# Optimizing a Trainium2 kernel written in Bass

```python
import jax, jax.numpy as jnp
from jax import lax
import numpy as np

D_MODEL = 1024
BATCH = 1
SEQ = 1024
DEPTH = 1

GRID_W = 64
CTX_LEN = 256
N_HEADS = 8
N_KV_HEADS = 2
HEAD_DIM = 64
WINDOW = 128
BLOCK = 128
ROPE_BASE = 10000.0
M_HEADS = 4
M_DIM = 128
CHUNK = 128
CONV_W = 3
ATT_WIDTH = N_HEADS * HEAD_DIM
KV_WIDTH = N_KV_HEADS * HEAD_DIM
M_WIDTH = M_HEADS * M_DIM
MIX_WIDTH = ATT_WIDTH + M_WIDTH
IN_SPLITS = (ATT_WIDTH, KV_WIDTH, KV_WIDTH, M_WIDTH, M_WIDTH, M_WIDTH, M_WIDTH, 4 * M_HEADS)
IN_COLS = sum(IN_SPLITS)
N_EXPERTS = 16
EXPERT_FF = 512
CAPACITY = 2
EPS = 1e-6
NEG = -1e30


f32 = jnp.float32

def rmsnorm(x, w):
    xf = x.astype(f32)
    y = xf * lax.rsqrt(jnp.mean(xf * xf, -1, keepdims=True) + EPS)
    return (y * w.astype(f32)).astype(x.dtype)

def modulate(h, shift, scale):
    return h * (1 + scale) + shift

def axial_rope_tables(n):
    rows = n // GRID_W
    row, col = jnp.meshgrid(jnp.arange(rows), jnp.arange(GRID_W), indexing='ij')
    n_freq = HEAD_DIM // 4
    freqs = ROPE_BASE ** (-jnp.arange(n_freq, dtype=f32) / n_freq)
    ang = jnp.concatenate([row.reshape(-1, 1).astype(f32) * freqs,
                           col.reshape(-1, 1).astype(f32) * freqs], -1)
    return jnp.cos(ang), jnp.sin(ang)

def apply_rope(x, cos, sin):
    shape = (1, cos.shape[0]) + (1,) * (x.ndim - 3) + (cos.shape[1],)
    cos = cos.reshape(shape)
    sin = sin.reshape(shape)
    x1, x2 = jnp.split(x.astype(f32), 2, -1)
    return jnp.concatenate([x1 * cos - x2 * sin, x2 * cos + x1 * sin], -1).astype(x.dtype)

def short_conv(u, w):
    n = u.shape[1]
    r = CONV_W // 2
    up = jnp.pad(u, ((0, 0), (r, r), (0, 0)))
    out = up[:, 0:n] * w[0]
    for j in range(1, CONV_W):
        out = out + up[:, j:j + n] * w[j]
    return out

def mixer_inputs(h, w_in, b_gates, conv_qk, q_norm_w, k_norm_w):
    B, N, _ = h.shape
    offs = np.cumsum(IN_SPLITS)[:-1].tolist()
    aq, ak, av, mq, mk, mv, mo, gates = jnp.split(h @ w_in, offs, -1)
    aq = rmsnorm(aq.reshape(B, N, N_KV_HEADS, N_HEADS // N_KV_HEADS, HEAD_DIM), q_norm_w)
    ak = rmsnorm(ak.reshape(B, N, N_KV_HEADS, HEAD_DIM), k_norm_w)
    av = av.reshape(B, N, N_KV_HEADS, HEAD_DIM)
    mqk = jax.nn.silu(short_conv(jnp.concatenate([mq, mk], -1), conv_qk))
    mq, mk = jnp.split(mqk, 2, -1)

    def heads(a):
        return a.reshape(B, N, M_HEADS, M_DIM).transpose(0, 2, 1, 3).astype(f32)

    g = (gates + b_gates).astype(f32).reshape(B, N, 4, M_HEADS).transpose(2, 0, 3, 1)
    li_f, f_f, li_b, f_b = g[0], g[1], g[2], g[3]
    return (aq, ak, av, heads(mq) * (M_DIM ** -0.5), heads(mk), heads(mv), mo,
            li_f, jax.nn.log_sigmoid(f_f), li_b, jax.nn.log_sigmoid(f_b))

def latent_attention(q, k, v, k_ctx, v_ctx, sink):
    B, N = q.shape[:2]
    L = k_ctx.shape[1]
    nb = N // BLOCK
    span = BLOCK + 2 * WINDOW
    pad = ((0, 0), (WINDOW, WINDOW), (0, 0), (0, 0))
    idx = jnp.arange(nb)[:, None] * BLOCK + jnp.arange(span)[None]
    k_blk = jnp.moveaxis(jnp.pad(k, pad)[:, idx], 1, 0)
    v_blk = jnp.moveaxis(jnp.pad(v, pad)[:, idx], 1, 0)
    q_blk = jnp.moveaxis(q.reshape((B, nb, BLOCK) + q.shape[2:]), 1, 0)
    scale = HEAD_DIM ** -0.5
    sink_f = sink.astype(f32)

    def one_block(args):
        qb, kb, vb, n = args
        qpos = n * BLOCK + jnp.arange(BLOCK)
        kpos = n * BLOCK - WINDOW + jnp.arange(span)
        ok = (kpos[None] >= 0) & (kpos[None] < N) & (jnp.abs(qpos[:, None] - kpos[None]) <= WINDOW)
        s_loc = jnp.einsum('bqkgd,bskd->bkgqs', qb, kb, preferred_element_type=f32) * scale
        s_loc = jnp.where(ok, s_loc, NEG)
        s_ctx = jnp.einsum('bqkgd,bckd->bkgqc', qb, k_ctx, preferred_element_type=f32) * scale
        s_sink = jnp.broadcast_to(sink_f[None, :, :, None, None], s_loc.shape[:-1] + (1,))
        p = jax.nn.softmax(jnp.concatenate([s_loc, s_ctx, s_sink], -1), -1)
        p_loc = p[..., :span].astype(vb.dtype)
        p_ctx = p[..., span:span + L].astype(vb.dtype)
        return (jnp.einsum('bkgqs,bskd->bqkgd', p_loc, vb)
                + jnp.einsum('bkgqc,bckd->bqkgd', p_ctx, v_ctx))

    o = lax.map(one_block, (q_blk, k_blk, v_blk, jnp.arange(nb)))
    return jnp.moveaxis(o, 0, 1).reshape(B, N, ATT_WIDTH)

def context_attention(q, k, v, sink):
    B, L = q.shape[:2]
    s = jnp.einsum('bqkgd,bckd->bkgqc', q, k, preferred_element_type=f32) * (HEAD_DIM ** -0.5)
    s_sink = jnp.broadcast_to(sink.astype(f32)[None, :, :, None, None], s.shape[:-1] + (1,))
    p = jax.nn.softmax(jnp.concatenate([s, s_sink], -1), -1)[..., :L].astype(v.dtype)
    return jnp.einsum('bkgqc,bckd->bqkgd', p, v).reshape(B, L, ATT_WIDTH)

def zero_state(batch):
    return (jnp.zeros((batch, M_HEADS, M_DIM, M_DIM), f32),
            jnp.zeros((batch, M_HEADS, M_DIM), f32),
            jnp.zeros((batch, M_HEADS), f32))

def mlstm_state_update(state, k, v, li, lf):
    C, n, m = state
    b = jnp.cumsum(lf, -1)
    b_last = b[..., -1]
    w = b_last[..., None] - b + li
    m_new = jnp.maximum(b_last + m, w.max(-1))
    a = jnp.exp(b_last + m - m_new)
    ws = jnp.exp(w - m_new[..., None])
    C_new = a[..., None, None] * C + jnp.einsum('bhs,bhsd,bhsv->bhdv', ws, k, v)
    n_new = a[..., None] * n + jnp.einsum('bhs,bhsd->bhd', ws, k)
    return (C_new, n_new, m_new)

def mlstm_chunk(state, xs):
    q, k, v, li, lf = xs
    C, n, m = state
    b = jnp.cumsum(lf, -1)
    within = jnp.tril(jnp.ones((CHUNK, CHUNK), bool))
    d = jnp.where(within, b[..., :, None] - b[..., None, :] + li[..., None, :], -jnp.inf)
    inter = b + m[..., None]
    m_t = jnp.maximum(inter, d.max(-1))
    wts = jnp.exp(d - m_t[..., None]) * jnp.einsum('bhtd,bhsd->bhts', q, k)
    decay = jnp.exp(inter - m_t)
    num = jnp.einsum('bhts,bhsv->bhtv', wts, v) + decay[..., None] * jnp.einsum('bhtd,bhdv->bhtv', q, C)
    den = wts.sum(-1) + decay * jnp.einsum('bhtd,bhd->bht', q, n)
    h = num / jnp.maximum(jnp.abs(den), jnp.exp(-m_t))[..., None]
    return mlstm_state_update(state, k, v, li, lf), h

def mlstm_scan(q, k, v, li, lf, state):
    B, H, N, _ = q.shape
    nc = N // CHUNK

    def chunks(a):
        return jnp.moveaxis(a.reshape((B, H, nc, CHUNK) + a.shape[3:]), 2, 0)

    state, h = lax.scan(mlstm_chunk, state, (chunks(q), chunks(k), chunks(v), chunks(li), chunks(lf)))
    return jnp.moveaxis(h, 0, 2).reshape(B, H, N, M_DIM), state

def flip(a):
    return jnp.flip(a, 2)

def bidir_mlstm(mq, mk, mv, li_f, lf_f, li_b, lf_b, st_f, st_b):
    h_f, end_f = mlstm_scan(mq, mk, mv, li_f, lf_f, st_f)
    h_b, end_b = mlstm_scan(flip(mq), flip(mk), flip(mv), flip(li_b), flip(lf_b), st_b)
    return h_f + flip(h_b), end_f, end_b

def mlstm_out(h_sum, mo, norm_w):
    B, H, N, _ = h_sum.shape
    h = jnp.moveaxis(h_sum, 1, 2)
    h = h * lax.rsqrt(jnp.mean(h * h, -1, keepdims=True) + EPS) * norm_w.astype(f32).reshape(M_HEADS, M_DIM)
    return (h.reshape(B, N, M_WIDTH) * jax.nn.sigmoid(mo.astype(f32))).astype(mo.dtype)

def expert_choice_ffn(h, w_router, w_gate, w_up, w_down):
    B, N, _ = h.shape
    cap = CAPACITY * N // N_EXPERTS
    aff = jax.nn.softmax((h @ w_router).astype(f32), -1)
    gate, idx = lax.top_k(jnp.swapaxes(aff, 1, 2), cap)
    bidx = jnp.arange(B)[:, None, None]
    xg = h[bidx, idx]
    g = jnp.einsum('becd,edf->becf', xg, w_gate)
    u = jnp.einsum('becd,edf->becf', xg, w_up)
    y = jnp.einsum('becf,efd->becd', jax.nn.silu(g) * u, w_down) * gate[..., None].astype(h.dtype)
    return jnp.zeros_like(h).at[bidx, idx].add(y)

def layer(x, ctx, mod_x, mod_c, norm1_w, norm2_w, w_in, b_gates, conv_qk, q_norm_w, k_norm_w,
          sink, mlstm_norm_w, w_out, w_router, w_gate, w_up, w_down, update_ctx):
    B = x.shape[0]
    sh1, sc1, g1, sh2, sc2, g2 = jnp.split(mod_x[:, None, :], 6, -1)
    csh1, csc1, cg1, csh2, csc2, cg2 = jnp.split(mod_c, 6, -1)
    sink_r = sink.reshape(N_KV_HEADS, N_HEADS // N_KV_HEADS)

    hx = modulate(rmsnorm(x, norm1_w), sh1, sc1)
    hc = modulate(rmsnorm(ctx, norm1_w), csh1, csc1)
    aq, ak, av, mq, mk, mv, mo, li_f, lf_f, li_b, lf_b = mixer_inputs(hx, w_in, b_gates, conv_qk, q_norm_w, k_norm_w)
    caq, cak, cav, cmq, cmk, cmv, cmo, cli_f, clf_f, cli_b, clf_b = mixer_inputs(hc, w_in, b_gates, conv_qk, q_norm_w, k_norm_w)

    cos, sin = axial_rope_tables(x.shape[1])
    att = latent_attention(apply_rope(aq, cos, sin), apply_rope(ak, cos, sin), av, cak, cav, sink_r)

    if update_ctx:
        hc_sum, st_f, st_b = bidir_mlstm(cmq, cmk, cmv, cli_f, clf_f, cli_b, clf_b, zero_state(B), zero_state(B))
        c_mix = jnp.concatenate([context_attention(caq, cak, cav, sink_r), mlstm_out(hc_sum, cmo, mlstm_norm_w)], -1)
        ctx_new = ctx + cg1 * (c_mix @ w_out)
        hc2 = modulate(rmsnorm(ctx_new, norm2_w), csh2, csc2)
        ctx_new = ctx_new + cg2 * expert_choice_ffn(hc2, w_router, w_gate, w_up, w_down)
    else:
        st_f = mlstm_state_update(zero_state(B), cmk, cmv, cli_f, clf_f)
        st_b = mlstm_state_update(zero_state(B), flip(cmk), flip(cmv), flip(cli_b), flip(clf_b))
        ctx_new = ctx

    h_sum, _, _ = bidir_mlstm(mq, mk, mv, li_f, lf_f, li_b, lf_b, st_f, st_b)
    mix = jnp.concatenate([att, mlstm_out(h_sum, mo, mlstm_norm_w)], -1)
    x = x + g1 * (mix @ w_out)

    hx2 = modulate(rmsnorm(x, norm2_w), sh2, sc2)
    x = x + g2 * expert_choice_ffn(hx2, w_router, w_gate, w_up, w_down)
    return x, ctx_new

def first_inputs(seed: int = 0) -> dict:
    key = jax.random.key(seed)
    ks = jax.random.split(key, 24)
    D = D_MODEL

    def nrm(k, shape, scale):
        return jax.random.normal(k, shape, f32) * scale

    f_bias = 3.0 + 0.5 * jax.random.normal(ks[20], (DEPTH, 2, M_HEADS), f32)
    i_bias = 0.1 * jax.random.normal(ks[21], (DEPTH, 2, M_HEADS), f32)
    b_gates = jnp.stack([i_bias[:, 0], f_bias[:, 0], i_bias[:, 1], f_bias[:, 1]], 1).reshape(DEPTH, 4 * M_HEADS)
    return {
        'x': nrm(ks[0], (BATCH, SEQ, D), 1.0),
        'c': nrm(ks[1], (BATCH, D), 1.0),
        'ctx': nrm(ks[2], (BATCH, CTX_LEN, D), 1.0),
        'c_ctx': nrm(ks[3], (D,), 1.0),
        'w_mod': nrm(ks[4], (DEPTH, D, 6 * D), 0.5 * D ** -0.5),
        'b_mod': nrm(ks[5], (DEPTH, 6 * D), 0.02),
        'norm1_w': 1.0 + nrm(ks[6], (DEPTH, D), 0.02),
        'norm2_w': 1.0 + nrm(ks[7], (DEPTH, D), 0.02),
        'w_in': nrm(ks[8], (DEPTH, D, IN_COLS), D ** -0.5),
        'b_gates': b_gates,
        'conv_qk': nrm(ks[9], (DEPTH, CONV_W, 2 * M_WIDTH), CONV_W ** -0.5),
        'q_norm_w': 1.0 + nrm(ks[10], (DEPTH, HEAD_DIM), 0.02),
        'k_norm_w': 1.0 + nrm(ks[11], (DEPTH, HEAD_DIM), 0.02),
        'sink': nrm(ks[12], (DEPTH, N_HEADS), 0.5),
        'mlstm_norm_w': 1.0 + nrm(ks[13], (DEPTH, M_WIDTH), 0.02),
        'w_out': nrm(ks[14], (DEPTH, MIX_WIDTH, D), MIX_WIDTH ** -0.5),
        'w_router': nrm(ks[15], (DEPTH, D, N_EXPERTS), D ** -0.5),
        'w_gate': nrm(ks[16], (DEPTH, N_EXPERTS, D, EXPERT_FF), D ** -0.5),
        'w_up': nrm(ks[17], (DEPTH, N_EXPERTS, D, EXPERT_FF), D ** -0.5),
        'w_down': nrm(ks[18], (DEPTH, N_EXPERTS, EXPERT_FF, D), EXPERT_FF ** -0.5),
    }

def first_block(x, c, ctx, c_ctx, w_mod, b_mod, norm1_w, norm2_w, w_in, b_gates, conv_qk, q_norm_w,
              k_norm_w, sink, mlstm_norm_w, w_out, w_router, w_gate, w_up, w_down):
    for l in range(DEPTH):
        mod_x = jax.nn.silu(c) @ w_mod[l] + b_mod[l]
        mod_c = jax.nn.silu(c_ctx) @ w_mod[l] + b_mod[l]
        x, ctx = layer(x, ctx, mod_x, mod_c, norm1_w[l], norm2_w[l], w_in[l], b_gates[l], conv_qk[l],
                       q_norm_w[l], k_norm_w[l], sink[l], mlstm_norm_w[l], w_out[l], w_router[l],
                       w_gate[l], w_up[l], w_down[l], l < DEPTH - 1)
    return x


DEPTH_2 = 2

EXPAND = 2
D_INNER = EXPAND * D_MODEL
NEG_2 = -1e30

A_WIDTH = D_INNER // 2
POOL_SIZES = (2, 4, 8, 16)
A_GROUPS = len(POOL_SIZES)
A_GROUP_DIM = A_WIDTH // A_GROUPS
B_WIDTH = D_INNER - A_WIDTH
B_GROUPS = 4
B_GROUP_DIM = B_WIDTH // B_GROUPS
EVEN_IN = 2 * A_WIDTH + 3 * B_WIDTH

DILATED = ((128, 1), (512, 4), (2048, 16))
N_DIL = len(DILATED)
HEAD_DIM_2 = 128
C_SLOTS = 8
C_HEADS = C_SLOTS * N_DIL
C_WIDTH = C_SLOTS * HEAD_DIM_2
D_WIDTH = D_INNER - C_WIDTH
ATTN_BLOCK = 128
QKV_WIDTH = 3 * C_HEADS * HEAD_DIM_2
ODD_IN = QKV_WIDTH + C_WIDTH + 4 * D_WIDTH

N_EVEN = (DEPTH_2 + 1) // 2
N_ODD = DEPTH_2 // 2


def rmsnorm_2(x, g):
    xf = x.astype(jnp.float32)
    y = xf * lax.rsqrt(jnp.mean(xf * xf, axis=-1, keepdims=True) + EPS)
    return (y * g.astype(jnp.float32)).astype(x.dtype)

def alibi_slopes(n):
    return jnp.asarray(2.0 ** (-8.0 * (np.arange(n) + 1) / n), dtype=jnp.float32)

def multiscale_pool(a, pool_w, pool_scale):
    Bn, S, _ = a.shape
    ag = a.reshape(Bn, S, A_GROUPS, A_GROUP_DIM).astype(jnp.float32)
    cs = jnp.pad(jnp.cumsum(ag, axis=1), ((0, 0), (1, 0), (0, 0), (0, 0)))
    t = jnp.arange(S)
    means = []
    for g, w in enumerate(POOL_SIZES):
        lo = jnp.maximum(t + 1 - w, 0)
        cnt = (t + 1 - lo).astype(jnp.float32)
        means.append((cs[:, 1:, g] - cs[:, lo, g]) / cnt[None, :, None])
    pooled = (jnp.stack(means, axis=2) - ag).astype(a.dtype)
    mixed = jnp.einsum('bsgc,gcd->bsgd', pooled, pool_w)
    return mixed.reshape(Bn, S, A_WIDTH) * pool_scale

def chunk_spatial_gate(u, v, ws, bs):
    Bn, S, _ = v.shape
    nc = S // CHUNK
    vg = v.reshape(Bn, nc, CHUNK, B_GROUPS, B_GROUP_DIM)
    causal = jnp.tril(jnp.ones((CHUNK, CHUNK), dtype=bool))
    w = jnp.where(causal[None], ws, jnp.zeros_like(ws))
    mixed = jnp.einsum('gts,bnsgc->bntgc', w, vg) + bs.T[None, None, :, :, None]
    return u * mixed.reshape(Bn, S, B_WIDTH)

def dilated_group_attention(q, k, v, window, dilation, slopes):
    Bn, S, H, Dh = q.shape
    unit = dilation * ATTN_BLOCK
    Sp = -(-S // unit) * unit
    pad = Sp - S
    L = Sp // dilation
    nb = L // ATTN_BLOCK
    span = window // dilation

    def to_sub(x):
        x = jnp.pad(x, ((0, 0), (0, pad), (0, 0), (0, 0)))
        return x.reshape(Bn, L, dilation, H, Dh).transpose(0, 2, 1, 3, 4)

    def band(x):
        x = jnp.pad(x, ((0, 0), (0, 0), (ATTN_BLOCK, 0), (0, 0), (0, 0)))
        x = x.reshape(Bn, dilation, nb + 1, ATTN_BLOCK, H, Dh)
        return jnp.concatenate([x[:, :, :-1], x[:, :, 1:]], axis=3)

    qb = to_sub(q).reshape(Bn, dilation, nb, ATTN_BLOCK, H, Dh)
    kb = band(to_sub(k))
    vb = band(to_sub(v))
    s = jnp.einsum('bdnqhe,bdnkhe->bdnhqk', qb, kb,
                   preferred_element_type=jnp.float32) * (Dh ** -0.5)
    qi = jnp.arange(ATTN_BLOCK)[:, None] + ATTN_BLOCK
    ki = jnp.arange(2 * ATTN_BLOCK)[None, :]
    steps = qi - ki
    band_ok = (steps >= 0) & (steps <= span)
    blk = jnp.arange(nb)[:, None, None]
    valid = band_ok[None] & ((blk > 0) | (ki >= ATTN_BLOCK)[None])
    dist = (steps * dilation).astype(jnp.float32)
    s = s - slopes[:, None, None] * dist
    s = jnp.where(valid[:, None], s, NEG_2)
    lse = jax.nn.logsumexp(s, axis=-1)
    p = jnp.exp(s - lse[..., None])
    o = jnp.einsum('bdnhqk,bdnkhe->bdnqhe', p.astype(v.dtype), vb)
    o = o.reshape(Bn, dilation, L, H, Dh).transpose(0, 2, 1, 3, 4).reshape(Bn, Sp, H, Dh)[:, :S]
    lse = lse.transpose(0, 1, 2, 4, 3).reshape(Bn, dilation, L, H)
    lse = lse.transpose(0, 2, 1, 3).reshape(Bn, Sp, H)[:, :S]
    return o, lse

def short_gated_conv(gb, gc, xt, conv_w):
    S = xt.shape[1]
    z = jnp.pad(gc * xt, ((0, 0), (CONV_W - 1, 0), (0, 0)))
    conv = conv_w[0] * z[:, 0:S]
    for j in range(1, CONV_W):
        conv = conv + conv_w[j] * z[:, j:j + S]
    return gb * conv

def even_layer(x, norm_g, w_in, pool_w, pool_scale, ws, bs, w_out):
    h = rmsnorm_2(x, norm_g)
    z = h @ w_in
    a, g_a, u, v, g_b = jnp.split(
        z, [A_WIDTH, 2 * A_WIDTH, 2 * A_WIDTH + B_WIDTH, 2 * A_WIDTH + 2 * B_WIDTH], axis=-1)
    y_a = multiscale_pool(a, pool_w, pool_scale) * jax.nn.silu(g_a)
    y_b = chunk_spatial_gate(u, v, ws, bs) * jax.nn.silu(g_b)
    return x + jnp.concatenate([y_a, y_b], axis=-1) @ w_out

def odd_layer(x, norm_g, w_in, conv_w, w_out):
    Bn, S, _ = x.shape
    h = rmsnorm_2(x, norm_g)
    z = h @ w_in
    o1 = QKV_WIDTH
    o2 = o1 + C_WIDTH
    qkv, g_c, d_b, d_c, d_x, g_d = jnp.split(
        z, [o1, o2, o2 + D_WIDTH, o2 + 2 * D_WIDTH, o2 + 3 * D_WIDTH], axis=-1)
    qkv = qkv.reshape(Bn, S, 3, N_DIL, C_SLOTS, HEAD_DIM_2)
    slopes = alibi_slopes(C_HEADS).reshape(N_DIL, C_SLOTS)
    outs, lses = [], []
    for gi, (window, dil) in enumerate(DILATED):
        o, l = dilated_group_attention(qkv[:, :, 0, gi], qkv[:, :, 1, gi], qkv[:, :, 2, gi],
                                       window, dil, slopes[gi])
        outs.append(o)
        lses.append(l)
    alpha = jax.nn.softmax(jnp.stack(lses, axis=0), axis=0)
    y_c = jnp.einsum('gbsh,gbshe->bshe', alpha.astype(x.dtype), jnp.stack(outs, axis=0))
    y_c = y_c.reshape(Bn, S, C_WIDTH) * jax.nn.silu(g_c)
    y_d = short_gated_conv(d_b, d_c, d_x, conv_w) * jax.nn.silu(g_d)
    return x + jnp.concatenate([y_c, y_d], axis=-1) @ w_out

def second_inputs(seed: int = 0) -> dict:
    key = jax.random.key(seed)
    ks = jax.random.split(key, 16)
    nrm = jax.random.normal
    f32 = jnp.float32
    return {
        "x": nrm(ks[0], (BATCH, SEQ, D_MODEL), f32),
        "even_norm": 1.0 + 0.05 * nrm(ks[1], (N_EVEN, D_MODEL), f32),
        "even_w_in": nrm(ks[2], (N_EVEN, D_MODEL, EVEN_IN), f32) * D_MODEL ** -0.5,
        "even_pool_w": nrm(ks[3], (N_EVEN, A_GROUPS, A_GROUP_DIM, A_GROUP_DIM), f32) * A_GROUP_DIM ** -0.5,
        "even_pool_scale": 1.0 + 0.1 * nrm(ks[4], (N_EVEN, A_WIDTH), f32),
        "even_ws": nrm(ks[5], (N_EVEN, B_GROUPS, CHUNK, CHUNK), f32) * CHUNK ** -0.5,
        "even_bs": 1.0 + 0.1 * nrm(ks[6], (N_EVEN, B_GROUPS, CHUNK), f32),
        "even_w_out": nrm(ks[7], (N_EVEN, D_INNER, D_MODEL), f32) * D_INNER ** -0.5,
        "odd_norm": 1.0 + 0.05 * nrm(ks[8], (N_ODD, D_MODEL), f32),
        "odd_w_in": nrm(ks[9], (N_ODD, D_MODEL, ODD_IN), f32) * D_MODEL ** -0.5,
        "odd_conv_w": nrm(ks[10], (N_ODD, CONV_W, D_WIDTH), f32) * CONV_W ** -0.5,
        "odd_w_out": nrm(ks[11], (N_ODD, D_INNER, D_MODEL), f32) * D_INNER ** -0.5,
        "final_norm": 1.0 + 0.05 * nrm(ks[12], (D_MODEL,), f32),
    }

def second_block(x, even_norm, even_w_in, even_pool_w, even_pool_scale, even_ws, even_bs,
              even_w_out, odd_norm, odd_w_in, odd_conv_w, odd_w_out, final_norm):
    h = x
    for layer in range(DEPTH_2):
        i = layer // 2
        if layer % 2 == 0:
            h = even_layer(h, even_norm[i], even_w_in[i], even_pool_w[i], even_pool_scale[i],
                           even_ws[i], even_bs[i], even_w_out[i])
        else:
            h = odd_layer(h, odd_norm[i], odd_w_in[i], odd_conv_w[i], odd_w_out[i])
    return rmsnorm_2(h, final_norm)


def setup_inputs(seed=0):
    out = dict(first_inputs(seed))
    for name, value in second_inputs(seed + 1).items():
        if name != "x":
            out[name + "_2"] = value
    return out


def reference(
    x, c, ctx, c_ctx, w_mod, b_mod, norm1_w, norm2_w, w_in, b_gates, conv_qk, q_norm_w,
    k_norm_w, sink, mlstm_norm_w, w_out, w_router, w_gate, w_up, w_down, even_norm_2,
    even_w_in_2, even_pool_w_2, even_pool_scale_2, even_ws_2, even_bs_2, even_w_out_2,
    odd_norm_2, odd_w_in_2, odd_conv_w_2, odd_w_out_2, final_norm_2,
):
    x = first_block(
        x, c, ctx, c_ctx, w_mod, b_mod, norm1_w, norm2_w, w_in, b_gates, conv_qk, q_norm_w,
        k_norm_w, sink, mlstm_norm_w, w_out, w_router, w_gate, w_up, w_down,
    )
    return second_block(
        x, even_norm_2, even_w_in_2, even_pool_w_2, even_pool_scale_2, even_ws_2, even_bs_2,
        even_w_out_2, odd_norm_2, odd_w_in_2, odd_conv_w_2, odd_w_out_2, final_norm_2,
    )


_drawn_inputs = setup_inputs


def setup_inputs(seed=0):
    import zlib

    import numpy as np

    out = dict(_drawn_inputs(seed))
    spreads = {}
    factors = {'ctx': 2.717,
     'b_mod': 2.789,
     'norm1_w': 8.0,
     'norm2_w': 6.298,
     'q_norm_w': 8.0,
     'k_norm_w': 8.0,
     'sink': 8.0,
     'mlstm_norm_w': 8.0,
     'even_norm_2': 8.0,
     'even_pool_scale_2': 8.0,
     'even_bs_2': 8.0,
     'odd_norm_2': 8.0}
    for name, (base, spread) in spreads.items():
        noise = np.random.default_rng([zlib.crc32(name.encode()), seed]).standard_normal(out[name].shape)
        drawn = base * np.exp(spread * noise) if base else spread * noise
        out[name] = __import__('jax').numpy.asarray(drawn.astype(out[name].dtype))
    for name, factor in factors.items():
        out[name] = (out[name] * factor).astype(out[name].dtype)
    return out
```

```python
from contextlib import ExitStack

import numpy as np

import concourse.bass as bass
from concourse import mybir

F32 = mybir.dt.float32
F32R = mybir.dt.float32r
U32 = mybir.dt.uint32
ALU = mybir.AluOpType
ACT = mybir.ActivationFunctionType
AX_X = mybir.AxisListType.X

P = 128
D = 1024
KT = D // P
SEQ = 1024
CTX = 256
TOK = CTX + SEQ
HALF = 512
EPS = 1e-6
NEG = -1e30
GRID_W = 64
N_HEADS, HEAD_DIM = 8, 64
M_HEADS, M_DIM = 4, 128
CHUNK = 128
XCH = SEQ // CHUNK
ALLCH = TOK // CHUNK
CCH = CTX // CHUNK
N_EXPERTS, EXPERT_FF = 16, 512
SLOTS = 2 * SEQ // N_EXPERTS
POOL_SIZES = (2, 4, 8, 16)
C_SLOTS, N_DIL = 8, 3
DILATION = (1, 4, 16)
BLOCKS = SEQ // P
Q_COL, K_COL, V_COL, MQ_COL, MK_COL, MV_COL, MO_COL, G_COL = 0, 512, 640, 768, 1280, 1792, 2304, 2816
GATE_ROWS = 36

CONST_PARTS = (("ident", P), ("ones", P), ("head_ones", P), ("rotate", P), ("near_mask", 3 * P), ("chunk_mask", 2 * P),
               ("dist", 2 * P), ("dist16", P), ("slopes", N_DIL * C_SLOTS), ("pool_inv", len(POOL_SIZES) * 16))
CONST_AT, _n = {}, 0
for _name, _w in CONST_PARTS:
    CONST_AT[_name] = (_n, _w)
    _n += _w
CONST_W = _n
ROWS_A = (("b_mod", 48), ("norm1_w", 8), ("norm2_w", 8), ("even_norm_2", 8), ("odd_norm_2", 8), ("final_norm_2", 8),
          ("even_pool_scale_2", 8))
ROWS_B = (("conv_qk", 24), ("odd_conv_w_2", 24), ("mlstm_norm_w", 4), ("c", 8), ("c_ctx", 8))
SH1, SC1, G1, SH2, SC2, G2 = range(0, 48, 8)


def columns_of(parts):
    at, n = {}, 0
    for name, rows in parts:
        at[name] = (n, rows)
        n += rows
    return at, n


AT_A, N_A = columns_of(ROWS_A)
AT_B, N_B = columns_of(ROWS_B)


def constant_tables():
    i = np.arange(P)
    table = np.zeros((P, CONST_W), np.float32)

    def put(name, value):
        at, width = CONST_AT[name]
        table[:, at:at + width] = value

    put("ident", np.eye(P))
    put("ones", 1.0)
    put("head_ones", (i[:, None] // HEAD_DIM == i[None] // HEAD_DIM))
    rotate = np.zeros((P, P))
    for m in range(P):
        if m % HEAD_DIM < HEAD_DIM // 2:
            rotate[m + HEAD_DIM // 2, m] = -1.0
        else:
            rotate[m - HEAD_DIM // 2, m] = 1.0
    put("rotate", rotate)
    q, k = i[:, None], np.arange(3 * P)[None]
    put("near_mask", np.where(np.abs(q + P - k) <= P, 0.0, NEG))
    put("chunk_mask", np.concatenate([np.where(q <= i[None], 0.0, NEG), np.where(q >= i[None], 0.0, NEG)], 1))
    steps = q + P - np.arange(2 * P)[None]
    put("dist", np.where((steps >= 0) & (steps <= P), -steps, NEG))
    half = P // 2
    same = (q // half == i[None] // half) & (i[None] % half <= q % half)
    put("dist16", np.where(same, -(q % half - i[None] % half), NEG))
    n = N_DIL * C_SLOTS
    slopes = 2.0 ** (-8.0 * (np.arange(n) + 1) / n)
    put("slopes", np.repeat(slopes[None] * np.repeat(DILATION, C_SLOTS)[None], P, 0))
    t = np.arange(16)
    put("pool_inv", np.repeat(np.concatenate([1.0 / np.minimum(t + 1, w) for w in POOL_SIZES])[None], P, 0))

    pos = np.arange(SEQ)
    n_freq = HEAD_DIM // 4
    freqs = (np.float32(10000.0) ** (-np.arange(n_freq, dtype=np.float32) / np.float32(n_freq))).astype(np.float32)
    ang = np.concatenate([(pos // GRID_W)[:, None].astype(np.float32) * freqs,
                          (pos % GRID_W)[:, None].astype(np.float32) * freqs], 1)
    ang = np.concatenate([ang, ang, ang, ang], 1).T
    rope = np.stack([np.cos(ang), np.sin(ang)], 1).astype(np.float32)

    pick = np.zeros((GATE_ROWS, 8, P), np.float32)
    for r in range(8):
        pick[32 * (r // M_HEADS) + r % M_HEADS, r] = 1.0
    keep = np.ones((GATE_ROWS, TOK), np.float32)
    keep[:, ::CHUNK] = 0.0
    return {"const_table": table, "rope_table": rope, "pick_table": pick.reshape(GATE_ROWS, 8 * P), "keep_table": keep}


class Steps:

    def __init__(self, eng, sem, base=0):
        self.eng, self.sem, self.base, self.done = eng, sem, base, 0

    def __call__(self, ins):
        ins.then_inc(self.sem, 1)
        self.done += 1
        return ins

    def wait(self):
        self.eng.wait_ge(self.sem, self.base + self.done)


class Arena:

    def __init__(self, nc, at):
        self.nc, self.at = nc, at

    def __call__(self, name, shape, dtype=F32):
        words = 1
        for s in shape[1:]:
            words *= s
        t = self.nc.alloc_sbuf_tensor_at(name, list(shape), dtype, offset=self.at)
        self.at += (words * 4 + 31) // 32 * 32
        assert self.at <= self.nc.sbuf_usable_end, (name, self.at)
        return t


class PhaseSemaphores:

    def __init__(self, nc):
        self.nc = nc
        free = sorted(nc.free_semaphores)
        self.kept, free = free[:8], free[8:]
        self.sets = [free[:len(free) // 2], free[len(free) // 2:]]
        self.used = []

    def start(self):
        if self.used:
            self.nc.gpsimd.sem_clear(range(self.used[0].num, self.used[-1].num + 1))
            for s in self.used:
                self.nc.release_semaphore(s)
        self.used = []
        self.sets.reverse()

    def keep(self, name):
        return self.nc.alloc_semaphore(name, num=self.kept.pop())

    def sem(self, name):
        self.used.append(self.nc.alloc_semaphore(name, num=self.sets[0][len(self.used)]))
        return self.used[-1]


def build_program(nc, A, out):
    with ExitStack() as ctx:
        phases = PhaseSemaphores(nc)
        sem = phases.sem

        def dram(name, shape):
            return nc.dram_tensor(name, shape, F32, kind="Internal").ap()

        x_cm = dram("x_cm", (D, SEQ))
        att_cm = dram("att_cm", (N_HEADS * HEAD_DIM, SEQ))
        h2_rows = dram("h2_rows", (SEQ, D))
        ffn_rows = dram("ffn_rows", (SEQ, D))
        stat_dram = dram("stat_dram", (2, N_DIL, SEQ))
        factor_dram = dram("factor_dram", (N_DIL, SEQ))
        x_cm_k = x_cm.rearrange("(k p) t -> p k t", p=P)

        start = (nc.sbuf_base + 63) // 32 * 32
        fixed = Arena(nc, start)
        const = fixed("const", [P, CONST_W])
        par_a = fixed("par_a", [P, N_A])
        par_b = fixed("par_b", [P, N_B])
        mod = fixed("mod", [P, 48, 2])
        gain1 = fixed("gain1", [P, KT, 2])
        gain2 = fixed("gain2", [P, KT])
        sinks = fixed("sinks", [P, N_HEADS])
        qk_gain = fixed("qk_gain", [P, 2])
        gate_bias = fixed("gate_bias", [P, 1])
        ring_at = fixed.at
        w_raw = fixed("w_raw", [P, 2, KT, P])
        w_hi = fixed("w_hi", [P, 2, KT, P], F32R)
        w_lo = fixed("w_lo", [P, 2, KT, P], F32R)
        zero_col = fixed("zero_col", [P, 1])
        free_at = fixed.at

        def cst(name):
            at, width = CONST_AT[name]
            return const[:, at:at + width]

        def pa(name):
            at, width = AT_A[name]
            return par_a[:, at:at + width]

        def pb(name):
            at, width = AT_B[name]
            return par_b[:, at:at + width]

        ident, ones = cst("ident"), cst("ones")
        passed = phases.keep("passed")

        def pass_waits(eng):
            eng.sem_inc(passed, 1)

        class Ring:

            def __init__(self, tag, pieces=1):
                self.pieces = pieces
                self.loaded = [sem(f"{tag}_w_loaded{u}") for u in range(2)]
                self.hi_done = sem(f"{tag}_w_hi_done")
                self.split = sem(f"{tag}_w_split")
                self.projected = sem(f"{tag}_projected")

            def load(self, sp, n, u, parts):
                sp.wait_ge(self.split, n + 1)
                if not isinstance(n, int):
                    pass_waits(sp)
                assert len(parts) == self.pieces
                for dst, src in parts:
                    sp.dma_start(dst, src).then_inc(self.loaded[u], 16)

            def credits(self, pool, pe):
                if pool is not None:
                    pool.sem_inc(self.split, 2)
                if pe is not None:
                    pe.sem_inc(self.projected, 2)

            def do_split(self, pool, n, u, round_):
                pool.wait_ge(self.loaded[u], 16 * self.pieces * (round_ + 1))
                pool.wait_ge(self.projected, n + 1)
                pool.tensor_tensor(w_hi[:, u], w_raw[:, u], zero_col[:, 0:1].to_broadcast([P, KT * P]).rearrange("p (k n) -> p k n", k=KT),
                                   ALU.add).then_inc(self.hi_done, 1)
                pool.wait_ge(self.hi_done, n + 1)
                pool.tensor_tensor(w_lo[:, u], w_raw[:, u], w_hi[:, u].bitcast(F32), ALU.subtract).then_inc(self.split, 1)

            def project(self, pe, n, u, z_free, targets, rhs_hi, rhs_lo, between=None):
                pe.wait_ge(self.split, n + 3)
                pe.wait_ge(z_free, n + 1)
                for kt in range(KT):
                    for w, rhs, first, last in ((w_hi, rhs_hi, kt == 0, False), (w_hi, rhs_lo, False, False),
                                                (w_lo, rhs_hi, False, kt == KT - 1)):
                        for z, c0, width in targets:
                            ins = pe.matmul(z, w[:, u, kt], rhs[:, kt, c0:c0 + width], start=first, stop=last)
                    if between and kt in between:
                        between[kt]()
                ins.then_inc(self.projected, 1)

        def phase_modulation():
            phases.start()
            mem = Arena(nc, free_at)
            rows_a = mem("rows_a", [N_A, P])
            rows_b = mem("rows_b", [N_B, P])
            sink_row = mem("sink_row", [1, N_HEADS])
            silu_c = mem("silu_c", [P, KT, 2])
            zeros = mem("zeros", [P, D])
            w_mod = [mem(f"w_mod{u}", [P, KT, HALF]) for u in range(3)]
            rows_sb = mem("mod_rows_sb", [2, 6 * D])
            rows_out = sem("mod_rows_out")
            columns_done = sem("mod_columns_done")
            small = sem("mod_small_loaded")
            w_loaded = [sem(f"mod_w_loaded{u}") for u in range(3)]
            w_used = sem("mod_w_used")
            zeroed = sem("mod_zeroed")
            bias_zeroed = sem("mod_bias_zeroed")
            cleared = sem("mod_ffn_cleared")
            turned = sem("mod_params_turned")
            params_ready = sem("mod_params_ready")
            silu_done = sem("mod_silu_done")
            done = sem("mod_done")
            dve_step = sem("mod_dve_step")
            n_small = 0
            with nc.psum_tensor("mod_turn", [P, 4, HALF], F32) as turn, nc.psum_tensor("mod_acc", [P, HALF], F32) as acc, \
                    nc.psum_tensor("mod_row_acc", [2, 2, HALF], F32) as row_acc, nc.Block() as block:
                @block.sync
                def _(sp):
                    nonlocal n_small
                    parts = [(const[:], A["const_table"])]
                    for rows, names, at in ((rows_a, ROWS_A, AT_A), (rows_b, ROWS_B, AT_B)):
                        for name, count in names:
                            src = A[name]
                            letters = "abcd"[:len(src.shape)]
                            flat = src.rearrange(f"{' '.join(letters)} -> ({' '.join(letters)})") if len(src.shape) > 1 else src
                            parts.append((rows[at[name][0]:at[name][0] + count, :], flat.rearrange("(r q) -> r q", q=P)))
                    parts.append((sink_row[:], A["sink"]))
                    for col, name in ((0, "q_norm_w"), (1, "k_norm_w")):
                        for half in range(2):
                            parts.append((qk_gain[half * HEAD_DIM:(half + 1) * HEAD_DIM, col:col + 1], A[name].rearrange("o p -> p o")))
                    for dst, src in parts:
                        sp.dma_start(dst, src).then_inc(small, 16)
                    n_small = len(parts)
                    sp.wait_ge(bias_zeroed, 1)
                    for row, at in ((0, 0), (64, 4), (32, 8), (96, 12)):
                        sp.dma_start(gate_bias[row:row + M_HEADS, :], A["b_gates"][0:1, at:at + M_HEADS].rearrange("o p -> p o")).then_inc(small, 16)
                    n_small += 4
                    w_src = A["w_mod"].rearrange("o (k p) n -> p (o k) n", p=P)
                    for j in range(12):
                        if j >= 3:
                            sp.wait_ge(w_used, j - 2)
                        sp.dma_start(w_mod[j % 3][:], w_src[:, :, j * HALF:(j + 1) * HALF]).then_inc(w_loaded[j % 3], 16)
                    sp.wait_ge(small, 16 * n_small)

                @block.gpsimd
                def _(pool):
                    pool.memset(gate_bias[:], 0.0).then_inc(bias_zeroed, 1)
                    pool.memset(zero_col[:], 0.0)
                    pool.memset(zeros[:], 0.0).then_inc(zeroed, 1)

                @block.tensor
                def _(pe):
                    pe.wait_ge(small, 16 * n_small)
                    pe.transpose(turn[:, 0, 0:N_A], rows_a[:], ident[0:N_A, 0:N_A]).then_inc(turned, 1)
                    pe.transpose(turn[:, 1, 0:N_B], rows_b[:], ident[0:N_B, 0:N_B]).then_inc(turned, 1)
                    pe.matmul(turn[:, 2, 0:N_HEADS], ones[0:1, :], sink_row[:], start=True, stop=True).then_inc(turned, 1)
                    pe.wait_ge(silu_done, 2)

                    def columns(j):
                        pe.wait_ge(rows_out, j + 1)
                        for q in range(4):
                            at = 4 * j + q
                            ins = pe.transpose(acc[:, 2 * at:2 * at + 2], rows_sb[:, at * P:(at + 1) * P], ident[0:2, 0:2])
                        ins.then_inc(columns_done, 1)

                    for j in range(12):
                        pe.wait_ge(w_loaded[j % 3], 16 * (j // 3 + 1))
                        if j >= 2:
                            pe.wait_ge(rows_out, j - 1)
                        for kt in range(KT):
                            ins = pe.matmul(row_acc[:, j % 2, :], silu_c[:, kt, :], w_mod[j % 3][:, kt, :], start=(kt == 0), stop=(kt == KT - 1))
                        ins.then_inc(w_used, 1)
                        if j >= 1:
                            columns(j - 1)
                    columns(11)

                @block.scalar
                def _(act):
                    act.wait_ge(zeroed, 1)
                    for j in range(BLOCKS):
                        act.dma_start(ffn_rows[j * P:(j + 1) * P, :], zeros[:]).then_inc(cleared, 16)
                    act.wait_ge(turned, 2)
                    act.copy(par_b[:], turn[:, 1, 0:N_B]).then_inc(params_ready, 1)
                    act.wait_ge(params_ready, 1)
                    act.activation(silu_c[:, :, 0], pb("c"), ACT.Silu).then_inc(silu_done, 1)
                    act.activation(silu_c[:, :, 1], pb("c_ctx"), ACT.Silu).then_inc(silu_done, 1)
                    for j in range(12):
                        act.wait_ge(w_used, j + 1)
                        act.copy(rows_sb[:, j * HALF:(j + 1) * HALF], row_acc[:, j % 2, :]).then_inc(rows_out, 1)
                    act.wait_ge(cleared, 16 * BLOCKS)

                @block.vector
                def _(dve):
                    step = Steps(dve, dve_step)
                    dve.wait_ge(turned, 3)
                    step(dve.tensor_copy(par_a[:], turn[:, 0, 0:N_A]))
                    step(dve.tensor_copy(sinks[:], turn[:, 2, 0:N_HEADS]))
                    step.wait()
                    dve.wait_ge(columns_done, 12)
                    step(dve.tensor_tensor(mod[:], acc[:, 0:96].rearrange("p (j s) -> p j s", s=2),
                                           pa("b_mod").unsqueeze(2).to_broadcast([P, 48, 2]), ALU.add))
                    step.wait()
                    for s in range(2):
                        dve.scalar_tensor_tensor(out=gain1[:, :, s], in0=mod[:, SC1:SC1 + KT, s], scalar=1.0, in1=pa("norm1_w"),
                                                 op0=ALU.add, op1=ALU.mult).then_inc(done, 1)
                    dve.scalar_tensor_tensor(out=gain2[:], in0=mod[:, SC2:SC2 + KT, 0], scalar=1.0, in1=pa("norm2_w"),
                                             op0=ALU.add, op1=ALU.mult).then_inc(done, 1)

        def phase_norm(tag, mem, source, affines, n_tok, h_hi=None, h_lo=None, h_plain=None, finish=None):
            phases.start()
            groups = [(0, CTX), (CTX, HALF), (CTX + HALF, HALF)] if n_tok == TOK else [(0, HALF), (HALF, HALF)]
            ng = len(groups)
            pieces = KT * ng
            xt = mem(f"{tag}_xt", [P, KT, n_tok])
            sq = mem(f"{tag}_sq", [P, 2, HALF])
            rstd = mem(f"{tag}_rstd", [P, n_tok])
            scaled = mem(f"{tag}_scaled", [P, 2, n_tok])
            shifted = mem(f"{tag}_shifted", [P, 2, n_tok]) if h_plain is None else None
            rows = None
            if source == "rows":
                rows = mem(f"{tag}_rows", [P, n_tok // P, D])
            elif source == "stream+ffn":
                rows = mem(f"{tag}_rows", [P, BLOCKS, D])
            in_loaded = sem(f"{tag}_in_loaded")
            rows_turned = sem(f"{tag}_rows_turned")
            x_done = sem(f"{tag}_x_done")
            sq_done = sem(f"{tag}_sq_done")
            sq_used = sem(f"{tag}_sq_used")
            mean_done = sem(f"{tag}_mean_done")
            root_done = sem(f"{tag}_root_done")
            scaled_done = sem(f"{tag}_scaled_done")
            shifted_done = sem(f"{tag}_shifted_done")
            hi_done = sem(f"{tag}_hi_done")
            lo_done = sem(f"{tag}_lo_done")
            stored = sem(f"{tag}_stored")
            dve_step = sem(f"{tag}_dve_step")
            n_in = {"rows": 2, "stream": 1, "stream+ffn": 2}[source]
            x_at = n_tok - SEQ
            turning = source != "stream"
            with nc.psum_tensor(f"{tag}_turn", [P, 2, HALF], F32) as turn, nc.psum_tensor(f"{tag}_ssq", [P, 3, HALF], F32) as ssq, \
                    nc.Block() as block:
                @block.sync
                def _(sp):
                    if source == "rows":
                        sp.dma_start(rows[:, 0:CCH, :], A["ctx"].rearrange("o (j p) d -> p (o j) d", p=P)).then_inc(in_loaded, 16)
                        sp.dma_start(rows[:, CCH:, :], A["x"].rearrange("o (j p) d -> p (o j) d", p=P)).then_inc(in_loaded, 16)
                    else:
                        sp.dma_start(xt[:], x_cm_k).then_inc(in_loaded, 16)
                        if source == "stream+ffn":
                            sp.dma_start(rows[:], ffn_rows.rearrange("(j p) d -> p j d", p=P)).then_inc(in_loaded, 16)
                    if turning:
                        for kt in range(KT):
                            sp.wait_ge(x_done, ng * (kt + 1) + 2)
                            sp.dma_start(x_cm_k[:, kt, :], xt[:, kt, x_at:]).then_inc(stored, 16)
                        sp.wait_ge(stored, 16 * KT)

                @block.tensor
                def _(pe):
                    pe.wait_ge(in_loaded, 16 * n_in)

                    def turn_piece(p):
                        kt, (c0, width) = p // ng, groups[p % ng]
                        pe.wait_ge(x_done, p + 1)
                        for j in range(width // P):
                            ins = pe.transpose(turn[:, p % 2, j * P:(j + 1) * P], rows[:, c0 // P + j, kt * P:(kt + 1) * P], ident)
                        ins.then_inc(rows_turned, 1)

                    if turning:
                        turn_piece(0)
                    for p in range(pieces):
                        if turning and p + 1 < pieces:
                            turn_piece(p + 1)
                        kt, (c0, width) = p // ng, groups[p % ng]
                        pe.wait_ge(sq_done, p + 1)
                        pe.matmul(ssq[:, p % ng, 0:width], ones, sq[:, p % 2, 0:width], start=(kt == 0), stop=(kt == KT - 1)).then_inc(sq_used, 1)

                @block.scalar
                def _(act):
                    if source == "rows":
                        act.sem_inc(x_done, 2)
                        for p in range(pieces):
                            kt, (c0, width) = p // ng, groups[p % ng]
                            act.wait_ge(rows_turned, p + 1)
                            act.copy(xt[:, kt, c0:c0 + width], turn[:, p % 2, 0:width]).then_inc(x_done, 1)
                    act.wait_ge(mean_done, ng)
                    act.activation(rstd[:], rstd[:], ACT.Sqrt).then_inc(root_done, 1)
                    for kt in range(KT):
                        act.wait_ge(scaled_done, kt + 1)
                        if h_plain is None and kt >= 2:
                            act.wait_ge(lo_done, kt - 1)
                        to = h_plain[:, kt] if h_plain is not None else shifted[:, kt % 2]
                        for c0, width, gain, shift in affines:
                            ins = act.activation(to[:, c0:c0 + width], scaled[:, kt % 2, c0:c0 + width], ACT.Identity,
                                                 scale=gain(kt), bias=0.0 if shift is None else shift(kt))
                            ins.then_inc(shifted_done, 1)
                        if h_plain is None:
                            act.wait_ge(shifted_done, len(affines) * (kt + 1))
                            act.copy(h_hi[:, kt, :], shifted[:, kt % 2]).then_inc(hi_done, 1)

                @block.vector
                def _(dve):
                    step = Steps(dve, dve_step)
                    dve.sem_inc(sq_used, 2)
                    if source == "stream+ffn":
                        dve.sem_inc(x_done, 2)
                    dve.wait_ge(in_loaded, 16 * n_in)
                    for p in range(pieces):
                        kt, (c0, width) = p // ng, groups[p % ng]
                        piece = xt[:, kt, c0:c0 + width]
                        if source == "stream+ffn":
                            dve.wait_ge(rows_turned, p + 1)
                            dve.scalar_tensor_tensor(out=piece, in0=turn[:, p % 2, 0:width], scalar=mod[:, G2 + kt, 0:1], in1=piece,
                                                     op0=ALU.mult, op1=ALU.add).then_inc(x_done, 1)
                        if turning:
                            dve.wait_ge(x_done, p + 3)
                        dve.wait_ge(sq_used, p + 1)
                        dve.tensor_tensor(sq[:, p % 2, 0:width], piece, piece, ALU.mult).then_inc(sq_done, 1)
                    dve.wait_ge(sq_used, pieces + 2)
                    for g, (c0, width) in enumerate(groups):
                        dve.tensor_scalar(rstd[:, c0:c0 + width], ssq[:, g, 0:width], 1.0 / D, EPS, ALU.mult, ALU.add).then_inc(mean_done, 1)
                    dve.wait_ge(root_done, 1)
                    step(dve.reciprocal(rstd[:], rstd[:]))
                    step.wait()
                    for kt in range(KT):
                        if kt >= 2:
                            dve.wait_ge(shifted_done, len(affines) * (kt - 1))
                        dve.tensor_tensor(scaled[:, kt % 2], xt[:, kt, :], rstd[:], ALU.mult).then_inc(scaled_done, 1)
                        if h_plain is None and kt >= 1:
                            dve.wait_ge(hi_done, kt)
                            dve.tensor_tensor(h_lo[:, kt - 1, :], shifted[:, (kt - 1) % 2], h_hi[:, kt - 1, :].bitcast(F32),
                                              ALU.subtract).then_inc(lo_done, 1)
                    if h_plain is None:
                        dve.wait_ge(hi_done, KT)
                        dve.tensor_tensor(h_lo[:, KT - 1, :], shifted[:, (KT - 1) % 2], h_hi[:, KT - 1, :].bitcast(F32),
                                          ALU.subtract).then_inc(lo_done, 1)

        def plain_gain(name):
            return lambda kt: pa(name)[:, kt:kt + 1]

        phase_modulation()
        h_mem = Arena(nc, nc.sbuf_usable_end // 32 * 32 - 2 * KT * TOK * 4)
        h_hi = h_mem("h1_hi", [P, KT, TOK], F32R)
        h_lo = h_mem("h1_lo", [P, KT, TOK], F32R)
        shift = [lambda kt, s=s: mod[:, SH1 + kt, s:s + 1] for s in range(2)]
        gain = [lambda kt, s=s: gain1[:, kt, s:s + 1] for s in range(2)]
        phase_norm("norm1", Arena(nc, free_at), "rows", [(0, CTX, gain[1], shift[1]), (CTX, SEQ, gain[0], shift[0])], TOK, h_hi, h_lo)

        w_in_k = A["w_in"].rearrange("o (k p) n -> p (o k) n", p=P)
        att_mem = Arena(nc, free_at)
        q_cm = att_mem("q_cm", [P, N_HEADS // 2, SEQ])
        k_cm = att_mem("k_cm", [P, TOK])
        v_rows = att_mem("v_rows", [P, ALLCH, P])
        X0, X1, CX = (0, CTX, HALF, 0), (1, CTX + HALF, HALF, HALF), (2, 0, CTX, SEQ)

        def phase_attention_inputs():
            phases.start()
            mem = Arena(nc, att_mem.at)
            rope = mem("rope", [P, 2, SEQ])
            raw = mem("raw", [P, 2, TOK])
            sq = mem("qk_sq", [P, 2, TOK])
            rstd = mem("qk_rstd", [P, TOK])
            normed = mem("qk_normed", [P, 2, TOK])
            turned = mem("qk_turned", [P, SEQ])
            ring = Ring("att", pieces=2)
            rope_loaded = sem("att_rope_loaded")
            z_free = sem("att_z_free")
            sq_done = sem("att_sq_done")
            raw_done = sem("att_raw_done")
            sums_done = sem("att_sums_done")
            mean_done = sem("att_mean_done")
            root_done = sem("att_root_done")
            normed_done = sem("att_normed_done")
            rotated = sem("att_rotated")
            rotated_used = sem("att_rotated_used")
            v_turned = sem("att_v_turned")
            v_out = sem("att_v_out")
            roped = sem("att_roped")
            dve_step = sem("att_dve_step")
            tiles = [(Q_COL + j * HEAD_DIM, Q_COL + (4 + j) * HEAD_DIM) for j in range(4)]
            tiles += [(K_COL, K_COL + HEAD_DIM), (V_COL, V_COL + HEAD_DIM)]
            groups = [[X0, X1]] * 4 + [[X0, X1, CX]] * 2
            KTILE, VTILE = 4, 5
            with nc.psum_tensor("att_z", [P, 2, 3, HALF], F32) as z, nc.psum_tensor("att_aux", [P, 2, HALF], F32) as aux, nc.Block() as block:
                @block.sync
                def _(sp):
                    sp.dma_start(rope[:], A["rope_table"]).then_inc(rope_loaded, 16)
                    for n, cols in enumerate(tiles):
                        ring.load(sp, n, n % 2, [(w_raw[:, n % 2, :, i * HEAD_DIM:(i + 1) * HEAD_DIM], w_in_k[:, :, c:c + HEAD_DIM])
                                                 for i, c in enumerate(cols)])

                @block.gpsimd
                def _(pool):
                    ring.credits(pool, None)
                    for n in range(len(tiles)):
                        ring.do_split(pool, n, n % 2, n // 2)

                @block.tensor
                def _(pe):
                    ring.credits(None, pe)

                    def proj(n):
                        ring.project(pe, n, n % 2, z_free, [(z[:, n % 2, b, 0:w], c0, w) for b, c0, w, _ in groups[n]], h_hi, h_lo)

                    sums = [0]

                    def head_sums(n):
                        pe.wait_ge(sq_done, n + 1)
                        for _, _, w, r0 in groups[n]:
                            if sums[0]:
                                pe.wait_ge(mean_done, sums[0])
                            pe.matmul(aux[:, 0, 0:w], cst("head_ones"), sq[:, n % 2, r0:r0 + w], start=True, stop=True).then_inc(sums_done, 1)
                            sums[0] += 1

                    def rotate(n):
                        pe.wait_ge(normed_done, n + 1)
                        for half in range(2):
                            if n or half:
                                pe.wait_ge(rotated_used, 2 * n + half)
                            pe.matmul(aux[:, 1, :], cst("rotate"), normed[:, n % 2, half * HALF:(half + 1) * HALF], start=True, stop=True).then_inc(rotated, 1)

                    proj(0)
                    proj(1)
                    head_sums(0)
                    for n in range(2, 6):
                        proj(n)
                        rotate(n - 2)
                        head_sums(n - 1)
                    rotate(KTILE)
                    pe.wait_ge(raw_done, VTILE + 1)
                    pe.wait_ge(mean_done, sums[0])
                    pe.wait_ge(rotated_used, 2 * (KTILE + 1))
                    for g, (t0, count) in enumerate(((0, 4), (4, 4), (8, 2))):
                        if g == 2:
                            pe.wait_ge(v_out, 1)
                        for j in range(count):
                            at = (t0 + j) * P
                            ins = pe.transpose(aux[:, g % 2, j * P:(j + 1) * P], raw[:, VTILE % 2, at:at + P], ident)
                        ins.then_inc(v_turned, 1)

                @block.scalar
                def _(act):
                    act.sem_inc(z_free, 2)
                    for n in range(6):
                        act.wait_ge(ring.projected, n + 3)
                        if 2 <= n:
                            act.wait_ge(normed_done, n - 1)
                        if n != VTILE:
                            for i, (b, _, w, r0) in enumerate(groups[n]):
                                ins = act.activation(sq[:, n % 2, r0:r0 + w], z[:, n % 2, b, 0:w], ACT.Square)
                            ins.then_inc(sq_done, 1)
                        for i, (b, _, w, r0) in enumerate(groups[n]):
                            ins = act.copy(raw[:, n % 2, r0:r0 + w], z[:, n % 2, b, 0:w])
                        ins.then_inc(z_free, 1)
                        act.wait_ge(z_free, n + 3)
                        act.sem_inc(raw_done, 1)
                        if 1 <= n:
                            width = sum(w for _, _, w, _ in groups[n - 1])
                            act.wait_ge(mean_done, sum(len(g) for g in groups[:n]))
                            act.activation(rstd[:, 0:width], rstd[:, 0:width], ACT.Sqrt).then_inc(root_done, 1)

                @block.vector
                def _(dve):
                    step = Steps(dve, dve_step)
                    sums = 0
                    dve.wait_ge(rope_loaded, 16)
                    for n in range(5):
                        width = sum(w for _, _, w, _ in groups[n])
                        for _, _, w, r0 in groups[n]:
                            sums += 1
                            dve.wait_ge(sums_done, sums)
                            dve.tensor_scalar(rstd[:, r0:r0 + w], aux[:, 0, 0:w], 1.0 / HEAD_DIM, EPS, ALU.mult, ALU.add).then_inc(mean_done, 1)
                        dve.wait_ge(root_done, n + 1)
                        step(dve.reciprocal(rstd[:, 0:width], rstd[:, 0:width]))
                        step.wait()
                        dve.wait_ge(raw_done, n + 1)
                        g = 1 if n == KTILE else 0
                        dve.scalar_tensor_tensor(out=normed[:, n % 2, 0:width], in0=raw[:, n % 2, 0:width], scalar=qk_gain[:, g:g + 1],
                                                 in1=rstd[:, 0:width], op0=ALU.mult, op1=ALU.mult).then_inc(normed_done, 1)
                        dve.wait_ge(normed_done, n + 1)
                        to = k_cm[:, CTX:] if n == KTILE else q_cm[:, n, :]
                        if n == KTILE:
                            step(dve.tensor_copy(k_cm[:, 0:CTX], normed[:, n % 2, SEQ:TOK]))
                        step(dve.tensor_tensor(to, normed[:, n % 2, 0:SEQ], rope[:, 0], ALU.mult))
                        for half in range(2):
                            cols = slice(half * HALF, (half + 1) * HALF)
                            dve.wait_ge(rotated, 2 * n + half + 1)
                            dve.tensor_tensor(turned[:, cols], aux[:, 1, :], rope[:, 1, cols], ALU.mult).then_inc(rotated_used, 1)
                        dve.wait_ge(rotated_used, 2 * n + 2)
                        step.wait()
                        step(dve.tensor_tensor(to, to, turned[:], ALU.add))
                        step.wait()
                    for g, (t0, count) in enumerate(((0, 4), (4, 4), (8, 2))):
                        dve.wait_ge(v_turned, g + 1)
                        at = [(t0 + j + CCH) % ALLCH for j in range(count)]
                        split = next((j for j in range(1, count) if at[j] != at[j - 1] + 1), count)
                        for a, b in ((0, split), (split, count)):
                            if b > a:
                                ins = dve.tensor_copy(v_rows[:, at[a]:at[a] + b - a, :], aux[:, g % 2, a * P:b * P].rearrange("p (j n) -> p j n", n=P))
                        ins.then_inc(v_out, 1)

        def phase_attention():
            phases.start()
            mem = Arena(nc, att_mem.at)
            q_now = mem("q_now", [P, SEQ])
            out_now = mem("att_out_now", [P, SEQ])
            s = [mem(f"att_s{a}", [P, 1 + 5 * P]) for a in range(2)]
            p = [mem(f"att_p{a}", [P, 1 + 5 * P]) for a in range(2)]
            p_t = mem("att_p_t", [P, 2, 5, P])
            neg_max = mem("att_neg_max", [P, 2])
            den = mem("att_den", [P, 2])
            q_copied = sem("win_q_copied")
            scores = sem("win_scores")
            local_in = sem("win_local_in")
            ctx_in = sem("win_ctx_in")
            max_done = sem("win_max_done")
            probs = sem("win_probs")
            scaled = sem("win_scaled")
            p_turned = sem("win_p_turned")
            near_out = sem("win_near_out")
            last_out = sem("win_last_out")
            pv_done = sem("win_pv_done")
            o_out = sem("win_o_out")
            stored = sem("win_stored")
            dve_step = sem("win_dve_step")
            U = 2 * BLOCKS
            near = [range(max(n - 1, 0), min(n + 2, BLOCKS)) for n in range(BLOCKS)]
            with nc.psum_tensor("win_s", [P, 2, 2, HALF], F32) as ps, nc.psum_tensor("win_t", [P, 2, HALF], F32) as pt, \
                    nc.psum_tensor("win_o", [P, 2, HALF], F32) as po, nc.Block() as block:
                @block.tensor
                def _(pe):
                    with pe.Fori(0, 4) as j:
                        def score(u):
                            n, a = u // 2, u % 2
                            rows = slice(a * HEAD_DIM, (a + 1) * HEAD_DIM)
                            w, k0 = len(near[n]) * P, CTX + near[n][0] * P
                            pe.wait_ge(local_in, j * U + u + 1)
                            pe.wait_ge(ctx_in, j * U + u + 1)
                            pe.matmul(ps[:, a, 0, 0:w], q_now[rows, n * P:(n + 1) * P], k_cm[rows, k0:k0 + w], start=True, stop=True)
                            pe.matmul(ps[:, a, 1, 0:CTX], q_now[rows, n * P:(n + 1) * P], k_cm[rows, 0:CTX], start=True, stop=True).then_inc(scores, 1)

                        def turn_and_sum(u):
                            n, a = u // 2, u % 2
                            tiles = [CCH + t for t in near[n]] + [0, 1]
                            nt = len(tiles)
                            pe.wait_ge(near_out, j * U + u + 1)
                            pe.wait_ge(last_out, j * U + u + 1)
                            pe.wait_ge(scaled, j * U + u + 1)
                            for t in range(nt):
                                to = pt[:, 1, 0:P] if t == nt - 1 else pt[:, 0, t * P:(t + 1) * P]
                                ins = pe.transpose(to, p[a][:, 1 + t * P:1 + (t + 1) * P], ident)
                            ins.then_inc(p_turned, 1)
                            if a == 0:
                                pe.wait_ge(o_out, j * BLOCKS + n + 1)
                            pe.wait_ge(near_out, j * U + u + 2)
                            pe.wait_ge(last_out, j * U + u + 2)
                            cols = slice(a * HEAD_DIM, (a + 1) * HEAD_DIM)
                            for t in range(nt):
                                ins = pe.matmul(po[cols, n % 2, 0:P], v_rows[:, tiles[t], cols], p_t[:, a, 4 if t == nt - 1 else t, :],
                                                start=(t == 0), stop=(t == nt - 1))
                            ins.then_inc(pv_done, 1)

                        pe.wait_ge(q_copied, j + 1)
                        score(0)
                        score(1)
                        for u in range(U):
                            if u + 2 < U:
                                score(u + 2)
                            turn_and_sum(u)

                @block.scalar
                def _(act):
                    act.sem_inc(ctx_in, 2)
                    act.sem_inc(last_out, 1)
                    act.sem_inc(o_out, 2)
                    act.sem_inc(probs, 2)
                    act.sem_inc(stored, 16)
                    with act.Fori(0, 4) as j:
                        def take_ctx(u):
                            n, a = u // 2, u % 2
                            at = 1 + len(near[n]) * P
                            act.wait_ge(scores, j * U + u + 2)
                            act.wait_ge(probs, j * U + u + 1)
                            act.copy(s[a][:, at:at + CTX], ps[:, a, 1, 0:CTX]).then_inc(ctx_in, 1)

                        take_ctx(0)
                        for u in range(U):
                            n, a = u // 2, u % 2
                            if u + 1 < U:
                                take_ctx(u + 1)
                            w = 1 + len(near[n]) * P + CTX
                            act.wait_ge(max_done, j * U + u + 1)
                            act.wait_ge(pv_done, j * U + u + 1)
                            act.activation(p[a][:, 0:w], s[a][:, 0:w], ACT.Exp, bias=neg_max[:, a:a + 1],
                                           accum_out=den[:, a:a + 1]).then_inc(probs, 1)
                            act.wait_ge(p_turned, j * U + u + 1)
                            act.copy(p_t[:, a, 4, :], pt[:, 1, 0:P]).then_inc(last_out, 1)
                            if a == 1:
                                if n == 0:
                                    act.wait_ge(stored, 16 * j + 16)
                                act.wait_ge(pv_done, j * U + u + 3)
                                act.copy(out_now[:, n * P:(n + 1) * P], po[:, n % 2, 0:P]).then_inc(o_out, 1)
                        act.wait_ge(o_out, j * BLOCKS + BLOCKS + 2)
                        act.dma_start(att_cm.rearrange("(j p) t -> p j t", p=P)[:, bass.ds(j, 1), :],
                                      out_now[:].rearrange("p (o t) -> p o t", o=1)).then_inc(stored, 16)
                    act.wait_ge(stored, 16 * 5)

                @block.vector
                def _(dve):
                    dve.sem_inc(local_in, 2)
                    dve.sem_inc(near_out, 1)
                    dve.sem_inc(pv_done, 2)
                    dve.sem_inc(scores, 1)
                    N_STEP = U
                    with dve.Fori(0, 4) as j:
                        def local_and_max(u):
                            n, a = u // 2, u % 2
                            w = len(near[n]) * P
                            m0 = (near[n][0] - n + 1) * P
                            dve.wait_ge(scores, j * U + u + 2)
                            dve.wait_ge(probs, j * U + u + 1)
                            dve.tensor_tensor(s[a][:, 1:1 + w], ps[:, a, 0, 0:w], cst("near_mask")[:, m0:m0 + w], ALU.add).then_inc(local_in, 1)
                            dve.wait_ge(local_in, j * U + u + 3)
                            dve.wait_ge(ctx_in, j * U + u + 3)
                            dve.tensor_reduce(neg_max[:, a:a + 1], s[a][:, 0:1 + w + CTX], AX_X, ALU.max, negate=True).then_inc(max_done, 1)

                        dve.wait_ge(probs, j * U + 2)
                        dve.wait_ge(scores, j * U + 1)
                        for a in range(2):
                            dve.tensor_scalar(s[a][:, 0:1], sinks[:, bass.ds(j + 4 * a, 1)], 0.0, None, ALU.add)
                        dve.tensor_scalar(q_now[:], q_cm[:, bass.ds(j, 1), :].rearrange("p o t -> p (o t)"), HEAD_DIM ** -0.5, None,
                                          ALU.mult).then_inc(q_copied, 1)
                        dve.wait_ge(q_copied, j + 1)
                        local_and_max(0)
                        for u in range(U):
                            n, a = u // 2, u % 2
                            if u + 1 < U:
                                local_and_max(u + 1)
                            w = len(near[n]) * P + CTX
                            dve.wait_ge(probs, j * U + u + 3)
                            dve.reciprocal(den[:, a:a + 1], den[:, a:a + 1]).then_inc(dve_step, 1)
                            dve.wait_ge(dve_step, j * N_STEP + u + 1)
                            dve.tensor_scalar(p[a][:, 1:1 + w], p[a][:, 1:1 + w], den[:, a:a + 1], None, ALU.mult).then_inc(scaled, 1)
                            dve.wait_ge(p_turned, j * U + u + 1)
                            nn = len(near[n]) + 1
                            dve.tensor_copy(p_t[:, a, 0:nn, :], pt[:, 0, 0:nn * P].rearrange("p (t q) -> p t q", q=P)).then_inc(near_out, 1)

        phase_attention_inputs()
        phase_attention()

        m_mem = Arena(nc, free_at)
        mq_cm = m_mem("mq_cm", [P, M_HEADS, SEQ])
        mk_cm = m_mem("mk_cm", [P, M_HEADS, TOK])
        v_ext = m_mem("v_ext", [P, ALLCH, M_HEADS, M_DIM + 1])
        out_gate = m_mem("out_gate", [P, M_HEADS, SEQ])
        gates_raw = m_mem("gates_raw", [P, TOK])

        def phase_mlstm_inputs():
            phases.start()
            mem = Arena(nc, m_mem.at)
            XPAD, CPAD = 1, SEQ + 3
            PADDED = SEQ + CTX + 4
            padded = mem("conv_padded", [P, PADDED])
            conv = mem("conv_sum", [P, PADDED - 2])
            taps = mem("conv_taps", [P, 3, 2, 1])
            ring = Ring("mls")
            z_free = sem("mls_z_free")
            padded_done = sem("mls_padded_done")
            pad_free = sem("mls_pad_free")
            conv_done = sem("mls_conv_done")
            conv_used = sem("mls_conv_used")
            v_turned = sem("mls_v_turned")
            v_out = sem("mls_v_out")
            gates_zeroed = sem("mls_gates_zeroed")
            gates_out = sem("mls_gates_out")
            dve_step = sem("mls_dve_step")
            cleared = sem("mls_cleared")
            groups = [[X0, X1], [X0, X1, CX], [X0, X1, CX], [X0, X1]]
            G = 4 * M_HEADS
            with nc.psum_tensor("mls_z", [P, 2, 3, HALF], F32) as z, nc.psum_tensor("mls_aux", [P, 2, HALF], F32) as aux, nc.Block() as block:
                @block.sync
                def _(sp):
                    with sp.Fori(0, M_HEADS) as h:
                        for i, col in enumerate((MQ_COL, MK_COL, MV_COL, MO_COL)):
                            ring.load(sp, 4 * h + i, i % 2, [(w_raw[:, i % 2], w_in_k[:, :, bass.ds(h * M_DIM + col, M_DIM)])])
                    sp.wait_ge(gates_zeroed, 1)
                    for row, at in ((0, 0), (64, 4), (32, 8), (96, 12)):
                        sp.dma_start(w_raw[:, 0, :, row:row + M_HEADS], w_in_k[:, :, G_COL + at:G_COL + at + M_HEADS]).then_inc(ring.loaded[0], 16)

                @block.gpsimd
                def _(pool):
                    ring.credits(pool, None)
                    with pool.Fori(0, M_HEADS) as h:
                        for i in range(4):
                            ring.do_split(pool, 4 * h + i, i % 2, 2 * h + i // 2)
                    pool.wait_ge(ring.split, G + 1)
                    pool.memset(w_raw[:, 0], 0.0).then_inc(gates_zeroed, 1)
                    ring.do_split(pool, G, 0, 2 * M_HEADS + 3)

                @block.tensor
                def _(pe):
                    ring.credits(None, pe)
                    pe.wait_ge(cleared, 1)

                    def proj(n, i, between=None):
                        ring.project(pe, n, i % 2, z_free, [(z[:, i % 2, b, 0:w], c0, w) for b, c0, w, _ in groups[i]], h_hi, h_lo, between)

                    def turn_v(h):
                        for g, (t0, count) in enumerate(((0, 4), (4, 4), (8, 2))):
                            if g == 0:
                                pe.wait_ge(padded_done, 3 * h + 3)
                            if g == 2:
                                pe.wait_ge(v_out, 3 * h + 1 + 1)
                            else:
                                pe.wait_ge(v_out, 3 * h + 1)
                            for t in range(t0, t0 + count):
                                at = CPAD + t * P if t < CCH else XPAD + (t - CCH) * P
                                ins = pe.transpose(aux[:, g % 2, (t - t0) * P:(t - t0 + 1) * P], padded[:, at:at + P], ident)
                            ins.then_inc(v_turned, 1)

                    with pe.Fori(0, M_HEADS) as h:
                        for i in range(4):
                            proj(4 * h + i, i)
                        turn_v(h)
                    ring.project(pe, G, 0, z_free, [(z[:, 0, b, 0:w], c0, w) for b, c0, w, _ in groups[1]], h_hi, h_lo)

                @block.scalar
                def _(act):
                    act.sem_inc(z_free, 2)
                    act.sem_inc(conv_used, 1)
                    act.wait_ge(cleared, 1)
                    with act.Fori(0, M_HEADS) as h:
                        def pad(i, round_):
                            act.wait_ge(ring.projected, 4 * h + i + 3)
                            act.wait_ge(pad_free, round_ + 1)
                            for b, _, w, r0 in groups[i]:
                                at = CPAD if b == 2 else XPAD + r0
                                ins = act.copy(padded[:, at:at + w], z[:, i % 2, b, 0:w])
                            ins.then_inc(z_free, 1)
                            act.wait_ge(z_free, 4 * h + i + 3)
                            act.sem_inc(padded_done, 1)

                        pad(0, 3 * h)
                        act.wait_ge(conv_done, 2 * h + 1)
                        pass_waits(act)
                        act.activation(mq_cm[:, bass.ds(h, 1), :].rearrange("p o t -> p (o t)"), conv[:, 0:SEQ], ACT.Silu).then_inc(conv_used, 1)
                        pad(1, 3 * h + 1)
                        act.wait_ge(conv_done, 2 * h + 2)
                        pass_waits(act)
                        act.activation(mk_cm[:, bass.ds(h, 1), CTX:].rearrange("p o t -> p (o t)"), conv[:, 0:SEQ], ACT.Silu)
                        act.activation(mk_cm[:, bass.ds(h, 1), 0:CTX].rearrange("p o t -> p (o t)"), conv[:, SEQ + 2:SEQ + 2 + CTX],
                                       ACT.Silu).then_inc(conv_used, 1)
                        pad(2, 3 * h + 2)
                        act.wait_ge(ring.projected, 4 * h + 3 + 3)
                        pass_waits(act)
                        for half in range(2):
                            ins = act.activation(out_gate[:, bass.ds(h, 1), half * HALF:(half + 1) * HALF].rearrange("p o t -> p (o t)"),
                                                 z[:, 1, half, :], ACT.Sigmoid)
                        ins.then_inc(z_free, 1)
                    act.wait_ge(ring.projected, G + 3)
                    for b, c0, w, _ in groups[1]:
                        act.copy(gates_raw[:, c0:c0 + w], z[:, 0, b, 0:w]).then_inc(gates_out, 1)

                @block.vector
                def _(dve):
                    dve.memset(padded[:], 0.0).then_inc(dve_step, 1)
                    dve.memset(v_ext[:].rearrange("p t h n -> p (t h) n")[:, :, M_DIM:M_DIM + 1], 1.0).then_inc(dve_step, 1)
                    dve.wait_ge(dve_step, 2)
                    dve.sem_inc(pad_free, 1)
                    dve.sem_inc(v_out, 1)
                    dve.sem_inc(cleared, 1)
                    N_STEP = 5
                    with dve.Fori(0, M_HEADS) as h:
                        step = Steps(dve, dve_step, h * N_STEP + 2)
                        dve.wait_ge(conv_used, 2 * h + 1)
                        pass_waits(dve)
                        step(dve.tensor_copy(taps[:], pb("conv_qk").rearrange("p (j s h) -> p j s h", j=3, s=2)[:, :, :, bass.ds(h, 1)]))
                        step.wait()
                        for s in range(2):
                            width = SEQ if s == 0 else PADDED - 2
                            dve.wait_ge(padded_done, 3 * h + s + 1)
                            dve.wait_ge(conv_used, 2 * h + s + 1)
                            step(dve.tensor_scalar(conv[:, 0:width], padded[:, 0:width], taps[:, 0, s, :], None, ALU.mult))
                            step.wait()
                            step(dve.scalar_tensor_tensor(out=conv[:, 0:width], in0=padded[:, 1:1 + width], scalar=taps[:, 1, s, :],
                                                          in1=conv[:, 0:width], op0=ALU.mult, op1=ALU.add))
                            step.wait()
                            dve.scalar_tensor_tensor(out=conv[:, 0:width], in0=padded[:, 2:2 + width], scalar=taps[:, 2, s, :],
                                                     in1=conv[:, 0:width], op0=ALU.mult, op1=ALU.add).then_inc(conv_done, 1)
                            dve.wait_ge(conv_done, 2 * h + s + 1)
                            dve.sem_inc(pad_free, 1)
                        assert step.done == N_STEP
                        for g, (t0, count) in enumerate(((0, 4), (4, 4), (8, 2))):
                            dve.wait_ge(v_turned, 3 * h + g + 1)
                            pass_waits(dve)
                            ins = dve.tensor_copy(v_ext[:, t0:t0 + count, bass.ds(h, 1), 0:M_DIM].rearrange("p t o n -> p t (o n)"),
                                                  aux[:, g % 2, 0:count * P].rearrange("p (t n) -> p t n", n=P))
                            ins.then_inc(v_out, 1)
                        dve.wait_ge(v_out, 3 * h + 3 + 1)
                        dve.sem_inc(pad_free, 1)

        s_mem = Arena(nc, m_mem.at)
        neg_m = s_mem("neg_m", [GATE_ROWS, TOK])
        pick = s_mem("pick", [GATE_ROWS, 8, P])
        tok_gate = s_mem("tok_gate", [P, 4, ALLCH, GATE_ROWS])
        carry = s_mem("carry", [P, 8, ALLCH])
        GG, WS, DECAY, FLOOR = range(4)

        def phase_gate_scans():
            phases.start()
            mem = Arena(nc, s_mem.at)
            names = ("keep", "log_i", "log_f", "tmp", "b", "g", "run_max", "jump", "pre_ws", "pre_decay", "pre_floor", "time_gate")
            t = {n: mem(f"scan_{n}", [GATE_ROWS, TOK] if n != "time_gate" else [GATE_ROWS, 4, TOK]) for n in names}
            start_m = mem("scan_start_m", [GATE_ROWS, ALLCH])
            step_decay = mem("scan_step_decay", [GATE_ROWS, ALLCH])
            loaded = sem("scan_loaded")
            dve_step = sem("scan_dve_step")
            act_step = sem("scan_act_step")
            f_ready = sem("scan_f_ready")
            log_done = sem("scan_log_done")
            pre_done = sem("scan_pre_done")
            exp_done = sem("scan_exp_done")
            g_done = sem("scan_g_done")
            turned = sem("scan_turned")
            copied = sem("scan_copied")
            B0 = 32

            def by_time(dst, rows=GATE_ROWS):
                return [(dst[0:B0], slice(0, B0), slice(None)), (dst[B0:GATE_ROWS, CTX - 1::-1], slice(B0, GATE_ROWS), slice(0, CTX)),
                        (dst[B0:GATE_ROWS, TOK - 1:CTX - 1:-1], slice(B0, GATE_ROWS), slice(CTX, TOK))]

            def chunks(x):
                return x.rearrange("p (c t) -> p c t", t=CHUNK)

            with nc.psum_tensor("scan_turn", [P, 4, HALF], F32) as turn, nc.psum_tensor("scan_carry", [P, HALF], F32) as cps, nc.Block() as block:
                @block.sync
                def _(sp):
                    sp.dma_start(t["keep"][:], A["keep_table"]).then_inc(loaded, 16)
                    sp.dma_start(pick[:].rearrange("p r n -> p (r n)"), A["pick_table"]).then_inc(loaded, 16)

                @block.vector
                def _(dve):
                    step = Steps(dve, dve_step)
                    for name, at in (("log_i", 0), ("log_f", 64)):
                        rows = gates_raw[at:at + GATE_ROWS]
                        bias = gate_bias[at:at + GATE_ROWS]
                        for dst, r, cols in by_time(t[name]):
                            step(dve.tensor_scalar(dst, rows[r, cols], bias[r], None, ALU.add))
                    step.wait()
                    dve.sem_inc(f_ready, 1)
                    step(dve.tensor_scalar(t["jump"][:], t["log_f"][:], 0.0, None, ALU.min))
                    step.wait()
                    dve.wait_ge(log_done, 1)
                    step(dve.tensor_tensor(t["log_f"][:], t["jump"][:], t["tmp"][:], ALU.subtract))
                    step.wait()
                    dve.wait_ge(loaded, 32)
                    step(dve.tensor_tensor_scan(t["b"][:], t["keep"][:], t["log_f"][:], 0.0, ALU.mult, ALU.add))
                    step(dve.memset(t["jump"][:], 0.0))
                    step.wait()
                    last_b = chunks(t["b"][:])[:, :, CHUNK - 1]
                    step(dve.tensor_copy(chunks(t["jump"][:])[:, 1:, 0], last_b[:, 0:ALLCH - 1]))
                    step(dve.tensor_tensor(t["g"][:], t["log_i"][:], t["b"][:], ALU.subtract))
                    step.wait()
                    step(dve.tensor_tensor_scan(t["run_max"][:], t["jump"][:], t["g"][:], 0.0, ALU.add, ALU.max))
                    step(dve.memset(start_m[:], 0.0))
                    step.wait()
                    last_max = chunks(t["run_max"][:])[:, :, CHUNK - 1]
                    step(dve.tensor_tensor(start_m[:, 1:], last_b[:, 0:ALLCH - 1], last_max[:, 0:ALLCH - 1], ALU.add))
                    for dst, r, cols in by_time(neg_m[:]):
                        step(dve.tensor_scalar(dst, t["run_max"][r, cols], -1.0, None, ALU.mult))
                    step.wait()
                    wide = [GATE_ROWS, ALLCH, CHUNK]
                    step(dve.tensor_tensor(step_decay[:], start_m[:], last_max, ALU.subtract))
                    step(dve.tensor_tensor(chunks(t["pre_ws"][:]), chunks(t["g"][:]), last_max.unsqueeze(2).to_broadcast(wide), ALU.subtract))
                    step(dve.tensor_tensor(chunks(t["pre_decay"][:]), start_m[:].unsqueeze(2).to_broadcast(wide), chunks(t["run_max"][:]), ALU.subtract))
                    step(dve.tensor_tensor(t["pre_floor"][:], t["b"][:], t["run_max"][:], ALU.add))
                    step.wait()
                    dve.sem_inc(pre_done, 1)
                    for dst, r, cols in by_time(t["time_gate"][:, GG, :]):
                        step(dve.tensor_copy(dst, t["g"][r, cols]))
                    step.wait()
                    dve.sem_inc(g_done, 1)
                    dve.wait_ge(turned, 5)
                    step(dve.tensor_copy(carry[:], cps[:, 0:8 * ALLCH].rearrange("p (r c) -> p r c", c=ALLCH)))
                    dve.wait_ge(copied, 4)
                    step(dve.tensor_scalar(tok_gate[:, DECAY], tok_gate[:, DECAY], M_DIM ** -0.5, None, ALU.mult))

                @block.scalar
                def _(act):
                    step = Steps(act, act_step)
                    act.wait_ge(f_ready, 1)
                    step(act.activation(t["tmp"][:], t["log_f"][:], ACT.Abs))
                    step.wait()
                    step(act.activation(t["tmp"][:], t["tmp"][:], ACT.Exp, scale=-1.0))
                    step.wait()
                    act.activation(t["tmp"][:], t["tmp"][:], ACT.Ln, bias=1.0).then_inc(log_done, 1)
                    act.wait_ge(pre_done, 1)
                    act.activation(step_decay[:], step_decay[:], ACT.Exp).then_inc(exp_done, 1)
                    for q, name, sign in ((WS, "pre_ws", 1.0), (DECAY, "pre_decay", 1.0), (FLOOR, "pre_floor", -1.0)):
                        for dst, r, cols in by_time(t["time_gate"][:, q, :]):
                            act.activation(dst, t[name][r, cols], ACT.Exp, scale=sign).then_inc(exp_done, 1)
                    for i, q in enumerate((GG, WS, DECAY, FLOOR)):
                        act.wait_ge(turned, i + 2)
                        act.copy(tok_gate[:, q], turn[:, q, 0:ALLCH * GATE_ROWS].rearrange("p (c r) -> p c r", r=GATE_ROWS)).then_inc(copied, 1)

                @block.tensor
                def _(pe):
                    pe.wait_ge(loaded, 32)
                    pe.wait_ge(exp_done, 1)
                    for r in range(8):
                        ins = pe.matmul(cps[:, r * ALLCH:(r + 1) * ALLCH], pick[:, r, :], step_decay[:], start=True, stop=True)
                    ins.then_inc(turned, 1)
                    for i, q in enumerate((GG, WS, DECAY, FLOOR)):
                        if q == GG:
                            pe.wait_ge(g_done, 1)
                        else:
                            pe.wait_ge(exp_done, 1 + 3 * i)
                        for c in range(ALLCH):
                            ins = pe.transpose(turn[:, q, c * GATE_ROWS:(c + 1) * GATE_ROWS], t["time_gate"][:, q, c * CHUNK:(c + 1) * CHUNK],
                                               ident[0:GATE_ROWS, 0:GATE_ROWS])
                        ins.then_inc(turned, 1)

        r_mem = Arena(nc, s_mem.at)
        h_sum = r_mem("h_sum", [P, XCH, M_HEADS, M_DIM])

        def phase_mlstm():
            phases.start()
            mem = Arena(nc, r_mem.at)
            E1 = M_DIM + 1
            state = mem("state", [P, 8, E1])
            k_now = mem("k_now", [P, 2, 2, M_HEADS, CHUNK])
            q_now = mem("mq_now", [P, 2, 2, M_HEADS, CHUNK])
            g_now = mem("g_now", [P, 2, 2, 4, M_HEADS])
            a_now = mem("a_now", [P, 2, 8])
            weight = mem("m_weight", [P, 2, CHUNK])
            w_qk = mem("m_w_qk", [P, 2, CHUNK])
            k_w = mem("m_k_w", [P, 2, M_DIM])
            inter = mem("m_inter", [P, 2, E1])
            total = mem("m_total", [P, 2, E1])
            size = mem("m_size", [P, 2, 1])
            fetched = sem("mlc_fetched")
            first_done = sem("mlc_first_done")
            second_done = sem("mlc_second_done")
            weight_done = sem("mlc_weight_done")
            k_w_done = sem("mlc_k_w_done")
            w_qk_done = sem("mlc_w_qk_done")
            inter_done = sem("mlc_inter_done")
            state_done = sem("mlc_state_done")
            unit_done = sem("mlc_unit_done")
            dve_step = sem("mlc_dve_step")
            cleared = sem("mlc_cleared")
            U = 16
            with nc.psum_tensor("mlc_wk", [P, 2, HALF], F32) as p_wk, nc.psum_tensor("mlc_qk", [P, 2, HALF], F32) as p_qk, \
                    nc.psum_tensor("mlc_num", [P, 2, HALF], F32) as p_num, nc.psum_tensor("mlc_inter", [P, 2, HALF], F32) as p_int, nc.Block() as block:

                def unit(u):
                    return u // 8, u % 8, (u % 8) // M_HEADS, u % M_HEADS, u % 2

                @block.gpsimd
                def _(pool):
                    pool.wait_ge(cleared, 1)

                    def fetch(par, chunk, s, with_q):
                        for d in range(2):
                            for now, all_, off in ((k_now, mk_cm, 0),) + (((q_now, mq_cm, CTX),) if with_q else ()):
                                at = chunk[d] * CHUNK - off
                                pool.tensor_copy(now[:, par, d], all_[:, :, bass.ds(at, CHUNK)]).then_inc(fetched, 1)
                            pool.tensor_copy(g_now[:, par, d].rearrange("p q (c h) -> p q c h", c=1),
                                             tok_gate[:, :, bass.ds(chunk[d], 1), 32 * d:32 * d + M_HEADS]).then_inc(fetched, 1)
                        pool.tensor_copy(a_now[:, par, :].rearrange("p (r c) -> p r c", c=1), carry[:, :, bass.ds(s, 1)]).then_inc(fetched, 1)

                    for s in range(CCH):
                        fetch(s % 2, (s, CCH - 1 - s), s, False)
                    with pool.Fori(0, XCH // 2) as i:
                        for par in range(2):
                            pool.wait_ge(unit_done, i * U + 8 * (par + 1) + 2)
                            pass_waits(pool)
                            fetch(par, (2 * i + par + CCH, ALLCH - 1 - par - 2 * i), 2 * i + par + CCH, True)

                C_FETCH, X_FETCH = 5, 7

                @block.tensor
                def _(pe):
                    def first(u, base, x):
                        par, r, d, h, b = unit(u)
                        pe.wait_ge(k_w_done, base + u + 1)
                        if x is not None:
                            pe.wait_ge(weight_done, x * U + u + 1)
                            pe.wait_ge(w_qk_done, x * U + u + 1)
                            c = 2 * x + par + CCH if d == 0 else ALLCH - 1 - par - 2 * x
                            pass_waits(pe)
                            pe.matmul(p_wk[:, b, 0:CHUNK], pick[:, r, :], neg_m[:, bass.ds(c * CHUNK, CHUNK)], start=True, stop=False)
                            pe.matmul(p_wk[:, b, 0:CHUNK], ident, cst("chunk_mask")[:, d * P:(d + 1) * P], start=False, stop=True)
                            pe.matmul(p_qk[:, b, 0:CHUNK], k_now[:, par, d, h, :], q_now[:, par, d, h, :], start=True, stop=True)
                        pe.transpose(p_wk[:, b, CHUNK:2 * CHUNK], k_now[:, par, d, h, :], ident).then_inc(first_done, 1)

                    def second(u, base, x):
                        par, r, d, h, b = unit(u)
                        pe.wait_ge(unit_done, base + u + 1)
                        if x is not None:
                            c = 2 * x + par + CCH if d == 0 else ALLCH - 1 - par - 2 * x
                            values = v_ext[:, bass.ds(c, 1), h, :].rearrange("p o n -> p (o n)")
                            pe.wait_ge(inter_done, x * U + u + 1)
                            pe.wait_ge(w_qk_done, x * U + u + 3)
                            pass_waits(pe)
                            pe.matmul(p_num[:, b, 0:E1], w_qk[:, b, :], values, start=True, stop=True)
                            pe.wait_ge(state_done, base + u - 5)
                            pe.matmul(p_int[:, b, 0:E1], q_now[:, par, d, h, :], state[:, r, :], start=True, stop=True)
                        else:
                            c = par if d == 0 else CCH - 1 - par
                            values = v_ext[:, c, h, :]
                        pe.wait_ge(k_w_done, base + u + 3)
                        if x is not None:
                            pass_waits(pe)
                        pe.matmul(p_num[:, b, 256:256 + E1], k_w[:, b, :], values, start=True, stop=True).then_inc(second_done, 1)

                    def units(base, x, fetches):
                        for u in range(U):
                            if u == 0:
                                pe.wait_ge(fetched, fetches[0])
                                first(0, base, x)
                            if u + 1 < U:
                                if u + 1 == 8:
                                    pe.wait_ge(fetched, fetches[1])
                                first(u + 1, base, x)
                            second(u, base, x)

                    units(0, None, (C_FETCH, 2 * C_FETCH))
                    with pe.Fori(0, XCH // 2) as i:
                        done = 2 * C_FETCH + 2 * X_FETCH * i
                        units((i + 1) * U, i, (done + X_FETCH, done + 2 * X_FETCH))

                @block.scalar
                def _(act):
                    act.sem_inc(k_w_done, 2)
                    act.sem_inc(weight_done, 2)
                    act.sem_inc(inter_done, 2)

                    def first(u, base, x):
                        par, r, d, h, b = unit(u)
                        act.wait_ge(first_done, base + u + 1)
                        if x is not None:
                            act.wait_ge(w_qk_done, x * U + u + 1)
                            act.activation(weight[:, b, :], p_wk[:, b, 0:CHUNK], ACT.Exp, bias=g_now[:, par, d, GG, h:h + 1]).then_inc(weight_done, 1)
                        act.wait_ge(unit_done, base + u + 1)
                        act.activation(k_w[:, b, :], p_wk[:, b, CHUNK:2 * CHUNK], ACT.Copy, scale=g_now[:, par, d, WS, h:h + 1]).then_inc(k_w_done, 1)

                    def second(u, base, x):
                        par, r, d, h, b = unit(u)
                        if x is not None:
                            act.wait_ge(second_done, base + u + 1)
                            act.activation(inter[:, b, :], p_int[:, b, 0:E1], ACT.Copy, scale=g_now[:, par, d, DECAY, h:h + 1]).then_inc(inter_done, 1)

                    def units(base, x):
                        first(0, base, x)
                        for u in range(U):
                            if u + 1 < U:
                                first(u + 1, base, x)
                            second(u, base, x)

                    units(0, None)
                    with act.Fori(0, XCH // 2) as i:
                        units((i + 1) * U, i)

                @block.vector
                def _(dve):
                    dve.memset(state[:], 0.0).then_inc(dve_step, 1)
                    dve.memset(h_sum[:], 0.0).then_inc(dve_step, 1)
                    dve.wait_ge(dve_step, 2)
                    dve.sem_inc(w_qk_done, 2)
                    dve.sem_inc(unit_done, 2)
                    dve.sem_inc(state_done, 2)
                    dve.sem_inc(cleared, 1)

                    def first(u, base, x):
                        par, r, d, h, b = unit(u)
                        if x is not None:
                            dve.wait_ge(weight_done, x * U + u + 3)
                            dve.wait_ge(second_done, base + u - 1)
                            dve.scalar_tensor_tensor(out=w_qk[:, b, :], in0=p_qk[:, b, 0:CHUNK], scalar=M_DIM ** -0.5, in1=weight[:, b, :],
                                                     op0=ALU.mult, op1=ALU.mult).then_inc(w_qk_done, 1)

                    def second(u, base, x, steps):
                        par, r, d, h, b = unit(u)
                        dve.wait_ge(second_done, base + u + 1)
                        dve.scalar_tensor_tensor(out=state[:, r, :], in0=state[:, r, :], scalar=a_now[:, par, r:r + 1], in1=p_num[:, b, 256:256 + E1],
                                                 op0=ALU.mult, op1=ALU.add).then_inc(state_done, 1)
                        if x is not None:
                            dve.wait_ge(inter_done, x * U + u + 3)
                            steps(dve.tensor_tensor(total[:, b, :], p_num[:, b, 0:E1], inter[:, b, :], ALU.add))
                            steps.wait()
                            steps(dve.scalar_tensor_tensor(out=size[:, b, :], in0=total[:, b, M_DIM:E1], scalar=-1.0, in1=total[:, b, M_DIM:E1],
                                                           op0=ALU.mult, op1=ALU.max))
                            steps.wait()
                            steps(dve.tensor_scalar(size[:, b, :], size[:, b, :], g_now[:, par, d, FLOOR, h:h + 1], None, ALU.max))
                            steps.wait()
                            steps(dve.reciprocal(size[:, b, :], size[:, b, :]))
                            steps.wait()
                            pass_waits(dve)
                            c = 2 * x + par if d == 0 else XCH - 1 - par - 2 * x
                            to = h_sum[:, bass.ds(c, 1), h, :].rearrange("p o n -> p (o n)")
                            steps(dve.scalar_tensor_tensor(out=to, in0=total[:, b, 0:M_DIM], scalar=size[:, b, :], in1=to, op0=ALU.mult, op1=ALU.add))
                            steps.wait()
                        dve.wait_ge(state_done, base + u + 3)
                        dve.sem_inc(unit_done, 1)

                    def units(base, x):
                        steps = Steps(dve, dve_step, 2 + (0 if x is None else x * (5 * U)))
                        first(0, base, x)
                        for u in range(U):
                            if u + 1 < U:
                                first(u + 1, base, x)
                            second(u, base, x, steps)

                    units(0, None)
                    with dve.Fori(0, XCH // 2) as i:
                        units((i + 1) * U, i)

        mix_at = nc.sbuf_usable_end // 32 * 32 - 2 * KT * SEQ * 4
        mix_mem = Arena(nc, mix_at)
        mix_hi = mix_mem("mix_hi", [P, KT, SEQ], F32R)
        mix_lo = mix_mem("mix_lo", [P, KT, SEQ], F32R)

        def phase_mix():
            phases.start()
            mem = Arena(nc, free_at)
            att = mem("mix_att", [P, M_HEADS, SEQ])
            normed = mem("mix_normed", [P, XCH * M_HEADS, M_DIM])
            mixed = mem("mix_mixed", [P, 2, HALF])
            sums = mem("mix_sums", [P, XCH * M_HEADS])
            assert mem.at <= free_at + 57 * 1024
            loaded = sem("mix_loaded")
            mean_done = sem("mix_mean_done")
            root_done = sem("mix_root_done")
            normed_done = sem("mix_normed_done")
            turned = sem("mix_turned")
            mixed_done = sem("mix_mixed_done")
            hi_done = sem("mix_hi_done")
            lo_done = sem("mix_lo_done")
            att_hi = sem("mix_att_hi")
            dve_step = sem("mix_dve_step")
            with nc.psum_tensor("mix_turn", [P, 2, HALF], F32) as turn, nc.Block() as block:
                @block.sync
                def _(sp):
                    sp.dma_start(att[:], att_cm.rearrange("(j p) t -> p j t", p=P)).then_inc(loaded, 16)

                @block.gpsimd
                def _(pool):
                    for j in range(M_HEADS):
                        pool.wait_ge(att_hi, j + 1)
                        pool.tensor_tensor(mix_lo[:, j, :], att[:, j, :], mix_hi[:, j, :].bitcast(F32), ALU.subtract)

                @block.vector
                def _(dve):
                    step = Steps(dve, dve_step)
                    rows = h_sum[:].rearrange("p c h n -> p (c h) n")
                    step(dve.tensor_tensor(normed[:], rows, rows, ALU.mult))
                    step.wait()
                    step(dve.tensor_reduce(sums[:], normed[:], AX_X, ALU.add))
                    step.wait()
                    dve.tensor_scalar(sums[:], sums[:], 1.0 / M_DIM, EPS, ALU.mult, ALU.add).then_inc(mean_done, 1)
                    dve.wait_ge(root_done, 1)
                    step(dve.reciprocal(sums[:], sums[:]))
                    step.wait()
                    dve.tensor_tensor(normed[:], rows, sums[:].unsqueeze(2).to_broadcast([P, XCH * M_HEADS, M_DIM]), ALU.mult).then_inc(normed_done, 1)
                    dve.sem_inc(mixed_done, 2)
                    for n in range(2 * M_HEADS):
                        h, half = n // 2, n % 2
                        cols = slice(half * HALF, (half + 1) * HALF)
                        dve.wait_ge(turned, n + 1)
                        if n >= 2:
                            dve.wait_ge(lo_done, n - 1)
                        dve.scalar_tensor_tensor(out=mixed[:, n % 2, :], in0=turn[:, n % 2, :], scalar=pb("mlstm_norm_w")[:, h:h + 1],
                                                 in1=out_gate[:, h, cols], op0=ALU.mult, op1=ALU.mult).then_inc(mixed_done, 1)
                        dve.wait_ge(hi_done, n + 1)
                        dve.tensor_tensor(mix_lo[:, M_HEADS + h, cols], mixed[:, n % 2, :], mix_hi[:, M_HEADS + h, cols].bitcast(F32),
                                          ALU.subtract).then_inc(lo_done, 1)

                @block.scalar
                def _(act):
                    act.wait_ge(mean_done, 1)
                    act.activation(sums[:], sums[:], ACT.Sqrt).then_inc(root_done, 1)
                    act.wait_ge(loaded, 16)
                    for j in range(M_HEADS):
                        act.copy(mix_hi[:, j, :], att[:, j, :]).then_inc(att_hi, 1)
                    for n in range(2 * M_HEADS):
                        h, half = n // 2, n % 2
                        act.wait_ge(mixed_done, n + 3)
                        act.copy(mix_hi[:, M_HEADS + h, half * HALF:(half + 1) * HALF], mixed[:, n % 2, :]).then_inc(hi_done, 1)

                @block.tensor
                def _(pe):
                    pe.wait_ge(normed_done, 1)
                    for n in range(2 * M_HEADS):
                        h, half = n // 2, n % 2
                        pe.wait_ge(mixed_done, n + 1)
                        for c in range(4):
                            ins = pe.transpose(turn[:, n % 2, c * P:(c + 1) * P], normed[:, (4 * half + c) * M_HEADS + h, :], ident)
                        ins.then_inc(turned, 1)

        def phase_out(tag, mem, y_hi, y_lo, weights, pieces, gain):
            phases.start()
            x_in = mem(f"{tag}_x_in", [P, 2, SEQ])
            x_new = mem(f"{tag}_x_new", [P, 2, SEQ])
            ring = Ring(tag, pieces)
            z_free = sem(f"{tag}_z_free")
            x_loaded = [sem(f"{tag}_x_loaded{u}") for u in range(2)]
            x_done = sem(f"{tag}_x_done")
            stored = [sem(f"{tag}_stored{u}") for u in range(2)]
            with nc.psum_tensor(f"{tag}_z", [P, 2, 2, HALF], F32) as z, nc.Block() as block:
                @block.sync
                def _(sp):
                    for n in range(KT):
                        ring.load(sp, n, n % 2, weights(n))
                        if n >= 2:
                            sp.wait_ge(x_done, 2 * (n - 1))
                        sp.dma_start(x_in[:, n % 2, :], x_cm_k[:, n, :]).then_inc(x_loaded[n % 2], 16)

                @block.gpsimd
                def _(pool):
                    ring.credits(pool, None)
                    for n in range(KT):
                        ring.do_split(pool, n, n % 2, n // 2)

                @block.tensor
                def _(pe):
                    ring.credits(None, pe)
                    with pe.Fori(0, KT // 2) as i:
                        for u in range(2):
                            ring.project(pe, 2 * i + u, u, z_free, [(z[:, u, b, :], b * HALF, HALF) for b in range(2)], y_hi, y_lo)

                @block.vector
                def _(dve):
                    dve.sem_inc(z_free, 2)
                    for n in range(KT):
                        u = n % 2
                        dve.wait_ge(ring.projected, n + 3)
                        dve.wait_ge(x_loaded[u], 16 * (n // 2 + 1))
                        if n >= 2:
                            dve.wait_ge(stored[u], 16 * (n // 2))
                        for b in range(2):
                            cols = slice(b * HALF, (b + 1) * HALF)
                            dve.scalar_tensor_tensor(out=x_new[:, u, cols], in0=z[:, u, b, :], scalar=1.0 if gain is None else gain(n),
                                                     in1=x_in[:, u, cols], op0=ALU.mult, op1=ALU.add).then_inc(x_done, 1)
                        dve.wait_ge(x_done, 2 * n + 2)
                        dve.sem_inc(z_free, 1)

                @block.scalar
                def _(act):
                    for n in range(KT):
                        act.wait_ge(x_done, 2 * n + 2)
                        act.dma_start(x_cm_k[:, n, :], x_new[:, n % 2, :]).then_inc(stored[n % 2], 16)
                    for u in range(2):
                        act.wait_ge(stored[u], 16 * (KT // 2))

        def mix_weights(n):
            src = A["w_out"].rearrange("o k n -> (o k) n")
            cols = slice(n * P, (n + 1) * P)
            half = N_HEADS // 2 * HEAD_DIM
            parts = [(w_raw[HEAD_DIM * a:HEAD_DIM * (a + 1), n % 2, 0:4, :],
                      src[half * a:half * (a + 1), cols].rearrange("(k p) n -> p k n", p=HEAD_DIM)) for a in range(2)]
            return parts + [(w_raw[:, n % 2, 4:, :], src[2 * half:, cols].rearrange("(k p) n -> p k n", p=P))]

        phase_mlstm_inputs()
        phase_gate_scans()
        phase_mlstm()
        phase_mix()
        phase_out("out1", Arena(nc, free_at), mix_hi, mix_lo, mix_weights, 3, lambda n: mod[:, G1 + n, 0:1])

        route_mem = Arena(nc, free_at)
        slot_gate = route_mem("slot_gate", [P, N_EXPERTS])
        slot_token = route_mem("slot_token", [P, N_EXPERTS], U32)
        h2_at = nc.sbuf_usable_end // 32 * 32 - KT * SEQ * 4
        h2_cm = Arena(nc, h2_at)("h2_cm", [P, KT, SEQ])

        def phase_router():
            phases.start()
            mem = Arena(nc, route_mem.at)
            w_router = mem("w_router", [P, KT, N_EXPERTS])
            rows = mem("h2_rows_sb", [P, 2, D])
            aff = mem("aff", [P, BLOCKS, N_EXPERTS])
            peak = mem("aff_peak", [P, BLOCKS])
            total = mem("aff_total", [P, BLOCKS])
            left = [mem(f"aff_left{u}", [N_EXPERTS, SEQ]) for u in range(2)]
            top = mem("aff_top", [N_EXPERTS, SLOTS])
            top_at = mem("aff_top_at", [N_EXPERTS, SLOTS], U32)
            top_at_f = mem("aff_top_at_f", [N_EXPERTS, SLOTS])
            w_loaded = sem("route_w_loaded")
            logits_done = sem("route_logits_done")
            shifted = sem("route_shifted")
            exp_done = sem("route_exp_done")
            aff_done = sem("route_aff_done")
            aff_turned = sem("route_aff_turned")
            rows_turned = sem("route_rows_turned")
            rows_out = sem("route_rows_out")
            stored = [sem(f"route_stored{u}") for u in range(2)]
            top_done = sem("route_top_done")
            top_turned = sem("route_top_turned")
            dve_step = sem("route_dve_step")
            wide = [P, BLOCKS, N_EXPERTS]
            with nc.psum_tensor("route_logits", [P, HALF], F32) as logits, nc.psum_tensor("route_aff_t", [N_EXPERTS, 2, HALF], F32) as aff_t, \
                    nc.psum_tensor("route_turn", [P, 2, 2, HALF], F32) as turn, nc.psum_tensor("route_top_t", [P, 2, N_EXPERTS], F32) as top_t, \
                    nc.Block() as block:
                @block.sync
                def _(sp):
                    sp.dma_start(w_router[:], A["w_router"].rearrange("o (k p) n -> p (o k) n", p=P)).then_inc(w_loaded, 16)
                    for j in range(BLOCKS):
                        sp.wait_ge(rows_out, 2 * (j + 1))
                        sp.dma_start(h2_rows[j * P:(j + 1) * P, :], rows[:, j % 2, :]).then_inc(stored[j % 2], 16)
                    for u in range(2):
                        sp.wait_ge(stored[u], 16 * (BLOCKS // 2))

                @block.tensor
                def _(pe):
                    pe.wait_ge(w_loaded, 16)
                    for j in range(BLOCKS):
                        for kt in range(KT):
                            ins = pe.matmul(logits[:, j * N_EXPERTS:(j + 1) * N_EXPERTS], h2_cm[:, kt, j * P:(j + 1) * P], w_router[:, kt, :],
                                            start=(kt == 0), stop=(kt == KT - 1))
                    ins.then_inc(logits_done, 1)
                    for j in range(BLOCKS):
                        if j >= 2:
                            pe.wait_ge(rows_out, 2 * (j - 1))
                        for kt in range(KT):
                            ins = pe.transpose(turn[:, j % 2, kt // 4, (kt % 4) * P:(kt % 4 + 1) * P], h2_cm[:, kt, j * P:(j + 1) * P], ident)
                            if kt % 4 == 3:
                                ins.then_inc(rows_turned, 1)
                        if j == 2:
                            pe.wait_ge(aff_done, 1)
                            for b in range(BLOCKS):
                                ins = pe.transpose(aff_t[:, b // 4, (b % 4) * P:(b % 4 + 1) * P], aff[:, b, :], ident)
                            ins.then_inc(aff_turned, 1)
                    pe.wait_ge(top_done, 1)
                    pe.transpose(top_t[:, 0, :], top[:], ident[0:N_EXPERTS, 0:N_EXPERTS])
                    pe.transpose(top_t[:, 1, :], top_at_f[:], ident[0:N_EXPERTS, 0:N_EXPERTS]).then_inc(top_turned, 1)

                @block.scalar
                def _(act):
                    act.wait_ge(shifted, 1)
                    act.activation(aff[:], aff[:], ACT.Exp).then_inc(exp_done, 1)
                    for j in range(BLOCKS):
                        if j >= 2:
                            act.wait_ge(stored[j % 2], 16 * (j // 2))
                        for half in range(2):
                            act.wait_ge(rows_turned, 2 * j + half + 1)
                            act.copy(rows[:, j % 2, half * HALF:(half + 1) * HALF], turn[:, j % 2, half, :]).then_inc(rows_out, 1)

                @block.vector
                def _(dve):
                    step = Steps(dve, dve_step)
                    dve.wait_ge(logits_done, 1)
                    lg = logits[:, 0:BLOCKS * N_EXPERTS].rearrange("p (j n) -> p j n", n=N_EXPERTS)
                    step(dve.tensor_reduce(peak[:], lg, AX_X, ALU.max))
                    step.wait()
                    dve.tensor_tensor(aff[:], lg, peak[:].unsqueeze(2).to_broadcast(wide), ALU.subtract).then_inc(shifted, 1)
                    dve.wait_ge(exp_done, 1)
                    step(dve.tensor_reduce(total[:], aff[:], AX_X, ALU.add))
                    step.wait()
                    step(dve.reciprocal(total[:], total[:]))
                    step.wait()
                    dve.tensor_tensor(aff[:], aff[:], total[:].unsqueeze(2).to_broadcast(wide), ALU.mult).then_inc(aff_done, 1)
                    dve.wait_ge(aff_turned, 1)
                    step(dve.tensor_copy(left[0][:], aff_t[:].rearrange("p a b -> p (a b)")))
                    step.wait()
                    for r in range(SLOTS // 8):
                        now, nxt = left[r % 2], left[(r + 1) % 2]
                        eight = slice(8 * r, 8 * (r + 1))
                        step(dve.max(top[:, eight], now[:]))
                        step.wait()
                        step(dve.max_index(top_at[:, eight], top[:, eight], now[:]))
                        if r + 1 < SLOTS // 8:
                            step(dve.match_replace(nxt[:], top[:, eight], now[:], -1.0))
                        step.wait()
                    dve.tensor_copy(top_at_f[:], top_at[:]).then_inc(top_done, 1)
                    dve.wait_ge(top_turned, 1)
                    step(dve.tensor_copy(slot_gate[:], top_t[:, 0, :]))
                    step(dve.tensor_copy(slot_token[:], top_t[:, 1, :]))

        def phase_experts():
            phases.start()
            mem = Arena(nc, route_mem.at)
            FK = EXPERT_FF // P
            xg = mem("x_gathered", [P, 2, D])
            x_hi = mem("x_hi", [P, KT, P], F32R)
            x_lo = mem("x_lo", [P, KT, P], F32R)
            shapes = {"gate": [P, KT, EXPERT_FF], "up": [P, KT, EXPERT_FF], "down": [P, FK, D]}
            raw = {w: mem(f"raw_{w}", s) for w, s in shapes.items() if w != "down"}
            raw["down"] = Arena(nc, ring_at)("raw_down", shapes["down"])
            w_hi_ = {w: mem(f"hi_{w}", s, F32R) for w, s in shapes.items()}
            w_lo_ = {w: mem(f"lo_{w}", s, F32R) for w, s in shapes.items()}
            silu = mem("silu_gate", [P, EXPERT_FF])
            prod = mem("gate_up", [P, EXPERT_FF])
            f_hi = mem("f_hi", [P, FK, P], F32R)
            f_lo = mem("f_lo", [P, FK, P], F32R)
            y = mem("expert_y", [P, 2, D])
            token_in = mem("token_in", [P, 2], U32)
            token_out = mem("token_out", [P, 2], U32)
            gate_now = mem("gate_now", [P, 2])
            src = {"gate": A["w_gate"].rearrange("o e (k p) n -> p (o e) k n", p=P), "up": A["w_up"].rearrange("o e (k p) n -> p (o e) k n", p=P),
                   "down": A["w_down"].rearrange("o e (k p) n -> p (o e) k n", p=P)}
            loaded = {w: sem(f"exp_{w}_loaded") for w in shapes}
            hi_done = {w: sem(f"exp_{w}_hi_done") for w in shapes}
            split = {w: sem(f"exp_{w}_split") for w in shapes}
            used = {w: sem(f"exp_{w}_used") for w in shapes}
            token_in_copied = sem("exp_token_in_copied")
            token_out_copied = sem("exp_token_out_copied")
            gathered = [phases.keep(f"exp_gathered{u}") for u in range(2)]
            turned = sem("exp_turned")
            x_hi_done = sem("exp_x_hi_done")
            x_lo_done = sem("exp_x_lo_done")
            silu_done = sem("exp_silu_done")
            prod_done = sem("exp_prod_done")
            f_turned = sem("exp_f_turned")
            f_hi_done = sem("exp_f_hi_done")
            f_lo_done = sem("exp_f_lo_done")
            gate_copied = sem("exp_gate_copied")
            y_out = sem("exp_y_out")
            y_free = sem("exp_y_free")
            scattered = phases.keep("exp_scattered")
            PAIRS = N_EXPERTS // 2
            with nc.psum_tensor("exp_turn", [P, 2, HALF], F32) as p_x, nc.psum_tensor("exp_gate", [P, 2, HALF], F32) as p_gu, \
                    nc.psum_tensor("exp_f", [P, FK, P], F32) as p_f, nc.psum_tensor("exp_y", [P, 2, HALF], F32) as p_y, nc.Block() as block:

                def pairs(eng, run):
                    with eng.Fori(0, PAIRS - 1) as i:
                        for u in range(2):
                            run(2 * i + u, u, i, False)
                    for u in range(2):
                        run(2 * (PAIRS - 1) + u, u, PAIRS - 1, u == 1)

                @block.sync
                def _(sp):
                    with sp.Fori(0, N_EXPERTS) as e:
                        for w in shapes:
                            sp.wait_ge(split[w], e + 1)
                            sp.dma_start(raw[w][:].rearrange("p (o k) n -> p o k n", o=1), src[w][:, bass.ds(e, 1)]).then_inc(loaded[w], 16)

                @block.gpsimd
                def _(pool):
                    pool.sem_inc(split["down"], 1)

                    def gather(e, slot, round_):
                        pool.wait_ge(turned, e + 1)
                        pass_waits(pool)
                        pool.tensor_copy(token_in[:, slot:slot + 1], slot_token[:, bass.ds(e, 1)]).then_inc(token_in_copied, 1)
                        pool.wait_ge(token_in_copied, e + 1)
                        pass_waits(pool)
                        pool.indirect_dma_start(xg[:, slot, :], None, h2_rows, bass.IndirectOffsetOnAxis(ap=token_in[:, slot:slot + 1], axis=0),
                                                bounds_check=SEQ - 1).then_inc(gathered[slot], 16)

                    def lo_down(e):
                        pool.wait_ge(hi_done["down"], e + 1)
                        pool.tensor_tensor(w_lo_["down"][:], raw["down"][:], w_hi_["down"][:].bitcast(F32), ALU.subtract).then_inc(split["down"], 1)

                    def scatter(e, slot):
                        pass_waits(pool)
                        pool.tensor_copy(token_out[:, slot:slot + 1], slot_token[:, bass.ds(e, 1)]).then_inc(token_out_copied, 1)
                        pool.wait_ge(token_out_copied, e + 1)
                        pool.wait_ge(y_out, e + 2)
                        if not (isinstance(e, int) and e == 0):
                            pool.wait_ge(scattered, 16 * e)
                        pool.sem_inc(y_free, 1)
                        pass_waits(pool)
                        pool.indirect_dma_start(ffn_rows, bass.IndirectOffsetOnAxis(ap=token_out[:, slot:slot + 1], axis=0), y[:, slot, :], None,
                                                bounds_check=SEQ - 1, compute_op=ALU.add).then_inc(scattered, 16)

                    pool.sem_inc(turned, 2)
                    pool.sem_inc(y_free, 1)
                    gather(0, 0, 0)
                    gather(1, 1, 0)
                    lo_down(0)
                    gather(2, 0, 1)
                    lo_down(1)
                    scatter(0, 0)
                    with pool.Fori(1, PAIRS - 1) as i:
                        for u in range(2):
                            gather(2 * i + u + 1, (u + 1) % 2, i + u)
                            lo_down(2 * i + u)
                            scatter(2 * i + u - 1, (u + 1) % 2)
                    for e in (N_EXPERTS - 2, N_EXPERTS - 1):
                        if e + 1 < N_EXPERTS:
                            gather(e + 1, (e + 1) % 2, (e + 1) // 2)
                        lo_down(e)
                        scatter(e - 1, (e - 1) % 2)
                    scatter(N_EXPERTS - 1, 1)
                    pool.wait_ge(scattered, 16 * N_EXPERTS)

                @block.tensor
                def _(pe):
                    for w in shapes:
                        pe.sem_inc(used[w], 1)

                    def turn(e, slot, round_):
                        pe.wait_ge(gathered[slot], 16 * (round_ + 1))
                        pe.wait_ge(x_lo_done, e + 1)
                        for kt in range(KT):
                            ins = pe.transpose(p_x[:, kt // 4, (kt % 4) * P:(kt % 4 + 1) * P], xg[:, slot, kt * P:(kt + 1) * P], ident)
                        ins.then_inc(turned, 1)

                    def product(to, w, x_parts, kts, cols):
                        for kt in range(kts):
                            for x, part, first, last in ((x_parts[0], w_hi_, kt == 0, False), (x_parts[1], w_hi_, False, False),
                                                         (x_parts[0], w_lo_, False, kt == kts - 1)):
                                ins = pe.matmul(to, x[:, kt, :], part[w][:, kt, cols], start=first, stop=last)
                        return ins

                    def run(e, slot, round_, last):
                        pe.wait_ge(x_lo_done, e + 2)
                        pe.wait_ge(prod_done, e + 1)
                        for b, w in enumerate(("gate", "up")):
                            pe.wait_ge(split[w], e + 2)
                            product(p_gu[:, b, :], w, (x_hi, x_lo), KT, slice(None)).then_inc(used[w], 1)
                        if not last:
                            turn(e + 1, 1 - slot, round_ + slot)
                        pe.wait_ge(prod_done, e + 2)
                        pe.wait_ge(f_lo_done, e + 1)
                        for kt in range(FK):
                            ins = pe.transpose(p_f[:, kt, :], prod[:, kt * P:(kt + 1) * P], ident)
                        ins.then_inc(f_turned, 1)
                        pe.wait_ge(f_lo_done, e + 2)
                        pe.wait_ge(split["down"], e + 2)
                        pe.wait_ge(y_out, e + 1)
                        for half in range(2):
                            ins = product(p_y[:, half, :], "down", (f_hi, f_lo), FK, slice(half * HALF, (half + 1) * HALF))
                        ins.then_inc(used["down"], 1)

                    turn(0, 0, 0)
                    pairs(pe, run)

                @block.scalar
                def _(act):
                    def hi(w, e):
                        act.wait_ge(loaded[w], 16 * (e + 1))
                        act.wait_ge(used[w], e + 1)
                        act.copy(w_hi_[w][:], raw[w][:]).then_inc(hi_done[w], 1)

                    def hi_x(e):
                        act.wait_ge(turned, e + 3)
                        act.copy(x_hi[:].rearrange("p (a k) n -> p a (k n)", a=2), p_x[:]).then_inc(x_hi_done, 1)

                    def run(e, slot, round_, last):
                        act.wait_ge(used["gate"], e + 2)
                        act.wait_ge(prod_done, e + 1)
                        act.activation(silu[:], p_gu[:, 0, :], ACT.Silu).then_inc(silu_done, 1)
                        if not last:
                            hi("gate", e + 1)
                            hi_x(e + 1)
                        act.wait_ge(f_turned, e + 1)
                        act.copy(f_hi[:], p_f[:]).then_inc(f_hi_done, 1)
                        if not last:
                            hi("up", e + 1)
                            hi("down", e + 1)

                    hi("gate", 0)
                    hi_x(0)
                    hi("up", 0)
                    hi("down", 0)
                    pairs(act, run)

                @block.vector
                def _(dve):
                    dve.sem_inc(split["gate"], 1)
                    dve.sem_inc(split["up"], 1)
                    dve.sem_inc(x_lo_done, 1)
                    dve.sem_inc(prod_done, 1)
                    dve.sem_inc(f_lo_done, 1)
                    dve.sem_inc(y_out, 1)
                    dve.sem_inc(gate_copied, 1)

                    def lo(w, e):
                        dve.wait_ge(hi_done[w], e + 1)
                        dve.tensor_tensor(w_lo_[w][:], raw[w][:], w_hi_[w][:].bitcast(F32), ALU.subtract).then_inc(split[w], 1)

                    def lo_x(e):
                        dve.wait_ge(x_hi_done, e + 1)
                        dve.tensor_tensor(x_lo[:].rearrange("p (a k) n -> p a (k n)", a=2), p_x[:],
                                          x_hi[:].rearrange("p (a k) n -> p a (k n)", a=2).bitcast(F32), ALU.subtract).then_inc(x_lo_done, 1)

                    def run(e, slot, round_, last):
                        dve.wait_ge(silu_done, e + 1)
                        dve.wait_ge(used["up"], e + 2)
                        dve.tensor_tensor(prod[:], silu[:], p_gu[:, 1, :], ALU.mult).then_inc(prod_done, 1)
                        if not last:
                            lo_x(e + 1)
                        dve.wait_ge(f_hi_done, e + 1)
                        dve.tensor_tensor(f_lo[:], p_f[:], f_hi[:].bitcast(F32), ALU.subtract).then_inc(f_lo_done, 1)
                        if not last:
                            lo("gate", e + 1)
                            lo("up", e + 1)
                        pass_waits(dve)
                        dve.tensor_scalar(gate_now[:, slot:slot + 1], slot_gate[:, bass.ds(e, 1)], 0.0, None, ALU.add).then_inc(gate_copied, 1)
                        dve.wait_ge(gate_copied, e + 2)
                        dve.wait_ge(used["down"], e + 2)
                        dve.wait_ge(y_free, e + 1)
                        dve.tensor_scalar(y[:, slot, :], p_y[:].rearrange("p a b -> p (a b)"), gate_now[:, slot:slot + 1], None,
                                          ALU.mult).then_inc(y_out, 1)

                    lo("gate", 0)
                    lo_x(0)
                    lo("up", 0)
                    pairs(dve, run)

        phase_norm("norm2", Arena(nc, route_mem.at), "stream", [(0, SEQ, lambda kt: gain2[:, kt:kt + 1], lambda kt: mod[:, SH2 + kt, 0:1])],
                   SEQ, h_plain=h2_cm)
        phase_router()
        phase_experts()

        top = nc.sbuf_usable_end // 32 * 32
        h_split = Arena(nc, top - 2 * KT * SEQ * 4)
        h_hi = h_split("h_hi", [P, KT, SEQ], F32R)
        h_lo = h_split("h_lo", [P, KT, SEQ], F32R)
        y_split = Arena(nc, top - 4 * KT * SEQ * 4)
        y_hi = y_split("y_hi", [P, KT, SEQ], F32R)
        y_lo = y_split("y_lo", [P, KT, SEQ], F32R)
        work_end = top - 4 * KT * SEQ * 4
        BOTH = [(0, 0, HALF), (1, HALF, HALF)]

        def weight_cols(w, first_row=0):
            src = w.rearrange("o (k p) n -> p (o k) n", p=P)
            return lambda u, cols: [(w_raw[:, u], src[:, first_row // P:first_row // P + KT, cols])]

        def out_weights(w, first_row):
            part = weight_cols(w, first_row)
            return lambda n: part(n % 2, slice(n * P, (n + 1) * P))

        def phase_pool():
            phases.start()
            mem = Arena(nc, free_at)
            PAD, G = max(POOL_SIZES), len(POOL_SIZES)
            a_pad = mem("pool_a", [P, 2, PAD + SEQ])
            sums = mem("pool_sums", [P, 2, PAD + SEQ])
            pooled = mem("pool_pooled", [P, 2, SEQ])
            silu = mem("pool_silu", [P, 2, SEQ])
            y = mem("pool_y", [P, 2, SEQ])
            w_pool = mem("pool_w", [P, 2, 2, 2 * P])
            assert mem.at <= work_end
            ring = Ring("pool")
            z_out = sem("pool_z_out")
            w_loaded = [sem(f"pool_matrix_loaded{u}") for u in range(2)]
            pooled_done = sem("pool_pooled_done")
            mixed_done = sem("pool_mixed_done")
            y_done = sem("pool_y_done")
            hi_done = sem("pool_hi_done")
            lo_done = sem("pool_lo_done")
            cleared = sem("pool_cleared")
            dve_step = sem("pool_dve_step")
            w_cols = weight_cols(A["even_w_in_2"])
            src_pool = A["even_pool_w_2"].rearrange("o g (k p) n -> p (o g) k n", p=P)
            with nc.psum_tensor("pool_z", [P, 2, 2, HALF], F32) as z, nc.psum_tensor("pool_mixed", [P, 2, 2, HALF], F32) as mixed, nc.Block() as block:
                @block.sync
                def _(sp):
                    with sp.Fori(0, G // 2) as i:
                        for s in range(2):
                            g = 2 * i + s
                            sp.wait_ge(mixed_done, g + 1)
                            sp.dma_start(w_pool[:, s].rearrange("p (o k) n -> p o k n", o=1), src_pool[:, bass.ds(g, 1)]).then_inc(w_loaded[s], 16)
                            for t in range(4):
                                ring.load(sp, 4 * g + t, t % 2, w_cols(t % 2, bass.ds(g * 2 * P + (t // 2) * D + (t % 2) * P, P)))

                @block.gpsimd
                def _(pool):
                    ring.credits(pool, None)
                    with pool.Fori(0, G) as g:
                        for t in range(4):
                            ring.do_split(pool, 4 * g + t, t % 2, 2 * g + t // 2)

                @block.tensor
                def _(pe):
                    ring.credits(None, pe)
                    pe.sem_inc(mixed_done, 2)
                    with pe.Fori(0, G // 2) as i:
                        for s in range(2):
                            g = 2 * i + s
                            for t in range(4):
                                ring.project(pe, 4 * g + t, t % 2, z_out, [(z[:, t % 2, b, :], c0, w) for b, c0, w in BOTH], h_hi, h_lo)
                            pe.wait_ge(w_loaded[s], 16 * (i + 1))
                            pe.wait_ge(pooled_done, 2 * g + 2)
                            pe.wait_ge(y_done, 2 * g + 2)
                            for d in range(2):
                                for b, c0, w in BOTH:
                                    for k in range(2):
                                        ins = pe.matmul(mixed[:, d, b, :], w_pool[:, s, k, d * P:(d + 1) * P], pooled[:, k, c0:c0 + w],
                                                        start=(k == 0), stop=(k == 1))
                            ins.then_inc(mixed_done, 1)

                @block.scalar
                def _(act):
                    act.sem_inc(z_out, 2)
                    act.wait_ge(cleared, 1)
                    for g in range(G):
                        for t in range(4):
                            act.wait_ge(ring.projected, 4 * g + t + 3)
                            tile = z[:, t % 2].rearrange("p b n -> p (b n)")
                            if t < 2:
                                if g:
                                    act.wait_ge(pooled_done, 2 * (g - 1) + t + 1)
                                act.copy(a_pad[:, t, PAD:], tile).then_inc(z_out, 1)
                            else:
                                act.wait_ge(y_done, 2 * g + t - 2 + 1)
                                act.activation(silu[:, t - 2, :], tile, ACT.Silu).then_inc(z_out, 1)
                        for d in range(2):
                            act.wait_ge(y_done, 2 * g + d + 3)
                            act.copy(y_hi[:, 2 * g + d, :], y[:, d, :]).then_inc(hi_done, 1)

                @block.vector
                def _(dve):
                    step = Steps(dve, dve_step)
                    dve.sem_inc(y_done, 2)
                    step(dve.memset(a_pad[:], 0.0))
                    step(dve.memset(sums[:], 0.0))
                    step.wait()
                    dve.sem_inc(cleared, 1)
                    for g, w in enumerate(POOL_SIZES):
                        for t in range(2):
                            dve.wait_ge(z_out, 4 * g + t + 3)
                            now = a_pad[:, t]
                            for k in range(g + 1):
                                nxt = sums[:, k % 2]
                                step(dve.tensor_tensor(nxt[:, PAD:], now[:, PAD:], now[:, PAD - (1 << k):PAD + SEQ - (1 << k)], ALU.add))
                                step.wait()
                                now = nxt
                            dve.wait_ge(mixed_done, g + 2)
                            head = pooled[:, t, 0:PAD]
                            step(dve.tensor_tensor(head, now[:, PAD:2 * PAD], cst("pool_inv")[:, g * PAD:(g + 1) * PAD], ALU.mult))
                            step.wait()
                            step(dve.tensor_tensor(head, head, a_pad[:, t, PAD:2 * PAD], ALU.subtract))
                            step.wait()
                            dve.scalar_tensor_tensor(out=pooled[:, t, PAD:], in0=now[:, 2 * PAD:], scalar=1.0 / w, in1=a_pad[:, t, 2 * PAD:],
                                                     op0=ALU.mult, op1=ALU.subtract).then_inc(pooled_done, 1)
                            dve.wait_ge(pooled_done, 2 * g + t + 1)
                        dve.wait_ge(mixed_done, g + 3)
                        for d in range(2):
                            dve.wait_ge(z_out, 4 * g + 2 + d + 3)
                            if g:
                                dve.wait_ge(lo_done, 2 * (g - 1) + d + 1)
                            dve.scalar_tensor_tensor(out=y[:, d, :], in0=mixed[:, d].rearrange("p b n -> p (b n)"),
                                                     scalar=pa("even_pool_scale_2")[:, 2 * g + d:2 * g + d + 1], in1=silu[:, d, :],
                                                     op0=ALU.mult, op1=ALU.mult).then_inc(y_done, 1)
                        for d in range(2):
                            dve.wait_ge(hi_done, 2 * g + d + 1)
                            dve.tensor_tensor(y_lo[:, 2 * g + d, :], y[:, d, :], y_hi[:, 2 * g + d, :].bitcast(F32), ALU.subtract).then_inc(lo_done, 1)

        def phase_spatial():
            phases.start()
            mem = Arena(nc, free_at)
            G, U_AT, V_AT, B_AT = 4, 2 * D, 3 * D, 4 * D
            ws = mem("spat_ws", [P, G, CHUNK])
            ws_low = mem("spat_ws_low", [P, G, CHUNK])
            ws_t = mem("spat_ws_t", [P, G, CHUNK])
            bias = mem("spat_bias", [1, G, 4, CHUNK])
            v_cm = mem("spat_v_cm", [P, SEQ])
            v_rows_ = mem("spat_v_rows", [P, XCH, P])
            u_cm = mem("spat_u_cm", [P, SEQ])
            silu = mem("spat_silu", [P, SEQ])
            gated = mem("spat_gated", [P, SEQ])
            y = mem("spat_y", [P, SEQ])
            assert mem.at <= work_end
            ring = Ring("spat")
            z_out = sem("spat_z_out")
            loaded = sem("spat_loaded")
            masked = sem("spat_masked")
            ws_turned = sem("spat_ws_turned")
            ws_ready = sem("spat_ws_ready")
            v_turned = sem("spat_v_turned")
            rows_out = sem("spat_rows_out")
            gated_done = sem("spat_gated_done")
            mixed_done = sem("spat_mixed_done")
            y_done = sem("spat_y_done")
            hi_done = sem("spat_hi_done")
            lo_done = sem("spat_lo_done")
            w_cols = weight_cols(A["even_w_in_2"])
            with nc.psum_tensor("spat_z", [P, 2, 2, HALF], F32) as z, nc.psum_tensor("spat_turn", [P, 2, HALF], F32) as turn, \
                    nc.psum_tensor("spat_mixed", [P, 2, HALF], F32) as mixed, nc.Block() as block:
                @block.sync
                def _(sp):
                    sp.dma_start(ws[:], A["even_ws_2"].rearrange("o g t s -> t (o g) s")).then_inc(loaded, 16)
                    for r in range(4):
                        sp.dma_start(bias[:, :, r, :], A["even_bs_2"]).then_inc(loaded, 16)
                    with sp.Fori(0, G) as i:
                        for s in range(2):
                            for t, col in enumerate((V_AT, B_AT, U_AT)):
                                m = 3 * s + t
                                ring.load(sp, 6 * i + m, m % 2, w_cols(m % 2, bass.ds(i * 2 * P + s * P + col, P)))

                @block.gpsimd
                def _(pool):
                    ring.credits(pool, None)
                    pool.wait_ge(loaded, 16 * 5)
                    pool.affine_select(ws_low[:], ws[:], [[0, G], [-1, CHUNK]], ALU.is_ge, 0.0, base=0, channel_multiplier=1).then_inc(masked, 1)
                    with pool.Fori(0, G) as i:
                        for m in range(6):
                            ring.do_split(pool, 6 * i + m, m % 2, 3 * i + m // 2)

                @block.tensor
                def _(pe):
                    ring.credits(None, pe)
                    pe.wait_ge(masked, 1)
                    for g in range(G):
                        ins = pe.transpose(turn[:, 0, g * CHUNK:(g + 1) * CHUNK], ws_low[:, g, :], ident)
                    ins.then_inc(ws_turned, 1)

                    def proj(n, m):
                        ring.project(pe, n, m % 2, z_out, [(z[:, m % 2, b, :], c0, w) for b, c0, w in BOTH], h_hi, h_lo)

                    with pe.Fori(0, G) as i:
                        for s in range(2):
                            c = 2 * i + s
                            proj(6 * i + 3 * s, 3 * s)
                            proj(6 * i + 3 * s + 1, 3 * s + 1)
                            pe.wait_ge(z_out, 6 * i + 3 * s + 3)
                            pe.wait_ge(rows_out, c + 1)
                            for j in range(XCH):
                                ins = pe.transpose(turn[:, j // 4, (j % 4) * P:(j % 4 + 1) * P], v_cm[:, j * P:(j + 1) * P], ident)
                            ins.then_inc(v_turned, 1)
                            proj(6 * i + 3 * s + 2, 3 * s + 2)
                            pe.wait_ge(rows_out, c + 2)
                            pe.wait_ge(y_done, c + 1)
                            pass_waits(pe)
                            for b in range(2):
                                pe.matmul(mixed[:, b, :], ones[0:1, :], bias[:, bass.ds(i, 1), :, :].rearrange("p o r t -> p (o r t)"), start=True, stop=False)
                                for j in range(4):
                                    ins = pe.matmul(mixed[:, b, j * CHUNK:(j + 1) * CHUNK], v_rows_[:, 4 * b + j, :],
                                                    ws_t[:, bass.ds(i, 1), :].rearrange("p o t -> p (o t)"), start=False, stop=(j == 3))
                            ins.then_inc(mixed_done, 1)

                @block.scalar
                def _(act):
                    act.sem_inc(z_out, 2)
                    with act.Fori(0, G) as i:
                        for s in range(2):
                            c = 2 * i + s
                            for t, to in enumerate((v_cm, silu, u_cm)):
                                m = 3 * s + t
                                act.wait_ge(ring.projected, 6 * i + m + 3)
                                if t == 0:
                                    act.wait_ge(v_turned, c + 1)
                                else:
                                    act.wait_ge(gated_done, c + 1)
                                act.activation(to[:], z[:, m % 2].rearrange("p b n -> p (b n)"), ACT.Silu if t == 1 else ACT.Copy).then_inc(z_out, 1)
                            act.wait_ge(y_done, c + 2)
                            pass_waits(act)
                            act.copy(y_hi[:, bass.ds(c, 1), :].rearrange("p o t -> p (o t)"), y[:]).then_inc(hi_done, 1)

                @block.vector
                def _(dve):
                    dve.sem_inc(v_turned, 1)
                    dve.sem_inc(gated_done, 1)
                    dve.sem_inc(y_done, 1)
                    dve.sem_inc(lo_done, 1)
                    dve.wait_ge(ws_turned, 1)
                    dve.tensor_copy(ws_t[:], turn[:, 0, :].rearrange("p (g t) -> p g t", g=G)).then_inc(rows_out, 1)
                    with dve.Fori(0, G) as i:
                        for s in range(2):
                            c = 2 * i + s
                            dve.wait_ge(v_turned, c + 2)
                            dve.tensor_copy(v_rows_[:].rearrange("p (a j) n -> p a (j n)", a=2), turn[:]).then_inc(rows_out, 1)
                            dve.wait_ge(z_out, 6 * i + 3 * s + 2 + 3)
                            dve.wait_ge(y_done, c + 1)
                            dve.tensor_tensor(gated[:], u_cm[:], silu[:], ALU.mult).then_inc(gated_done, 1)
                            dve.wait_ge(mixed_done, c + 1)
                            dve.wait_ge(gated_done, c + 2)
                            dve.wait_ge(lo_done, c + 1)
                            dve.tensor_tensor(y[:], mixed[:].rearrange("p b n -> p (b n)"), gated[:], ALU.mult).then_inc(y_done, 1)
                            dve.wait_ge(hi_done, c + 1)
                            at = bass.ds(c, 1)
                            dve.tensor_tensor(y_lo[:, at, :].rearrange("p o t -> p (o t)"), y[:], y_hi[:, at, :].rearrange("p o t -> p (o t)").bitcast(F32),
                                              ALU.subtract).then_inc(lo_done, 1)

        phase_norm("even", Arena(nc, free_at), "stream+ffn", [(0, SEQ, plain_gain("even_norm_2"), None)], SEQ, h_hi, h_lo)
        phase_pool()
        phase_out("even_a_out", Arena(nc, free_at), y_hi, y_lo, out_weights(A["even_w_out_2"], 0), 1, None)
        phase_spatial()
        phase_out("even_b_out", Arena(nc, free_at), y_hi, y_lo, out_weights(A["even_w_out_2"], D), 1, None)

        odd_cols = weight_cols(A["odd_w_in_2"])
        GC_COL = 3 * N_DIL * C_SLOTS * P
        DB_COL, DC_COL, DX_COL, GD_COL = (GC_COL + (1 + k) * D for k in range(4))

        def phase_conv():
            phases.start()
            mem = Arena(nc, free_at)
            PAD, TAPS = 2, 3
            taken = [mem(f"conv_{name}", [P, SEQ]) for name in ("c", "x", "silu", "b")]
            c_cm, x_cm_, silu, b_cm = taken
            prod = mem("conv_prod", [P, PAD + SEQ])
            acc = mem("conv_acc", [P, SEQ])
            gated = mem("conv_gated", [P, SEQ])
            y = mem("conv_y", [P, SEQ])
            taps = mem("gated_conv_taps", [P, TAPS, 1])
            assert mem.at <= work_end
            ring = Ring("conv")
            z_out = sem("conv_z_out")
            taken_used = sem("conv_taken_used")
            y_done = sem("conv_y_done")
            hi_done = sem("conv_hi_done")
            lo_done = sem("conv_lo_done")
            dve_step = sem("conv_dve_step")
            with nc.psum_tensor("conv_z", [P, 2, 2, HALF], F32) as z, nc.Block() as block:
                @block.sync
                def _(sp):
                    with sp.Fori(0, KT) as c:
                        for t, col in enumerate((DC_COL, DX_COL, GD_COL, DB_COL)):
                            ring.load(sp, 4 * c + t, t % 2, odd_cols(t % 2, bass.ds(c * P + col, P)))

                @block.gpsimd
                def _(pool):
                    ring.credits(pool, None)
                    with pool.Fori(0, KT) as c:
                        for t in range(4):
                            ring.do_split(pool, 4 * c + t, t % 2, 2 * c + t // 2)

                @block.tensor
                def _(pe):
                    ring.credits(None, pe)
                    with pe.Fori(0, KT) as c:
                        for t in range(4):
                            ring.project(pe, 4 * c + t, t % 2, z_out, [(z[:, t % 2, b, :], c0, w) for b, c0, w in BOTH], h_hi, h_lo)

                @block.scalar
                def _(act):
                    act.sem_inc(z_out, 2)
                    with act.Fori(0, KT) as c:
                        for t, to in enumerate(taken):
                            act.wait_ge(ring.projected, 4 * c + t + 3)
                            act.wait_ge(taken_used, c + 1)
                            act.activation(to[:], z[:, t % 2].rearrange("p b n -> p (b n)"), ACT.Silu if to is silu else ACT.Copy).then_inc(z_out, 1)
                        act.wait_ge(y_done, c + 1)
                        pass_waits(act)
                        act.copy(y_hi[:, bass.ds(c, 1), :].rearrange("p o t -> p (o t)"), y[:]).then_inc(hi_done, 1)

                @block.vector
                def _(dve):
                    dve.memset(prod[:], 0.0).then_inc(dve_step, 1)
                    dve.wait_ge(dve_step, 1)
                    dve.sem_inc(taken_used, 1)
                    N_STEP = TAPS + 3
                    with dve.Fori(0, KT) as c:
                        step = Steps(dve, dve_step, N_STEP * c + 1)
                        step.wait()
                        pass_waits(dve)
                        step(dve.tensor_copy(taps[:], pb("odd_conv_w_2").rearrange("p (j c) -> p j c", j=TAPS)[:, :, bass.ds(c, 1)]))
                        dve.wait_ge(z_out, 4 * c + 1 + 3)
                        step(dve.tensor_tensor(prod[:, PAD:], c_cm[:], x_cm_[:], ALU.mult))
                        step.wait()
                        step(dve.tensor_scalar(acc[:], prod[:, 0:SEQ], taps[:, 0, :], None, ALU.mult))
                        step.wait()
                        for j in range(1, TAPS):
                            step(dve.scalar_tensor_tensor(out=acc[:], in0=prod[:, j:j + SEQ], scalar=taps[:, j, :], in1=acc[:], op0=ALU.mult, op1=ALU.add))
                            step.wait()
                        dve.wait_ge(z_out, 4 * c + 3 + 3)
                        step(dve.tensor_tensor(gated[:], b_cm[:], silu[:], ALU.mult))
                        step.wait()
                        dve.sem_inc(taken_used, 1)
                        assert step.done == N_STEP
                        dve.tensor_tensor(y[:], acc[:], gated[:], ALU.mult).then_inc(y_done, 1)
                        dve.wait_ge(hi_done, c + 1)
                        at = bass.ds(c, 1)
                        dve.tensor_tensor(y_lo[:, at, :].rearrange("p o t -> p (o t)"), y[:], y_hi[:, at, :].rearrange("p o t -> p (o t)").bitcast(F32),
                                          ALU.subtract).then_inc(lo_done, 1)
                        dve.wait_ge(lo_done, c + 1)

        y_plain = Arena(nc, top - 3 * KT * SEQ * 4)("y_plain", [P, KT, SEQ])

        def phase_dilated():
            phases.start()
            mem = Arena(nc, free_at)
            q_cm_ = mem("dil_q", [P, N_DIL, SEQ])
            k_cm_ = mem("dil_k", [P, N_DIL, SEQ])
            v_cm = mem("dil_v", [P, SEQ])
            v_rows_ = mem("dil_v_rows", [P, N_DIL, BLOCKS, P])
            silu = mem("dil_silu", [P, SEQ])
            biased = mem("dil_biased", [P, 2, 2 * P])
            p_t = mem("dil_p_t", [P, 2, 2 * P])
            NU = N_DIL * BLOCKS
            neg_max = mem("dil_neg_max", [P, NU])
            den = mem("dil_den", [P, NU])
            log_den = mem("dil_log_den", [P, NU])
            lse = mem("dil_lse", [P, NU])
            slope_now = mem("dil_slope_now", [P, N_DIL, 1])
            joint = mem("dil_joint", [P, N_DIL, 8])
            joint_max = mem("dil_joint_max", [P, 8])
            joint_sum = mem("dil_joint_sum", [P, 8])
            share = mem("dil_share", [P, NU])

            units = []
            for g in range(N_DIL):
                for b in range(BLOCKS):
                    has_prev = (b > 0, b % 2 == 1, False)[g]
                    units.append((g, b, b - 1 if has_prev else b, 2 if has_prev else 1))
            probs = [mem(f"dil_p{u}", [P, n * P]) for u, (_, _, _, n) in enumerate(units)]
            assert mem.at <= top - 3 * KT * SEQ * 4
            ring = Ring("dil")
            z_out = sem("dil_z_out")
            scores = sem("dil_scores")
            bias_done = sem("dil_bias_done")
            max_done = sem("dil_max_done")
            exp_done = sem("dil_exp_done")
            aux_free = [sem(f"dil_aux_free{b}") for b in range(2)]
            log_done = sem("dil_log_done")
            lse_done = sem("dil_lse_done")
            lse_stored = sem("dil_lse_stored")
            joint_loaded = sem("dil_joint_loaded")
            joint_shifted = sem("dil_joint_shifted")
            joint_exp = sem("dil_joint_exp")
            share_done = sem("dil_share_done")
            share_stored = sem("dil_share_stored")
            share_loaded = sem("dil_share_loaded")
            factor_done = sem("dil_factor_done")
            scaled = sem("dil_scaled")
            v_turned = sem("dil_v_turned")
            rows_out = sem("dil_rows_out")
            p_turned = sem("dil_p_turned")
            p_t_out = sem("dil_p_t_out")
            summed = sem("dil_summed")
            y_done = sem("dil_y_done")
            dve_step = sem("dil_dve_step")
            NT = 3 * N_DIL + 1
            cols = [first + g * D for g in range(N_DIL) for first in (N_DIL * D, 0)] + [2 * N_DIL * D + g * D for g in range(N_DIL)] + [GC_COL]
            VT, GT = 2 * N_DIL, 3 * N_DIL
            AUX = NU + 2 * N_DIL + NU

            def reordered(x, g):
                r = DILATION[g]
                return x.rearrange("p (r b m) -> p b m r", r=r, b=2) if g else x.rearrange("p (b m) -> p b m", b=2)

            def in_banks(x, g):
                return x.rearrange("p b (m r) -> p b m r", r=DILATION[g]) if g else x

            def token_order(row, tile, g):
                if g == 0:
                    return [(row.rearrange("(b p) -> p b", p=P), tile)]
                if g == 1:
                    return [(row.rearrange("(m p r) -> p r m", p=P, r=4)[:, r, :], tile[:, 2 * r:2 * r + 2]) for r in range(4)]
                by_half = row.rearrange("(i b a) -> a i b", b=8, a=2)
                return [(by_half[a], tile[a * 64:(a + 1) * 64, :]) for a in range(2)]

            moves = sum(len(token_order(stat_dram[0, g], share[:, 0:8], g)) for g in range(N_DIL))

            with nc.psum_tensor("dil_z", [P, 2, 2, HALF], F32) as z, nc.psum_tensor("dil_aux", [P, 2, HALF], F32) as aux, \
                    nc.psum_tensor("dil_acc", [P, 2, HALF], F32) as acc, nc.Block() as block:
                @block.sync
                def _(sp):
                    with sp.Fori(0, C_SLOTS) as h:
                        for t in range(NT):
                            ring.load(sp, NT * h + t, t % 2, odd_cols(t % 2, bass.ds(h * P + cols[t], P)))

                @block.gpsimd
                def _(pool):
                    ring.credits(pool, None)
                    with pool.Fori(0, C_SLOTS) as h:
                        for t in range(NT):
                            ring.do_split(pool, NT * h + t, t % 2, NT // 2 * h + t // 2)

                @block.tensor
                def _(pe):
                    ring.credits(None, pe)
                    with pe.Fori(0, C_SLOTS) as h:
                        uses = [0]

                        def take_aux():
                            a = uses[0]
                            pe.wait_ge(aux_free[a % 2], AUX // 2 * h + a // 2 + 1)
                            uses[0] += 1
                            return aux[:, a % 2, :]

                        def score(u):
                            g, b, k0, n = units[u]
                            to = take_aux()
                            pe.wait_ge(z_out, NT * h + 2 * g + 2 + 2)
                            pe.matmul(to[:, 0:n * P], q_cm_[:, g, b * P:(b + 1) * P], k_cm_[:, g, k0 * P:(k0 + n) * P], start=True, stop=True).then_inc(scores, 1)

                        def proj(t, first_unit=None):
                            between = None
                            if first_unit is not None:
                                between = {2 * k + 1: (lambda u=first_unit + k: score(u)) for k in range(4)}
                            ring.project(pe, NT * h + t, t % 2, z_out, [(z[:, t % 2, b, :], c0, w) for b, c0, w in BOTH], h_hi, h_lo, between)

                        def turn_v(g):
                            pe.wait_ge(z_out, NT * h + VT + g + 3)
                            for half in range(2):
                                to = take_aux()
                                for j in range(4):
                                    at = (4 * half + j) * P
                                    ins = pe.transpose(to[:, j * P:(j + 1) * P], v_cm[:, at:at + P], ident)
                                ins.then_inc(v_turned, 1)

                        def turn_p(u):
                            to = take_aux()
                            pe.wait_ge(scaled, NU * h + u + 1)
                            for j in range(units[u][3]):
                                ins = pe.transpose(to[:, j * P:(j + 1) * P], probs[u][:, j * P:(j + 1) * P], ident)
                            ins.then_inc(p_turned, 1)

                        def weigh_v(u):
                            g, b, k0, n = units[u]
                            pe.wait_ge(p_t_out, NU * h + u + 1)
                            for j in range(n):
                                pt = p_t[:, u % 2, j * P:(j + 1) * P]
                                v = v_rows_[:, g, k0 + j, :]
                                if g == 0:
                                    ins = pe.matmul(acc[:, b // 4, (b % 4) * P:(b % 4 + 1) * P], v, pt, start=False, stop=False)
                                elif g == 1:
                                    ins = pe.matmul(acc[:, b % 2, :].rearrange("p (m r) -> p r m", r=4)[:, b // 2, :], v, pt, start=False, stop=False)
                                else:
                                    for bank in range(2):
                                        to = acc[:, bank, :].rearrange("p (i c a) -> p c a i", c=8, a=2)[:, b]
                                        ins = pe.matmul(to, v, pt.rearrange("p (a s i) -> p s a i", a=2, s=2)[:, bank], start=False, stop=(b == BLOCKS - 1))
                            ins.then_inc(summed, 1)

                        for t in range(2):
                            proj(t)
                        for t in range(6):
                            proj(2 + t, 4 * t)
                        turn_v(0)
                        proj(VT + 2)
                        turn_v(1)
                        proj(GT)
                        turn_v(2)
                        turn_p(0)
                        pe.wait_ge(y_done, h + 1)
                        for bank in range(2):
                            pe.matmul(acc[:, bank, :], ones[0:1, :], zero_col[0:1, :].to_broadcast([1, HALF]), start=True, stop=False)
                        pe.wait_ge(rows_out, 6 * h + 6)
                        for u in range(NU):
                            if u + 1 < NU:
                                turn_p(u + 1)
                            weigh_v(u)
                        assert uses[0] == AUX

                @block.scalar
                def _(act):
                    act.sem_inc(z_out, 2)
                    with act.Fori(0, C_SLOTS) as h:
                        def take(t, to):
                            act.wait_ge(ring.projected, NT * h + t + 3)
                            act.activation(to, in_banks(z[:, t % 2], t // 2) if t < VT else in_banks(z[:, t % 2], t - VT), ACT.Copy,
                                           scale=P ** -0.5 if t < VT and t % 2 else 1.0).then_inc(z_out, 1)

                        def exps(u0):
                            for u in range(u0, u0 + 4):
                                w = units[u][3] * P
                                act.wait_ge(max_done, NU * h + u + 1)
                                act.activation(probs[u][:], biased[:, u % 2, 0:w], ACT.Exp, bias=neg_max[:, u:u + 1],
                                               accum_out=den[:, u:u + 1]).then_inc(exp_done, 1)

                        for t in range(2 * N_DIL):
                            if t >= 2:
                                exps(4 * (t - 2))
                            take(t, reordered((q_cm_ if t % 2 else k_cm_)[:, t // 2, :], t // 2))
                        for g in range(N_DIL):
                            if g < 2:
                                exps(16 + 4 * g)
                            if g == 2:
                                act.wait_ge(exp_done, NU * h + NU + 2)
                                act.activation(log_den[:], den[:], ACT.Ln).then_inc(log_done, 1)
                                act.wait_ge(lse_done, h + 1)
                                for q in range(N_DIL):
                                    for row, tile in token_order(stat_dram[0, q], lse[:, 8 * q:8 * q + 8], q):
                                        act.dma_start(row, tile, allow_slow_non_contiguous=True).then_inc(lse_stored, 16)
                                act.wait_ge(lse_stored, 16 * moves * (h + 1))
                                act.dma_start(joint[:], stat_dram[0].rearrange("q (p j) -> p q j", j=8)).then_inc(joint_loaded, 16)
                                act.wait_ge(joint_shifted, h + 1)
                                act.activation(joint[:], joint[:], ACT.Exp).then_inc(joint_exp, 1)
                                act.wait_ge(share_done, h + 1)
                                act.dma_start(factor_dram.rearrange("q (p j) -> p q j", j=8), joint[:]).then_inc(share_stored, 16)
                                act.wait_ge(share_stored, 16 * (h + 1))
                                for q in range(N_DIL):
                                    for row, tile in token_order(factor_dram[q], share[:, 8 * q:8 * q + 8], q):
                                        act.dma_start(tile, row, allow_slow_non_contiguous=True).then_inc(share_loaded, 16)
                            act.wait_ge(v_turned, 6 * h + 2 * g)
                            take(VT + g, reordered(v_cm[:], g))
                        act.wait_ge(ring.projected, NT * h + GT + 3)
                        act.wait_ge(y_done, h + 1)
                        act.activation(silu[:], z[:, GT % 2].rearrange("p b n -> p (b n)"), ACT.Silu).then_inc(z_out, 1)
                        act.wait_ge(factor_done, h + 1)
                        for u in range(NU):
                            act.activation(probs[u][:], probs[u][:], ACT.Copy, scale=share[:, u:u + 1]).then_inc(scaled, 1)

                @block.vector
                def _(dve):
                    for b in range(2):
                        dve.sem_inc(aux_free[b], 1)
                    dve.sem_inc(exp_done, 2)
                    dve.sem_inc(y_done, 1)
                    dve.sem_inc(dve_step, 1)
                    N_STEP = 10
                    with dve.Fori(0, C_SLOTS) as h:
                        step = Steps(dve, dve_step, N_STEP * h + 1)
                        uses = 0
                        step.wait()
                        pass_waits(dve)
                        step(dve.tensor_copy(slope_now[:], cst("slopes").rearrange("p (g s) -> p g s", g=N_DIL)[:, :, bass.ds(h, 1)]))
                        step.wait()
                        for u, (g, b, k0, n) in enumerate(units):
                            w = n * P
                            dist = cst("dist16") if g == 2 else cst("dist")[:, (2 - n) * P:]
                            dve.wait_ge(scores, NU * h + u + 1)
                            dve.wait_ge(exp_done, NU * h + u + 1)
                            dve.scalar_tensor_tensor(out=biased[:, u % 2, 0:w], in0=dist, scalar=slope_now[:, g, :], in1=aux[:, uses % 2, 0:w],
                                                     op0=ALU.mult, op1=ALU.add).then_inc(aux_free[uses % 2], 1)
                            uses += 1
                            dve.wait_ge(aux_free[u % 2], AUX // 2 * h + u // 2 + 2)
                            dve.tensor_reduce(neg_max[:, u:u + 1], biased[:, u % 2, 0:w], AX_X, ALU.max, negate=True).then_inc(max_done, 1)

                        def rows(g):
                            nonlocal uses
                            for half in range(2):
                                dve.wait_ge(v_turned, 6 * h + 2 * g + half + 1)
                                dve.tensor_copy(v_rows_[:, g, 4 * half:4 * half + 4, :].rearrange("p j n -> p (j n)"), aux[:, uses % 2, :]).then_inc(aux_free[uses % 2], 1)
                                uses += 1
                                dve.wait_ge(aux_free[(uses - 1) % 2], AUX // 2 * h + (uses - 1) // 2 + 2)
                                dve.sem_inc(rows_out, 1)

                        dve.wait_ge(log_done, h + 1)
                        dve.wait_ge(max_done, NU * h + NU)
                        dve.tensor_tensor(lse[:], log_den[:], neg_max[:], ALU.subtract).then_inc(lse_done, 1)
                        step(dve.reciprocal(den[:], den[:]))
                        rows(0)
                        dve.wait_ge(joint_loaded, 16 * (h + 1))
                        step(dve.tensor_tensor(joint_max[:], joint[:, 0], joint[:, 1], ALU.max))
                        step.wait()
                        step(dve.tensor_tensor(joint_max[:], joint_max[:], joint[:, 2], ALU.max))
                        step.wait()
                        dve.tensor_tensor(joint[:], joint[:], joint_max[:].unsqueeze(1).to_broadcast([P, N_DIL, 8]), ALU.subtract).then_inc(joint_shifted, 1)
                        dve.wait_ge(joint_exp, h + 1)
                        step(dve.tensor_tensor(joint_sum[:], joint[:, 0], joint[:, 1], ALU.add))
                        step.wait()
                        step(dve.tensor_tensor(joint_sum[:], joint_sum[:], joint[:, 2], ALU.add))
                        step.wait()
                        step(dve.reciprocal(joint_sum[:], joint_sum[:]))
                        step.wait()
                        dve.tensor_tensor(joint[:], joint[:], joint_sum[:].unsqueeze(1).to_broadcast([P, N_DIL, 8]), ALU.mult).then_inc(share_done, 1)
                        rows(1)
                        rows(2)
                        dve.wait_ge(share_loaded, 16 * moves * (h + 1))
                        dve.tensor_tensor(share[:], share[:], den[:], ALU.mult).then_inc(factor_done, 1)
                        for u in range(NU):
                            w = units[u][3] * P
                            dve.wait_ge(p_turned, NU * h + u + 1)
                            if u >= 2:
                                dve.wait_ge(summed, NU * h + u - 1)
                            dve.tensor_copy(p_t[:, u % 2, 0:w], aux[:, uses % 2, 0:w]).then_inc(aux_free[uses % 2], 1)
                            uses += 1
                            dve.wait_ge(aux_free[(uses - 1) % 2], AUX // 2 * h + (uses - 1) // 2 + 2)
                            dve.sem_inc(p_t_out, 1)
                        dve.wait_ge(summed, NU * h + NU)
                        dve.wait_ge(z_out, NT * h + NT + 2)
                        dve.tensor_tensor(y_plain[:, bass.ds(h, 1), :].rearrange("p o t -> p (o t)"), acc[:].rearrange("p b n -> p (b n)"), silu[:],
                                          ALU.mult).then_inc(y_done, 1)
                        dve.wait_ge(y_done, h + 2)
                        dve.sem_inc(dve_step, N_STEP - step.done)

        def phase_split_y():
            phases.start()
            hi_done = sem("split_hi_done")
            with nc.Block() as block:
                @block.scalar
                def _(act):
                    for kt in range(KT):
                        act.copy(h_hi[:, kt, :], y_plain[:, kt, :]).then_inc(hi_done, 1)

                @block.vector
                def _(dve):
                    for kt in range(KT):
                        dve.wait_ge(hi_done, kt + 1)
                        dve.tensor_tensor(h_lo[:, kt, :], y_plain[:, kt, :], h_hi[:, kt, :].bitcast(F32), ALU.subtract)

        def phase_rows_out():
            phases.start()
            rows = Arena(nc, free_at)("out_rows", [P, 2, D])
            turned = sem("rows_turned")
            rows_out = sem("rows_out")
            stored = [sem(f"rows_stored{u}") for u in range(2)]
            with nc.psum_tensor("rows_turn", [P, 2, 2, HALF], F32) as turn, nc.Block() as block:
                @block.tensor
                def _(pe):
                    for j in range(BLOCKS):
                        if j >= 2:
                            pe.wait_ge(rows_out, 2 * (j - 1))
                        for kt in range(KT):
                            ins = pe.transpose(turn[:, j % 2, kt // 4, (kt % 4) * P:(kt % 4 + 1) * P], h2_cm[:, kt, j * P:(j + 1) * P], ident)
                            if kt % 4 == 3:
                                ins.then_inc(turned, 1)

                @block.scalar
                def _(act):
                    for j in range(BLOCKS):
                        if j >= 2:
                            act.wait_ge(stored[j % 2], 16 * (j // 2))
                        for half in range(2):
                            act.wait_ge(turned, 2 * j + half + 1)
                            act.copy(rows[:, j % 2, half * HALF:(half + 1) * HALF], turn[:, j % 2, half, :]).then_inc(rows_out, 1)

                @block.sync
                def _(sp):
                    for j in range(BLOCKS):
                        sp.wait_ge(rows_out, 2 * (j + 1))
                        sp.dma_start(out[0, j * P:(j + 1) * P, :], rows[:, j % 2, :]).then_inc(stored[j % 2], 16)
                    for u in range(2):
                        sp.wait_ge(stored[u], 16 * (BLOCKS // 2))

        phase_norm("odd", Arena(nc, free_at), "stream", [(0, SEQ, plain_gain("odd_norm_2"), None)], SEQ, h_hi, h_lo)
        phase_conv()
        phase_out("odd_d_out", Arena(nc, free_at), y_hi, y_lo, out_weights(A["odd_w_out_2"], D), 1, None)
        phase_dilated()
        phase_split_y()
        phase_out("odd_c_out", Arena(nc, free_at), h_hi, h_lo, out_weights(A["odd_w_out_2"], 0), 1, None)
        phase_norm("final", Arena(nc, free_at), "stream", [(0, SEQ, plain_gain("final_norm_2"), None)], SEQ, h_plain=h2_cm)
        phase_rows_out()


_USED = ["x", "c", "ctx", "c_ctx", "w_mod", "b_mod", "norm1_w", "norm2_w", "w_in", "b_gates", "conv_qk", "q_norm_w", "k_norm_w",
         "sink", "mlstm_norm_w", "w_out", "w_router", "w_gate", "w_up", "w_down", "even_norm_2", "even_w_in_2", "even_pool_w_2",
         "even_pool_scale_2", "even_ws_2", "even_bs_2", "even_w_out_2", "odd_norm_2", "odd_w_in_2", "odd_conv_w_2", "odd_w_out_2",
         "final_norm_2"]


def declare(nc, inputs):
    arrays, args = {}, {}
    for name, a in {**{n: inputs[n] for n in _USED}, **constant_tables()}.items():
        a = np.ascontiguousarray(a)
        arrays[f"in_{name}"] = a
        args[name] = nc.dram_tensor(f"in_{name}", a.shape, F32, kind="ExternalInput").ap()
    out = nc.dram_tensor("out", (1, SEQ, D), F32, kind="ExternalOutput").ap()
    return arrays, args, out


def kernel(**inputs):
    import concourse.bacc as bacc
    from concourse.bass_utils import run_bass_kernel_spmd

    nc = bacc.Bacc("TRN2", target_bir_lowering=False, num_devices=1)
    arrays, args, out = declare(nc, inputs)
    build_program(nc, args, out)
    result = run_bass_kernel_spmd(nc, [arrays], core_ids=[0])
    return result.results[0]["out"]
```

```python
from contextlib import ExitStack

import numpy as np

import concourse.bass as bass
from concourse import mybir

F32 = mybir.dt.float32
F32R = mybir.dt.float32r
U32 = mybir.dt.uint32
ALU = mybir.AluOpType
ACT = mybir.ActivationFunctionType
AX_X = mybir.AxisListType.X

P = 128
D = 1024
KT = D // P
SEQ = 1024
CTX = 256
TOK = CTX + SEQ
HALF = 512
EPS = 1e-6
NEG = -1e30
GRID_W = 64
N_HEADS, HEAD_DIM = 8, 64
M_HEADS, M_DIM = 4, 128
CHUNK = 128
XCH = SEQ // CHUNK
ALLCH = TOK // CHUNK
CCH = CTX // CHUNK
N_EXPERTS, EXPERT_FF = 16, 512
SLOTS = 2 * SEQ // N_EXPERTS
POOL_SIZES = (2, 4, 8, 16)
C_SLOTS, N_DIL = 8, 3
DILATION = (1, 4, 16)
BLOCKS = SEQ // P
Q_COL, K_COL, V_COL, MQ_COL, MK_COL, MV_COL, MO_COL, G_COL = 0, 512, 640, 768, 1280, 1792, 2304, 2816
GATE_ROWS = 36

CONST_PARTS = (("ident", P), ("ones", P), ("head_ones", P), ("rotate", P), ("near_mask", 3 * P), ("chunk_mask", 2 * P),
               ("dist", 2 * P), ("dist16", P), ("slopes", N_DIL * C_SLOTS), ("pool_inv", len(POOL_SIZES) * 16))
CONST_AT, _n = {}, 0
for _name, _w in CONST_PARTS:
    CONST_AT[_name] = (_n, _w)
    _n += _w
CONST_W = _n
ROWS_A = (("b_mod", 48), ("norm1_w", 8), ("norm2_w", 8), ("even_norm_2", 8), ("odd_norm_2", 8), ("final_norm_2", 8),
          ("even_pool_scale_2", 8))
ROWS_B = (("conv_qk", 24), ("odd_conv_w_2", 24), ("mlstm_norm_w", 4), ("c", 8), ("c_ctx", 8))
SH1, SC1, G1, SH2, SC2, G2 = range(0, 48, 8)


def columns_of(parts):
    at, n = {}, 0
    for name, rows in parts:
        at[name] = (n, rows)
        n += rows
    return at, n


AT_A, N_A = columns_of(ROWS_A)
AT_B, N_B = columns_of(ROWS_B)


def constant_tables():
    i = np.arange(P)
    table = np.zeros((P, CONST_W), np.float32)

    def put(name, value):
        at, width = CONST_AT[name]
        table[:, at:at + width] = value

    put("ident", np.eye(P))
    put("ones", 1.0)
    put("head_ones", (i[:, None] // HEAD_DIM == i[None] // HEAD_DIM))
    rotate = np.zeros((P, P))
    for m in range(P):
        if m % HEAD_DIM < HEAD_DIM // 2:
            rotate[m + HEAD_DIM // 2, m] = -1.0
        else:
            rotate[m - HEAD_DIM // 2, m] = 1.0
    put("rotate", rotate)
    q, k = i[:, None], np.arange(3 * P)[None]
    put("near_mask", np.where(np.abs(q + P - k) <= P, 0.0, NEG))
    put("chunk_mask", np.concatenate([np.where(q <= i[None], 0.0, NEG), np.where(q >= i[None], 0.0, NEG)], 1))
    steps = q + P - np.arange(2 * P)[None]
    put("dist", np.where((steps >= 0) & (steps <= P), -steps, NEG))
    half = P // 2
    same = (q // half == i[None] // half) & (i[None] % half <= q % half)
    put("dist16", np.where(same, -(q % half - i[None] % half), NEG))
    n = N_DIL * C_SLOTS
    slopes = 2.0 ** (-8.0 * (np.arange(n) + 1) / n)
    put("slopes", np.repeat(slopes[None] * np.repeat(DILATION, C_SLOTS)[None], P, 0))
    t = np.arange(16)
    put("pool_inv", np.repeat(np.concatenate([1.0 / np.minimum(t + 1, w) for w in POOL_SIZES])[None], P, 0))

    pos = np.arange(SEQ)
    n_freq = HEAD_DIM // 4
    freqs = (np.float32(10000.0) ** (-np.arange(n_freq, dtype=np.float32) / np.float32(n_freq))).astype(np.float32)
    ang = np.concatenate([(pos // GRID_W)[:, None].astype(np.float32) * freqs,
                          (pos % GRID_W)[:, None].astype(np.float32) * freqs], 1)
    ang = np.concatenate([ang, ang, ang, ang], 1).T
    rope = np.stack([np.cos(ang), np.sin(ang)], 1).astype(np.float32)

    pick = np.zeros((GATE_ROWS, 8, P), np.float32)
    for r in range(8):
        pick[32 * (r // M_HEADS) + r % M_HEADS, r] = 1.0
    keep = np.ones((GATE_ROWS, TOK), np.float32)
    keep[:, ::CHUNK] = 0.0
    return {"const_table": table, "rope_table": rope, "pick_table": pick.reshape(GATE_ROWS, 8 * P), "keep_table": keep}


class Steps:

    def __init__(self, eng, sem, base=0):
        self.eng, self.sem, self.base, self.done = eng, sem, base, 0

    def __call__(self, ins):
        ins.then_inc(self.sem, 1)
        self.done += 1
        return ins

    def wait(self):
        self.eng.wait_ge(self.sem, self.base + self.done)


class Arena:

    def __init__(self, nc, at):
        self.nc, self.at = nc, at

    def __call__(self, name, shape, dtype=F32):
        words = 1
        for s in shape[1:]:
            words *= s
        t = self.nc.alloc_sbuf_tensor_at(name, list(shape), dtype, offset=self.at)
        self.at += (words * 4 + 31) // 32 * 32
        assert self.at <= self.nc.sbuf_usable_end, (name, self.at)
        return t


class PhaseSemaphores:

    def __init__(self, nc):
        self.nc = nc
        free = sorted(nc.free_semaphores)
        self.kept, free = free[:8], free[8:]
        self.sets = [free[:len(free) // 2], free[len(free) // 2:]]
        self.used = []

    def start(self):
        if self.used:
            self.nc.gpsimd.sem_clear(range(self.used[0].num, self.used[-1].num + 1))
            for s in self.used:
                self.nc.release_semaphore(s)
        self.used = []
        self.sets.reverse()

    def keep(self, name):
        return self.nc.alloc_semaphore(name, num=self.kept.pop())

    def sem(self, name):
        self.used.append(self.nc.alloc_semaphore(name, num=self.sets[0][len(self.used)]))
        return self.used[-1]


def build_program(nc, A, out):
    with ExitStack() as ctx:
        phases = PhaseSemaphores(nc)
        sem = phases.sem

        def dram(name, shape):
            return nc.dram_tensor(name, shape, F32, kind="Internal").ap()

        x_cm = dram("x_cm", (D, SEQ))
        att_cm = dram("att_cm", (N_HEADS * HEAD_DIM, SEQ))
        h2_rows = dram("h2_rows", (SEQ, D))
        ffn_rows = dram("ffn_rows", (SEQ, D))
        stat_dram = dram("stat_dram", (2, N_DIL, SEQ))
        factor_dram = dram("factor_dram", (N_DIL, SEQ))
        x_cm_k = x_cm.rearrange("(k p) t -> p k t", p=P)

        start = (nc.sbuf_base + 63) // 32 * 32
        fixed = Arena(nc, start)
        const = fixed("const", [P, CONST_W])
        par_a = fixed("par_a", [P, N_A])
        par_b = fixed("par_b", [P, N_B])
        mod = fixed("mod", [P, 48, 2])
        gain1 = fixed("gain1", [P, KT, 2])
        gain2 = fixed("gain2", [P, KT])
        sinks = fixed("sinks", [P, N_HEADS])
        qk_gain = fixed("qk_gain", [P, 2])
        gate_bias = fixed("gate_bias", [P, 1])
        ring_at = fixed.at
        w_raw = fixed("w_raw", [P, 2, KT, P])
        w_hi = fixed("w_hi", [P, 2, KT, P], F32R)
        w_lo = fixed("w_lo", [P, 2, KT, P], F32R)
        zero_col = fixed("zero_col", [P, 1])
        eps_col = fixed("eps_col", [P, 1])
        free_at = fixed.at

        def cst(name):
            at, width = CONST_AT[name]
            return const[:, at:at + width]

        def pa(name):
            at, width = AT_A[name]
            return par_a[:, at:at + width]

        def pb(name):
            at, width = AT_B[name]
            return par_b[:, at:at + width]

        ident, ones = cst("ident"), cst("ones")
        passed = phases.keep("passed")

        def pass_waits(eng):
            eng.sem_inc(passed, 1)

        class Ring:

            def __init__(self, tag, pieces=1, ready=2):
                self.pieces, self.ready = pieces, ready
                self.loaded = [sem(f"{tag}_w_loaded{u}") for u in range(2)]
                self.hi_done = sem(f"{tag}_w_hi_done")
                self.split = sem(f"{tag}_w_split")
                self.projected = sem(f"{tag}_projected")

            def load(self, sp, n, u, parts):
                sp.wait_ge(self.split, n + 1)
                if not isinstance(n, int):
                    pass_waits(sp)
                assert len(parts) == self.pieces
                for dst, src in parts:
                    sp.dma_start(dst, src).then_inc(self.loaded[u], 16)

            def credits(self, pool, pe):
                if pool is not None:
                    pool.sem_inc(self.split, 2 + self.ready)
                    if self.ready:
                        pool.sem_inc(self.hi_done, self.ready)
                if pe is not None:
                    pe.sem_inc(self.projected, 2)

            def do_split(self, pool, n, u, round_):
                pool.wait_ge(self.loaded[u], 16 * self.pieces * (round_ + 1 - self.ready // 2))
                pool.wait_ge(self.projected, n + 1)
                pool.tensor_tensor(w_hi[:, u], w_raw[:, u], zero_col[:, 0:1].to_broadcast([P, KT * P]).rearrange("p (k n) -> p k n", k=KT),
                                   ALU.add).then_inc(self.hi_done, 1)
                pool.wait_ge(self.hi_done, n + 1)
                pool.tensor_tensor(w_lo[:, u], w_raw[:, u], w_hi[:, u].bitcast(F32), ALU.subtract).then_inc(self.split, 1)

            def load_all(self, sp, groups, tiles, parts, before=None):
                def load(g, t):
                    self.load(sp, tiles * g + t, t % 2, parts(g + t // tiles, t % tiles))

                with sp.Fori(0, groups - 1) as g:
                    if before:
                        before(g)
                    for t in range(2, tiles + 2):
                        load(g, t)
                if before:
                    before(groups - 1)
                for t in range(2, tiles):
                    load(groups - 1, t)

            def split_all(self, pool, groups, tiles):
                with pool.Fori(0, groups - 1) as g:
                    for t in range(2, tiles + 2):
                        self.do_split(pool, tiles * g + t, t % 2, tiles // 2 * g + t // 2)
                for t in range(2, tiles):
                    self.do_split(pool, tiles * (groups - 1) + t, t % 2, tiles // 2 * (groups - 1) + t // 2)

            def project(self, pe, n, u, z_free, targets, rhs_hi, rhs_lo, between=None):
                pe.wait_ge(self.split, n + 3)
                pe.wait_ge(z_free, n + 1)
                for kt in range(KT):
                    for w, rhs, first, last in ((w_hi, rhs_hi, kt == 0, False), (w_hi, rhs_lo, False, False),
                                                (w_lo, rhs_hi, False, kt == KT - 1)):
                        for z, c0, width in targets:
                            ins = pe.matmul(z, w[:, u, kt], rhs[:, kt, c0:c0 + width], start=first, stop=last)
                    if between and kt in between:
                        between[kt]()
                ins.then_inc(self.projected, 1)

        class Prefetch:

            def __init__(self, tag, parts, ring=None, n=0):
                self.parts, self.ring, self.n = parts, ring, n
                self.loaded = [sem(f"{tag}_next_loaded{u}") for u in range(2)]
                self.hi_done = sem(f"{tag}_next_hi_done")

            def load(self, sp):
                for u in range(2):
                    if self.ring:
                        sp.wait_ge(self.ring.split, self.n + u + 1)
                    for dst, src in self.parts[u]:
                        sp.dma_start(dst, src).then_inc(self.loaded[u], 16)

            def split(self, pool):
                for u in range(2):
                    pool.wait_ge(self.loaded[u], 16 * len(self.parts[u]))
                    if self.ring:
                        pool.wait_ge(self.ring.projected, self.n + u + 1)
                    pool.tensor_tensor(w_hi[:, u], w_raw[:, u], zero_col[:, 0:1].to_broadcast([P, KT * P]).rearrange("p (k n) -> p k n", k=KT),
                                       ALU.add).then_inc(self.hi_done, 1)
                    pool.wait_ge(self.hi_done, u + 1)
                    pool.tensor_tensor(w_lo[:, u], w_raw[:, u], w_hi[:, u].bitcast(F32), ALU.subtract)

        class NormTail:

            def __init__(self, tag, mem, x, n_tok, affines, h_hi=None, h_lo=None, h_plain=None, diag=None):
                self.x, self.n_tok, self.affines = x, n_tok, affines
                self.h_hi, self.h_lo, self.h_plain = h_hi, h_lo, h_plain
                self.blocks = n_tok // P
                self.rstd = mem(f"{tag}_rstd", [P, self.blocks])
                self.diag = diag if diag is not None else mem(f"{tag}_diag", [P, n_tok])[:]
                self.summed = sem(f"{tag}_norm_summed")
                self.mean_done = sem(f"{tag}_norm_mean_done")
                self.root_done = sem(f"{tag}_norm_root_done")
                self.inverse_done = sem(f"{tag}_norm_inverse_done")
                self.diag_done = sem(f"{tag}_norm_diag_done")
                self.spread = sem(f"{tag}_norm_spread")
                self.scaled = sem(f"{tag}_norm_scaled")
                self.shifted = sem(f"{tag}_norm_shifted")
                self.hi_done = sem(f"{tag}_norm_hi_done")
                self.lo_done = sem(f"{tag}_norm_lo_done")

            def through_shift(self, kt):
                return kt % 2 == 0 or any(shift for _, _, _, shift in self.affines)

            def pe(self, pe, spread):
                pe.wait_ge(self.diag_done, 1)
                for g, c0 in enumerate(range(0, self.n_tok, HALF)):
                    width = min(HALF, self.n_tok - c0)
                    ins = pe.matmul(spread[:, g, 0:width], ones, self.diag[:, c0:c0 + width], start=True, stop=True)
                ins.then_inc(self.spread, 1)

            def dve(self, dve, sums, spread, x_free=None):
                wide = [P, self.blocks, P]
                dve.wait_ge(self.summed, 1)
                dve.tensor_scalar(self.rstd[:], sums, 1.0 / D, EPS, ALU.mult, ALU.add).then_inc(self.mean_done, 1)
                dve.wait_ge(self.root_done, 1)
                dve.reciprocal(self.rstd[:], self.rstd[:]).then_inc(self.inverse_done, 1)
                dve.wait_ge(self.inverse_done, 1)
                dve.tensor_tensor(self.diag.rearrange("p (j n) -> p j n", n=P), ident.unsqueeze(1).to_broadcast(wide),
                                  self.rstd[:].unsqueeze(2).to_broadcast(wide), ALU.mult).then_inc(self.diag_done, 1)
                dve.wait_ge(self.spread, 1)
                flat = spread.rearrange("p g n -> p (g n)")[:, 0:self.n_tok]

                def lo(kt):
                    dve.wait_ge(self.hi_done, kt + 1)
                    if self.through_shift(kt):
                        dve.tensor_tensor(self.h_lo[:, kt, :], self.x[:, kt, :], self.h_hi[:, kt, :].bitcast(F32), ALU.subtract).then_inc(self.lo_done, 1)
                    else:
                        dve.scalar_tensor_tensor(out=self.h_lo[:, kt, :], in0=self.x[:, kt, :], scalar=self.affines[0][2](kt),
                                                 in1=self.h_hi[:, kt, :].bitcast(F32), op0=ALU.mult, op1=ALU.subtract).then_inc(self.lo_done, 1)

                for kt in range(KT):
                    if x_free:
                        x_free(kt)
                    dve.tensor_tensor(self.x[:, kt, :], self.x[:, kt, :], flat, ALU.mult).then_inc(self.scaled, 1)
                    if self.h_plain is None and kt >= 3 and kt % 2 == 1:
                        lo(kt - 2)
                if self.h_plain is None:
                    lo(KT - 1)

            def act(self, act):
                act.wait_ge(self.mean_done, 1)
                act.activation(self.rstd[:], self.rstd[:], ACT.Sqrt).then_inc(self.root_done, 1)
                n = 0
                for kt in range(KT):
                    act.wait_ge(self.scaled, kt + 1)
                    if self.h_plain is None and not self.through_shift(kt):
                        act.activation(self.h_hi[:, kt, :], self.x[:, kt, :], ACT.Copy, scale=self.affines[0][2](kt)).then_inc(self.hi_done, 1)
                        continue
                    to = (self.x if self.h_plain is None else self.h_plain)[:, kt, :]
                    for c0, width, gain, shift in self.affines:
                        act.activation(to[:, c0:c0 + width], self.x[:, kt, c0:c0 + width], ACT.Identity, scale=gain(kt),
                                       bias=0.0 if shift is None else shift(kt)).then_inc(self.shifted, 1)
                        n += 1
                    if self.h_plain is None:
                        act.wait_ge(self.shifted, n)
                        act.copy(self.h_hi[:, kt, :], self.x[:, kt, :]).then_inc(self.hi_done, 1)

            def pool(self, pool):
                if self.h_plain is None:
                    for kt in range(0, KT, 2):
                        pool.wait_ge(self.hi_done, kt + 1)
                        pool.tensor_tensor(self.h_lo[:, kt, :], self.x[:, kt, :], self.h_hi[:, kt, :].bitcast(F32), ALU.subtract)

        class Modulation:

            CHUNKS, SLOTS_W = 6 * D // HALF, 4

            def __init__(self, mem, w_at):
                self.rows_a = mem("rows_a", [N_A, P])
                self.rows_b = mem("rows_b", [N_B, P])
                self.sink_row = mem("sink_row", [1, N_HEADS])
                self.silu_c = mem("silu_c", [P, KT, 2])
                self.rows_sb = mem("mod_rows_sb", [2, 3, HALF])
                self.w = [w_at(f"w_mod{u}", [P, KT, HALF]) for u in range(self.SLOTS_W)]
                self.small = sem("mod_small_loaded")
                self.w_loaded = [sem(f"mod_w_loaded{u}") for u in range(self.SLOTS_W)]
                self.w_used = sem("mod_w_used")
                self.rows_out = sem("mod_rows_out")
                self.columns_done = sem("mod_columns_done")
                self.bias_zeroed = sem("mod_bias_zeroed")
                self.bias_loaded = sem("mod_bias_loaded")
                self.turned = sem("mod_params_turned")
                self.params_ready = sem("mod_params_ready")
                self.silu_done = sem("mod_silu_done")
                self.done = sem("mod_done")
                self.dve_step = sem("mod_dve_step")
                self.src = A["w_mod"].rearrange("o (k p) n -> p (o k) n", p=P)
                self.parts = [(const[:], A["const_table"])]
                for rows, names, at in ((self.rows_a, ROWS_A, AT_A), (self.rows_b, ROWS_B, AT_B)):
                    for name, count in names:
                        src = A[name]
                        letters = "abcd"[:len(src.shape)]
                        flat = src.rearrange(f"{' '.join(letters)} -> ({' '.join(letters)})") if len(src.shape) > 1 else src
                        self.parts.append((rows[at[name][0]:at[name][0] + count, :], flat.rearrange("(r q) -> r q", q=P)))
                self.parts.append((self.sink_row[:], A["sink"]))
                for col, name in ((0, "q_norm_w"), (1, "k_norm_w")):
                    for half in range(2):
                        self.parts.append((qk_gain[half * HEAD_DIM:(half + 1) * HEAD_DIM, col:col + 1], A[name].rearrange("o p -> p o")))
                self.biases = [(gate_bias[row:row + M_HEADS, :], A["b_gates"][0:1, at:at + M_HEADS].rearrange("o p -> p o"))
                               for row, at in ((0, 0), (64, 4), (32, 8), (96, 12))]

            def sp_start(self, sp):
                for dst, src in self.parts[0::2]:
                    sp.dma_start(dst, src).then_inc(self.small, 16)

            def sp(self, sp, j):
                if j >= self.SLOTS_W:
                    sp.wait_ge(self.w_used, j - self.SLOTS_W + 1)
                sp.dma_start(self.w[j % self.SLOTS_W][:], self.src[:, :, j * HALF:(j + 1) * HALF]).then_inc(self.w_loaded[j % self.SLOTS_W], 16)

            def pool(self, pool):
                pool.memset(gate_bias[:], 0.0).then_inc(self.bias_zeroed, 1)
                pool.memset(zero_col[:], 0.0).then_inc(self.bias_zeroed, 1)
                pool.memset(eps_col[:], EPS).then_inc(self.bias_zeroed, 1)
                pool.wait_ge(self.bias_zeroed, 3)

            def pe_start(self, pe, spare):
                pe.wait_ge(self.small, 16 * len(self.parts))
                pe.transpose(spare[:, 0, 0:N_A], self.rows_a[:], ident[0:N_A, 0:N_A])
                pe.transpose(spare[:, 1, 0:N_B], self.rows_b[:], ident[0:N_B, 0:N_B])
                pe.matmul(spare[:, 2, 0:N_HEADS], ones[0:1, :], self.sink_row[:], start=True, stop=True).then_inc(self.turned, 1)
                pe.wait_ge(self.silu_done, 2)
                pe.wait_ge(self.dve_step, 2)

            def pe(self, pe, j, row_acc, acc):
                pe.wait_ge(self.w_loaded[j % self.SLOTS_W], 16 * (j // self.SLOTS_W + 1))
                if j >= 2:
                    pe.wait_ge(self.rows_out, j - 1)
                for kt in range(KT):
                    ins = pe.matmul(row_acc[:, j % 2, :], self.silu_c[:, kt, :], self.w[j % self.SLOTS_W][:, kt, :], start=(kt == 0), stop=(kt == KT - 1))
                ins.then_inc(self.w_used, 1)
                if j:
                    self.pe_columns(pe, j - 1, acc)

            def pe_columns(self, pe, j, acc):
                pe.wait_ge(self.rows_out, j + 1)
                for q in range(4):
                    at = 4 * j + q
                    ins = pe.transpose(acc[:, 2 * at:2 * at + 2], self.rows_sb[:, j % 3, q * P:(q + 1) * P], ident[0:2, 0:2])
                ins.then_inc(self.columns_done, 1)

            def act_start(self, act, spare):
                for dst, src in self.parts[1::2]:
                    act.dma_start(dst, src).then_inc(self.small, 16)
                act.wait_ge(self.bias_zeroed, 3)
                for dst, src in self.biases:
                    act.dma_start(dst, src).then_inc(self.bias_loaded, 16)
                act.wait_ge(self.turned, 1)
                act.copy(par_b[:], spare[:, 1, 0:N_B]).then_inc(self.params_ready, 1)
                act.wait_ge(self.params_ready, 1)
                act.activation(self.silu_c[:, :, 0], pb("c"), ACT.Silu).then_inc(self.silu_done, 1)
                act.activation(self.silu_c[:, :, 1], pb("c_ctx"), ACT.Silu).then_inc(self.silu_done, 1)

            def act(self, act, j, row_acc):
                act.wait_ge(self.w_used, j + 1)
                if j >= 3:
                    act.wait_ge(self.columns_done, j - 2)
                act.copy(self.rows_sb[:, j % 3, :], row_acc[:, j % 2, :]).then_inc(self.rows_out, 1)

            def dve_start(self, dve, spare):
                dve.wait_ge(self.turned, 1)
                dve.tensor_copy(par_a[:], spare[:, 0, 0:N_A]).then_inc(self.dve_step, 1)
                dve.tensor_copy(sinks[:], spare[:, 2, 0:N_HEADS]).then_inc(self.dve_step, 1)
                dve.wait_ge(self.dve_step, 2)

            def dve_end(self, dve, acc):
                dve.wait_ge(self.columns_done, self.CHUNKS)
                dve.tensor_tensor(mod[:], acc[:, 0:96].rearrange("p (j s) -> p j s", s=2), pa("b_mod").unsqueeze(2).to_broadcast([P, 48, 2]),
                                  ALU.add).then_inc(self.dve_step, 1)
                dve.wait_ge(self.dve_step, 3)
                for s in range(2):
                    dve.scalar_tensor_tensor(out=gain1[:, :, s], in0=mod[:, SC1:SC1 + KT, s], scalar=1.0, in1=pa("norm1_w"),
                                             op0=ALU.add, op1=ALU.mult).then_inc(self.done, 1)
                dve.scalar_tensor_tensor(out=gain2[:], in0=mod[:, SC2:SC2 + KT, 0], scalar=1.0, in1=pa("norm2_w"),
                                         op0=ALU.add, op1=ALU.mult).then_inc(self.done, 1)

        def phase_rows_norm(tag, mem, n_tok, affines, h_hi, h_lo, next_parts, beside=None):
            ffn = beside is None
            blocks = n_tok // P
            xt = mem(f"{tag}_xt", [P, KT, n_tok])
            rows = mem(f"{tag}_rows", [P, 4, D])
            sq = mem(f"{tag}_sq", [P, 2, KT, P])
            part = mem(f"{tag}_part", [P, 2, P])
            scaled = mem(f"{tag}_ffn", [P, 2, KT, P]) if ffn else None
            tail = NormTail(tag, mem, xt, n_tok, affines, h_hi, h_lo)
            pre = Prefetch(tag, next_parts)
            rows_loaded = [sem(f"{tag}_rows_loaded{r}") for r in range(4)]
            turned = sem(f"{tag}_turned")
            turn_out = sem(f"{tag}_turn_out")
            x_done = sem(f"{tag}_x_done")
            sq_done = sem(f"{tag}_sq_done")
            part_done = sem(f"{tag}_part_done")
            part_used = sem(f"{tag}_part_used")
            stored = sem(f"{tag}_stored")
            x_at = n_tok - SEQ

            def block(x, j):
                return x[:, :, j * P:(j + 1) * P]

            def source(j):
                if ffn:
                    return ffn_rows[j * P:(j + 1) * P, :]
                return A["ctx"][0, j * P:(j + 1) * P, :] if j < CCH else A["x"][0, (j - CCH) * P:(j - CCH + 1) * P, :]

            with nc.psum_tensor(f"{tag}_turn", [P, 2, KT, P], F32) as turn, nc.psum_tensor(f"{tag}_sums", [P, HALF], F32) as sums, \
                    nc.psum_tensor(f"{tag}_mod_rows", [2, 2, HALF], F32) as mod_rows, nc.psum_tensor(f"{tag}_mod_columns", [P, HALF], F32) as mod_columns, \
                    nc.Block() as blk:
                banks = turn[:].rearrange("p a k n -> p (a k n)").rearrange("p (b n) -> p b n", n=HALF)
                spread = banks[:, 0:3, :]

                @blk.sync
                def _(sp):
                    if beside:
                        beside.sp_start(sp)
                    for j in range(blocks):
                        if j >= 4:
                            sp.wait_ge(turned, j - 3)
                        sp.dma_start(rows[:, j % 4, :], source(j)).then_inc(rows_loaded[j % 4], 16)
                        if ffn:
                            sp.dma_start(block(xt, j), block(x_cm_k, j)).then_inc(rows_loaded[j % 4], 16)
                        if beside:
                            beside.sp(sp, j)
                    if beside:
                        for j in range(blocks, beside.CHUNKS):
                            beside.sp(sp, j)
                    pre.load(sp)

                @blk.tensor
                def _(pe):
                    def sum_up(j):
                        pe.wait_ge(part_done, j + 1)
                        pe.matmul(sums[:, j:j + 1], part[:, j % 2, :], ones[:, 0:1], start=True, stop=True).then_inc(part_used, 1)

                    if beside:
                        beside.pe_start(pe, banks)
                    for j in range(blocks):
                        pe.wait_ge(rows_loaded[j % 4], (32 if ffn else 16) * (j // 4 + 1))
                        if j >= 2:
                            pe.wait_ge(turn_out, j - 1)
                        for kt in range(KT):
                            ins = pe.transpose(turn[:, j % 2, kt, :], rows[:, j % 4, kt * P:(kt + 1) * P], ident)
                        ins.then_inc(turned, 1)
                        if beside:
                            beside.pe(pe, j, mod_rows, mod_columns)
                        if j >= 2:
                            sum_up(j - 2)
                    if beside:
                        for j in range(blocks, beside.CHUNKS):
                            beside.pe(pe, j, mod_rows, mod_columns)
                        beside.pe_columns(pe, beside.CHUNKS - 1, mod_columns)
                    sum_up(blocks - 2)
                    sum_up(blocks - 1)
                    pe.wait_ge(part_used, blocks)
                    pe.sem_inc(tail.summed, 1)
                    tail.pe(pe, spread)

                @blk.gpsimd
                def _(pool):
                    if ffn:
                        for j in range(blocks):
                            pool.wait_ge(turn_out, j + 1)
                            pool.tensor_tensor(block(xt, j), block(xt, j), scaled[:, j % 2], ALU.add).then_inc(x_done, 1)
                    else:
                        beside.pool(pool)
                    pre.split(pool)
                    tail.pool(pool)

                @blk.scalar
                def _(act):
                    def square(j):
                        act.wait_ge(x_done, j + 1)
                        if j >= 2:
                            act.wait_ge(part_done, j - 1)
                        act.activation(sq[:, j % 2], block(xt, j), ACT.Square).then_inc(sq_done, 1)
                        if j * P >= x_at:
                            act.dma_start(block(x_cm_k, j - x_at // P), block(xt, j)).then_inc(stored, 16)

                    if beside:
                        beside.act_start(act, banks)
                    for j in range(blocks):
                        if beside:
                            act.wait_ge(turned, j + 1)
                            act.copy(block(xt, j), turn[:, j % 2]).then_inc(turn_out, 1)
                            act.wait_ge(turn_out, j + 1)
                            act.sem_inc(x_done, 1)
                        square(j)
                        if beside:
                            beside.act(act, j, mod_rows)
                    if beside:
                        for j in range(blocks, beside.CHUNKS):
                            beside.act(act, j, mod_rows)
                        act.wait_ge(beside.bias_loaded, 16 * len(beside.biases))
                        act.wait_ge(beside.done, 3)
                    tail.act(act)

                @blk.vector
                def _(dve):
                    def add_up(j):
                        dve.wait_ge(sq_done, j + 1)
                        if j >= 2:
                            dve.wait_ge(part_used, j - 1)
                        dve.tensor_reduce(part[:, j % 2, :], sq[:, j % 2].rearrange("p k t -> p t k"), AX_X, ALU.add).then_inc(part_done, 1)

                    if beside:
                        beside.dve_start(dve, banks)
                    for j in range(blocks):
                        if ffn:
                            dve.wait_ge(turned, j + 1)
                            if j >= 2:
                                dve.wait_ge(x_done, j - 1)
                            dve.tensor_tensor(scaled[:, j % 2], turn[:, j % 2], mod[:, G2:G2 + KT, 0:1].to_broadcast([P, KT, P]), ALU.mult).then_inc(turn_out, 1)
                            if j >= 1:
                                add_up(j - 1)
                        else:
                            add_up(j)
                    if ffn:
                        add_up(blocks - 1)
                    if beside:
                        beside.dve_end(dve, mod_columns)
                    dve.wait_ge(stored, 16 * BLOCKS)
                    tail.dve(dve, sums[:, 0:blocks], spread)

        def plain_gain(name):
            return lambda kt: pa(name)[:, kt:kt + 1]

        h_mem = Arena(nc, nc.sbuf_usable_end // 32 * 32 - 2 * KT * TOK * 4)
        h_hi = h_mem("h1_hi", [P, KT, TOK], F32R)
        h_lo = h_mem("h1_lo", [P, KT, TOK], F32R)
        shift = [lambda kt, s=s: mod[:, SH1 + kt, s:s + 1] for s in range(2)]
        gain = [lambda kt, s=s: gain1[:, kt, s:s + 1] for s in range(2)]
        w_in_k = A["w_in"].rearrange("o (k p) n -> p (o k) n", p=P)
        ATT_TILES = [(K_COL, K_COL + HEAD_DIM)] + [(Q_COL + j * HEAD_DIM, Q_COL + (4 + j) * HEAD_DIM) for j in range(4)]
        ATT_TILES += [(V_COL, V_COL + HEAD_DIM)]

        def att_weights(n):
            return [(w_raw[:, n % 2, :, i * HEAD_DIM:(i + 1) * HEAD_DIM], w_in_k[:, :, c:c + HEAD_DIM]) for i, c in enumerate(ATT_TILES[n])]

        phases.start()
        start_mem = Arena(nc, free_at)
        modulation = Modulation(start_mem, Arena(nc, nc.sbuf_usable_end // 32 * 32 - 2 * KT * TOK * 4))
        phase_rows_norm("norm1", start_mem, TOK, [(0, CTX, gain[1], shift[1]), (CTX, SEQ, gain[0], shift[0])], h_hi, h_lo,
                        [att_weights(0), att_weights(1)], modulation)

        att_mem = Arena(nc, free_at)
        q_cm = att_mem("q_cm", [P, N_HEADS // 2, SEQ])
        k_cm = att_mem("k_cm", [P, TOK])
        v_rows = att_mem("v_rows", [P, ALLCH, P])
        X0, X1, CX = (0, CTX, HALF, 0), (1, CTX + HALF, HALF, HALF), (2, 0, CTX, SEQ)

        def phase_attention_inputs():
            phases.start()
            mem = Arena(nc, att_mem.at)
            rope = mem("rope", [P, 2, SEQ])
            raw = mem("raw", [P, 2, TOK])
            sq = mem("qk_sq", [P, 2, TOK])
            rstd = mem("qk_rstd", [P, 2, TOK])
            normed = mem("qk_normed", [P, 2, TOK])
            turned = mem("qk_turned", [P, SEQ])
            ring = Ring("att", pieces=2)
            rope_loaded = sem("att_rope_loaded")
            z_free = sem("att_z_free")
            sq_done = sem("att_sq_done")
            raw_done = sem("att_raw_done")
            sums_done = sem("att_sums_done")
            root_done = sem("att_root_done")
            normed_done = sem("att_normed_done")
            rotated = sem("att_rotated")
            rotated_used = sem("att_rotated_used")
            v_turned = sem("att_v_turned")
            v_out = sem("att_v_out")
            roped = sem("att_roped")
            dve_step = sem("att_dve_step")
            groups = [[X0, X1, CX]] + [[X0, X1]] * 4 + [[X0, X1, CX]]
            KTILE, VTILE = 0, 5
            with nc.psum_tensor("att_z", [P, 2, 3, HALF], F32) as z, nc.psum_tensor("att_aux", [P, 2, HALF], F32) as aux, nc.Block() as block:
                @block.sync
                def _(sp):
                    sp.dma_start(rope[:], A["rope_table"]).then_inc(rope_loaded, 16)
                    for n in range(2, len(ATT_TILES)):
                        ring.load(sp, n, n % 2, att_weights(n))

                @block.gpsimd
                def _(pool):
                    ring.credits(pool, None)
                    for n in range(2, len(ATT_TILES)):
                        ring.do_split(pool, n, n % 2, n // 2)

                @block.tensor
                def _(pe):
                    ring.credits(None, pe)

                    first_sum = [sum(len(g) for g in groups[:n]) for n in range(len(groups))]

                    def proj(n, between=None):
                        ring.project(pe, n, n % 2, z_free, [(z[:, n % 2, b, 0:w], c0, w) for b, c0, w, _ in groups[n]], h_hi, h_lo, between)

                    def head_sums(n, g):
                        _, _, w, r0 = groups[n][g]
                        pe.wait_ge(sq_done, n + 1)
                        if first_sum[n] + g:
                            pe.wait_ge(root_done, first_sum[n] + g)
                        pe.matmul(aux[:, 0, 0:w], cst("head_ones"), sq[:, n % 2, r0:r0 + w], start=True, stop=True).then_inc(sums_done, 1)

                    def rotate(n, half):
                        pe.wait_ge(normed_done, n + 1)
                        if n or half:
                            pe.wait_ge(rotated_used, 2 * n + half)
                        pe.matmul(aux[:, 1, :], cst("rotate"), normed[:, n % 2, half * HALF:(half + 1) * HALF], start=True, stop=True).then_inc(rotated, 1)

                    proj(0)
                    for n in range(1, VTILE + 1):
                        beside = {2 + g: (lambda n=n, g=g: head_sums(n - 1, g)) for g in range(len(groups[n - 1]))}
                        if n >= 2:
                            beside.update({6 + half: (lambda n=n, half=half: rotate(n - 2, half)) for half in range(2)})
                        proj(n, beside)
                    for half in range(2):
                        rotate(VTILE - 1, half)
                    pe.wait_ge(raw_done, VTILE + 1)
                    pe.wait_ge(rotated_used, 2 * VTILE)
                    for g, (t0, count) in enumerate(((0, 4), (4, 4), (8, 2))):
                        if g == 2:
                            pe.wait_ge(v_out, 1)
                        for j in range(count):
                            at = (t0 + j) * P
                            ins = pe.transpose(aux[:, g % 2, j * P:(j + 1) * P], raw[:, VTILE % 2, at:at + P], ident)
                        ins.then_inc(v_turned, 1)

                @block.scalar
                def _(act):
                    act.sem_inc(z_free, 2)
                    sums = 0
                    for n in range(6):
                        if n:
                            for _, _, w, r0 in groups[n - 1]:
                                sums += 1
                                act.wait_ge(sums_done, sums)
                                if n >= 3:
                                    act.wait_ge(normed_done, n - 2)
                                act.activation(rstd[:, (n - 1) % 2, r0:r0 + w], aux[:, 0, 0:w], ACT.Sqrt, scale=1.0 / HEAD_DIM, bias=eps_col[:, 0:1]).then_inc(root_done, 1)
                        act.wait_ge(ring.projected, n + 3)
                        if 2 <= n:
                            act.wait_ge(normed_done, n - 1)
                        if n != VTILE:
                            for i, (b, _, w, r0) in enumerate(groups[n]):
                                ins = act.activation(sq[:, n % 2, r0:r0 + w], z[:, n % 2, b, 0:w], ACT.Square)
                            ins.then_inc(sq_done, 1)
                        for i, (b, _, w, r0) in enumerate(groups[n]):
                            ins = act.copy(raw[:, n % 2, r0:r0 + w], z[:, n % 2, b, 0:w])
                        ins.then_inc(z_free, 1)
                        act.wait_ge(z_free, n + 3)
                        act.sem_inc(raw_done, 1)

                @block.vector
                def _(dve):
                    step = Steps(dve, dve_step)
                    sums = 0
                    dve.wait_ge(rope_loaded, 16)
                    for n in range(5):
                        width = sum(w for _, _, w, _ in groups[n])
                        sums += len(groups[n])
                        dve.wait_ge(root_done, sums)
                        step(dve.reciprocal(rstd[:, n % 2, 0:width], rstd[:, n % 2, 0:width]))
                        step.wait()
                        dve.wait_ge(raw_done, n + 1)
                        g = 1 if n == KTILE else 0
                        dve.scalar_tensor_tensor(out=normed[:, n % 2, 0:width], in0=raw[:, n % 2, 0:width], scalar=qk_gain[:, g:g + 1],
                                                 in1=rstd[:, n % 2, 0:width], op0=ALU.mult, op1=ALU.mult).then_inc(normed_done, 1)
                        dve.wait_ge(normed_done, n + 1)
                        to = k_cm[:, CTX:] if n == KTILE else q_cm[:, n - 1, :]
                        if n == KTILE:
                            step(dve.tensor_copy(k_cm[:, 0:CTX], normed[:, n % 2, SEQ:TOK]))
                        step(dve.tensor_tensor(to, normed[:, n % 2, 0:SEQ], rope[:, 0], ALU.mult))
                        for half in range(2):
                            cols = slice(half * HALF, (half + 1) * HALF)
                            dve.wait_ge(rotated, 2 * n + half + 1)
                            dve.tensor_tensor(turned[:, cols], aux[:, 1, :], rope[:, 1, cols], ALU.mult).then_inc(rotated_used, 1)
                        dve.wait_ge(rotated_used, 2 * n + 2)
                        step.wait()
                        step(dve.tensor_tensor(to, to, turned[:], ALU.add))
                        step.wait()
                    for g, (t0, count) in enumerate(((0, 4), (4, 4), (8, 2))):
                        dve.wait_ge(v_turned, g + 1)
                        at = [(t0 + j + CCH) % ALLCH for j in range(count)]
                        split = next((j for j in range(1, count) if at[j] != at[j - 1] + 1), count)
                        for a, b in ((0, split), (split, count)):
                            if b > a:
                                ins = dve.tensor_copy(v_rows[:, at[a]:at[a] + b - a, :], aux[:, g % 2, a * P:b * P].rearrange("p (j n) -> p j n", n=P))
                        ins.then_inc(v_out, 1)

        def phase_attention():
            phases.start()
            mem = Arena(nc, att_mem.at)
            q_now = mem("q_now", [P, SEQ])
            out_now = mem("att_out_now", [P, SEQ])
            s = [mem(f"att_s{a}", [P, 1 + 5 * P]) for a in range(2)]
            p = [mem(f"att_p{a}", [P, 1 + 5 * P]) for a in range(2)]
            p_t = mem("att_p_t", [P, 2, 5, P])
            neg_max = mem("att_neg_max", [P, 2])
            den = mem("att_den", [P, 2])
            zeros = mem("att_zeros", [P, D])
            zeroed = sem("win_zeroed")
            cleared = sem("win_ffn_cleared")
            q_copied = sem("win_q_copied")
            scores = sem("win_scores")
            local_in = sem("win_local_in")
            ctx_in = sem("win_ctx_in")
            max_done = sem("win_max_done")
            probs = sem("win_probs")
            scaled = sem("win_scaled")
            p_turned = sem("win_p_turned")
            near_out = sem("win_near_out")
            last_out = sem("win_last_out")
            pv_done = sem("win_pv_done")
            o_out = sem("win_o_out")
            stored = sem("win_stored")
            dve_step = sem("win_dve_step")
            pre = Prefetch("win", [[(w_raw[:, i], w_in_k[:, :, col:col + M_DIM])] for i, col in enumerate((MQ_COL, MK_COL))])
            U = 2 * BLOCKS
            near = [range(max(n - 1, 0), min(n + 2, BLOCKS)) for n in range(BLOCKS)]
            with nc.psum_tensor("win_s", [P, 2, 2, HALF], F32) as ps, nc.psum_tensor("win_t", [P, 2, HALF], F32) as pt, \
                    nc.psum_tensor("win_o", [P, 2, HALF], F32) as po, nc.Block() as block:
                @block.sync
                def _(sp):
                    pre.load(sp)
                    sp.wait_ge(zeroed, 1)
                    for j in range(BLOCKS):
                        sp.dma_start(ffn_rows[j * P:(j + 1) * P, :], zeros[:]).then_inc(cleared, 16)
                    sp.wait_ge(cleared, 16 * BLOCKS)

                @block.gpsimd
                def _(pool):
                    pool.memset(zeros[:], 0.0).then_inc(zeroed, 1)
                    pre.split(pool)

                @block.tensor
                def _(pe):
                    with pe.Fori(0, 4) as j:
                        def score(u):
                            n, a = u // 2, u % 2
                            rows = slice(a * HEAD_DIM, (a + 1) * HEAD_DIM)
                            w, k0 = len(near[n]) * P, CTX + near[n][0] * P
                            pe.wait_ge(local_in, j * U + u + 1)
                            pe.wait_ge(ctx_in, j * U + u + 1)
                            pe.matmul(ps[:, a, 0, 0:w], q_now[rows, n * P:(n + 1) * P], k_cm[rows, k0:k0 + w], start=True, stop=True)
                            pe.matmul(ps[:, a, 1, 0:CTX], q_now[rows, n * P:(n + 1) * P], k_cm[rows, 0:CTX], start=True, stop=True).then_inc(scores, 1)

                        def value_tiles(n):
                            return [CCH + t for t in near[n]] + [0, 1]

                        def turn(u):
                            n, a = u // 2, u % 2
                            nt = len(value_tiles(n))
                            pe.wait_ge(near_out, j * U + u + 1)
                            pe.wait_ge(last_out, j * U + u + 1)
                            pe.wait_ge(scaled, j * U + u + 2)
                            for t in range(nt):
                                to = pt[:, 1, 0:P] if t == nt - 1 else pt[:, 0, t * P:(t + 1) * P]
                                ins = pe.transpose(to, p[a][:, 1 + t * P:1 + (t + 1) * P], ident)
                            ins.then_inc(p_turned, 1)

                        def weigh(u):
                            n, a = u // 2, u % 2
                            tiles = value_tiles(n)
                            nt = len(tiles)
                            if a == 0:
                                pe.wait_ge(o_out, j * BLOCKS + n + 1)
                            pe.wait_ge(near_out, j * U + u + 2)
                            pe.wait_ge(last_out, j * U + u + 2)
                            cols = slice(a * HEAD_DIM, (a + 1) * HEAD_DIM)
                            for t in range(nt):
                                ins = pe.matmul(po[cols, n % 2, 0:P], v_rows[:, tiles[t], cols], p_t[:, a, 4 if t == nt - 1 else t, :],
                                                start=(t == 0), stop=(t == nt - 1))
                            ins.then_inc(pv_done, 1)

                        pe.wait_ge(q_copied, j + 1)
                        score(0)
                        score(1)
                        for u in range(U):
                            if u + 2 < U:
                                score(u + 2)
                            if u:
                                weigh(u - 1)
                            turn(u)
                        weigh(U - 1)

                @block.scalar
                def _(act):
                    act.sem_inc(ctx_in, 2)
                    act.sem_inc(last_out, 1)
                    act.sem_inc(o_out, 2)
                    act.sem_inc(probs, 2)
                    act.sem_inc(stored, 16)
                    with act.Fori(0, 4) as j:
                        def take_ctx(u):
                            n, a = u // 2, u % 2
                            at = 1 + len(near[n]) * P
                            act.wait_ge(scores, j * U + u + 2)
                            act.wait_ge(probs, j * U + u + 1)
                            act.copy(s[a][:, at:at + CTX], ps[:, a, 1, 0:CTX]).then_inc(ctx_in, 1)

                        def exps(u):
                            n, a = u // 2, u % 2
                            w = 1 + len(near[n]) * P + CTX
                            act.wait_ge(max_done, j * U + u + 1)
                            act.wait_ge(p_turned, j * U + u)
                            act.wait_ge(scaled, j * U + u)
                            act.activation(p[a][:, 0:w], s[a][:, 0:w], ACT.Exp, bias=neg_max[:, a:a + 1],
                                           accum_out=den[:, a:a + 1]).then_inc(probs, 1)

                        def take_last(u):
                            act.wait_ge(p_turned, j * U + u + 2)
                            act.wait_ge(pv_done, j * U + u + 1)
                            act.copy(p_t[:, u % 2, 4, :], pt[:, 1, 0:P]).then_inc(last_out, 1)

                        def take_out(u):
                            n, a = u // 2, u % 2
                            if a == 1:
                                if n == 0:
                                    act.wait_ge(stored, 16 * j + 16)
                                act.wait_ge(pv_done, j * U + u + 3)
                                act.copy(out_now[:, n * P:(n + 1) * P], po[:, n % 2, 0:P]).then_inc(o_out, 1)

                        take_ctx(0)
                        exps(0)
                        take_ctx(1)
                        for u in range(U):
                            if u + 1 < U:
                                exps(u + 1)
                            if u:
                                take_out(u - 1)
                            if u + 2 < U:
                                take_ctx(u + 2)
                            take_last(u)
                        take_out(U - 1)
                        act.wait_ge(o_out, j * BLOCKS + BLOCKS + 2)
                        act.dma_start(att_cm.rearrange("(j p) t -> p j t", p=P)[:, bass.ds(j, 1), :],
                                      out_now[:].rearrange("p (o t) -> p o t", o=1)).then_inc(stored, 16)
                    act.wait_ge(stored, 16 * 5)

                @block.vector
                def _(dve):
                    dve.sem_inc(local_in, 2)
                    dve.sem_inc(near_out, 1)
                    dve.sem_inc(pv_done, 2)
                    dve.sem_inc(scores, 1)
                    dve.sem_inc(p_turned, 1)
                    dve.sem_inc(scaled, 1)
                    N_STEP = U
                    with dve.Fori(0, 4) as j:
                        def local_and_max(u):
                            n, a = u // 2, u % 2
                            w = len(near[n]) * P
                            m0 = (near[n][0] - n + 1) * P
                            dve.wait_ge(scores, j * U + u + 2)
                            dve.wait_ge(probs, j * U + u + 1)
                            dve.tensor_tensor(s[a][:, 1:1 + w], ps[:, a, 0, 0:w], cst("near_mask")[:, m0:m0 + w], ALU.add).then_inc(local_in, 1)
                            dve.wait_ge(local_in, j * U + u + 3)
                            dve.wait_ge(ctx_in, j * U + u + 3)
                            dve.tensor_reduce(neg_max[:, a:a + 1], s[a][:, 0:1 + w + CTX], AX_X, ALU.max, negate=True).then_inc(max_done, 1)

                        dve.wait_ge(probs, j * U + 2)
                        dve.wait_ge(scores, j * U + 1)
                        for a in range(2):
                            dve.tensor_scalar(s[a][:, 0:1], sinks[:, bass.ds(j + 4 * a, 1)], 0.0, None, ALU.add)
                        dve.tensor_scalar(q_now[:], q_cm[:, bass.ds(j, 1), :].rearrange("p o t -> p (o t)"), HEAD_DIM ** -0.5, None,
                                          ALU.mult).then_inc(q_copied, 1)
                        dve.wait_ge(q_copied, j + 1)
                        local_and_max(0)
                        local_and_max(1)
                        for u in range(U):
                            n, a = u // 2, u % 2
                            w = len(near[n]) * P + CTX
                            dve.wait_ge(probs, j * U + u + 3)
                            dve.reciprocal(den[:, a:a + 1], den[:, a:a + 1]).then_inc(dve_step, 1)
                            dve.wait_ge(dve_step, j * N_STEP + u + 1)
                            dve.tensor_scalar(p[a][:, 1:1 + w], p[a][:, 1:1 + w], den[:, a:a + 1], None, ALU.mult).then_inc(scaled, 1)
                            if u + 2 < U:
                                local_and_max(u + 2)
                            dve.wait_ge(p_turned, j * U + u + 2)
                            dve.wait_ge(pv_done, j * U + u + 1)
                            nn = len(near[n]) + 1
                            dve.tensor_copy(p_t[:, a, 0:nn, :], pt[:, 0, 0:nn * P].rearrange("p (t q) -> p t q", q=P)).then_inc(near_out, 1)

        phase_attention_inputs()
        phase_attention()

        m_mem = Arena(nc, free_at)
        mq_cm = m_mem("mq_cm", [P, M_HEADS, SEQ])
        mk_cm = m_mem("mk_cm", [P, M_HEADS, TOK])
        v_ext = m_mem("v_ext", [P, ALLCH, M_HEADS, M_DIM + 1])
        out_gate = m_mem("out_gate", [P, M_HEADS, SEQ])
        gates_raw = m_mem("gates_raw", [P, TOK])

        def phase_mlstm_inputs():
            phases.start()
            mem = Arena(nc, m_mem.at)
            XPAD, CPAD = 1, SEQ + 3
            PADDED = SEQ + CTX + 4
            padded = mem("conv_padded", [P, PADDED])
            conv = mem("conv_sum", [P, PADDED - 2])
            taps = mem("conv_taps", [P, 3, 2, 1])
            ring = Ring("mls")
            z_free = sem("mls_z_free")
            padded_done = sem("mls_padded_done")
            pad_free = sem("mls_pad_free")
            conv_done = sem("mls_conv_done")
            conv_used = sem("mls_conv_used")
            v_turned = sem("mls_v_turned")
            v_out = sem("mls_v_out")
            gates_zeroed = sem("mls_gates_zeroed")
            gates_out = sem("mls_gates_out")
            dve_step = sem("mls_dve_step")
            cleared = sem("mls_cleared")
            groups = [[X0, X1], [X0, X1, CX], [X0, X1, CX], [X0, X1]]
            G = 4 * M_HEADS
            with nc.psum_tensor("mls_z", [P, 2, 3, HALF], F32) as z, nc.psum_tensor("mls_aux", [P, 2, HALF], F32) as aux, nc.Block() as block:
                @block.sync
                def _(sp):
                    ring.load_all(sp, M_HEADS, 4, lambda h, i: [(w_raw[:, i % 2], w_in_k[:, :, bass.ds(h * M_DIM + (MQ_COL, MK_COL, MV_COL, MO_COL)[i], M_DIM)])])
                    sp.wait_ge(gates_zeroed, 1)
                    for row, at in ((0, 0), (64, 4), (32, 8), (96, 12)):
                        sp.dma_start(w_raw[:, 0, :, row:row + M_HEADS], w_in_k[:, :, G_COL + at:G_COL + at + M_HEADS]).then_inc(ring.loaded[0], 16)

                @block.gpsimd
                def _(pool):
                    ring.credits(pool, None)
                    ring.split_all(pool, M_HEADS, 4)
                    pool.wait_ge(ring.split, G + 1)
                    pool.memset(w_raw[:, 0], 0.0).then_inc(gates_zeroed, 1)
                    ring.do_split(pool, G, 0, 2 * M_HEADS + 3)

                @block.tensor
                def _(pe):
                    ring.credits(None, pe)
                    pe.wait_ge(cleared, 1)

                    def proj(n, i, between=None):
                        ring.project(pe, n, i % 2, z_free, [(z[:, i % 2, b, 0:w], c0, w) for b, c0, w, _ in groups[i]], h_hi, h_lo, between)

                    def turn_v(h):
                        for g, (t0, count) in enumerate(((0, 4), (4, 4), (8, 2))):
                            if g == 0:
                                pe.wait_ge(padded_done, 3 * h + 3)
                            if g == 2:
                                pe.wait_ge(v_out, 3 * h + 1 + 1)
                            else:
                                pe.wait_ge(v_out, 3 * h + 1)
                            for t in range(t0, t0 + count):
                                at = CPAD + t * P if t < CCH else XPAD + (t - CCH) * P
                                ins = pe.transpose(aux[:, g % 2, (t - t0) * P:(t - t0 + 1) * P], padded[:, at:at + P], ident)
                            ins.then_inc(v_turned, 1)

                    with pe.Fori(0, M_HEADS) as h:
                        for i in range(4):
                            proj(4 * h + i, i)
                        turn_v(h)
                    ring.project(pe, G, 0, z_free, [(z[:, 0, b, 0:w], c0, w) for b, c0, w, _ in groups[1]], h_hi, h_lo)

                @block.scalar
                def _(act):
                    act.sem_inc(z_free, 2)
                    act.sem_inc(conv_used, 1)
                    act.wait_ge(cleared, 1)
                    with act.Fori(0, M_HEADS) as h:
                        def pad(i, round_):
                            act.wait_ge(ring.projected, 4 * h + i + 3)
                            act.wait_ge(pad_free, round_ + 1)
                            for b, _, w, r0 in groups[i]:
                                at = CPAD if b == 2 else XPAD + r0
                                ins = act.copy(padded[:, at:at + w], z[:, i % 2, b, 0:w])
                            ins.then_inc(z_free, 1)
                            act.wait_ge(z_free, 4 * h + i + 3)
                            act.sem_inc(padded_done, 1)

                        pad(0, 3 * h)
                        act.wait_ge(conv_done, 2 * h + 1)
                        pass_waits(act)
                        act.activation(mq_cm[:, bass.ds(h, 1), :].rearrange("p o t -> p (o t)"), conv[:, 0:SEQ], ACT.Silu).then_inc(conv_used, 1)
                        pad(1, 3 * h + 1)
                        act.wait_ge(conv_done, 2 * h + 2)
                        pass_waits(act)
                        act.activation(mk_cm[:, bass.ds(h, 1), CTX:].rearrange("p o t -> p (o t)"), conv[:, 0:SEQ], ACT.Silu)
                        act.activation(mk_cm[:, bass.ds(h, 1), 0:CTX].rearrange("p o t -> p (o t)"), conv[:, SEQ + 2:SEQ + 2 + CTX],
                                       ACT.Silu).then_inc(conv_used, 1)
                        pad(2, 3 * h + 2)
                        act.wait_ge(ring.projected, 4 * h + 3 + 3)
                        pass_waits(act)
                        for half in range(2):
                            ins = act.activation(out_gate[:, bass.ds(h, 1), half * HALF:(half + 1) * HALF].rearrange("p o t -> p (o t)"),
                                                 z[:, 1, half, :], ACT.Sigmoid)
                        ins.then_inc(z_free, 1)
                    act.wait_ge(ring.projected, G + 3)
                    for b, c0, w, _ in groups[1]:
                        act.copy(gates_raw[:, c0:c0 + w], z[:, 0, b, 0:w]).then_inc(gates_out, 1)

                @block.vector
                def _(dve):
                    dve.memset(padded[:], 0.0).then_inc(dve_step, 1)
                    dve.memset(v_ext[:].rearrange("p t h n -> p (t h) n")[:, :, M_DIM:M_DIM + 1], 1.0).then_inc(dve_step, 1)
                    dve.wait_ge(dve_step, 2)
                    dve.sem_inc(pad_free, 1)
                    dve.sem_inc(v_out, 1)
                    dve.sem_inc(cleared, 1)
                    N_STEP = 5
                    with dve.Fori(0, M_HEADS) as h:
                        step = Steps(dve, dve_step, h * N_STEP + 2)
                        dve.wait_ge(conv_used, 2 * h + 1)
                        pass_waits(dve)
                        step(dve.tensor_copy(taps[:], pb("conv_qk").rearrange("p (j s h) -> p j s h", j=3, s=2)[:, :, :, bass.ds(h, 1)]))
                        step.wait()
                        for s in range(2):
                            width = SEQ if s == 0 else PADDED - 2
                            dve.wait_ge(padded_done, 3 * h + s + 1)
                            dve.wait_ge(conv_used, 2 * h + s + 1)
                            step(dve.tensor_scalar(conv[:, 0:width], padded[:, 0:width], taps[:, 0, s, :], None, ALU.mult))
                            step.wait()
                            step(dve.scalar_tensor_tensor(out=conv[:, 0:width], in0=padded[:, 1:1 + width], scalar=taps[:, 1, s, :],
                                                          in1=conv[:, 0:width], op0=ALU.mult, op1=ALU.add))
                            step.wait()
                            dve.scalar_tensor_tensor(out=conv[:, 0:width], in0=padded[:, 2:2 + width], scalar=taps[:, 2, s, :],
                                                     in1=conv[:, 0:width], op0=ALU.mult, op1=ALU.add).then_inc(conv_done, 1)
                            dve.wait_ge(conv_done, 2 * h + s + 1)
                            dve.sem_inc(pad_free, 1)
                        assert step.done == N_STEP
                        for g, (t0, count) in enumerate(((0, 4), (4, 4), (8, 2))):
                            dve.wait_ge(v_turned, 3 * h + g + 1)
                            pass_waits(dve)
                            ins = dve.tensor_copy(v_ext[:, t0:t0 + count, bass.ds(h, 1), 0:M_DIM].rearrange("p t o n -> p t (o n)"),
                                                  aux[:, g % 2, 0:count * P].rearrange("p (t n) -> p t n", n=P))
                            ins.then_inc(v_out, 1)
                        dve.wait_ge(v_out, 3 * h + 3 + 1)
                        dve.sem_inc(pad_free, 1)

        s_mem = Arena(nc, m_mem.at)
        neg_m = s_mem("neg_m", [GATE_ROWS, TOK])
        pick = s_mem("pick", [GATE_ROWS, 8, P])
        tok_gate = s_mem("tok_gate", [P, 4, ALLCH, GATE_ROWS])
        carry = s_mem("carry", [P, 8, ALLCH])
        GG, WS, DECAY, FLOOR = range(4)

        def phase_gate_scans():
            phases.start()
            mem = Arena(nc, s_mem.at)
            names = ("keep", "log_i", "log_f", "tmp", "b", "g", "run_max", "jump", "pre_ws", "pre_decay", "pre_floor", "time_gate")
            t = {n: mem(f"scan_{n}", [GATE_ROWS, TOK] if n != "time_gate" else [GATE_ROWS, 4, TOK]) for n in names}
            start_m = mem("scan_start_m", [GATE_ROWS, ALLCH])
            step_decay = mem("scan_step_decay", [GATE_ROWS, ALLCH])
            loaded = sem("scan_loaded")
            dve_step = sem("scan_dve_step")
            act_step = sem("scan_act_step")
            f_ready = sem("scan_f_ready")
            log_done = sem("scan_log_done")
            pre_done = sem("scan_pre_done")
            exp_done = sem("scan_exp_done")
            g_done = sem("scan_g_done")
            turned = sem("scan_turned")
            copied = sem("scan_copied")
            B0 = 32

            def by_time(dst, rows=GATE_ROWS):
                return [(dst[0:B0], slice(0, B0), slice(None)), (dst[B0:GATE_ROWS, CTX - 1::-1], slice(B0, GATE_ROWS), slice(0, CTX)),
                        (dst[B0:GATE_ROWS, TOK - 1:CTX - 1:-1], slice(B0, GATE_ROWS), slice(CTX, TOK))]

            def chunks(x):
                return x.rearrange("p (c t) -> p c t", t=CHUNK)

            with nc.psum_tensor("scan_turn", [P, 4, HALF], F32) as turn, nc.psum_tensor("scan_carry", [P, HALF], F32) as cps, nc.Block() as block:
                @block.sync
                def _(sp):
                    sp.dma_start(t["keep"][:], A["keep_table"]).then_inc(loaded, 16)
                    sp.dma_start(pick[:].rearrange("p r n -> p (r n)"), A["pick_table"]).then_inc(loaded, 16)

                @block.vector
                def _(dve):
                    step = Steps(dve, dve_step)
                    for name, at in (("log_i", 0), ("log_f", 64)):
                        rows = gates_raw[at:at + GATE_ROWS]
                        bias = gate_bias[at:at + GATE_ROWS]
                        for dst, r, cols in by_time(t[name]):
                            step(dve.tensor_scalar(dst, rows[r, cols], bias[r], None, ALU.add))
                    step.wait()
                    dve.sem_inc(f_ready, 1)
                    step(dve.tensor_scalar(t["jump"][:], t["log_f"][:], 0.0, None, ALU.min))
                    step.wait()
                    dve.wait_ge(log_done, 1)
                    step(dve.tensor_tensor(t["log_f"][:], t["jump"][:], t["tmp"][:], ALU.subtract))
                    step.wait()
                    dve.wait_ge(loaded, 32)
                    step(dve.tensor_tensor_scan(t["b"][:], t["keep"][:], t["log_f"][:], 0.0, ALU.mult, ALU.add))
                    step(dve.memset(t["jump"][:], 0.0))
                    step.wait()
                    last_b = chunks(t["b"][:])[:, :, CHUNK - 1]
                    step(dve.tensor_copy(chunks(t["jump"][:])[:, 1:, 0], last_b[:, 0:ALLCH - 1]))
                    step(dve.tensor_tensor(t["g"][:], t["log_i"][:], t["b"][:], ALU.subtract))
                    step.wait()
                    step(dve.tensor_tensor_scan(t["run_max"][:], t["jump"][:], t["g"][:], 0.0, ALU.add, ALU.max))
                    step(dve.memset(start_m[:], 0.0))
                    step.wait()
                    last_max = chunks(t["run_max"][:])[:, :, CHUNK - 1]
                    step(dve.tensor_tensor(start_m[:, 1:], last_b[:, 0:ALLCH - 1], last_max[:, 0:ALLCH - 1], ALU.add))
                    for dst, r, cols in by_time(neg_m[:]):
                        step(dve.tensor_scalar(dst, t["run_max"][r, cols], -1.0, None, ALU.mult))
                    step.wait()
                    wide = [GATE_ROWS, ALLCH, CHUNK]
                    step(dve.tensor_tensor(step_decay[:], start_m[:], last_max, ALU.subtract))
                    step(dve.tensor_tensor(chunks(t["pre_ws"][:]), chunks(t["g"][:]), last_max.unsqueeze(2).to_broadcast(wide), ALU.subtract))
                    step(dve.tensor_tensor(chunks(t["pre_decay"][:]), start_m[:].unsqueeze(2).to_broadcast(wide), chunks(t["run_max"][:]), ALU.subtract))
                    step(dve.tensor_tensor(t["pre_floor"][:], t["b"][:], t["run_max"][:], ALU.add))
                    step.wait()
                    dve.sem_inc(pre_done, 1)
                    for dst, r, cols in by_time(t["time_gate"][:, GG, :]):
                        step(dve.tensor_copy(dst, t["g"][r, cols]))
                    step.wait()
                    dve.sem_inc(g_done, 1)
                    dve.wait_ge(turned, 5)
                    step(dve.tensor_copy(carry[:], cps[:, 0:8 * ALLCH].rearrange("p (r c) -> p r c", c=ALLCH)))
                    dve.wait_ge(copied, 4)
                    step(dve.tensor_scalar(tok_gate[:, DECAY], tok_gate[:, DECAY], M_DIM ** -0.5, None, ALU.mult))

                @block.scalar
                def _(act):
                    step = Steps(act, act_step)
                    act.wait_ge(f_ready, 1)
                    step(act.activation(t["tmp"][:], t["log_f"][:], ACT.Abs))
                    step.wait()
                    step(act.activation(t["tmp"][:], t["tmp"][:], ACT.Exp, scale=-1.0))
                    step.wait()
                    act.activation(t["tmp"][:], t["tmp"][:], ACT.Ln, bias=1.0).then_inc(log_done, 1)
                    act.wait_ge(pre_done, 1)
                    act.activation(step_decay[:], step_decay[:], ACT.Exp).then_inc(exp_done, 1)
                    for q, name, sign in ((WS, "pre_ws", 1.0), (DECAY, "pre_decay", 1.0), (FLOOR, "pre_floor", -1.0)):
                        for dst, r, cols in by_time(t["time_gate"][:, q, :]):
                            act.activation(dst, t[name][r, cols], ACT.Exp, scale=sign).then_inc(exp_done, 1)
                    for i, q in enumerate((GG, WS, DECAY, FLOOR)):
                        act.wait_ge(turned, i + 2)
                        act.copy(tok_gate[:, q], turn[:, q, 0:ALLCH * GATE_ROWS].rearrange("p (c r) -> p c r", r=GATE_ROWS)).then_inc(copied, 1)

                @block.tensor
                def _(pe):
                    pe.wait_ge(loaded, 32)
                    pe.wait_ge(exp_done, 1)
                    for r in range(8):
                        ins = pe.matmul(cps[:, r * ALLCH:(r + 1) * ALLCH], pick[:, r, :], step_decay[:], start=True, stop=True)
                    ins.then_inc(turned, 1)
                    for i, q in enumerate((GG, WS, DECAY, FLOOR)):
                        if q == GG:
                            pe.wait_ge(g_done, 1)
                        else:
                            pe.wait_ge(exp_done, 1 + 3 * i)
                        for c in range(ALLCH):
                            ins = pe.transpose(turn[:, q, c * GATE_ROWS:(c + 1) * GATE_ROWS], t["time_gate"][:, q, c * CHUNK:(c + 1) * CHUNK],
                                               ident[0:GATE_ROWS, 0:GATE_ROWS])
                        ins.then_inc(turned, 1)

        r_mem = Arena(nc, s_mem.at)
        h_sum = r_mem("h_sum", [P, XCH, M_HEADS, M_DIM])

        def phase_mlstm():
            phases.start()
            mem = Arena(nc, r_mem.at)
            E1 = M_DIM + 1
            state = mem("state", [P, 8, E1])
            k_now = mem("k_now", [P, 2, 2, M_HEADS, CHUNK])
            q_now = mem("mq_now", [P, 2, 2, M_HEADS, CHUNK])
            g_now = mem("g_now", [P, 2, 2, 4, M_HEADS])
            a_now = mem("a_now", [P, 2, 8])
            weight = mem("m_weight", [P, 2, CHUNK])
            w_qk = mem("m_w_qk", [P, 2, CHUNK])
            k_w = mem("m_k_w", [P, 2, M_DIM])
            inter = mem("m_inter", [P, 2, E1])
            total = mem("m_total", [P, 2, M_HEADS, E1])
            size = mem("m_size", [P, 2, M_HEADS, 1])
            fetched = sem("mlc_fetched")
            first_done = sem("mlc_first_done")
            second_done = sem("mlc_second_done")
            weight_done = sem("mlc_weight_done")
            k_w_done = sem("mlc_k_w_done")
            w_qk_done = sem("mlc_w_qk_done")
            inter_done = sem("mlc_inter_done")
            state_done = sem("mlc_state_done")
            total_done = sem("mlc_total_done")
            group_done = sem("mlc_group_done")
            dve_step = sem("mlc_dve_step")
            cleared = sem("mlc_cleared")
            U = 16
            with nc.psum_tensor("mlc_wk", [P, 2, HALF], F32) as p_wk, nc.psum_tensor("mlc_qk", [P, 2, HALF], F32) as p_qk, \
                    nc.psum_tensor("mlc_num", [P, 2, HALF], F32) as p_num, nc.psum_tensor("mlc_inter", [P, 2, HALF], F32) as p_int, nc.Block() as block:

                def unit(u):
                    return u // 8, u % 8, (u % 8) // M_HEADS, u % M_HEADS, u % 2

                @block.gpsimd
                def _(pool):
                    pool.wait_ge(cleared, 1)

                    def fetch(par, chunk, s, with_q):
                        for d in range(2):
                            for now, all_, off in ((k_now, mk_cm, 0),) + (((q_now, mq_cm, CTX),) if with_q else ()):
                                at = chunk[d] * CHUNK - off
                                pool.tensor_copy(now[:, par, d], all_[:, :, bass.ds(at, CHUNK)]).then_inc(fetched, 1)
                            pool.tensor_copy(g_now[:, par, d].rearrange("p q (c h) -> p q c h", c=1),
                                             tok_gate[:, :, bass.ds(chunk[d], 1), 32 * d:32 * d + M_HEADS]).then_inc(fetched, 1)
                        pool.tensor_copy(a_now[:, par, :].rearrange("p (r c) -> p r c", c=1), carry[:, :, bass.ds(s, 1)]).then_inc(fetched, 1)

                    for s in range(CCH):
                        fetch(s % 2, (s, CCH - 1 - s), s, False)
                    with pool.Fori(0, XCH // 2) as i:
                        for par in range(2):
                            pool.wait_ge(state_done, i * U + 8 * (par + 1) + 2)
                            pool.wait_ge(group_done, 4 * i + 2 * (par + 1))
                            pass_waits(pool)
                            fetch(par, (2 * i + par + CCH, ALLCH - 1 - par - 2 * i), 2 * i + par + CCH, True)

                C_FETCH, X_FETCH = 5, 7

                @block.tensor
                def _(pe):
                    def first(u, base, x):
                        par, r, d, h, b = unit(u)
                        pe.wait_ge(k_w_done, base + u + 1)
                        if x is not None:
                            pe.wait_ge(weight_done, x * U + u + 1)
                            pe.wait_ge(w_qk_done, x * U + u + 1)
                            c = 2 * x + par + CCH if d == 0 else ALLCH - 1 - par - 2 * x
                            pass_waits(pe)
                            pe.matmul(p_wk[:, b, 0:CHUNK], pick[:, r, :], neg_m[:, bass.ds(c * CHUNK, CHUNK)], start=True, stop=False)
                            pe.matmul(p_wk[:, b, 0:CHUNK], ident, cst("chunk_mask")[:, d * P:(d + 1) * P], start=False, stop=True)
                            pe.matmul(p_qk[:, b, 0:CHUNK], k_now[:, par, d, h, :], q_now[:, par, d, h, :], start=True, stop=True)
                        pe.transpose(p_wk[:, b, CHUNK:2 * CHUNK], k_now[:, par, d, h, :], ident).then_inc(first_done, 1)

                    def second(u, base, x):
                        par, r, d, h, b = unit(u)
                        pe.wait_ge(state_done, base + u + 1)
                        if x is not None:
                            pe.wait_ge(total_done, x * U + u + 1)
                            c = 2 * x + par + CCH if d == 0 else ALLCH - 1 - par - 2 * x
                            values = v_ext[:, bass.ds(c, 1), h, :].rearrange("p o n -> p (o n)")
                            pe.wait_ge(inter_done, x * U + u + 1)
                            pe.wait_ge(w_qk_done, x * U + u + 3)
                            pass_waits(pe)
                            pe.matmul(p_num[:, b, 0:E1], w_qk[:, b, :], values, start=True, stop=True)
                            pe.matmul(p_int[:, b, 0:E1], q_now[:, par, d, h, :], state[:, r, :], start=True, stop=True)
                        else:
                            c = par if d == 0 else CCH - 1 - par
                            values = v_ext[:, c, h, :]
                        pe.wait_ge(k_w_done, base + u + 3)
                        if x is not None:
                            pass_waits(pe)
                        pe.matmul(p_num[:, b, 256:256 + E1], k_w[:, b, :], values, start=True, stop=True).then_inc(second_done, 1)

                    def units(base, x, fetches):
                        pe.wait_ge(fetched, fetches[0])
                        first(0, base, x)
                        first(1, base, x)
                        for u in range(U):
                            second(u, base, x)
                            if u + 2 < U:
                                if u + 2 == U // 2:
                                    pe.wait_ge(fetched, fetches[1])
                                first(u + 2, base, x)

                    units(0, None, (C_FETCH, 2 * C_FETCH))
                    with pe.Fori(0, XCH // 2) as i:
                        done = 2 * C_FETCH + 2 * X_FETCH * i
                        units((i + 1) * U, i, (done + X_FETCH, done + 2 * X_FETCH))

                @block.scalar
                def _(act):
                    act.sem_inc(k_w_done, 2)
                    act.sem_inc(weight_done, 2)
                    act.sem_inc(inter_done, 2)

                    def first(u, base, x):
                        par, r, d, h, b = unit(u)
                        act.wait_ge(first_done, base + u + 1)
                        if x is not None:
                            act.wait_ge(w_qk_done, x * U + u + 1)
                            act.activation(weight[:, b, :], p_wk[:, b, 0:CHUNK], ACT.Exp, bias=g_now[:, par, d, GG, h:h + 1]).then_inc(weight_done, 1)
                        act.wait_ge(state_done, base + u + 1)
                        act.activation(k_w[:, b, :], p_wk[:, b, CHUNK:2 * CHUNK], ACT.Copy, scale=g_now[:, par, d, WS, h:h + 1]).then_inc(k_w_done, 1)

                    def second(u, base, x):
                        par, r, d, h, b = unit(u)
                        if x is not None:
                            act.wait_ge(second_done, base + u + 1)
                            act.activation(inter[:, b, :], p_int[:, b, 0:E1], ACT.Copy, scale=g_now[:, par, d, DECAY, h:h + 1]).then_inc(inter_done, 1)

                    def units(base, x):
                        first(0, base, x)
                        first(1, base, x)
                        for u in range(U):
                            second(u, base, x)
                            if u + 2 < U:
                                first(u + 2, base, x)

                    units(0, None)
                    with act.Fori(0, XCH // 2) as i:
                        units((i + 1) * U, i)

                @block.vector
                def _(dve):
                    dve.memset(state[:], 0.0).then_inc(dve_step, 1)
                    dve.memset(h_sum[:], 0.0).then_inc(dve_step, 1)
                    dve.wait_ge(dve_step, 2)
                    dve.sem_inc(w_qk_done, 2)
                    dve.sem_inc(total_done, 2)
                    dve.sem_inc(group_done, 4)
                    dve.sem_inc(state_done, 2)
                    dve.sem_inc(cleared, 1)

                    def first(u, base, x):
                        par, r, d, h, b = unit(u)
                        if x is not None:
                            dve.wait_ge(weight_done, x * U + u + 3)
                            dve.wait_ge(second_done, base + u - 1)
                            dve.scalar_tensor_tensor(out=w_qk[:, b, :], in0=p_qk[:, b, 0:CHUNK], scalar=M_DIM ** -0.5, in1=weight[:, b, :],
                                                     op0=ALU.mult, op1=ALU.mult).then_inc(w_qk_done, 1)

                    def second(u, base, x, steps):
                        par, r, d, h, b = unit(u)
                        dve.wait_ge(second_done, base + u + 1)
                        dve.scalar_tensor_tensor(out=state[:, r, :], in0=state[:, r, :], scalar=a_now[:, par, r:r + 1], in1=p_num[:, b, 256:256 + E1],
                                                 op0=ALU.mult, op1=ALU.add).then_inc(state_done, 1)
                        if x is not None:
                            dve.wait_ge(inter_done, x * U + u + 3)
                            dve.tensor_tensor(total[:, (u // M_HEADS) % 2, h, :], p_num[:, b, 0:E1], inter[:, b, :], ALU.add).then_inc(total_done, 1)
                            if h == M_HEADS - 1:
                                finish(u // M_HEADS, par, d, x, steps)

                    def finish(q, par, d, x, steps):
                        sums, den, by = total[:, q % 2, :, 0:M_DIM], total[:, q % 2, :, M_DIM:E1], size[:, q % 2]
                        dve.wait_ge(total_done, x * U + (q + 1) * M_HEADS + 2)
                        steps(dve.scalar_tensor_tensor(out=by, in0=den, scalar=-1.0, in1=den, op0=ALU.mult, op1=ALU.max))
                        steps.wait()
                        steps(dve.tensor_tensor(by, by, g_now[:, par, d, FLOOR, :].unsqueeze(2), ALU.max))
                        steps.wait()
                        steps(dve.reciprocal(by, by))
                        steps.wait()
                        steps(dve.tensor_tensor(sums, sums, by.to_broadcast([P, M_HEADS, M_DIM]), ALU.mult))
                        steps.wait()
                        pass_waits(dve)
                        c = 2 * x + par if d == 0 else XCH - 1 - par - 2 * x
                        to = h_sum[:, bass.ds(c, 1), :, :].rearrange("p o h n -> p (o h) n")
                        steps(dve.tensor_tensor(to, to, sums, ALU.add))
                        steps.wait()
                        dve.sem_inc(group_done, 1)

                    def units(base, x):
                        steps = Steps(dve, dve_step, 2 + (0 if x is None else x * (5 * U // M_HEADS)))
                        first(0, base, x)
                        for u in range(U):
                            if u + 1 < U:
                                first(u + 1, base, x)
                            second(u, base, x, steps)

                    units(0, None)
                    with dve.Fori(0, XCH // 2) as i:
                        units((i + 1) * U, i)

        mix_at = nc.sbuf_usable_end // 32 * 32 - 2 * KT * SEQ * 4
        mix_mem = Arena(nc, mix_at)
        mix_hi = mix_mem("mix_hi", [P, KT, SEQ], F32R)
        mix_lo = mix_mem("mix_lo", [P, KT, SEQ], F32R)

        def mix_weights(n):
            src = A["w_out"].rearrange("o k n -> (o k) n")
            cols = slice(n * P, (n + 1) * P)
            half = N_HEADS // 2 * HEAD_DIM
            parts = [(w_raw[HEAD_DIM * a:HEAD_DIM * (a + 1), n % 2, 0:4, :],
                      src[half * a:half * (a + 1), cols].rearrange("(k p) n -> p k n", p=HEAD_DIM)) for a in range(2)]
            return parts + [(w_raw[:, n % 2, 4:, :], src[2 * half:, cols].rearrange("(k p) n -> p k n", p=P))]

        def phase_mix():
            phases.start()
            mem = Arena(nc, free_at)
            att = mem("mix_att", [P, M_HEADS, SEQ])
            normed = mem("mix_normed", [P, XCH * M_HEADS, M_DIM])
            mixed = mem("mix_mixed", [P, 2, HALF])
            sums = mem("mix_sums", [P, XCH * M_HEADS])
            assert mem.at <= free_at + 57 * 1024
            loaded = sem("mix_loaded")
            mean_done = sem("mix_mean_done")
            root_done = sem("mix_root_done")
            normed_done = sem("mix_normed_done")
            turned = sem("mix_turned")
            mixed_done = sem("mix_mixed_done")
            hi_done = sem("mix_hi_done")
            lo_done = sem("mix_lo_done")
            att_hi = sem("mix_att_hi")
            dve_step = sem("mix_dve_step")
            pre = Prefetch("mix", [mix_weights(0), mix_weights(1)])
            with nc.psum_tensor("mix_turn", [P, 2, HALF], F32) as turn, nc.Block() as block:
                @block.sync
                def _(sp):
                    sp.dma_start(att[:], att_cm.rearrange("(j p) t -> p j t", p=P)).then_inc(loaded, 16)
                    pre.load(sp)

                @block.gpsimd
                def _(pool):
                    pre.split(pool)
                    for j in range(M_HEADS):
                        pool.wait_ge(att_hi, j + 1)
                        pool.tensor_tensor(mix_lo[:, j, :], att[:, j, :], mix_hi[:, j, :].bitcast(F32), ALU.subtract)

                @block.vector
                def _(dve):
                    step = Steps(dve, dve_step)
                    rows = h_sum[:].rearrange("p c h n -> p (c h) n")
                    step(dve.tensor_tensor(normed[:], rows, rows, ALU.mult))
                    step.wait()
                    step(dve.tensor_reduce(sums[:], normed[:], AX_X, ALU.add))
                    step.wait()
                    dve.tensor_scalar(sums[:], sums[:], 1.0 / M_DIM, EPS, ALU.mult, ALU.add).then_inc(mean_done, 1)
                    dve.wait_ge(root_done, 1)
                    step(dve.reciprocal(sums[:], sums[:]))
                    step.wait()
                    dve.tensor_tensor(normed[:], rows, sums[:].unsqueeze(2).to_broadcast([P, XCH * M_HEADS, M_DIM]), ALU.mult).then_inc(normed_done, 1)
                    dve.sem_inc(mixed_done, 2)
                    for n in range(2 * M_HEADS):
                        h, half = n // 2, n % 2
                        cols = slice(half * HALF, (half + 1) * HALF)
                        dve.wait_ge(turned, n + 1)
                        if n >= 2:
                            dve.wait_ge(lo_done, n - 1)
                        dve.scalar_tensor_tensor(out=mixed[:, n % 2, :], in0=turn[:, n % 2, :], scalar=pb("mlstm_norm_w")[:, h:h + 1],
                                                 in1=out_gate[:, h, cols], op0=ALU.mult, op1=ALU.mult).then_inc(mixed_done, 1)
                        dve.wait_ge(hi_done, n + 1)
                        dve.tensor_tensor(mix_lo[:, M_HEADS + h, cols], mixed[:, n % 2, :], mix_hi[:, M_HEADS + h, cols].bitcast(F32),
                                          ALU.subtract).then_inc(lo_done, 1)

                @block.scalar
                def _(act):
                    act.wait_ge(mean_done, 1)
                    act.activation(sums[:], sums[:], ACT.Sqrt).then_inc(root_done, 1)
                    act.wait_ge(loaded, 16)
                    for j in range(M_HEADS):
                        act.copy(mix_hi[:, j, :], att[:, j, :]).then_inc(att_hi, 1)
                    for n in range(2 * M_HEADS):
                        h, half = n // 2, n % 2
                        act.wait_ge(mixed_done, n + 3)
                        act.copy(mix_hi[:, M_HEADS + h, half * HALF:(half + 1) * HALF], mixed[:, n % 2, :]).then_inc(hi_done, 1)

                @block.tensor
                def _(pe):
                    pe.wait_ge(normed_done, 1)
                    for n in range(2 * M_HEADS):
                        h, half = n // 2, n % 2
                        pe.wait_ge(mixed_done, n + 1)
                        for c in range(4):
                            ins = pe.transpose(turn[:, n % 2, c * P:(c + 1) * P], normed[:, (4 * half + c) * M_HEADS + h, :], ident)
                        ins.then_inc(turned, 1)

        def phase_out(tag, y_hi, y_lo, weights, pieces, gain, next_parts=None, norm=None, split_from=None):
            phases.start()
            mem = Arena(nc, free_at)
            x = mem(f"{tag}_x", [P, KT, SEQ])
            sq = mem(f"{tag}_sq", [P, 2, SEQ]) if norm else None
            sq_sum = mem(f"{tag}_sq_sum", [P, SEQ]) if norm else None
            ring = Ring(tag, pieces)
            pre = Prefetch(tag, next_parts, ring, KT) if next_parts else None
            tail = NormTail(tag, mem, x, SEQ, norm["affines"], norm.get("h_hi"), norm.get("h_lo"), norm.get("h_plain"), diag=sq[:, 0, :]) if norm else None
            z_free = sem(f"{tag}_z_free")
            x_loaded = [sem(f"{tag}_x_loaded{n}") for n in range(KT)]
            x_done = sem(f"{tag}_x_done")
            stored = [sem(f"{tag}_stored{u}") for u in range(2)]
            y_hi_done = sem(f"{tag}_y_hi_done")
            y_ready = sem(f"{tag}_y_ready")
            sq_done = sem(f"{tag}_sq_done")
            sum_done = sem(f"{tag}_sum_done")
            sums_out = sem(f"{tag}_sums_out")
            with nc.psum_tensor(f"{tag}_z", [P, 2, 2, HALF], F32) as z, nc.psum_tensor(f"{tag}_sums", [P, HALF], F32) as sums, \
                    nc.psum_tensor(f"{tag}_spread", [P, 2, HALF], F32) as spread, nc.Block() as block:
                @block.sync
                def _(sp):
                    for n in range(KT):
                        sp.dma_start(x[:, n, :], x_cm_k[:, n, :]).then_inc(x_loaded[n], 16)
                        if n >= 2:
                            ring.load(sp, n, n % 2, weights(n))
                    if pre:
                        pre.load(sp)

                @block.gpsimd
                def _(pool):
                    ring.credits(pool, None)
                    for n in range(2, KT):
                        ring.do_split(pool, n, n % 2, n // 2)
                    if pre:
                        pre.split(pool)
                    if norm:
                        tail.pool(pool)

                @block.tensor
                def _(pe):
                    ring.credits(None, pe)
                    if split_from is not None:
                        pe.wait_ge(y_ready, KT)
                    with pe.Fori(0, KT // 2) as i:
                        for u in range(2):
                            ring.project(pe, 2 * i + u, u, z_free, [(z[:, u, b, :], b * HALF, HALF) for b in range(2)], y_hi, y_lo)
                    if norm:
                        pe.wait_ge(sum_done, KT)
                        for j in range(BLOCKS):
                            ins = pe.matmul(sums[:, j:j + 1], sq_sum[:, j * P:(j + 1) * P], ones[:, 0:1], start=True, stop=True)
                        ins.then_inc(tail.summed, 1)
                        tail.pe(pe, spread)

                @block.vector
                def _(dve):
                    dve.sem_inc(z_free, 2)

                    def add_up(n):
                        dve.wait_ge(sq_done, n + 1)
                        if n:
                            dve.wait_ge(sum_done, n)
                            dve.tensor_tensor(sq_sum[:], sq_sum[:], sq[:, n % 2, :], ALU.add).then_inc(sum_done, 1)
                        else:
                            dve.tensor_copy(sq_sum[:], sq[:, 0, :]).then_inc(sum_done, 1)

                    if split_from is not None:
                        for kt in range(KT):
                            dve.wait_ge(y_hi_done, kt + 1)
                            dve.tensor_tensor(y_lo[:, kt, :], split_from[:, kt, :], y_hi[:, kt, :].bitcast(F32), ALU.subtract).then_inc(y_ready, 1)
                    for n in range(KT):
                        u = n % 2
                        dve.wait_ge(ring.projected, n + 3)
                        dve.wait_ge(x_loaded[n], 16)
                        for b in range(2):
                            cols = slice(b * HALF, (b + 1) * HALF)
                            dve.scalar_tensor_tensor(out=x[:, n, cols], in0=z[:, u, b, :], scalar=1.0 if gain is None else gain(n),
                                                     in1=x[:, n, cols], op0=ALU.mult, op1=ALU.add).then_inc(x_done, 1)
                        dve.wait_ge(x_done, 2 * n + 2)
                        dve.sem_inc(z_free, 1)
                        if norm and n:
                            add_up(n - 1)
                    if norm:
                        add_up(KT - 1)
                        tail.dve(dve, sums[:, 0:BLOCKS], spread, lambda kt: dve.wait_ge(stored[kt % 2], 16 * (kt // 2 + 1)))

                @block.scalar
                def _(act):
                    if split_from is not None:
                        for kt in range(KT):
                            act.copy(y_hi[:, kt, :], split_from[:, kt, :]).then_inc(y_hi_done, 1)
                    for n in range(KT):
                        act.wait_ge(x_done, 2 * n + 2)
                        act.dma_start(x_cm_k[:, n, :], x[:, n, :]).then_inc(stored[n % 2], 16)
                        if norm:
                            if n >= 2:
                                act.wait_ge(sum_done, n - 1)
                            act.activation(sq[:, n % 2, :], x[:, n, :], ACT.Square).then_inc(sq_done, 1)
                    for u in range(2):
                        act.wait_ge(stored[u], 16 * (KT // 2))
                    if norm:
                        tail.act(act)

        phase_mlstm_inputs()
        phase_gate_scans()
        phase_mlstm()
        phase_mix()
        h2_at = nc.sbuf_usable_end // 32 * 32 - KT * SEQ * 4
        h2_cm = Arena(nc, h2_at)("h2_cm", [P, KT, SEQ])
        phase_out("out1", mix_hi, mix_lo, mix_weights, 3, lambda n: mod[:, G1 + n, 0:1],
                  norm=dict(affines=[(0, SEQ, lambda kt: gain2[:, kt:kt + 1], lambda kt: mod[:, SH2 + kt, 0:1])], h_plain=h2_cm))

        route_mem = Arena(nc, free_at)
        slot_gate = route_mem("slot_gate", [P, N_EXPERTS])
        slot_token = route_mem("slot_token", [P, N_EXPERTS], U32)
        FFK = EXPERT_FF // P
        EXP_SHAPES = {"gate": [P, KT, EXPERT_FF], "up": [P, KT, EXPERT_FF], "down": [P, FFK, D]}
        exp_mem = Arena(nc, route_mem.at)
        exp_hi = {w: exp_mem(f"hi_{w}", s, F32R) for w, s in EXP_SHAPES.items()}
        exp_raw, exp_lo = {}, {}
        for w, s in EXP_SHAPES.items():
            for u in range(2):
                at = Arena(nc, ring_at) if (w, u) == ("down", 0) else exp_mem
                again = Arena(nc, at.at)
                exp_raw[w, u] = at(f"raw_{w}{u}", s)
                exp_lo[w, u] = again(f"lo_{w}{u}", s, F32R)
        exp_src = {w: A[f"w_{w}"].rearrange("o e (k p) n -> p (o e) k n", p=P) for w in EXP_SHAPES}

        def phase_router():
            phases.start()
            mem = Arena(nc, exp_mem.at)
            ROWS = 32 + N_EXPERTS
            w_router = mem("w_router", [P, KT, N_EXPERTS])
            rows = mem("h2_rows_sb", [P, 2, HALF])
            aff = mem("aff", [P, BLOCKS, N_EXPERTS])
            peak = mem("aff_peak", [P, BLOCKS])
            total = mem("aff_total", [P, BLOCKS])
            by_half = mem("aff_by_half", [P, BLOCKS // 2, ROWS])
            left = [mem(f"aff_left{u}", [ROWS, HALF]) for u in range(2)]
            top = mem("aff_top", [ROWS, SLOTS])
            top_at = mem("aff_top_at", [ROWS, SLOTS], U32)
            top_at_f = mem("aff_top_at_f", [ROWS, SLOTS])
            top_back, top_at_back = mem("aff_top_back", [ROWS, SLOTS]), mem("aff_top_at_back", [ROWS, SLOTS])
            second = mem("aff_second", [P, 2, N_EXPERTS])
            of_first = mem("aff_of_first", [P, N_EXPERTS])
            apart = mem("aff_apart", [P, N_EXPERTS])
            w_loaded = sem("route_w_loaded")
            logits_done = sem("route_logits_done")
            shifted = sem("route_shifted")
            exp_done = sem("route_exp_done")
            aff_done = sem("route_aff_done")
            aff_turned = sem("route_aff_turned")
            rows_turned = sem("route_rows_turned")
            rows_out = sem("route_rows_out")
            stored = [sem(f"route_stored{u}") for u in range(2)]
            top_done = sem("route_top_done")
            top_turned = sem("route_top_turned")
            raw_loaded = [sem(f"route_{w}_loaded") for w in EXP_SHAPES]
            next_loaded = sem("route_next_loaded")
            hi_done = sem("route_hi_done")
            assert mem.at <= h2_at, (mem.at, h2_at, free_at)
            dve_step = sem("route_dve_step")
            wide = [P, BLOCKS, N_EXPERTS]
            with nc.psum_tensor("route_logits", [P, HALF], F32) as logits, nc.psum_tensor("route_aff_t", [ROWS, HALF], F32) as aff_t, \
                    nc.psum_tensor("route_turn", [P, 2, 2, HALF], F32) as turn, nc.psum_tensor("route_top_t", [P, 4, N_EXPERTS], F32) as top_t, \
                    nc.Block() as block:
                @block.sync
                def _(sp):
                    sp.dma_start(w_router[:], A["w_router"].rearrange("o (k p) n -> p (o k) n", p=P)).then_inc(w_loaded, 16)
                    for n, w in enumerate(EXP_SHAPES):
                        sp.dma_start(exp_raw[w, 0][:], exp_src[w][:, 0]).then_inc(raw_loaded[n], 16)
                    for j in range(BLOCKS):
                        for half in range(2):
                            sp.wait_ge(rows_out, 2 * j + half + 1)
                            sp.dma_start(h2_rows[j * P:(j + 1) * P, half * HALF:(half + 1) * HALF], rows[:, half, :]).then_inc(stored[half], 16)
                    for half in range(2):
                        sp.wait_ge(stored[half], 16 * BLOCKS)
                    for w in EXP_SHAPES:
                        sp.dma_start(exp_raw[w, 1][:], exp_src[w][:, 1]).then_inc(next_loaded, 16)
                    sp.wait_ge(next_loaded, 16 * len(EXP_SHAPES))

                @block.gpsimd
                def _(pool):
                    for n, w in enumerate(EXP_SHAPES):
                        pool.wait_ge(hi_done, n + 1)
                        pool.tensor_tensor(exp_lo[w, 0][:], exp_raw[w, 0][:], exp_hi[w][:].bitcast(F32), ALU.subtract)

                @block.tensor
                def _(pe):
                    pe.wait_ge(w_loaded, 16)
                    for j in range(BLOCKS):
                        for kt in range(KT):
                            ins = pe.matmul(logits[:, j * N_EXPERTS:(j + 1) * N_EXPERTS], h2_cm[:, kt, j * P:(j + 1) * P], w_router[:, kt, :],
                                            start=(kt == 0), stop=(kt == KT - 1))
                    ins.then_inc(logits_done, 1)
                    for j in range(BLOCKS):
                        if j >= 2:
                            pe.wait_ge(rows_out, 2 * (j - 1))
                        for kt in range(KT):
                            ins = pe.transpose(turn[:, j % 2, kt // 4, (kt % 4) * P:(kt % 4 + 1) * P], h2_cm[:, kt, j * P:(j + 1) * P], ident)
                            if kt % 4 == 3:
                                ins.then_inc(rows_turned, 1)
                        if j == 2:
                            pe.wait_ge(aff_done, 1)
                            for b in range(BLOCKS // 2):
                                ins = pe.transpose(aff_t[:, b * P:(b + 1) * P], by_half[:, b, :], ident)
                            ins.then_inc(aff_turned, 1)
                    pe.wait_ge(top_done, 1)
                    for n, (x, back) in enumerate(((top, top_back), (top_at_f, top_at_back))):
                        pe.matmul(top_t[:, 2 * n, :], x[:], ident[0:ROWS, 0:N_EXPERTS], start=True, stop=True)
                        ins = pe.matmul(top_t[:, 2 * n + 1, :], back[:], ident[0:ROWS, 32:ROWS], start=True, stop=True)
                    ins.then_inc(top_turned, 1)

                @block.scalar
                def _(act):
                    act.wait_ge(shifted, 1)
                    act.activation(aff[:], aff[:], ACT.Exp).then_inc(exp_done, 1)
                    for j in range(BLOCKS):
                        for half in range(2):
                            act.wait_ge(rows_turned, 2 * j + half + 1)
                            if j:
                                act.wait_ge(stored[half], 16 * j)
                            act.copy(rows[:, half, :], turn[:, j % 2, half, :]).then_inc(rows_out, 1)
                    for n, w in enumerate(EXP_SHAPES):
                        act.wait_ge(raw_loaded[n], 16)
                        act.copy(exp_hi[w][:], exp_raw[w, 0][:]).then_inc(hi_done, 1)

                @block.vector
                def _(dve):
                    step = Steps(dve, dve_step)
                    step(dve.memset(by_half[:], 0.0))
                    dve.wait_ge(logits_done, 1)
                    lg = logits[:, 0:BLOCKS * N_EXPERTS].rearrange("p (j n) -> p j n", n=N_EXPERTS)
                    step(dve.tensor_reduce(peak[:], lg, AX_X, ALU.max))
                    step.wait()
                    dve.tensor_tensor(aff[:], lg, peak[:].unsqueeze(2).to_broadcast(wide), ALU.subtract).then_inc(shifted, 1)
                    dve.wait_ge(exp_done, 1)
                    step(dve.tensor_reduce(total[:], aff[:], AX_X, ALU.add))
                    step.wait()
                    step(dve.reciprocal(total[:], total[:]))
                    step.wait()
                    for half in range(2):
                        blocks = slice(half * (BLOCKS // 2), (half + 1) * (BLOCKS // 2))
                        step(dve.tensor_tensor(by_half[:, :, 32 * half:32 * half + N_EXPERTS], aff[:, blocks, :],
                                               total[:, blocks].unsqueeze(2).to_broadcast([P, BLOCKS // 2, N_EXPERTS]), ALU.mult))
                    step.wait()
                    dve.sem_inc(aff_done, 1)
                    dve.wait_ge(aff_turned, 1)
                    step(dve.tensor_copy(left[0][:], aff_t[:]))
                    step.wait()
                    for r in range(SLOTS // 8):
                        now, nxt = left[r % 2], left[(r + 1) % 2]
                        eight = slice(8 * r, 8 * (r + 1))
                        step(dve.max(top[:, eight], now[:]))
                        step.wait()
                        step(dve.max_index(top_at[:, eight], top[:, eight], now[:]))
                        if r + 1 < SLOTS // 8:
                            step(dve.match_replace(nxt[:], top[:, eight], now[:], -1.0))
                        step.wait()
                    step(dve.tensor_copy(top_at_f[:], top_at[:]))
                    step(dve.tensor_copy(top_back[:], top[:, ::-1]))
                    step(dve.tensor_copy(top_at_back[:], top_at[:, ::-1]))
                    step.wait()
                    dve.sem_inc(top_done, 1)
                    dve.wait_ge(top_turned, 1)
                    step(dve.tensor_copy(second[:, 0, :], top_t[:, 1, :]))
                    step(dve.tensor_scalar(second[:, 1, :], top_t[:, 3, :], float(HALF), None, ALU.add))
                    step.wait()
                    step(dve.tensor_tensor(of_first[:], top_t[:, 0, :], second[:, 0, :], ALU.is_ge))
                    step(dve.tensor_tensor(slot_gate[:], top_t[:, 0, :], second[:, 0, :], ALU.max))
                    step(dve.tensor_tensor(apart[:], top_t[:, 2, :], second[:, 1, :], ALU.subtract))
                    step.wait()
                    step(dve.tensor_tensor(apart[:], apart[:], of_first[:], ALU.mult))
                    step.wait()
                    step(dve.tensor_tensor(slot_token[:], apart[:], second[:, 1, :], ALU.add))

        def phase_experts():
            phases.start()
            mem = Arena(nc, exp_mem.at)
            FK, shapes, raw, w_hi_, w_lo_ = FFK, EXP_SHAPES, exp_raw, exp_hi, exp_lo
            xg = mem("x_gathered", [P, 2, D])
            x_hi = mem("x_hi", [P, 2, KT, P], F32R)
            x_lo = mem("x_lo", [P, 2, KT, P], F32R)
            silu = mem("silu_gate", [P, EXPERT_FF])
            prod = mem("gate_up", [P, EXPERT_FF])
            f_hi = mem("f_hi", [P, FK, P], F32R)
            f_lo = mem("f_lo", [P, FK, P], F32R)
            y = mem("expert_y", [P, 2, D])
            token_in = mem("token_in", [P, 2], U32)
            token_out = mem("token_out", [P, 2], U32)
            gate_now = mem("gate_now", [P, 2])
            loaded = {(w, u): sem(f"exp_{w}_loaded{u}") for w in shapes for u in range(2)}
            hi_done = {w: sem(f"exp_{w}_hi_done") for w in shapes}
            split = {w: sem(f"exp_{w}_split") for w in shapes}
            used = {w: sem(f"exp_{w}_used") for w in shapes}
            token_in_copied = sem("exp_token_in_copied")
            token_out_copied = sem("exp_token_out_copied")
            gathered = [phases.keep(f"exp_gathered{u}") for u in range(2)]
            turned = sem("exp_turned")
            x_hi_done = sem("exp_x_hi_done")
            x_lo_done = sem("exp_x_lo_done")
            silu_done = sem("exp_silu_done")
            prod_done = sem("exp_prod_done")
            f_turned = sem("exp_f_turned")
            f_hi_done = sem("exp_f_hi_done")
            f_lo_done = sem("exp_f_lo_done")
            gate_copied = sem("exp_gate_copied")
            y_out = sem("exp_y_out")
            y_free = sem("exp_y_free")
            scattered = phases.keep("exp_scattered")
            PAIRS = N_EXPERTS // 2
            parts_of = {"gate": 2, "up": 1, "down": 1}
            gate_half = [slice(0, KT // 2), slice(KT // 2, KT)]
            with nc.psum_tensor("exp_turn", [P, 2, HALF], F32) as p_x, nc.psum_tensor("exp_gate", [P, 2, HALF], F32) as p_gu, \
                    nc.psum_tensor("exp_f", [P, FK, P], F32) as p_f, nc.psum_tensor("exp_y", [P, 2, HALF], F32) as p_y, nc.Block() as block:

                def pairs(eng, run):
                    with eng.Fori(0, PAIRS - 1) as i:
                        for u in range(2):
                            run(2 * i + u, u, i, False)
                    for u in range(2):
                        run(2 * (PAIRS - 1) + u, u, PAIRS - 1, u == 1)

                @block.sync
                def _(sp):
                    for place in loaded.values():
                        sp.sem_inc(place, 16)
                    with sp.Fori(1, PAIRS) as i:
                        for u in range(2):
                            for w in shapes:
                                sp.wait_ge(used[w], 2 * i + u)
                                pass_waits(sp)
                                sp.dma_start(raw[w, u][:].rearrange("p (o k) n -> p o k n", o=1), exp_src[w][:, bass.ds(2 * i + u, 1)]).then_inc(loaded[w, u], 16)

                @block.gpsimd
                def _(pool):
                    pool.sem_inc(split["down"], 2)

                    def gather(e, slot, round_):
                        pool.wait_ge(turned, e + 1)
                        pass_waits(pool)
                        pool.tensor_copy(token_in[:, slot:slot + 1], slot_token[:, bass.ds(e, 1)]).then_inc(token_in_copied, 1)
                        pool.wait_ge(token_in_copied, e + 1)
                        pass_waits(pool)
                        pool.indirect_dma_start(xg[:, slot, :], None, h2_rows, bass.IndirectOffsetOnAxis(ap=token_in[:, slot:slot + 1], axis=0),
                                                bounds_check=SEQ - 1).then_inc(gathered[slot], 16)

                    def lo_down(e, slot):
                        pool.wait_ge(hi_done["down"], e + 1)
                        pool.tensor_tensor(w_lo_["down", slot][:], raw["down", slot][:], w_hi_["down"][:].bitcast(F32), ALU.subtract).then_inc(split["down"], 1)

                    def scatter(e, slot):
                        pass_waits(pool)
                        pool.tensor_copy(token_out[:, slot:slot + 1], slot_token[:, bass.ds(e, 1)]).then_inc(token_out_copied, 1)
                        pool.wait_ge(token_out_copied, e + 1)
                        pool.wait_ge(y_out, e + 2)
                        if not (isinstance(e, int) and e == 0):
                            pool.wait_ge(scattered, 16 * e)
                        pool.sem_inc(y_free, 1)
                        pass_waits(pool)
                        pool.indirect_dma_start(ffn_rows, bass.IndirectOffsetOnAxis(ap=token_out[:, slot:slot + 1], axis=0), y[:, slot, :], None,
                                                bounds_check=SEQ - 1, compute_op=ALU.add).then_inc(scattered, 16)

                    pool.sem_inc(turned, 2)
                    pool.sem_inc(y_free, 1)
                    gather(0, 0, 0)
                    gather(1, 1, 0)
                    gather(2, 0, 1)
                    lo_down(1, 1)
                    scatter(0, 0)
                    with pool.Fori(1, PAIRS - 1) as i:
                        for u in range(2):
                            gather(2 * i + u + 1, (u + 1) % 2, i + u)
                            lo_down(2 * i + u, u)
                            scatter(2 * i + u - 1, (u + 1) % 2)
                    for e in (N_EXPERTS - 2, N_EXPERTS - 1):
                        if e + 1 < N_EXPERTS:
                            gather(e + 1, (e + 1) % 2, (e + 1) // 2)
                        lo_down(e, e % 2)
                        scatter(e - 1, (e - 1) % 2)
                    scatter(N_EXPERTS - 1, 1)
                    pool.wait_ge(scattered, 16 * N_EXPERTS)

                @block.tensor
                def _(pe):
                    for w in shapes:
                        pe.sem_inc(used[w], 1)

                    def turn(e, slot, round_):
                        pe.wait_ge(gathered[slot], 16 * (round_ + 1))
                        pe.wait_ge(x_lo_done, e + 1)
                        for kt in range(KT):
                            ins = pe.transpose(p_x[:, kt // 4, (kt % 4) * P:(kt % 4 + 1) * P], xg[:, slot, kt * P:(kt + 1) * P], ident)
                        ins.then_inc(turned, 1)

                    def product(to, w, slot, x_hi, x_lo, kts, cols, lo_ready=None):
                        for kt in range(kts):
                            pe.matmul(to, x_hi[:, kt, :], w_hi_[w][:, kt, cols], start=(kt == 0), stop=False)
                            pe.matmul(to, x_hi[:, kt, :], w_lo_[w, slot][:, kt, cols], start=False, stop=False)
                        if lo_ready:
                            lo_ready()
                        for kt in range(kts):
                            ins = pe.matmul(to, x_lo[:, kt, :], w_hi_[w][:, kt, cols], start=False, stop=(kt == kts - 1))
                        return ins

                    def run(e, slot, round_, last):
                        pe.wait_ge(x_lo_done, e + 2)
                        pe.wait_ge(prod_done, e + 1)
                        for b, w in enumerate(("gate", "up")):
                            pe.wait_ge(split[w], parts_of[w] * (e + 2))
                            product(p_gu[:, b, :], w, slot, x_hi[:, slot], x_lo[:, slot], KT, slice(None)).then_inc(used[w], 1)
                        if not last:
                            turn(e + 1, 1 - slot, round_ + slot)
                        pe.wait_ge(prod_done, e + 2)
                        pe.wait_ge(f_lo_done, e + 1)
                        for kt in range(FK):
                            ins = pe.transpose(p_f[:, kt, :], prod[:, kt * P:(kt + 1) * P], ident)
                        ins.then_inc(f_turned, 1)
                        pe.wait_ge(f_hi_done, e + 1)
                        pe.wait_ge(split["down"], e + 2)
                        pe.wait_ge(y_out, e + 1)
                        for half in range(2):
                            ins = product(p_y[:, half, :], "down", slot, f_hi, f_lo, FK, slice(half * HALF, (half + 1) * HALF),
                                          lambda: pe.wait_ge(f_lo_done, e + 2))
                        ins.then_inc(used["down"], 1)

                    turn(0, 0, 0)
                    pairs(pe, run)

                @block.scalar
                def _(act):
                    def hi(w, e, slot, round_):
                        act.wait_ge(loaded[w, slot], 16 * (round_ + 1))
                        act.wait_ge(used[w], e + 1)
                        for kts in gate_half if w == "gate" else [slice(None)]:
                            act.copy(w_hi_[w][:, kts], raw[w, slot][:, kts]).then_inc(hi_done[w], 1)

                    def hi_x(e, slot):
                        act.wait_ge(turned, e + 3)
                        act.copy(x_hi[:, slot].rearrange("p (a k) n -> p a (k n)", a=2), p_x[:]).then_inc(x_hi_done, 1)

                    def run(e, slot, round_, last):
                        act.wait_ge(used["gate"], e + 2)
                        act.wait_ge(prod_done, e + 1)
                        act.activation(silu[:], p_gu[:, 0, :], ACT.Silu).then_inc(silu_done, 1)
                        if not last:
                            hi("gate", e + 1, 1 - slot, round_ + slot)
                        act.wait_ge(f_turned, e + 1)
                        act.copy(f_hi[:], p_f[:]).then_inc(f_hi_done, 1)
                        if not last:
                            hi_x(e + 1, 1 - slot)
                            hi("up", e + 1, 1 - slot, round_ + slot)
                            hi("down", e + 1, 1 - slot, round_ + slot)

                    for w in shapes:
                        act.sem_inc(hi_done[w], parts_of[w])
                    hi_x(0, 0)
                    pairs(act, run)

                @block.vector
                def _(dve):
                    dve.sem_inc(split["gate"], 4)
                    dve.sem_inc(split["up"], 2)
                    dve.sem_inc(x_lo_done, 1)
                    dve.sem_inc(prod_done, 1)
                    dve.sem_inc(f_lo_done, 1)
                    dve.sem_inc(y_out, 1)
                    dve.sem_inc(gate_copied, 1)

                    def lo_up(e, slot):
                        dve.wait_ge(hi_done["up"], e + 1)
                        dve.tensor_tensor(w_lo_["up", slot][:], raw["up", slot][:], w_hi_["up"][:].bitcast(F32), ALU.subtract).then_inc(split["up"], 1)

                    def lo_gate(e, slot, half):
                        kts = gate_half[half]
                        dve.wait_ge(hi_done["gate"], 2 * e + half + 1)
                        dve.tensor_tensor(w_lo_["gate", slot][:, kts], raw["gate", slot][:, kts], w_hi_["gate"][:, kts].bitcast(F32), ALU.subtract).then_inc(split["gate"], 1)

                    def lo_x(e, slot):
                        dve.wait_ge(x_hi_done, e + 1)
                        dve.tensor_tensor(x_lo[:, slot].rearrange("p (a k) n -> p a (k n)", a=2), p_x[:],
                                          x_hi[:, slot].rearrange("p (a k) n -> p a (k n)", a=2).bitcast(F32), ALU.subtract).then_inc(x_lo_done, 1)

                    def run(e, slot, round_, last):
                        if not last:
                            lo_gate(e + 1, 1 - slot, 0)
                        dve.wait_ge(silu_done, e + 1)
                        dve.wait_ge(used["up"], e + 2)
                        dve.tensor_tensor(prod[:], silu[:], p_gu[:, 1, :], ALU.mult).then_inc(prod_done, 1)
                        dve.wait_ge(f_hi_done, e + 1)
                        dve.tensor_tensor(f_lo[:], p_f[:], f_hi[:].bitcast(F32), ALU.subtract).then_inc(f_lo_done, 1)
                        if not last:
                            lo_x(e + 1, 1 - slot)
                            lo_gate(e + 1, 1 - slot, 1)
                            lo_up(e + 1, 1 - slot)
                        pass_waits(dve)
                        dve.tensor_scalar(gate_now[:, slot:slot + 1], slot_gate[:, bass.ds(e, 1)], 0.0, None, ALU.add).then_inc(gate_copied, 1)
                        dve.wait_ge(gate_copied, e + 2)
                        dve.wait_ge(used["down"], e + 2)
                        dve.wait_ge(y_free, e + 1)
                        dve.tensor_scalar(y[:, slot, :], p_y[:].rearrange("p a b -> p (a b)"), gate_now[:, slot:slot + 1], None,
                                          ALU.mult).then_inc(y_out, 1)

                    lo_x(0, 0)
                    pairs(dve, run)

        phase_router()
        phase_experts()

        top = nc.sbuf_usable_end // 32 * 32
        h_split = Arena(nc, top - 2 * KT * SEQ * 4)
        h_hi = h_split("h_hi", [P, KT, SEQ], F32R)
        h_lo = h_split("h_lo", [P, KT, SEQ], F32R)
        y_split = Arena(nc, top - 4 * KT * SEQ * 4)
        y_hi = y_split("y_hi", [P, KT, SEQ], F32R)
        y_lo = y_split("y_lo", [P, KT, SEQ], F32R)
        work_end = top - 4 * KT * SEQ * 4
        BOTH = [(0, 0, HALF), (1, HALF, HALF)]

        def weight_cols(w, first_row=0):
            src = w.rearrange("o (k p) n -> p (o k) n", p=P)
            return lambda u, cols: [(w_raw[:, u], src[:, first_row // P:first_row // P + KT, cols])]

        def out_weights(w, first_row):
            part = weight_cols(w, first_row)
            return lambda n: part(n % 2, slice(n * P, (n + 1) * P))

        even_cols = weight_cols(A["even_w_in_2"])

        def pool_col(t):
            return t // 4 * 2 * P + (t % 4) // 2 * D + t % 2 * P

        SPATIAL_COLS = (3 * D, 4 * D, 2 * D)

        def phase_pool(next_parts):
            phases.start()
            mem = Arena(nc, free_at)
            PAD, G = max(POOL_SIZES), len(POOL_SIZES)
            a_pad = mem("pool_a", [P, 2, PAD + SEQ])
            sums = mem("pool_sums", [P, 2, PAD + SEQ])
            pooled = mem("pool_pooled", [P, 2, SEQ])
            silu = mem("pool_silu", [P, 2, SEQ])
            y = mem("pool_y", [P, 2, SEQ])
            w_pool = mem("pool_w", [P, 2, 2, 2 * P])
            assert mem.at <= work_end
            ring = Ring("pool")
            pre = Prefetch("pool", next_parts, ring, 4 * G)
            z_out = sem("pool_z_out")
            w_loaded = [sem(f"pool_matrix_loaded{u}") for u in range(2)]
            pooled_done = sem("pool_pooled_done")
            mixed_done = sem("pool_mixed_done")
            y_done = sem("pool_y_done")
            hi_done = sem("pool_hi_done")
            lo_done = sem("pool_lo_done")
            cleared = sem("pool_cleared")
            dve_step = sem("pool_dve_step")
            w_cols = even_cols
            src_pool = A["even_pool_w_2"].rearrange("o g (k p) n -> p (o g) k n", p=P)
            with nc.psum_tensor("pool_z", [P, 2, 2, HALF], F32) as z, nc.psum_tensor("pool_mixed", [P, 2, 2, HALF], F32) as mixed, nc.Block() as block:
                @block.sync
                def _(sp):
                    def matrices(i):
                        for s in range(2):
                            sp.wait_ge(mixed_done, 2 * i + s + 1)
                            if not isinstance(i, int):
                                pass_waits(sp)
                            sp.dma_start(w_pool[:, s].rearrange("p (o k) n -> p o k n", o=1), src_pool[:, bass.ds(2 * i + s, 1)]).then_inc(w_loaded[s], 16)

                    ring.load_all(sp, G // 2, 8, lambda i, t: w_cols(t % 2, bass.ds(i * 4 * P + pool_col(t), P)), matrices)
                    pre.load(sp)

                @block.gpsimd
                def _(pool):
                    ring.credits(pool, None)
                    ring.split_all(pool, G // 2, 8)
                    pre.split(pool)

                @block.tensor
                def _(pe):
                    ring.credits(None, pe)
                    pe.sem_inc(mixed_done, 2)
                    with pe.Fori(0, G // 2) as i:
                        for s in range(2):
                            g = 2 * i + s
                            for t in range(4):
                                ring.project(pe, 4 * g + t, t % 2, z_out, [(z[:, t % 2, b, :], c0, w) for b, c0, w in BOTH], h_hi, h_lo)
                            pe.wait_ge(w_loaded[s], 16 * (i + 1))
                            pe.wait_ge(pooled_done, 2 * g + 2)
                            pe.wait_ge(y_done, 2 * g + 2)
                            for d in range(2):
                                for b, c0, w in BOTH:
                                    for k in range(2):
                                        ins = pe.matmul(mixed[:, d, b, :], w_pool[:, s, k, d * P:(d + 1) * P], pooled[:, k, c0:c0 + w],
                                                        start=(k == 0), stop=(k == 1))
                            ins.then_inc(mixed_done, 1)

                @block.scalar
                def _(act):
                    act.sem_inc(z_out, 2)
                    act.wait_ge(cleared, 1)
                    for g in range(G):
                        for t in range(4):
                            act.wait_ge(ring.projected, 4 * g + t + 3)
                            tile = z[:, t % 2].rearrange("p b n -> p (b n)")
                            if t < 2:
                                if g:
                                    act.wait_ge(pooled_done, 2 * (g - 1) + t + 1)
                                act.copy(a_pad[:, t, PAD:], tile).then_inc(z_out, 1)
                            else:
                                act.wait_ge(y_done, 2 * g + t - 2 + 1)
                                act.activation(silu[:, t - 2, :], tile, ACT.Silu).then_inc(z_out, 1)
                        for d in range(2):
                            act.wait_ge(y_done, 2 * g + d + 3)
                            act.copy(y_hi[:, 2 * g + d, :], y[:, d, :]).then_inc(hi_done, 1)

                @block.vector
                def _(dve):
                    step = Steps(dve, dve_step)
                    dve.sem_inc(y_done, 2)
                    step(dve.memset(a_pad[:], 0.0))
                    step(dve.memset(sums[:], 0.0))
                    step.wait()
                    dve.sem_inc(cleared, 1)
                    for g, w in enumerate(POOL_SIZES):
                        for t in range(2):
                            dve.wait_ge(z_out, 4 * g + t + 3)
                            now = a_pad[:, t]
                            for k in range(g + 1):
                                nxt = sums[:, k % 2]
                                step(dve.tensor_tensor(nxt[:, PAD:], now[:, PAD:], now[:, PAD - (1 << k):PAD + SEQ - (1 << k)], ALU.add))
                                step.wait()
                                now = nxt
                            dve.wait_ge(mixed_done, g + 2)
                            head = pooled[:, t, 0:PAD]
                            step(dve.tensor_tensor(head, now[:, PAD:2 * PAD], cst("pool_inv")[:, g * PAD:(g + 1) * PAD], ALU.mult))
                            step.wait()
                            step(dve.tensor_tensor(head, head, a_pad[:, t, PAD:2 * PAD], ALU.subtract))
                            step.wait()
                            dve.scalar_tensor_tensor(out=pooled[:, t, PAD:], in0=now[:, 2 * PAD:], scalar=1.0 / w, in1=a_pad[:, t, 2 * PAD:],
                                                     op0=ALU.mult, op1=ALU.subtract).then_inc(pooled_done, 1)
                            dve.wait_ge(pooled_done, 2 * g + t + 1)
                        dve.wait_ge(mixed_done, g + 3)
                        for d in range(2):
                            dve.wait_ge(z_out, 4 * g + 2 + d + 3)
                            if g:
                                dve.wait_ge(lo_done, 2 * (g - 1) + d + 1)
                            dve.scalar_tensor_tensor(out=y[:, d, :], in0=mixed[:, d].rearrange("p b n -> p (b n)"),
                                                     scalar=pa("even_pool_scale_2")[:, 2 * g + d:2 * g + d + 1], in1=silu[:, d, :],
                                                     op0=ALU.mult, op1=ALU.mult).then_inc(y_done, 1)
                        for d in range(2):
                            dve.wait_ge(hi_done, 2 * g + d + 1)
                            dve.tensor_tensor(y_lo[:, 2 * g + d, :], y[:, d, :], y_hi[:, 2 * g + d, :].bitcast(F32), ALU.subtract).then_inc(lo_done, 1)

        def phase_spatial(next_parts):
            phases.start()
            mem = Arena(nc, free_at)
            G = 4
            ws = mem("spat_ws", [P, G, CHUNK])
            ws_low = mem("spat_ws_low", [P, G, CHUNK])
            ws_t = mem("spat_ws_t", [P, G, CHUNK])
            bias = mem("spat_bias", [1, G, 4, CHUNK])
            v_cm = mem("spat_v_cm", [P, SEQ])
            v_rows_ = mem("spat_v_rows", [P, XCH, P])
            u_cm = mem("spat_u_cm", [P, SEQ])
            silu = mem("spat_silu", [P, SEQ])
            gated = mem("spat_gated", [P, SEQ])
            y = mem("spat_y", [P, SEQ])
            assert mem.at <= work_end
            ring = Ring("spat")
            pre = Prefetch("spat", next_parts, ring, 6 * G)
            z_out = sem("spat_z_out")
            loaded = sem("spat_loaded")
            masked = sem("spat_masked")
            ws_turned = sem("spat_ws_turned")
            ws_ready = sem("spat_ws_ready")
            v_turned = sem("spat_v_turned")
            rows_out = sem("spat_rows_out")
            gated_done = sem("spat_gated_done")
            mixed_done = sem("spat_mixed_done")
            y_done = sem("spat_y_done")
            hi_done = sem("spat_hi_done")
            lo_done = sem("spat_lo_done")
            w_cols = even_cols
            with nc.psum_tensor("spat_z", [P, 2, 2, HALF], F32) as z, nc.psum_tensor("spat_turn", [P, 2, HALF], F32) as turn, \
                    nc.psum_tensor("spat_mixed", [P, 2, HALF], F32) as mixed, nc.Block() as block:
                @block.sync
                def _(sp):
                    sp.dma_start(ws[:], A["even_ws_2"].rearrange("o g t s -> t (o g) s")).then_inc(loaded, 16)
                    for r in range(4):
                        sp.dma_start(bias[:, :, r, :], A["even_bs_2"]).then_inc(loaded, 16)
                    ring.load_all(sp, G, 6, lambda i, m: w_cols(m % 2, bass.ds(i * 2 * P + m // 3 * P + SPATIAL_COLS[m % 3], P)))
                    pre.load(sp)

                @block.gpsimd
                def _(pool):
                    ring.credits(pool, None)
                    pool.wait_ge(loaded, 16 * 5)
                    pool.affine_select(ws_low[:], ws[:], [[0, G], [-1, CHUNK]], ALU.is_ge, 0.0, base=0, channel_multiplier=1).then_inc(masked, 1)
                    ring.split_all(pool, G, 6)
                    pre.split(pool)

                @block.tensor
                def _(pe):
                    ring.credits(None, pe)
                    pe.wait_ge(masked, 1)
                    for g in range(G):
                        ins = pe.transpose(turn[:, 0, g * CHUNK:(g + 1) * CHUNK], ws_low[:, g, :], ident)
                    ins.then_inc(ws_turned, 1)

                    def proj(n, m):
                        ring.project(pe, n, m % 2, z_out, [(z[:, m % 2, b, :], c0, w) for b, c0, w in BOTH], h_hi, h_lo)

                    with pe.Fori(0, G) as i:
                        for s in range(2):
                            c = 2 * i + s
                            proj(6 * i + 3 * s, 3 * s)
                            proj(6 * i + 3 * s + 1, 3 * s + 1)
                            pe.wait_ge(z_out, 6 * i + 3 * s + 3)
                            pe.wait_ge(rows_out, c + 1)
                            for j in range(XCH):
                                ins = pe.transpose(turn[:, j // 4, (j % 4) * P:(j % 4 + 1) * P], v_cm[:, j * P:(j + 1) * P], ident)
                            ins.then_inc(v_turned, 1)
                            proj(6 * i + 3 * s + 2, 3 * s + 2)
                            pe.wait_ge(rows_out, c + 2)
                            pe.wait_ge(y_done, c + 1)
                            pass_waits(pe)
                            for b in range(2):
                                pe.matmul(mixed[:, b, :], ones[0:1, :], bias[:, bass.ds(i, 1), :, :].rearrange("p o r t -> p (o r t)"), start=True, stop=False)
                                for j in range(4):
                                    ins = pe.matmul(mixed[:, b, j * CHUNK:(j + 1) * CHUNK], v_rows_[:, 4 * b + j, :],
                                                    ws_t[:, bass.ds(i, 1), :].rearrange("p o t -> p (o t)"), start=False, stop=(j == 3))
                            ins.then_inc(mixed_done, 1)

                @block.scalar
                def _(act):
                    act.sem_inc(z_out, 2)
                    with act.Fori(0, G) as i:
                        for s in range(2):
                            c = 2 * i + s
                            for t, to in enumerate((v_cm, silu, u_cm)):
                                m = 3 * s + t
                                act.wait_ge(ring.projected, 6 * i + m + 3)
                                if t == 0:
                                    act.wait_ge(v_turned, c + 1)
                                else:
                                    act.wait_ge(gated_done, c + 1)
                                act.activation(to[:], z[:, m % 2].rearrange("p b n -> p (b n)"), ACT.Silu if t == 1 else ACT.Copy).then_inc(z_out, 1)
                            act.wait_ge(y_done, c + 2)
                            pass_waits(act)
                            act.copy(y_hi[:, bass.ds(c, 1), :].rearrange("p o t -> p (o t)"), y[:]).then_inc(hi_done, 1)

                @block.vector
                def _(dve):
                    dve.sem_inc(v_turned, 1)
                    dve.sem_inc(gated_done, 1)
                    dve.sem_inc(y_done, 1)
                    dve.sem_inc(lo_done, 1)
                    dve.wait_ge(ws_turned, 1)
                    dve.tensor_copy(ws_t[:], turn[:, 0, :].rearrange("p (g t) -> p g t", g=G)).then_inc(rows_out, 1)
                    with dve.Fori(0, G) as i:
                        for s in range(2):
                            c = 2 * i + s
                            dve.wait_ge(v_turned, c + 2)
                            dve.tensor_copy(v_rows_[:].rearrange("p (a j) n -> p a (j n)", a=2), turn[:]).then_inc(rows_out, 1)
                            dve.wait_ge(z_out, 6 * i + 3 * s + 2 + 3)
                            dve.wait_ge(y_done, c + 1)
                            dve.tensor_tensor(gated[:], u_cm[:], silu[:], ALU.mult).then_inc(gated_done, 1)
                            dve.wait_ge(mixed_done, c + 1)
                            dve.wait_ge(gated_done, c + 2)
                            dve.wait_ge(lo_done, c + 1)
                            dve.tensor_tensor(y[:], mixed[:].rearrange("p b n -> p (b n)"), gated[:], ALU.mult).then_inc(y_done, 1)
                            dve.wait_ge(hi_done, c + 1)
                            at = bass.ds(c, 1)
                            dve.tensor_tensor(y_lo[:, at, :].rearrange("p o t -> p (o t)"), y[:], y_hi[:, at, :].rearrange("p o t -> p (o t)").bitcast(F32),
                                              ALU.subtract).then_inc(lo_done, 1)

        even_a_out, even_b_out = (out_weights(A["even_w_out_2"], row) for row in (0, D))
        odd_a_out, odd_b_out = (out_weights(A["odd_w_out_2"], row) for row in (0, D))
        phases.start()
        phase_rows_norm("even", Arena(nc, free_at), SEQ, [(0, SEQ, plain_gain("even_norm_2"), None)], h_hi, h_lo,
                        [even_cols(u, slice(pool_col(u), pool_col(u) + P)) for u in range(2)])
        phase_pool([even_a_out(u) for u in range(2)])
        phase_out("even_a_out", y_hi, y_lo, even_a_out, 1, None, [even_cols(u, slice(SPATIAL_COLS[u], SPATIAL_COLS[u] + P)) for u in range(2)])
        phase_spatial([even_b_out(u) for u in range(2)])
        odd_cols = weight_cols(A["odd_w_in_2"])
        GC_COL = 3 * N_DIL * C_SLOTS * P
        DB_COL, DC_COL, DX_COL, GD_COL = (GC_COL + (1 + k) * D for k in range(4))
        CONV_COLS = (DC_COL, DX_COL, GD_COL, DB_COL)
        phase_out("even_b_out", y_hi, y_lo, even_b_out, 1, None, [odd_cols(u, slice(CONV_COLS[u], CONV_COLS[u] + P)) for u in range(2)],
                  norm=dict(affines=[(0, SEQ, plain_gain("odd_norm_2"), None)], h_hi=h_hi, h_lo=h_lo))

        def phase_conv(next_parts):
            phases.start()
            mem = Arena(nc, free_at)
            PAD, TAPS = 2, 3
            taken = [mem(f"conv_{name}", [P, SEQ]) for name in ("c", "x", "silu", "b")]
            c_cm, x_cm_, silu, b_cm = taken
            prod = mem("conv_prod", [P, PAD + SEQ])
            acc = mem("conv_acc", [P, SEQ])
            gated = mem("conv_gated", [P, SEQ])
            y = mem("conv_y", [P, SEQ])
            taps = mem("gated_conv_taps", [P, TAPS, 1])
            assert mem.at <= work_end
            ring = Ring("conv")
            pre = Prefetch("conv", next_parts, ring, 4 * KT)
            z_out = sem("conv_z_out")
            taken_used = sem("conv_taken_used")
            y_done = sem("conv_y_done")
            hi_done = sem("conv_hi_done")
            lo_done = sem("conv_lo_done")
            dve_step = sem("conv_dve_step")
            with nc.psum_tensor("conv_z", [P, 2, 2, HALF], F32) as z, nc.Block() as block:
                @block.sync
                def _(sp):
                    ring.load_all(sp, KT, 4, lambda c, t: odd_cols(t % 2, bass.ds(c * P + CONV_COLS[t], P)))
                    pre.load(sp)

                @block.gpsimd
                def _(pool):
                    ring.credits(pool, None)
                    ring.split_all(pool, KT, 4)
                    pre.split(pool)

                @block.tensor
                def _(pe):
                    ring.credits(None, pe)
                    with pe.Fori(0, KT) as c:
                        for t in range(4):
                            ring.project(pe, 4 * c + t, t % 2, z_out, [(z[:, t % 2, b, :], c0, w) for b, c0, w in BOTH], h_hi, h_lo)

                @block.scalar
                def _(act):
                    act.sem_inc(z_out, 2)
                    with act.Fori(0, KT) as c:
                        for t, to in enumerate(taken):
                            act.wait_ge(ring.projected, 4 * c + t + 3)
                            act.wait_ge(taken_used, c + 1)
                            act.activation(to[:], z[:, t % 2].rearrange("p b n -> p (b n)"), ACT.Silu if to is silu else ACT.Copy).then_inc(z_out, 1)
                        act.wait_ge(y_done, c + 1)
                        pass_waits(act)
                        act.copy(y_hi[:, bass.ds(c, 1), :].rearrange("p o t -> p (o t)"), y[:]).then_inc(hi_done, 1)

                @block.vector
                def _(dve):
                    dve.memset(prod[:], 0.0).then_inc(dve_step, 1)
                    dve.wait_ge(dve_step, 1)
                    dve.sem_inc(taken_used, 1)
                    N_STEP = TAPS + 3
                    with dve.Fori(0, KT) as c:
                        step = Steps(dve, dve_step, N_STEP * c + 1)
                        step.wait()
                        pass_waits(dve)
                        step(dve.tensor_copy(taps[:], pb("odd_conv_w_2").rearrange("p (j c) -> p j c", j=TAPS)[:, :, bass.ds(c, 1)]))
                        dve.wait_ge(z_out, 4 * c + 1 + 3)
                        step(dve.tensor_tensor(prod[:, PAD:], c_cm[:], x_cm_[:], ALU.mult))
                        step.wait()
                        step(dve.tensor_scalar(acc[:], prod[:, 0:SEQ], taps[:, 0, :], None, ALU.mult))
                        step.wait()
                        for j in range(1, TAPS):
                            step(dve.scalar_tensor_tensor(out=acc[:], in0=prod[:, j:j + SEQ], scalar=taps[:, j, :], in1=acc[:], op0=ALU.mult, op1=ALU.add))
                            step.wait()
                        dve.wait_ge(z_out, 4 * c + 3 + 3)
                        step(dve.tensor_tensor(gated[:], b_cm[:], silu[:], ALU.mult))
                        step.wait()
                        dve.sem_inc(taken_used, 1)
                        assert step.done == N_STEP
                        dve.tensor_tensor(y[:], acc[:], gated[:], ALU.mult).then_inc(y_done, 1)
                        dve.wait_ge(hi_done, c + 1)
                        at = bass.ds(c, 1)
                        dve.tensor_tensor(y_lo[:, at, :].rearrange("p o t -> p (o t)"), y[:], y_hi[:, at, :].rearrange("p o t -> p (o t)").bitcast(F32),
                                          ALU.subtract).then_inc(lo_done, 1)
                        dve.wait_ge(lo_done, c + 1)

        y_plain = Arena(nc, top - 3 * KT * SEQ * 4)("y_plain", [P, KT, SEQ])

        DIL_COLS = [first + g * D for g in range(N_DIL) for first in (N_DIL * D, 0)]
        DIL_COLS += [2 * N_DIL * D + g * D for g in range(N_DIL)] + [GC_COL]

        def phase_dilated(next_parts):
            phases.start()
            mem = Arena(nc, free_at)
            q_cm_ = mem("dil_q", [P, N_DIL, SEQ])
            k_cm_ = mem("dil_k", [P, N_DIL, SEQ])
            v_cm = mem("dil_v", [P, SEQ])
            v_rows_ = mem("dil_v_rows", [P, N_DIL, BLOCKS, P])
            silu = mem("dil_silu", [P, SEQ])
            biased = mem("dil_biased", [P, 2, 2 * P])
            p_t = mem("dil_p_t", [P, 2, 2 * P])
            NU = N_DIL * BLOCKS
            neg_max = mem("dil_neg_max", [P, NU])
            den = mem("dil_den", [P, NU])
            log_den = mem("dil_log_den", [P, NU])
            lse = mem("dil_lse", [P, NU])
            slope_now = mem("dil_slope_now", [P, N_DIL, 1])
            joint = mem("dil_joint", [P, N_DIL, 8])
            joint_max = mem("dil_joint_max", [P, 8])
            joint_sum = mem("dil_joint_sum", [P, 8])
            share = mem("dil_share", [P, NU])

            units = []
            for g in range(N_DIL):
                for b in range(BLOCKS):
                    has_prev = (b > 0, b % 2 == 1, False)[g]
                    units.append((g, b, b - 1 if has_prev else b, 2 if has_prev else 1))
            probs = [mem(f"dil_p{u}", [P, n * P]) for u, (_, _, _, n) in enumerate(units)]
            assert mem.at <= top - 3 * KT * SEQ * 4
            ring = Ring("dil")
            pre = Prefetch("dil", next_parts, ring, C_SLOTS * len(DIL_COLS))
            z_out = sem("dil_z_out")
            scores = sem("dil_scores")
            bias_done = sem("dil_bias_done")
            max_done = sem("dil_max_done")
            exp_done = sem("dil_exp_done")
            aux_free = [sem(f"dil_aux_free{b}") for b in range(2)]
            log_done = sem("dil_log_done")
            lse_done = sem("dil_lse_done")
            lse_stored = sem("dil_lse_stored")
            joint_loaded = sem("dil_joint_loaded")
            joint_shifted = sem("dil_joint_shifted")
            joint_exp = sem("dil_joint_exp")
            share_done = sem("dil_share_done")
            share_stored = sem("dil_share_stored")
            share_loaded = sem("dil_share_loaded")
            factor_done = sem("dil_factor_done")
            scaled = sem("dil_scaled")
            v_turned = sem("dil_v_turned")
            rows_out = sem("dil_rows_out")
            p_turned = sem("dil_p_turned")
            p_t_out = sem("dil_p_t_out")
            summed = sem("dil_summed")
            y_done = sem("dil_y_done")
            dve_step = sem("dil_dve_step")
            NT = len(DIL_COLS)
            VT, GT = 2 * N_DIL, 3 * N_DIL
            AUX = NU + 2 * N_DIL + NU

            def reordered(x, g):
                r = DILATION[g]
                return x.rearrange("p (r b m) -> p b m r", r=r, b=2) if g else x.rearrange("p (b m) -> p b m", b=2)

            def in_banks(x, g):
                return x.rearrange("p b (m r) -> p b m r", r=DILATION[g]) if g else x

            def token_order(row, tile, g):
                if g == 0:
                    return [(row.rearrange("(b p) -> p b", p=P), tile)]
                if g == 1:
                    return [(row.rearrange("(m p r) -> p r m", p=P, r=4)[:, r, :], tile[:, 2 * r:2 * r + 2]) for r in range(4)]
                by_half = row.rearrange("(i b a) -> a i b", b=8, a=2)
                return [(by_half[a], tile[a * 64:(a + 1) * 64, :]) for a in range(2)]

            moves = sum(len(token_order(stat_dram[0, g], share[:, 0:8], g)) for g in range(N_DIL))

            with nc.psum_tensor("dil_z", [P, 2, 2, HALF], F32) as z, nc.psum_tensor("dil_aux", [P, 2, HALF], F32) as aux, \
                    nc.psum_tensor("dil_acc", [P, 2, HALF], F32) as acc, nc.Block() as block:
                @block.sync
                def _(sp):
                    ring.load_all(sp, C_SLOTS, NT, lambda h, t: odd_cols(t % 2, bass.ds(h * P + DIL_COLS[t], P)))
                    pre.load(sp)

                @block.gpsimd
                def _(pool):
                    ring.credits(pool, None)
                    ring.split_all(pool, C_SLOTS, NT)
                    pre.split(pool)

                @block.tensor
                def _(pe):
                    ring.credits(None, pe)
                    with pe.Fori(0, C_SLOTS) as h:
                        uses = [0]

                        def take_aux():
                            a = uses[0]
                            pe.wait_ge(aux_free[a % 2], AUX // 2 * h + a // 2 + 1)
                            uses[0] += 1
                            return aux[:, a % 2, :]

                        def score(u):
                            g, b, k0, n = units[u]
                            to = take_aux()
                            pe.wait_ge(z_out, NT * h + 2 * g + 2 + 2)
                            pe.matmul(to[:, 0:n * P], q_cm_[:, g, b * P:(b + 1) * P], k_cm_[:, g, k0 * P:(k0 + n) * P], start=True, stop=True).then_inc(scores, 1)

                        def proj(t, first_unit=None):
                            between = None
                            if first_unit is not None:
                                between = {2 * k + 1: (lambda u=first_unit + k: score(u)) for k in range(4)}
                            ring.project(pe, NT * h + t, t % 2, z_out, [(z[:, t % 2, b, :], c0, w) for b, c0, w in BOTH], h_hi, h_lo, between)

                        def turn_v(g):
                            pe.wait_ge(z_out, NT * h + VT + g + 3)
                            for half in range(2):
                                to = take_aux()
                                for j in range(4):
                                    at = (4 * half + j) * P
                                    ins = pe.transpose(to[:, j * P:(j + 1) * P], v_cm[:, at:at + P], ident)
                                ins.then_inc(v_turned, 1)

                        def turn_p(u):
                            to = take_aux()
                            pe.wait_ge(scaled, NU * h + u + 1)
                            for j in range(units[u][3]):
                                ins = pe.transpose(to[:, j * P:(j + 1) * P], probs[u][:, j * P:(j + 1) * P], ident)
                            ins.then_inc(p_turned, 1)

                        def weigh_v(u):
                            g, b, k0, n = units[u]
                            pe.wait_ge(p_t_out, NU * h + u + 1)
                            for j in range(n):
                                pt = p_t[:, u % 2, j * P:(j + 1) * P]
                                v = v_rows_[:, g, k0 + j, :]
                                if g == 0:
                                    ins = pe.matmul(acc[:, b // 4, (b % 4) * P:(b % 4 + 1) * P], v, pt, start=False, stop=False)
                                elif g == 1:
                                    ins = pe.matmul(acc[:, b % 2, :].rearrange("p (m r) -> p r m", r=4)[:, b // 2, :], v, pt, start=False, stop=False)
                                else:
                                    for bank in range(2):
                                        to = acc[:, bank, :].rearrange("p (i c a) -> p c a i", c=8, a=2)[:, b]
                                        ins = pe.matmul(to, v, pt.rearrange("p (a s i) -> p s a i", a=2, s=2)[:, bank], start=False, stop=(b == BLOCKS - 1))
                            ins.then_inc(summed, 1)

                        for t in range(2):
                            proj(t)
                        for t in range(6):
                            proj(2 + t, 4 * t)
                        turn_v(0)
                        proj(VT + 2)
                        turn_v(1)
                        proj(GT)
                        turn_v(2)
                        turn_p(0)
                        pe.wait_ge(y_done, h + 1)
                        for bank in range(2):
                            pe.matmul(acc[:, bank, :], ones[0:1, :], zero_col[0:1, :].to_broadcast([1, HALF]), start=True, stop=False)
                        pe.wait_ge(rows_out, 6 * h + 6)
                        for u in range(NU):
                            if u + 1 < NU:
                                turn_p(u + 1)
                            weigh_v(u)
                        assert uses[0] == AUX

                @block.scalar
                def _(act):
                    act.sem_inc(z_out, 2)
                    with act.Fori(0, C_SLOTS) as h:
                        def take(t, to):
                            act.wait_ge(ring.projected, NT * h + t + 3)
                            act.activation(to, in_banks(z[:, t % 2], t // 2) if t < VT else in_banks(z[:, t % 2], t - VT), ACT.Copy,
                                           scale=P ** -0.5 if t < VT and t % 2 else 1.0).then_inc(z_out, 1)

                        def exps(u0):
                            for u in range(u0, u0 + 4):
                                w = units[u][3] * P
                                act.wait_ge(max_done, NU * h + u + 1)
                                act.activation(probs[u][:], biased[:, u % 2, 0:w], ACT.Exp, bias=neg_max[:, u:u + 1],
                                               accum_out=den[:, u:u + 1]).then_inc(exp_done, 1)

                        for t in range(2 * N_DIL):
                            if t >= 2:
                                exps(4 * (t - 2))
                            take(t, reordered((q_cm_ if t % 2 else k_cm_)[:, t // 2, :], t // 2))
                        for g in range(N_DIL):
                            if g < 2:
                                exps(16 + 4 * g)
                            if g == 2:
                                act.wait_ge(exp_done, NU * h + NU + 2)
                                act.activation(log_den[:], den[:], ACT.Ln).then_inc(log_done, 1)
                                act.wait_ge(lse_done, h + 1)
                                for q in range(N_DIL):
                                    for row, tile in token_order(stat_dram[0, q], lse[:, 8 * q:8 * q + 8], q):
                                        act.dma_start(row, tile, allow_slow_non_contiguous=True).then_inc(lse_stored, 16)
                                act.wait_ge(lse_stored, 16 * moves * (h + 1))
                                act.dma_start(joint[:], stat_dram[0].rearrange("q (p j) -> p q j", j=8)).then_inc(joint_loaded, 16)
                                act.wait_ge(joint_shifted, h + 1)
                                act.activation(joint[:], joint[:], ACT.Exp).then_inc(joint_exp, 1)
                                act.wait_ge(share_done, h + 1)
                                act.dma_start(factor_dram.rearrange("q (p j) -> p q j", j=8), joint[:]).then_inc(share_stored, 16)
                                act.wait_ge(share_stored, 16 * (h + 1))
                                for q in range(N_DIL):
                                    for row, tile in token_order(factor_dram[q], share[:, 8 * q:8 * q + 8], q):
                                        act.dma_start(tile, row, allow_slow_non_contiguous=True).then_inc(share_loaded, 16)
                            act.wait_ge(v_turned, 6 * h + 2 * g)
                            take(VT + g, reordered(v_cm[:], g))
                        act.wait_ge(ring.projected, NT * h + GT + 3)
                        act.wait_ge(y_done, h + 1)
                        act.activation(silu[:], z[:, GT % 2].rearrange("p b n -> p (b n)"), ACT.Silu).then_inc(z_out, 1)
                        act.wait_ge(factor_done, h + 1)
                        for u in range(NU):
                            act.activation(probs[u][:], probs[u][:], ACT.Copy, scale=share[:, u:u + 1]).then_inc(scaled, 1)

                @block.vector
                def _(dve):
                    for b in range(2):
                        dve.sem_inc(aux_free[b], 1)
                    dve.sem_inc(exp_done, 2)
                    dve.sem_inc(y_done, 1)
                    dve.sem_inc(dve_step, 1)
                    N_STEP = 10
                    with dve.Fori(0, C_SLOTS) as h:
                        step = Steps(dve, dve_step, N_STEP * h + 1)
                        uses = 0
                        step.wait()
                        pass_waits(dve)
                        step(dve.tensor_copy(slope_now[:], cst("slopes").rearrange("p (g s) -> p g s", g=N_DIL)[:, :, bass.ds(h, 1)]))
                        step.wait()
                        for u, (g, b, k0, n) in enumerate(units):
                            w = n * P
                            dist = cst("dist16") if g == 2 else cst("dist")[:, (2 - n) * P:]
                            dve.wait_ge(scores, NU * h + u + 1)
                            dve.wait_ge(exp_done, NU * h + u + 1)
                            dve.scalar_tensor_tensor(out=biased[:, u % 2, 0:w], in0=dist, scalar=slope_now[:, g, :], in1=aux[:, uses % 2, 0:w],
                                                     op0=ALU.mult, op1=ALU.add).then_inc(aux_free[uses % 2], 1)
                            uses += 1
                            dve.wait_ge(aux_free[u % 2], AUX // 2 * h + u // 2 + 2)
                            dve.tensor_reduce(neg_max[:, u:u + 1], biased[:, u % 2, 0:w], AX_X, ALU.max, negate=True).then_inc(max_done, 1)

                        def rows(g):
                            nonlocal uses
                            for half in range(2):
                                dve.wait_ge(v_turned, 6 * h + 2 * g + half + 1)
                                dve.tensor_copy(v_rows_[:, g, 4 * half:4 * half + 4, :].rearrange("p j n -> p (j n)"), aux[:, uses % 2, :]).then_inc(aux_free[uses % 2], 1)
                                uses += 1
                                dve.wait_ge(aux_free[(uses - 1) % 2], AUX // 2 * h + (uses - 1) // 2 + 2)
                                dve.sem_inc(rows_out, 1)

                        dve.wait_ge(log_done, h + 1)
                        dve.wait_ge(max_done, NU * h + NU)
                        dve.tensor_tensor(lse[:], log_den[:], neg_max[:], ALU.subtract).then_inc(lse_done, 1)
                        step(dve.reciprocal(den[:], den[:]))
                        rows(0)
                        dve.wait_ge(joint_loaded, 16 * (h + 1))
                        step(dve.tensor_tensor(joint_max[:], joint[:, 0], joint[:, 1], ALU.max))
                        step.wait()
                        step(dve.tensor_tensor(joint_max[:], joint_max[:], joint[:, 2], ALU.max))
                        step.wait()
                        dve.tensor_tensor(joint[:], joint[:], joint_max[:].unsqueeze(1).to_broadcast([P, N_DIL, 8]), ALU.subtract).then_inc(joint_shifted, 1)
                        dve.wait_ge(joint_exp, h + 1)
                        step(dve.tensor_tensor(joint_sum[:], joint[:, 0], joint[:, 1], ALU.add))
                        step.wait()
                        step(dve.tensor_tensor(joint_sum[:], joint_sum[:], joint[:, 2], ALU.add))
                        step.wait()
                        step(dve.reciprocal(joint_sum[:], joint_sum[:]))
                        step.wait()
                        dve.tensor_tensor(joint[:], joint[:], joint_sum[:].unsqueeze(1).to_broadcast([P, N_DIL, 8]), ALU.mult).then_inc(share_done, 1)
                        rows(1)
                        rows(2)
                        dve.wait_ge(share_loaded, 16 * moves * (h + 1))
                        dve.tensor_tensor(share[:], share[:], den[:], ALU.mult).then_inc(factor_done, 1)
                        for u in range(NU):
                            w = units[u][3] * P
                            dve.wait_ge(p_turned, NU * h + u + 1)
                            if u >= 2:
                                dve.wait_ge(summed, NU * h + u - 1)
                            dve.tensor_copy(p_t[:, u % 2, 0:w], aux[:, uses % 2, 0:w]).then_inc(aux_free[uses % 2], 1)
                            uses += 1
                            dve.wait_ge(aux_free[(uses - 1) % 2], AUX // 2 * h + (uses - 1) // 2 + 2)
                            dve.sem_inc(p_t_out, 1)
                        dve.wait_ge(summed, NU * h + NU)
                        dve.wait_ge(z_out, NT * h + NT + 2)
                        dve.tensor_tensor(y_plain[:, bass.ds(h, 1), :].rearrange("p o t -> p (o t)"), acc[:].rearrange("p b n -> p (b n)"), silu[:],
                                          ALU.mult).then_inc(y_done, 1)
                        dve.wait_ge(y_done, h + 2)
                        dve.sem_inc(dve_step, N_STEP - step.done)

        def phase_rows_out():
            phases.start()
            rows = Arena(nc, free_at)("out_rows", [P, 2, D])
            turned = sem("rows_turned")
            rows_out = sem("rows_out")
            stored = [sem(f"rows_stored{u}") for u in range(2)]
            with nc.psum_tensor("rows_turn", [P, 2, 2, HALF], F32) as turn, nc.Block() as block:
                @block.tensor
                def _(pe):
                    for j in range(BLOCKS):
                        if j >= 2:
                            pe.wait_ge(rows_out, 2 * (j - 1))
                        for kt in range(KT):
                            ins = pe.transpose(turn[:, j % 2, kt // 4, (kt % 4) * P:(kt % 4 + 1) * P], h2_cm[:, kt, j * P:(j + 1) * P], ident)
                            if kt % 4 == 3:
                                ins.then_inc(turned, 1)

                @block.scalar
                def _(act):
                    for j in range(BLOCKS):
                        if j >= 2:
                            act.wait_ge(stored[j % 2], 16 * (j // 2))
                        for half in range(2):
                            act.wait_ge(turned, 2 * j + half + 1)
                            act.copy(rows[:, j % 2, half * HALF:(half + 1) * HALF], turn[:, j % 2, half, :]).then_inc(rows_out, 1)

                @block.sync
                def _(sp):
                    for j in range(BLOCKS):
                        sp.wait_ge(rows_out, 2 * (j + 1))
                        sp.dma_start(out[0, j * P:(j + 1) * P, :], rows[:, j % 2, :]).then_inc(stored[j % 2], 16)
                    for u in range(2):
                        sp.wait_ge(stored[u], 16 * (BLOCKS // 2))

        phase_conv([odd_b_out(u) for u in range(2)])
        phase_out("odd_b_out", y_hi, y_lo, odd_b_out, 1, None, [odd_cols(u, slice(DIL_COLS[u], DIL_COLS[u] + P)) for u in range(2)])
        phase_dilated([odd_a_out(u) for u in range(2)])
        phase_out("odd_a_out", h_hi, h_lo, odd_a_out, 1, None, split_from=y_plain,
                  norm=dict(affines=[(0, SEQ, plain_gain("final_norm_2"), None)], h_plain=h2_cm))
        phase_rows_out()


_USED = ["x", "c", "ctx", "c_ctx", "w_mod", "b_mod", "norm1_w", "norm2_w", "w_in", "b_gates", "conv_qk", "q_norm_w", "k_norm_w",
         "sink", "mlstm_norm_w", "w_out", "w_router", "w_gate", "w_up", "w_down", "even_norm_2", "even_w_in_2", "even_pool_w_2",
         "even_pool_scale_2", "even_ws_2", "even_bs_2", "even_w_out_2", "odd_norm_2", "odd_w_in_2", "odd_conv_w_2", "odd_w_out_2",
         "final_norm_2"]


def declare(nc, inputs):
    arrays, args = {}, {}
    for name, a in {**{n: inputs[n] for n in _USED}, **constant_tables()}.items():
        a = np.ascontiguousarray(a)
        arrays[f"in_{name}"] = a
        args[name] = nc.dram_tensor(f"in_{name}", a.shape, F32, kind="ExternalInput").ap()
    out = nc.dram_tensor("out", (1, SEQ, D), F32, kind="ExternalOutput").ap()
    return arrays, args, out


def kernel(**inputs):
    import concourse.bacc as bacc
    from concourse.bass_utils import run_bass_kernel_spmd

    nc = bacc.Bacc("TRN2", target_bir_lowering=False, num_devices=1)
    arrays, args, out = declare(nc, inputs)
    build_program(nc, args, out)
    result = run_bass_kernel_spmd(nc, [arrays], core_ids=[0])
    return result.results[0]["out"]
```

```python
from contextlib import ExitStack

import numpy as np

import concourse.bass as bass
from concourse import mybir

F32 = mybir.dt.float32
F32R = mybir.dt.float32r
U32 = mybir.dt.uint32
ALU = mybir.AluOpType
ACT = mybir.ActivationFunctionType
AX_X = mybir.AxisListType.X

P = 128
D = 1024
KT = D // P
SEQ = 1024
CTX = 256
TOK = CTX + SEQ
HALF = 512
EPS = 1e-6
NEG = -1e30
GRID_W = 64
N_HEADS, HEAD_DIM = 8, 64
M_HEADS, M_DIM = 4, 128
CHUNK = 128
XCH = SEQ // CHUNK
ALLCH = TOK // CHUNK
CCH = CTX // CHUNK
N_EXPERTS, EXPERT_FF = 16, 512
SLOTS = 2 * SEQ // N_EXPERTS
POOL_SIZES = (2, 4, 8, 16)
C_SLOTS, N_DIL = 8, 3
DILATION = (1, 4, 16)
BLOCKS = SEQ // P
Q_COL, K_COL, V_COL, MQ_COL, MK_COL, MV_COL, MO_COL, G_COL = 0, 512, 640, 768, 1280, 1792, 2304, 2816
GATE_ROWS = 36

CONST_PARTS = (("ident", P), ("ones", P), ("head_ones", P), ("rotate", P), ("near_mask", 3 * P), ("chunk_mask", 2 * P),
               ("dist", 2 * P), ("dist16", P), ("slopes", N_DIL * C_SLOTS), ("pool_inv", len(POOL_SIZES) * 16))
CONST_AT, _n = {}, 0
for _name, _w in CONST_PARTS:
    CONST_AT[_name] = (_n, _w)
    _n += _w
CONST_W = _n
ROWS_A = (("b_mod", 48), ("norm1_w", 8), ("norm2_w", 8), ("even_norm_2", 8), ("odd_norm_2", 8), ("final_norm_2", 8),
          ("even_pool_scale_2", 8))
ROWS_B = (("conv_qk", 24), ("odd_conv_w_2", 24), ("mlstm_norm_w", 4), ("c", 8), ("c_ctx", 8))
SH1, SC1, G1, SH2, SC2, G2 = range(0, 48, 8)


def columns_of(parts):
    at, n = {}, 0
    for name, rows in parts:
        at[name] = (n, rows)
        n += rows
    return at, n


AT_A, N_A = columns_of(ROWS_A)
AT_B, N_B = columns_of(ROWS_B)


def constant_tables():
    i = np.arange(P)
    table = np.zeros((P, CONST_W), np.float32)

    def put(name, value):
        at, width = CONST_AT[name]
        table[:, at:at + width] = value

    put("ident", np.eye(P))
    put("ones", 1.0)
    put("head_ones", (i[:, None] // HEAD_DIM == i[None] // HEAD_DIM))
    rotate = np.zeros((P, P))
    for m in range(P):
        if m % HEAD_DIM < HEAD_DIM // 2:
            rotate[m + HEAD_DIM // 2, m] = -1.0
        else:
            rotate[m - HEAD_DIM // 2, m] = 1.0
    put("rotate", rotate)
    q, k = i[:, None], np.arange(3 * P)[None]
    put("near_mask", np.where(np.abs(q + P - k) <= P, 0.0, NEG))
    put("chunk_mask", np.concatenate([np.where(q <= i[None], 0.0, NEG), np.where(q >= i[None], 0.0, NEG)], 1))
    steps = q + P - np.arange(2 * P)[None]
    put("dist", np.where((steps >= 0) & (steps <= P), -steps, NEG))
    half = P // 2
    same = (q // half == i[None] // half) & (i[None] % half <= q % half)
    put("dist16", np.where(same, -(q % half - i[None] % half), NEG))
    n = N_DIL * C_SLOTS
    slopes = 2.0 ** (-8.0 * (np.arange(n) + 1) / n)
    put("slopes", np.repeat(slopes[None] * np.repeat(DILATION, C_SLOTS)[None], P, 0))
    t = np.arange(16)
    put("pool_inv", np.repeat(np.concatenate([1.0 / np.minimum(t + 1, w) for w in POOL_SIZES])[None], P, 0))

    pos = np.arange(SEQ)
    n_freq = HEAD_DIM // 4
    freqs = (np.float32(10000.0) ** (-np.arange(n_freq, dtype=np.float32) / np.float32(n_freq))).astype(np.float32)
    ang = np.concatenate([(pos // GRID_W)[:, None].astype(np.float32) * freqs,
                          (pos % GRID_W)[:, None].astype(np.float32) * freqs], 1)
    ang = np.concatenate([ang, ang, ang, ang], 1).T
    rope = np.stack([np.cos(ang), np.sin(ang)], 1).astype(np.float32)

    pick = np.zeros((GATE_ROWS, 8, P), np.float32)
    for r in range(8):
        pick[32 * (r // M_HEADS) + r % M_HEADS, r] = 1.0
    keep = np.ones((GATE_ROWS, TOK), np.float32)
    keep[:, ::CHUNK] = 0.0
    return {"const_table": table, "rope_table": rope, "pick_table": pick.reshape(GATE_ROWS, 8 * P), "keep_table": keep}


class Steps:

    def __init__(self, eng, sem, base=0):
        self.eng, self.sem, self.base, self.done = eng, sem, base, 0

    def __call__(self, ins):
        ins.then_inc(self.sem, 1)
        self.done += 1
        return ins

    def wait(self):
        self.eng.wait_ge(self.sem, self.base + self.done)


class Arena:

    def __init__(self, nc, at):
        self.nc, self.at = nc, at

    def __call__(self, name, shape, dtype=F32):
        words = 1
        for s in shape[1:]:
            words *= s
        t = self.nc.alloc_sbuf_tensor_at(name, list(shape), dtype, offset=self.at)
        self.at += (words * 4 + 31) // 32 * 32
        assert self.at <= self.nc.sbuf_usable_end, (name, self.at)
        return t


class PhaseSemaphores:

    def __init__(self, nc):
        self.nc = nc
        free = sorted(nc.free_semaphores)
        self.kept, free = free[:8], free[8:]
        self.sets = [free[:len(free) // 2], free[len(free) // 2:]]
        self.used = []

    def start(self):
        if self.used:
            self.nc.gpsimd.sem_clear(range(self.used[0].num, self.used[-1].num + 1))
            for s in self.used:
                self.nc.release_semaphore(s)
        self.used = []
        self.sets.reverse()

    def keep(self, name):
        return self.nc.alloc_semaphore(name, num=self.kept.pop())

    def sem(self, name):
        self.used.append(self.nc.alloc_semaphore(name, num=self.sets[0][len(self.used)]))
        return self.used[-1]


def build_program(nc, A, out):
    with ExitStack() as ctx:
        phases = PhaseSemaphores(nc)
        sem = phases.sem

        def dram(name, shape):
            return nc.dram_tensor(name, shape, F32, kind="Internal").ap()

        x_cm = dram("x_cm", (D, SEQ))
        att_cm = dram("att_cm", (N_HEADS * HEAD_DIM, SEQ))
        h2_rows = dram("h2_rows", (SEQ, D))
        ffn_rows = dram("ffn_rows", (SEQ, D))
        stat_dram = dram("stat_dram", (2, N_DIL, SEQ))
        factor_dram = dram("factor_dram", (N_DIL, SEQ))
        x_cm_k = x_cm.rearrange("(k p) t -> p k t", p=P)

        start = (nc.sbuf_base + 63) // 32 * 32
        fixed = Arena(nc, start)
        const = fixed("const", [P, CONST_W])
        par_a = fixed("par_a", [P, N_A])
        par_b = fixed("par_b", [P, N_B])
        mod = fixed("mod", [P, 48, 2])
        gain1 = fixed("gain1", [P, KT, 2])
        gain2 = fixed("gain2", [P, KT])
        sinks = fixed("sinks", [P, N_HEADS])
        qk_gain = fixed("qk_gain", [P, 2])
        gate_bias = fixed("gate_bias", [P, 1])
        silu_c = fixed("silu_c", [P, KT, 2])
        ring_at = fixed.at
        w_raw = fixed("w_raw", [P, 2, KT, P])
        w_hi = fixed("w_hi", [P, 2, KT, P], F32R)
        w_lo = fixed("w_lo", [P, 2, KT, P], F32R)
        zero_col = fixed("zero_col", [P, 1])
        eps_col = fixed("eps_col", [P, 1])
        free_at = fixed.at

        def cst(name):
            at, width = CONST_AT[name]
            return const[:, at:at + width]

        def pa(name):
            at, width = AT_A[name]
            return par_a[:, at:at + width]

        def pb(name):
            at, width = AT_B[name]
            return par_b[:, at:at + width]

        ident, ones = cst("ident"), cst("ones")
        passed = phases.keep("passed")

        def pass_waits(eng):
            eng.sem_inc(passed, 1)

        class Ring:

            def __init__(self, tag, pieces=1, ready=2):
                self.pieces, self.ready = pieces, ready
                self.loaded = [sem(f"{tag}_w_loaded{u}") for u in range(2)]
                self.hi_done = sem(f"{tag}_w_hi_done")
                self.split = sem(f"{tag}_w_split")
                self.projected = sem(f"{tag}_projected")

            def load(self, sp, n, u, parts):
                sp.wait_ge(self.split, n + 1)
                if not isinstance(n, int):
                    pass_waits(sp)
                assert len(parts) == self.pieces
                for dst, src in parts:
                    sp.dma_start(dst, src).then_inc(self.loaded[u], 16)

            def credits(self, pool, pe):
                if pool is not None:
                    pool.sem_inc(self.split, 2 + self.ready)
                    if self.ready:
                        pool.sem_inc(self.hi_done, self.ready)
                if pe is not None:
                    pe.sem_inc(self.projected, 2)

            def do_split(self, pool, n, u, round_):
                pool.wait_ge(self.loaded[u], 16 * self.pieces * (round_ + 1 - self.ready // 2))
                pool.wait_ge(self.projected, n + 1)
                pool.tensor_tensor(w_hi[:, u], w_raw[:, u], zero_col[:, 0:1].to_broadcast([P, KT * P]).rearrange("p (k n) -> p k n", k=KT),
                                   ALU.add).then_inc(self.hi_done, 1)
                pool.wait_ge(self.hi_done, n + 1)
                pool.tensor_tensor(w_lo[:, u], w_raw[:, u], w_hi[:, u].bitcast(F32), ALU.subtract).then_inc(self.split, 1)

            def load_all(self, sp, groups, tiles, parts, before=None):
                def load(g, t):
                    self.load(sp, tiles * g + t, t % 2, parts(g + t // tiles, t % tiles))

                with sp.Fori(0, groups - 1) as g:
                    if before:
                        before(g)
                    for t in range(2, tiles + 2):
                        load(g, t)
                if before:
                    before(groups - 1)
                for t in range(2, tiles):
                    load(groups - 1, t)

            def split_all(self, pool, groups, tiles):
                with pool.Fori(0, groups - 1) as g:
                    for t in range(2, tiles + 2):
                        self.do_split(pool, tiles * g + t, t % 2, tiles // 2 * g + t // 2)
                for t in range(2, tiles):
                    self.do_split(pool, tiles * (groups - 1) + t, t % 2, tiles // 2 * (groups - 1) + t // 2)

            def project(self, pe, n, u, z_free, targets, rhs_hi, rhs_lo, between=None):
                pe.wait_ge(self.split, n + 3)
                pe.wait_ge(z_free, n + 1)
                for kt in range(KT):
                    for w, rhs, first, last in ((w_hi, rhs_hi, kt == 0, False), (w_hi, rhs_lo, False, False),
                                                (w_lo, rhs_hi, False, kt == KT - 1)):
                        for z, c0, width in targets:
                            ins = pe.matmul(z, w[:, u, kt], rhs[:, kt, c0:c0 + width], start=first, stop=last)
                    if between and kt in between:
                        between[kt]()
                ins.then_inc(self.projected, 1)

        class Prefetch:

            def __init__(self, tag, parts, ring=None, n=0):
                self.parts, self.ring, self.n = parts, ring, n
                self.loaded = [sem(f"{tag}_next_loaded{u}") for u in range(2)]
                self.hi_done = sem(f"{tag}_next_hi_done")

            def load(self, sp):
                for u in range(2):
                    if self.ring:
                        sp.wait_ge(self.ring.split, self.n + u + 1)
                    for dst, src in self.parts[u]:
                        sp.dma_start(dst, src).then_inc(self.loaded[u], 16)

            def split(self, pool):
                for u in range(2):
                    pool.wait_ge(self.loaded[u], 16 * len(self.parts[u]))
                    if self.ring:
                        pool.wait_ge(self.ring.projected, self.n + u + 1)
                    pool.tensor_tensor(w_hi[:, u], w_raw[:, u], zero_col[:, 0:1].to_broadcast([P, KT * P]).rearrange("p (k n) -> p k n", k=KT),
                                       ALU.add).then_inc(self.hi_done, 1)
                    pool.wait_ge(self.hi_done, u + 1)
                    pool.tensor_tensor(w_lo[:, u], w_raw[:, u], w_hi[:, u].bitcast(F32), ALU.subtract)

        class NormTail:

            def __init__(self, tag, mem, x, n_tok, affines, h_hi=None, h_lo=None, h_plain=None, away=None):
                self.x, self.n_tok, self.affines = x, n_tok, affines
                self.y = x if away is None else away
                self.h_hi, self.h_lo, self.h_plain = h_hi, h_lo, h_plain
                self.small = [a for a in affines if a[1] < HALF]
                self.large = [a for a in affines if a[1] >= HALF]
                self.blocks = n_tok // P
                self.rstd = mem(f"{tag}_rstd", [P, self.blocks])
                self.summed = sem(f"{tag}_norm_summed")
                self.mean_done = sem(f"{tag}_norm_mean_done")
                self.root_done = sem(f"{tag}_norm_root_done")
                self.inverse_done = sem(f"{tag}_norm_inverse_done")
                self.spread = sem(f"{tag}_norm_spread")
                self.scaled = sem(f"{tag}_norm_scaled")
                self.shifted = sem(f"{tag}_norm_shifted")
                self.small_shifted = sem(f"{tag}_norm_small_shifted")
                self.hi_done = sem(f"{tag}_norm_hi_done")
                self.lo_done = sem(f"{tag}_norm_lo_done")

            def through_shift(self, kt):
                return kt % 2 == 0 or any(shift for _, _, _, shift in self.affines)

            def pool_splits(self, kt):
                return kt % 2 == 0 or (kt % 4 == 1 and self.through_shift(kt) and self.y is not self.x)

            def pe(self, pe, spread):
                pe.wait_ge(self.inverse_done, 1)
                for j in range(self.blocks):
                    ins = pe.transpose(spread[:, j // 4, j % 4 * P:(j % 4 + 1) * P], self.rstd[:, j:j + 1].to_broadcast([P, P]), ident)
                ins.then_inc(self.spread, 1)

            def dve(self, dve, sums, spread, x_free=None):
                dve.wait_ge(self.summed, 1)
                dve.tensor_scalar(self.rstd[:], sums, 1.0 / D, EPS, ALU.mult, ALU.add).then_inc(self.mean_done, 1)
                dve.wait_ge(self.root_done, 1)
                dve.reciprocal(self.rstd[:], self.rstd[:]).then_inc(self.inverse_done, 1)
                dve.wait_ge(self.spread, 1)
                flat = spread.rearrange("p g n -> p (g n)")[:, 0:self.n_tok]

                def lo(kt):
                    dve.wait_ge(self.hi_done, kt + 1)
                    if self.through_shift(kt):
                        dve.tensor_tensor(self.h_lo[:, kt, :], self.y[:, kt, :], self.h_hi[:, kt, :].bitcast(F32), ALU.subtract).then_inc(self.lo_done, 1)
                    else:
                        dve.scalar_tensor_tensor(out=self.h_lo[:, kt, :], in0=self.y[:, kt, :], scalar=self.affines[0][2](kt),
                                                 in1=self.h_hi[:, kt, :].bitcast(F32), op0=ALU.mult, op1=ALU.subtract).then_inc(self.lo_done, 1)

                for kt in range(KT):
                    if x_free:
                        x_free(kt)
                    dve.tensor_tensor(self.y[:, kt, :], self.x[:, kt, :], flat, ALU.mult).then_inc(self.scaled, 1)
                    for c0, width, gain, shift in self.small:
                        dve.wait_ge(self.scaled, kt + 1)
                        dve.tensor_scalar(self.y[:, kt, c0:c0 + width], self.y[:, kt, c0:c0 + width], gain(kt), shift(kt),
                                          ALU.mult, ALU.add).then_inc(self.small_shifted, 1)
                    if self.h_plain is None and kt >= 2 and not self.pool_splits(kt - 2):
                        lo(kt - 2)
                if self.h_plain is None:
                    lo(KT - 1)

            def act(self, act):
                act.wait_ge(self.mean_done, 1)
                act.activation(self.rstd[:], self.rstd[:], ACT.Sqrt).then_inc(self.root_done, 1)
                n = 0
                for kt in range(KT):
                    act.wait_ge(self.scaled, kt + 1)
                    if self.h_plain is None and not self.through_shift(kt):
                        act.activation(self.h_hi[:, kt, :], self.y[:, kt, :], ACT.Copy, scale=self.affines[0][2](kt)).then_inc(self.hi_done, 1)
                        continue
                    to = (self.y if self.h_plain is None else self.h_plain)[:, kt, :]
                    for c0, width, gain, shift in self.large:
                        act.activation(to[:, c0:c0 + width], self.y[:, kt, c0:c0 + width], ACT.Identity, scale=gain(kt),
                                       bias=0.0 if shift is None else shift(kt)).then_inc(self.shifted, 1)
                        n += 1
                    if self.h_plain is None:
                        act.wait_ge(self.shifted, n)
                        if self.small:
                            act.wait_ge(self.small_shifted, len(self.small) * (kt + 1))
                        act.copy(self.h_hi[:, kt, :], self.y[:, kt, :]).then_inc(self.hi_done, 1)

            def pool(self, pool):
                if self.h_plain is None:
                    for kt in filter(self.pool_splits, range(KT)):
                        pool.wait_ge(self.hi_done, kt + 1)
                        pool.tensor_tensor(self.h_lo[:, kt, :], self.y[:, kt, :], self.h_hi[:, kt, :].bitcast(F32), ALU.subtract)

        SCAN_MOD, MIX_MOD, END_MOD = 16, 21, 24

        class Modulation:

            WIDTH = HALF // 2

            def __init__(self, tag, mem, w, first, count):
                self.w, self.first, self.count = w, first, count
                self.rows_sb = mem(f"{tag}_mod_rows_sb", [2, 3, self.WIDTH])
                self.w_loaded = [sem(f"{tag}_mod_w_loaded{u}") for u in range(len(w))]
                self.w_used = sem(f"{tag}_mod_w_used")
                self.rows_out = sem(f"{tag}_mod_rows_out")
                self.columns_done = sem(f"{tag}_mod_columns_done")
                self.bias_added = sem(f"{tag}_mod_bias_added")
                self.src = A["w_mod"].rearrange("o (k p) n -> p (o k) n", p=P)

            def sp(self, sp, j):
                u, at = j % len(self.w), (self.first + j) * self.WIDTH
                if j >= len(self.w):
                    sp.wait_ge(self.w_used, j - len(self.w) + 1)
                sp.dma_start(self.w[u][:], self.src[:, :, at:at + self.WIDTH]).then_inc(self.w_loaded[u], 16)

            def pe(self, pe, j, row_acc, acc):
                u = j % len(self.w)
                pe.wait_ge(self.w_loaded[u], 16 * (j // len(self.w) + 1))
                if j >= 2:
                    pe.wait_ge(self.rows_out, j - 1)
                for kt in range(KT):
                    ins = pe.matmul(row_acc[:, j % 2, 0:self.WIDTH], silu_c[:, kt, :], self.w[u][:, kt, :], start=(kt == 0), stop=(kt == KT - 1))
                ins.then_inc(self.w_used, 1)
                if j:
                    self.pe_columns(pe, j - 1, acc)
                if j == self.count - 1:
                    self.pe_columns(pe, j, acc)

            def pe_columns(self, pe, j, acc):
                pe.wait_ge(self.rows_out, j + 1)
                for q in range(self.WIDTH // P):
                    at = 2 * (j * self.WIDTH // P + q)
                    ins = pe.transpose(acc[:, at:at + 2], self.rows_sb[:, j % 3, q * P:(q + 1) * P], ident[0:2, 0:2])
                ins.then_inc(self.columns_done, 1)

            def copy_rows(self, eng, copy, j, row_acc):
                eng.wait_ge(self.w_used, j + 1)
                if j >= 3:
                    eng.wait_ge(self.columns_done, j - 2)
                copy(self.rows_sb[:, j % 3, :], row_acc[:, j % 2, 0:self.WIDTH]).then_inc(self.rows_out, 1)

            def act(self, act, j, row_acc):
                self.copy_rows(act, act.copy, j, row_acc)

            def dve(self, dve, j, row_acc):
                self.copy_rows(dve, dve.tensor_copy, j, row_acc)

            def dve_add(self, dve, acc, begin, end):
                each = self.WIDTH // P
                columns = (end - begin) * each
                to = slice((self.first + begin) * each, (self.first + end) * each)
                dve.wait_ge(self.columns_done, end)
                dve.tensor_tensor(mod[:, to], acc[:, 2 * each * begin:2 * each * end].rearrange("p (j s) -> p j s", s=2),
                                  pa("b_mod")[:, to].unsqueeze(2).to_broadcast([P, columns, 2]), ALU.add).then_inc(self.bias_added, 1)

        class FirstModulation(Modulation):

            NEEDED = 2 * D // Modulation.WIDTH

            def __init__(self, mem, w):
                Modulation.__init__(self, "start", mem, w, 0, SCAN_MOD)
                self.rows_a = mem("rows_a", [N_A, P])
                self.rows_b = mem("rows_b", [N_B, P])
                self.sink_row = mem("sink_row", [1, N_HEADS])
                self.small = sem("start_small_loaded")
                self.bias_zeroed = sem("start_bias_zeroed")
                self.bias_loaded = sem("start_bias_loaded")
                self.turned = sem("start_params_turned")
                self.params_ready = sem("start_params_ready")
                self.silu_done = sem("start_silu_done")
                self.gain_done = sem("start_gain_done")
                self.params_out = sem("start_params_out")
                self.parts = [(const[:], A["const_table"])]
                for rows, names, at in ((self.rows_a, ROWS_A, AT_A), (self.rows_b, ROWS_B, AT_B)):
                    for name, count in names:
                        src = A[name]
                        letters = "abcd"[:len(src.shape)]
                        flat = src.rearrange(f"{' '.join(letters)} -> ({' '.join(letters)})") if len(src.shape) > 1 else src
                        self.parts.append((rows[at[name][0]:at[name][0] + count, :], flat.rearrange("(r q) -> r q", q=P)))
                self.parts.append((self.sink_row[:], A["sink"]))
                for col, name in ((0, "q_norm_w"), (1, "k_norm_w")):
                    for half in range(2):
                        self.parts.append((qk_gain[half * HEAD_DIM:(half + 1) * HEAD_DIM, col:col + 1], A[name].rearrange("o p -> p o")))
                self.biases = [(gate_bias[row:row + M_HEADS, :], A["b_gates"][0:1, at:at + M_HEADS].rearrange("o p -> p o"))
                               for row, at in ((0, 0), (64, 4), (32, 8), (96, 12))]

            def sp_start(self, sp):
                for dst, src in self.parts[0::2]:
                    sp.dma_start(dst, src).then_inc(self.small, 16)

            def pool(self, pool):
                pool.memset(gate_bias[:], 0.0).then_inc(self.bias_zeroed, 1)
                pool.memset(zero_col[:], 0.0).then_inc(self.bias_zeroed, 1)
                pool.memset(eps_col[:], EPS).then_inc(self.bias_zeroed, 1)
                pool.wait_ge(self.bias_zeroed, 3)

            def pe_start(self, pe, spare):
                pe.wait_ge(self.small, 16 * len(self.parts))
                pe.transpose(spare[:, 0, 0:N_A], self.rows_a[:], ident[0:N_A, 0:N_A])
                pe.transpose(spare[:, 1, 0:N_B], self.rows_b[:], ident[0:N_B, 0:N_B])
                pe.matmul(spare[:, 2, 0:N_HEADS], ones[0:1, :], self.sink_row[:], start=True, stop=True).then_inc(self.turned, 1)
                pe.wait_ge(self.silu_done, 2)
                pe.wait_ge(self.params_out, 2)

            def act_start(self, act, spare):
                for dst, src in self.parts[1::2]:
                    act.dma_start(dst, src).then_inc(self.small, 16)
                act.wait_ge(self.bias_zeroed, 3)
                for dst, src in self.biases:
                    act.dma_start(dst, src).then_inc(self.bias_loaded, 16)
                act.wait_ge(self.turned, 1)
                act.copy(par_b[:], spare[:, 1, 0:N_B]).then_inc(self.params_ready, 1)
                act.wait_ge(self.params_ready, 1)
                act.activation(silu_c[:, :, 0], pb("c"), ACT.Silu).then_inc(self.silu_done, 1)
                act.activation(silu_c[:, :, 1], pb("c_ctx"), ACT.Silu).then_inc(self.silu_done, 1)

            def dve_start(self, dve, spare):
                dve.wait_ge(self.turned, 1)
                dve.tensor_copy(par_a[:], spare[:, 0, 0:N_A]).then_inc(self.params_out, 1)
                dve.tensor_copy(sinks[:], spare[:, 2, 0:N_HEADS]).then_inc(self.params_out, 1)
                dve.wait_ge(self.params_out, 2)

            def dve_gain(self, dve):
                dve.wait_ge(self.bias_added, 1)
                for s in range(2):
                    dve.scalar_tensor_tensor(out=gain1[:, :, s], in0=mod[:, SC1:SC1 + KT, s], scalar=1.0, in1=pa("norm1_w"),
                                             op0=ALU.add, op1=ALU.mult).then_inc(self.gain_done, 1)

        def phase_rows_norm(tag, mem, n_tok, affines, h_hi, h_lo, next_parts, beside=None):
            ffn = beside is None
            blocks = n_tok // P
            xt = mem(f"{tag}_xt", [P, KT, n_tok])
            rows = mem(f"{tag}_rows", [P, 4, D])
            sq = mem(f"{tag}_sq", [P, 2, KT, P])
            part = mem(f"{tag}_part", [P, 2, P])
            scaled = mem(f"{tag}_ffn", [P, 2, KT, P]) if ffn else None
            over_lo = Arena(nc, nc.sbuf_usable_end // 32 * 32 - KT * n_tok * 4)(f"{tag}_scaled", [P, KT, n_tok])
            tail = NormTail(tag, mem, xt, n_tok, affines, h_hi, h_lo, away=over_lo)
            pre = Prefetch(tag, next_parts)
            rows_loaded = [sem(f"{tag}_rows_loaded{r}") for r in range(4)]
            turned = sem(f"{tag}_turned")
            turn_out = sem(f"{tag}_turn_out")
            x_done = sem(f"{tag}_x_done")
            sq_done = sem(f"{tag}_sq_done")
            part_done = sem(f"{tag}_part_done")
            part_used = sem(f"{tag}_part_used")
            stored = sem(f"{tag}_stored")
            x_at = n_tok - SEQ

            def block(x, j):
                return x[:, :, j * P:(j + 1) * P]

            def source(j):
                if ffn:
                    return ffn_rows[j * P:(j + 1) * P, :]
                return A["ctx"][0, j * P:(j + 1) * P, :] if j < CCH else A["x"][0, (j - CCH) * P:(j - CCH + 1) * P, :]

            with nc.psum_tensor(f"{tag}_turn", [P, 2, KT, P], F32) as turn, nc.psum_tensor(f"{tag}_sums", [P, HALF], F32) as sums, \
                    nc.psum_tensor(f"{tag}_mod_rows", [2, 2, HALF], F32) as mod_rows, nc.psum_tensor(f"{tag}_mod_columns", [P, HALF], F32) as mod_columns, \
                    nc.Block() as blk:
                banks = turn[:].rearrange("p a k n -> p (a k n)").rearrange("p (b n) -> p b n", n=HALF)
                spread = banks[:, 0:3, :]

                @blk.sync
                def _(sp):
                    if beside:
                        beside.sp_start(sp)
                    for j in range(blocks):
                        if j >= 4:
                            sp.wait_ge(turned, j - 3)
                        sp.dma_start(rows[:, j % 4, :], source(j)).then_inc(rows_loaded[j % 4], 16)
                        if ffn:
                            sp.dma_start(block(xt, j), block(x_cm_k, j)).then_inc(rows_loaded[j % 4], 16)
                        if beside and j < beside.NEEDED:
                            beside.sp(sp, j)
                    if beside:
                        beside.sp(sp, beside.NEEDED)
                        beside.sp(sp, beside.NEEDED + 1)
                    pre.load(sp)
                    if beside:
                        for j in range(beside.NEEDED + 2, beside.count):
                            beside.sp(sp, j)
                    sp.wait_ge(stored, 16 * BLOCKS)

                @blk.tensor
                def _(pe):
                    def sum_up(j):
                        pe.wait_ge(part_done, j + 1)
                        pe.matmul(sums[:, j:j + 1], part[:, j % 2, :], ones[:, 0:1], start=True, stop=True).then_inc(part_used, 1)

                    if beside:
                        beside.pe_start(pe, banks)
                    for j in range(blocks):
                        pe.wait_ge(rows_loaded[j % 4], (32 if ffn else 16) * (j // 4 + 1))
                        if j >= 2:
                            pe.wait_ge(turn_out, j - 1)
                        for kt in range(KT):
                            ins = pe.transpose(turn[:, j % 2, kt, :], rows[:, j % 4, kt * P:(kt + 1) * P], ident)
                        ins.then_inc(turned, 1)
                        if beside and j < beside.NEEDED:
                            beside.pe(pe, j, mod_rows, mod_columns)
                        if j >= 2:
                            sum_up(j - 2)
                    if beside:
                        beside.pe(pe, beside.NEEDED, mod_rows, mod_columns)
                    sum_up(blocks - 2)
                    sum_up(blocks - 1)
                    pe.wait_ge(part_used, blocks)
                    pe.sem_inc(tail.summed, 1)
                    tail.pe(pe, spread)
                    if beside:
                        pe.wait_ge(beside.bias_added, 1)
                        for j in range(beside.NEEDED + 1, beside.count):
                            beside.pe(pe, j, mod_rows, mod_columns)

                @blk.gpsimd
                def _(pool):
                    if ffn:
                        for j in range(blocks):
                            pool.wait_ge(turn_out, j + 1)
                            pool.tensor_tensor(block(xt, j), block(xt, j), scaled[:, j % 2], ALU.add).then_inc(x_done, 1)
                    else:
                        beside.pool(pool)
                    pre.split(pool)
                    tail.pool(pool)

                @blk.scalar
                def _(act):
                    def square(j):
                        act.wait_ge(x_done, j + 1)
                        if j >= 2:
                            act.wait_ge(part_done, j - 1)
                        act.activation(sq[:, j % 2], block(xt, j), ACT.Square).then_inc(sq_done, 1)
                        if j * P >= x_at:
                            act.dma_start(block(x_cm_k, j - x_at // P), block(xt, j)).then_inc(stored, 16)

                    if beside:
                        beside.act_start(act, banks)
                    for j in range(blocks):
                        if beside:
                            act.wait_ge(turned, j + 1)
                            act.copy(block(xt, j), turn[:, j % 2]).then_inc(turn_out, 1)
                            act.wait_ge(turn_out, j + 1)
                            act.sem_inc(x_done, 1)
                        square(j)
                        if beside and j < beside.NEEDED:
                            beside.act(act, j, mod_rows)
                    if beside:
                        beside.act(act, beside.NEEDED, mod_rows)
                        act.wait_ge(beside.bias_loaded, 16 * len(beside.biases))
                        act.wait_ge(beside.gain_done, 2)
                    tail.act(act)

                @blk.vector
                def _(dve):
                    def add_up(j):
                        dve.wait_ge(sq_done, j + 1)
                        if j >= 2:
                            dve.wait_ge(part_used, j - 1)
                        dve.tensor_reduce(part[:, j % 2, :], sq[:, j % 2].rearrange("p k t -> p t k"), AX_X, ALU.add).then_inc(part_done, 1)

                    if beside:
                        beside.dve_start(dve, banks)
                    for j in range(blocks):
                        if ffn:
                            dve.wait_ge(turned, j + 1)
                            if j >= 2:
                                dve.wait_ge(x_done, j - 1)
                            dve.tensor_tensor(scaled[:, j % 2], turn[:, j % 2], mod[:, G2:G2 + KT, 0:1].to_broadcast([P, KT, P]), ALU.mult).then_inc(turn_out, 1)
                            if j >= 1:
                                add_up(j - 1)
                        else:
                            add_up(j)
                    if ffn:
                        add_up(blocks - 1)
                    if beside:
                        beside.dve_add(dve, mod_columns, 0, beside.NEEDED)
                        beside.dve_gain(dve)

                    def copy_late_rows(kt):
                        if beside and kt >= 2:
                            beside.dve(dve, beside.NEEDED + kt - 1, mod_rows)

                    tail.dve(dve, sums[:, 0:blocks], spread, copy_late_rows)
                    if beside:
                        beside.dve(dve, beside.NEEDED + KT - 1, mod_rows)
                        beside.dve_add(dve, mod_columns, beside.NEEDED, beside.count)

        def plain_gain(name):
            return lambda kt: pa(name)[:, kt:kt + 1]

        h_mem = Arena(nc, nc.sbuf_usable_end // 32 * 32 - 2 * KT * TOK * 4)
        h_hi = h_mem("h1_hi", [P, KT, TOK], F32R)
        h_lo = h_mem("h1_lo", [P, KT, TOK], F32R)
        shift = [lambda kt, s=s: mod[:, SH1 + kt, s:s + 1] for s in range(2)]
        gain = [lambda kt, s=s: gain1[:, kt, s:s + 1] for s in range(2)]
        w_in_k = A["w_in"].rearrange("o (k p) n -> p (o k) n", p=P)
        ATT_TILES = [(K_COL, K_COL + HEAD_DIM)] + [(Q_COL + j * HEAD_DIM, Q_COL + (4 + j) * HEAD_DIM) for j in range(4)]
        ATT_TILES += [(V_COL, V_COL + HEAD_DIM)]

        def att_weights(n):
            return [(w_raw[:, n % 2, :, i * HEAD_DIM:(i + 1) * HEAD_DIM], w_in_k[:, :, c:c + HEAD_DIM]) for i, c in enumerate(ATT_TILES[n])]

        phases.start()
        start_mem = Arena(nc, free_at)
        modulation = FirstModulation(start_mem, [start_mem(f"start_w_mod{u}", [P, KT, Modulation.WIDTH]) for u in range(3)])
        assert modulation.count == modulation.NEEDED + KT <= modulation.NEEDED + TOK // P
        phase_rows_norm("norm1", start_mem, TOK, [(0, CTX, gain[1], shift[1]), (CTX, SEQ, gain[0], shift[0])], h_hi, h_lo,
                        [att_weights(0), att_weights(1)], modulation)

        att_mem = Arena(nc, free_at)
        q_cm = att_mem("q_cm", [P, N_HEADS // 2, SEQ])
        k_cm = att_mem("k_cm", [P, TOK])
        v_rows = att_mem("v_rows", [P, ALLCH, P])
        X0, X1, CX = (0, CTX, HALF, 0), (1, CTX + HALF, HALF, HALF), (2, 0, CTX, SEQ)

        def phase_attention_inputs():
            phases.start()
            mem = Arena(nc, att_mem.at)
            rope = mem("rope", [P, 2, SEQ])
            raw = mem("raw", [P, 2, TOK])
            sq = mem("qk_sq", [P, 2, TOK])
            rstd = mem("qk_rstd", [P, 2, TOK])
            normed = mem("qk_normed", [P, 2, TOK])
            turned = mem("qk_turned", [P, SEQ])
            ring = Ring("att", pieces=2)
            rope_loaded = sem("att_rope_loaded")
            z_free = sem("att_z_free")
            sq_done = sem("att_sq_done")
            raw_done = sem("att_raw_done")
            sums_done = sem("att_sums_done")
            root_done = sem("att_root_done")
            normed_done = sem("att_normed_done")
            rotated = sem("att_rotated")
            rotated_used = sem("att_rotated_used")
            v_turned = sem("att_v_turned")
            v_out = sem("att_v_out")
            roped = sem("att_roped")
            dve_step = sem("att_dve_step")
            groups = [[X0, X1, CX]] + [[X0, X1]] * 4 + [[X0, X1, CX]]
            KTILE, VTILE = 0, 5
            with nc.psum_tensor("att_z", [P, 2, 3, HALF], F32) as z, nc.psum_tensor("att_aux", [P, 2, HALF], F32) as aux, nc.Block() as block:
                @block.sync
                def _(sp):
                    sp.dma_start(rope[:], A["rope_table"]).then_inc(rope_loaded, 16)
                    for n in range(2, len(ATT_TILES)):
                        ring.load(sp, n, n % 2, att_weights(n))

                @block.gpsimd
                def _(pool):
                    ring.credits(pool, None)
                    for n in range(2, len(ATT_TILES)):
                        ring.do_split(pool, n, n % 2, n // 2)

                @block.tensor
                def _(pe):
                    ring.credits(None, pe)

                    first_sum = [sum(len(g) for g in groups[:n]) for n in range(len(groups))]

                    def proj(n, between=None):
                        ring.project(pe, n, n % 2, z_free, [(z[:, n % 2, b, 0:w], c0, w) for b, c0, w, _ in groups[n]], h_hi, h_lo, between)

                    def head_sums(n, g):
                        _, _, w, r0 = groups[n][g]
                        pe.wait_ge(sq_done, n + 1)
                        if first_sum[n] + g:
                            pe.wait_ge(root_done, first_sum[n] + g)
                        pe.matmul(aux[:, 0, 0:w], cst("head_ones"), sq[:, n % 2, r0:r0 + w], start=True, stop=True).then_inc(sums_done, 1)

                    def rotate(n, half):
                        pe.wait_ge(normed_done, n + 1)
                        if n or half:
                            pe.wait_ge(rotated_used, 2 * n + half)
                        pe.matmul(aux[:, 1, :], cst("rotate"), normed[:, n % 2, half * HALF:(half + 1) * HALF], start=True, stop=True).then_inc(rotated, 1)

                    proj(0)
                    for n in range(1, VTILE + 1):
                        beside = {2 + g: (lambda n=n, g=g: head_sums(n - 1, g)) for g in range(len(groups[n - 1]))}
                        if n >= 2:
                            beside.update({6 + half: (lambda n=n, half=half: rotate(n - 2, half)) for half in range(2)})
                        proj(n, beside)
                    for half in range(2):
                        rotate(VTILE - 1, half)
                    pe.wait_ge(raw_done, VTILE + 1)
                    pe.wait_ge(rotated_used, 2 * VTILE)
                    for g, (t0, count) in enumerate(((0, 4), (4, 4), (8, 2))):
                        if g == 2:
                            pe.wait_ge(v_out, 1)
                        for j in range(count):
                            at = (t0 + j) * P
                            ins = pe.transpose(aux[:, g % 2, j * P:(j + 1) * P], raw[:, VTILE % 2, at:at + P], ident)
                        ins.then_inc(v_turned, 1)

                @block.scalar
                def _(act):
                    act.sem_inc(z_free, 2)
                    sums = 0
                    for n in range(6):
                        if n:
                            for _, _, w, r0 in groups[n - 1]:
                                sums += 1
                                act.wait_ge(sums_done, sums)
                                if n >= 3:
                                    act.wait_ge(normed_done, n - 2)
                                act.activation(rstd[:, (n - 1) % 2, r0:r0 + w], aux[:, 0, 0:w], ACT.Sqrt, scale=1.0 / HEAD_DIM, bias=eps_col[:, 0:1]).then_inc(root_done, 1)
                        act.wait_ge(ring.projected, n + 3)
                        if 2 <= n:
                            act.wait_ge(normed_done, n - 1)
                        if n != VTILE:
                            for i, (b, _, w, r0) in enumerate(groups[n]):
                                ins = act.activation(sq[:, n % 2, r0:r0 + w], z[:, n % 2, b, 0:w], ACT.Square)
                            ins.then_inc(sq_done, 1)
                        for i, (b, _, w, r0) in enumerate(groups[n]):
                            ins = act.copy(raw[:, n % 2, r0:r0 + w], z[:, n % 2, b, 0:w])
                        ins.then_inc(z_free, 1)
                        act.wait_ge(z_free, n + 3)
                        act.sem_inc(raw_done, 1)

                @block.vector
                def _(dve):
                    step = Steps(dve, dve_step)
                    sums = 0
                    dve.wait_ge(rope_loaded, 16)
                    for n in range(5):
                        width = sum(w for _, _, w, _ in groups[n])
                        sums += len(groups[n])
                        dve.wait_ge(root_done, sums)
                        step(dve.reciprocal(rstd[:, n % 2, 0:width], rstd[:, n % 2, 0:width]))
                        step.wait()
                        dve.wait_ge(raw_done, n + 1)
                        g = 1 if n == KTILE else 0
                        dve.scalar_tensor_tensor(out=normed[:, n % 2, 0:width], in0=raw[:, n % 2, 0:width], scalar=qk_gain[:, g:g + 1],
                                                 in1=rstd[:, n % 2, 0:width], op0=ALU.mult, op1=ALU.mult).then_inc(normed_done, 1)
                        dve.wait_ge(normed_done, n + 1)
                        to = k_cm[:, CTX:] if n == KTILE else q_cm[:, n - 1, :]
                        if n == KTILE:
                            step(dve.tensor_copy(k_cm[:, 0:CTX], normed[:, n % 2, SEQ:TOK]))
                        step(dve.tensor_tensor(to, normed[:, n % 2, 0:SEQ], rope[:, 0], ALU.mult))
                        for half in range(2):
                            cols = slice(half * HALF, (half + 1) * HALF)
                            dve.wait_ge(rotated, 2 * n + half + 1)
                            dve.tensor_tensor(turned[:, cols], aux[:, 1, :], rope[:, 1, cols], ALU.mult).then_inc(rotated_used, 1)
                        dve.wait_ge(rotated_used, 2 * n + 2)
                        step.wait()
                        step(dve.tensor_tensor(to, to, turned[:], ALU.add))
                        step.wait()
                    for g, (t0, count) in enumerate(((0, 4), (4, 4), (8, 2))):
                        dve.wait_ge(v_turned, g + 1)
                        at = [(t0 + j + CCH) % ALLCH for j in range(count)]
                        split = next((j for j in range(1, count) if at[j] != at[j - 1] + 1), count)
                        for a, b in ((0, split), (split, count)):
                            if b > a:
                                ins = dve.tensor_copy(v_rows[:, at[a]:at[a] + b - a, :], aux[:, g % 2, a * P:b * P].rearrange("p (j n) -> p j n", n=P))
                        ins.then_inc(v_out, 1)

        def phase_attention():
            phases.start()
            mem = Arena(nc, att_mem.at)
            q_now = mem("q_now", [P, 2, SEQ])
            out_now = mem("att_out_now", [P, 2, SEQ])
            NB = 4
            s = [mem(f"att_s{b}", [P, 1 + 5 * P]) for b in range(NB)]
            p = [mem(f"att_p{b}", [P, 1 + 5 * P]) for b in range(NB)]
            p_t = mem("att_p_t", [P, NB, 5, P])
            neg_max = mem("att_neg_max", [P, NB])
            den = mem("att_den", [P, NB])
            zeros = mem("att_zeros", [P, D])
            zeroed = sem("win_zeroed")
            cleared = sem("win_ffn_cleared")
            q_copied = sem("win_q_copied")
            scores = sem("win_scores")
            local_in = sem("win_local_in")
            ctx_in = sem("win_ctx_in")
            max_done = sem("win_max_done")
            probs = sem("win_probs")
            scaled = sem("win_scaled")
            p_turned = sem("win_p_turned")
            near_out = sem("win_near_out")
            last_out = sem("win_last_out")
            pv_done = sem("win_pv_done")
            o_out = sem("win_o_out")
            stored = [sem(f"win_stored{half}") for half in range(2)]
            inverse_done = sem("win_inverse_done")
            pre = Prefetch("win", [[(w_raw[:, i], w_in_k[:, :, col:col + M_DIM])] for i, col in enumerate((MQ_COL, MK_COL))])
            PAIR = 2 * BLOCKS
            U = 2 * PAIR
            near = [range(max(n - 1, 0), min(n + 2, BLOCKS)) for n in range(BLOCKS)]
            with nc.psum_tensor("win_s", [P, 2, 2, HALF], F32) as ps, nc.psum_tensor("win_t", [P, 2, HALF], F32) as pt, \
                    nc.psum_tensor("win_o", [P, 2, HALF], F32) as po, nc.Block() as block:
                @block.sync
                def _(sp):
                    pre.load(sp)
                    sp.wait_ge(zeroed, 1)
                    for j in range(BLOCKS):
                        sp.dma_start(ffn_rows[j * P:(j + 1) * P, :], zeros[:]).then_inc(cleared, 16)
                    sp.wait_ge(cleared, 16 * BLOCKS)

                @block.gpsimd
                def _(pool):
                    pool.memset(zeros[:], 0.0).then_inc(zeroed, 1)
                    pool.sem_inc(scaled, NB - 1)
                    with pool.Fori(0, 2) as i:
                        for u in range(U):
                            n, b = u % PAIR // 2, u % NB
                            w = len(near[n]) * P + CTX
                            pool.wait_ge(inverse_done, i * U + u + 1)
                            pool.tensor_tensor(p[b][:, 1:1 + w], p[b][:, 1:1 + w], den[:, b:b + 1].to_broadcast([P, w]), ALU.mult).then_inc(scaled, 1)
                    pre.split(pool)

                @block.tensor
                def _(pe):
                    with pe.Fori(0, 2) as i:
                        def score(u):
                            n, a = u % PAIR // 2, u % 2
                            rows = slice(a * HEAD_DIM, (a + 1) * HEAD_DIM)
                            w, k0 = len(near[n]) * P, CTX + near[n][0] * P
                            pe.wait_ge(local_in, i * U + u + 1)
                            pe.wait_ge(ctx_in, i * U + u + 1)
                            pe.matmul(ps[:, a, 0, 0:w], q_now[rows, u // PAIR, n * P:(n + 1) * P], k_cm[rows, k0:k0 + w], start=True, stop=True)
                            pe.matmul(ps[:, a, 1, 0:CTX], q_now[rows, u // PAIR, n * P:(n + 1) * P], k_cm[rows, 0:CTX], start=True, stop=True).then_inc(scores, 1)

                        def value_tiles(n):
                            return [CCH + t for t in near[n]] + [0, 1]

                        def turn(u):
                            n, a = u % PAIR // 2, u % 2
                            nt = len(value_tiles(n))
                            pe.wait_ge(near_out, i * U + u + 1)
                            pe.wait_ge(last_out, i * U + u + 1)
                            pe.wait_ge(scaled, i * U + u + NB)
                            for t in range(nt):
                                to = pt[:, 1, 0:P] if t == nt - 1 else pt[:, 0, t * P:(t + 1) * P]
                                ins = pe.transpose(to, p[u % NB][:, 1 + t * P:1 + (t + 1) * P], ident)
                            ins.then_inc(p_turned, 1)

                        def weigh(u):
                            n, a = u % PAIR // 2, u % 2
                            tiles = value_tiles(n)
                            nt = len(tiles)
                            if a == 0:
                                pe.wait_ge(o_out, i * 2 * BLOCKS + u // 2 + 1)
                            pe.wait_ge(near_out, i * U + u + 2)
                            pe.wait_ge(last_out, i * U + u + 2)
                            cols = slice(a * HEAD_DIM, (a + 1) * HEAD_DIM)
                            for t in range(nt):
                                ins = pe.matmul(po[cols, n % 2, 0:P], v_rows[:, tiles[t], cols], p_t[:, u % NB, 4 if t == nt - 1 else t, :],
                                                start=(t == 0), stop=(t == nt - 1))
                            ins.then_inc(pv_done, 1)

                        pe.wait_ge(q_copied, 2 * i + 2)
                        for u in range(3):
                            score(u)
                        for u in range(U):
                            if u + 3 < U:
                                score(u + 3)
                            if u:
                                weigh(u - 1)
                            turn(u)
                        weigh(U - 1)

                @block.scalar
                def _(act):
                    act.sem_inc(ctx_in, 2)
                    act.sem_inc(last_out, 1)
                    act.sem_inc(o_out, 2)
                    act.sem_inc(probs, NB)
                    for place in stored:
                        act.sem_inc(place, 16)
                    with act.Fori(0, 2) as i:
                        def take_ctx(u):
                            n, a = u % PAIR // 2, u % 2
                            at = 1 + len(near[n]) * P
                            act.wait_ge(scores, i * U + u + 2)
                            act.wait_ge(probs, i * U + u + 1)
                            act.copy(s[u % NB][:, at:at + CTX], ps[:, a, 1, 0:CTX]).then_inc(ctx_in, 1)

                        def exps(u):
                            n, a = u % PAIR // 2, u % 2
                            w = 1 + len(near[n]) * P + CTX
                            act.wait_ge(max_done, i * U + u + 1)
                            act.wait_ge(p_turned, i * U + u)
                            act.wait_ge(scaled, i * U + u)
                            b = u % NB
                            act.activation(p[b][:, 0:w], s[b][:, 0:w], ACT.Exp, bias=neg_max[:, b:b + 1],
                                           accum_out=den[:, b:b + 1]).then_inc(probs, 1)

                        def take_last(u):
                            act.wait_ge(p_turned, i * U + u + NB)
                            act.wait_ge(pv_done, i * U + u + 1)
                            act.copy(p_t[:, u % NB, 4, :], pt[:, 1, 0:P]).then_inc(last_out, 1)

                        def take_out(u):
                            n, a = u % PAIR // 2, u % 2
                            if a == 1:
                                if n == 0:
                                    act.wait_ge(stored[u // PAIR], 16 * i + 16)
                                act.wait_ge(pv_done, i * U + u + 1 + NB)
                                act.copy(out_now[:, u // PAIR, n * P:(n + 1) * P], po[:, n % 2, 0:P]).then_inc(o_out, 1)
                                if n == BLOCKS - 1:
                                    half = u // PAIR
                                    act.wait_ge(o_out, i * 2 * BLOCKS + (half + 1) * BLOCKS + 2)
                                    pass_waits(act)
                                    act.dma_start(att_cm.rearrange("(j p) t -> p j t", p=P)[:, bass.ds(2 * i + half, 1), :],
                                                  out_now[:, half:half + 1, :]).then_inc(stored[half], 16)

                        take_ctx(0)
                        exps(0)
                        take_ctx(1)
                        exps(1)
                        take_ctx(2)
                        for u in range(U):
                            if u + 2 < U:
                                exps(u + 2)
                            if u:
                                take_out(u - 1)
                            if u + 3 < U:
                                take_ctx(u + 3)
                            take_last(u)
                        take_out(U - 1)
                    for place in stored:
                        act.wait_ge(place, 16 * 3)

                @block.vector
                def _(dve):
                    dve.sem_inc(local_in, 2)
                    dve.sem_inc(near_out, 1)
                    dve.sem_inc(pv_done, NB)
                    dve.sem_inc(scores, 1)
                    dve.sem_inc(p_turned, NB - 1)
                    with dve.Fori(0, 2) as i:
                        def local_and_max(u):
                            n, a = u % PAIR // 2, u % 2
                            w = len(near[n]) * P
                            m0 = (near[n][0] - n + 1) * P
                            dve.wait_ge(scores, i * U + u + 2)
                            dve.wait_ge(probs, i * U + u + 1)
                            b = u % NB
                            if u % PAIR < NB:
                                pass_waits(dve)
                                dve.tensor_scalar(s[b][:, 0:1], sinks[:, bass.ds(2 * i + u // PAIR + 4 * a, 1)], 0.0, None, ALU.add)
                            dve.tensor_tensor(s[b][:, 1:1 + w], ps[:, a, 0, 0:w], cst("near_mask")[:, m0:m0 + w], ALU.add).then_inc(local_in, 1)
                            dve.wait_ge(local_in, i * U + u + 3)
                            dve.wait_ge(ctx_in, i * U + u + 3)
                            dve.tensor_reduce(neg_max[:, b:b + 1], s[b][:, 0:1 + w + CTX], AX_X, ALU.max, negate=True).then_inc(max_done, 1)

                        dve.wait_ge(scores, i * U + 1)
                        for half in range(2):
                            dve.tensor_scalar(q_now[:, half, :], q_cm[:, bass.ds(2 * i + half, 1), :].rearrange("p o t -> p (o t)"), HEAD_DIM ** -0.5, None,
                                              ALU.mult).then_inc(q_copied, 1)
                        def invert(u):
                            b = u % NB
                            dve.wait_ge(probs, i * U + u + 1 + NB)
                            dve.reciprocal(den[:, b:b + 1], den[:, b:b + 1]).then_inc(inverse_done, 1)

                        for u in range(3):
                            local_and_max(u)
                        invert(0)
                        for u in range(U):
                            n = u % PAIR // 2
                            if u + 1 < U:
                                invert(u + 1)
                            if u + 3 < U:
                                local_and_max(u + 3)
                            dve.wait_ge(p_turned, i * U + u + NB)
                            dve.wait_ge(pv_done, i * U + u + 1)
                            nn = len(near[n]) + 1
                            dve.tensor_copy(p_t[:, u % NB, 0:nn, :], pt[:, 0, 0:nn * P].rearrange("p (t q) -> p t q", q=P)).then_inc(near_out, 1)

        phase_attention_inputs()
        phase_attention()

        m_mem = Arena(nc, free_at)
        mq_cm = m_mem("mq_cm", [P, M_HEADS, SEQ])
        mk_cm = m_mem("mk_cm", [P, M_HEADS, TOK])
        v_ext = m_mem("v_ext", [P, ALLCH, M_HEADS, M_DIM + 1])
        out_gate_at = m_mem.at
        out_gate = m_mem("out_gate", [P, M_HEADS, SEQ])
        out_gate_end = m_mem.at
        gates_raw = m_mem("gates_raw", [P, TOK])

        def phase_mlstm_inputs():
            phases.start()
            mem = Arena(nc, m_mem.at)
            XPAD, CPAD = 1, SEQ + 3
            PADDED = SEQ + CTX + 4
            padded = mem("conv_padded", [P, PADDED])
            conv = mem("conv_sum", [P, PADDED - 2])
            taps = mem("conv_taps", [P, 3, 2, 1])
            ring = Ring("mls")
            z_free = sem("mls_z_free")
            padded_done = sem("mls_padded_done")
            pad_free = sem("mls_pad_free")
            conv_done = sem("mls_conv_done")
            conv_used = sem("mls_conv_used")
            v_turned = sem("mls_v_turned")
            v_out = sem("mls_v_out")
            gates_zeroed = sem("mls_gates_zeroed")
            gates_out = sem("mls_gates_out")
            dve_step = sem("mls_dve_step")
            cleared = sem("mls_cleared")
            groups = [[X0, X1], [X0, X1, CX], [X0, X1, CX], [X0, X1]]
            G = 4 * M_HEADS
            with nc.psum_tensor("mls_z", [P, 2, 3, HALF], F32) as z, nc.psum_tensor("mls_aux", [P, 2, HALF], F32) as aux, nc.Block() as block:
                @block.sync
                def _(sp):
                    ring.load_all(sp, M_HEADS, 4, lambda h, i: [(w_raw[:, i % 2], w_in_k[:, :, bass.ds(h * M_DIM + (MQ_COL, MK_COL, MV_COL, MO_COL)[i], M_DIM)])])
                    sp.wait_ge(gates_zeroed, 1)
                    for row, at in ((0, 0), (64, 4), (32, 8), (96, 12)):
                        sp.dma_start(w_raw[:, 0, :, row:row + M_HEADS], w_in_k[:, :, G_COL + at:G_COL + at + M_HEADS]).then_inc(ring.loaded[0], 16)

                @block.gpsimd
                def _(pool):
                    ring.credits(pool, None)
                    ring.split_all(pool, M_HEADS, 4)
                    pool.wait_ge(ring.split, G + 1)
                    pool.memset(w_raw[:, 0], 0.0).then_inc(gates_zeroed, 1)
                    ring.do_split(pool, G, 0, 2 * M_HEADS + 3)

                @block.tensor
                def _(pe):
                    ring.credits(None, pe)
                    pe.wait_ge(cleared, 1)

                    def proj(n, i, between=None):
                        ring.project(pe, n, i % 2, z_free, [(z[:, i % 2, b, 0:w], c0, w) for b, c0, w, _ in groups[i]], h_hi, h_lo, between)

                    def turn_v(h):
                        for g, (t0, count) in enumerate(((0, 4), (4, 4), (8, 2))):
                            if g == 0:
                                pe.wait_ge(padded_done, 3 * h + 3)
                            if g == 2:
                                pe.wait_ge(v_out, 3 * h + 1 + 1)
                            else:
                                pe.wait_ge(v_out, 3 * h + 1)
                            for t in range(t0, t0 + count):
                                at = CPAD + t * P if t < CCH else XPAD + (t - CCH) * P
                                ins = pe.transpose(aux[:, g % 2, (t - t0) * P:(t - t0 + 1) * P], padded[:, at:at + P], ident)
                            ins.then_inc(v_turned, 1)

                    with pe.Fori(0, M_HEADS) as h:
                        for i in range(4):
                            proj(4 * h + i, i)
                        turn_v(h)
                    ring.project(pe, G, 0, z_free, [(z[:, 0, b, 0:w], c0, w) for b, c0, w, _ in groups[1]], h_hi, h_lo)

                @block.scalar
                def _(act):
                    act.sem_inc(z_free, 2)
                    act.sem_inc(conv_used, 1)
                    act.wait_ge(cleared, 1)
                    with act.Fori(0, M_HEADS) as h:
                        def pad(i, round_):
                            act.wait_ge(ring.projected, 4 * h + i + 3)
                            act.wait_ge(pad_free, round_ + 1)
                            for b, _, w, r0 in groups[i]:
                                at = CPAD if b == 2 else XPAD + r0
                                ins = act.copy(padded[:, at:at + w], z[:, i % 2, b, 0:w])
                            ins.then_inc(z_free, 1)
                            act.wait_ge(z_free, 4 * h + i + 3)
                            act.sem_inc(padded_done, 1)

                        pad(0, 3 * h)
                        act.wait_ge(conv_done, 2 * h + 1)
                        pass_waits(act)
                        act.activation(mq_cm[:, bass.ds(h, 1), :].rearrange("p o t -> p (o t)"), conv[:, 0:SEQ], ACT.Silu).then_inc(conv_used, 1)
                        pad(1, 3 * h + 1)
                        act.wait_ge(conv_done, 2 * h + 2)
                        pass_waits(act)
                        act.activation(mk_cm[:, bass.ds(h, 1), CTX:].rearrange("p o t -> p (o t)"), conv[:, 0:SEQ], ACT.Silu)
                        act.activation(mk_cm[:, bass.ds(h, 1), 0:CTX].rearrange("p o t -> p (o t)"), conv[:, SEQ + 2:SEQ + 2 + CTX],
                                       ACT.Silu).then_inc(conv_used, 1)
                        pad(2, 3 * h + 2)
                        act.wait_ge(ring.projected, 4 * h + 3 + 3)
                        pass_waits(act)
                        for half in range(2):
                            ins = act.activation(out_gate[:, bass.ds(h, 1), half * HALF:(half + 1) * HALF].rearrange("p o t -> p (o t)"),
                                                 z[:, 1, half, :], ACT.Sigmoid)
                        ins.then_inc(z_free, 1)
                    act.wait_ge(ring.projected, G + 3)
                    for b, c0, w, _ in groups[1]:
                        act.copy(gates_raw[:, c0:c0 + w], z[:, 0, b, 0:w]).then_inc(gates_out, 1)

                @block.vector
                def _(dve):
                    dve.memset(padded[:], 0.0).then_inc(dve_step, 1)
                    dve.memset(v_ext[:].rearrange("p t h n -> p (t h) n")[:, :, M_DIM:M_DIM + 1], 1.0).then_inc(dve_step, 1)
                    dve.wait_ge(dve_step, 2)
                    dve.sem_inc(pad_free, 1)
                    dve.sem_inc(v_out, 1)
                    dve.sem_inc(cleared, 1)
                    N_STEP = 5
                    with dve.Fori(0, M_HEADS) as h:
                        step = Steps(dve, dve_step, h * N_STEP + 2)
                        dve.wait_ge(conv_used, 2 * h + 1)
                        pass_waits(dve)
                        step(dve.tensor_copy(taps[:], pb("conv_qk").rearrange("p (j s h) -> p j s h", j=3, s=2)[:, :, :, bass.ds(h, 1)]))
                        step.wait()
                        for s in range(2):
                            width = SEQ if s == 0 else PADDED - 2
                            dve.wait_ge(padded_done, 3 * h + s + 1)
                            dve.wait_ge(conv_used, 2 * h + s + 1)
                            step(dve.tensor_scalar(conv[:, 0:width], padded[:, 0:width], taps[:, 0, s, :], None, ALU.mult))
                            step.wait()
                            step(dve.scalar_tensor_tensor(out=conv[:, 0:width], in0=padded[:, 1:1 + width], scalar=taps[:, 1, s, :],
                                                          in1=conv[:, 0:width], op0=ALU.mult, op1=ALU.add))
                            step.wait()
                            dve.scalar_tensor_tensor(out=conv[:, 0:width], in0=padded[:, 2:2 + width], scalar=taps[:, 2, s, :],
                                                     in1=conv[:, 0:width], op0=ALU.mult, op1=ALU.add).then_inc(conv_done, 1)
                            dve.wait_ge(conv_done, 2 * h + s + 1)
                            dve.sem_inc(pad_free, 1)
                        assert step.done == N_STEP
                        for g, (t0, count) in enumerate(((0, 4), (4, 4), (8, 2))):
                            dve.wait_ge(v_turned, 3 * h + g + 1)
                            pass_waits(dve)
                            ins = dve.tensor_copy(v_ext[:, t0:t0 + count, bass.ds(h, 1), 0:M_DIM].rearrange("p t o n -> p t (o n)"),
                                                  aux[:, g % 2, 0:count * P].rearrange("p (t n) -> p t n", n=P))
                            ins.then_inc(v_out, 1)
                        dve.wait_ge(v_out, 3 * h + 3 + 1)
                        dve.sem_inc(pad_free, 1)

        s_mem = Arena(nc, m_mem.at)
        neg_m = s_mem("neg_m", [GATE_ROWS, TOK])
        pick = s_mem("pick", [GATE_ROWS, 8, P])
        tok_gate = s_mem("tok_gate", [P, 5, ALLCH, GATE_ROWS])
        carry = s_mem("carry", [P, 8, ALLCH])
        GG, WS, DECAY, FLOOR, NEG_MAX = range(5)

        def phase_gate_scans():
            phases.start()
            mem = Arena(nc, s_mem.at)
            t = {n: mem(f"scan_{n}", [GATE_ROWS, TOK]) for n in ("keep", "log_i", "log_f", "tmp", "g", "jump")}
            t["time_gate"] = mem("scan_time_gate", [GATE_ROWS, 4, TOK])
            t["b"], t["run_max"] = t["time_gate"][:, FLOOR, :], t["time_gate"][:, DECAY, :]
            t["pre_ws"], t["pre_decay"], t["pre_floor"] = t["tmp"], t["jump"], t["log_i"]
            modulation = Modulation("scan", mem, [mem(f"scan_w_mod{u}", [P, KT, Modulation.WIDTH]) for u in range(3)], SCAN_MOD, MIX_MOD - SCAN_MOD)
            start_m = mem("scan_start_m", [GATE_ROWS, ALLCH])
            step_decay = mem("scan_step_decay", [GATE_ROWS, ALLCH])
            loaded = sem("scan_loaded")
            dve_step = sem("scan_dve_step")
            act_step = sem("scan_act_step")
            f_ready = sem("scan_f_ready")
            log_done = sem("scan_log_done")
            pre_done = sem("scan_pre_done")
            exp_done = sem("scan_exp_done")
            g_done = sem("scan_g_done")
            neg_m_done = sem("scan_neg_m_done")
            turned = sem("scan_turned")
            copied = sem("scan_copied")
            B0 = 32
            EARLY = 5

            def by_time(dst, rows=GATE_ROWS):
                return [(dst[0:B0], slice(0, B0), slice(None)), (dst[B0:GATE_ROWS, CTX - 1::-1], slice(B0, GATE_ROWS), slice(0, CTX)),
                        (dst[B0:GATE_ROWS, TOK - 1:CTX - 1:-1], slice(B0, GATE_ROWS), slice(CTX, TOK))]

            def chunks(x):
                return x.rearrange("p (c t) -> p c t", t=CHUNK)

            with nc.psum_tensor("scan_turn", [P, 4, HALF], F32) as turn, nc.psum_tensor("scan_carry", [P, HALF], F32) as cps, \
                    nc.psum_tensor("scan_mod_rows", [2, 2, HALF], F32) as mod_rows, nc.psum_tensor("scan_mod_columns", [P, HALF], F32) as mod_columns, \
                    nc.Block() as block:
                def by_chunk(q):
                    return turn[:, q, 0:ALLCH * GATE_ROWS].rearrange("p (c r) -> p c r", r=GATE_ROWS)

                @block.sync
                def _(sp):
                    sp.dma_start(t["keep"][:], A["keep_table"]).then_inc(loaded, 16)
                    sp.dma_start(pick[:].rearrange("p r n -> p (r n)"), A["pick_table"]).then_inc(loaded, 16)
                    for j in range(modulation.count):
                        modulation.sp(sp, j)

                @block.vector
                def _(dve):
                    step = Steps(dve, dve_step)
                    for name, at in (("log_i", 0), ("log_f", 64)):
                        rows = gates_raw[at:at + GATE_ROWS]
                        bias = gate_bias[at:at + GATE_ROWS]
                        for dst, r, cols in by_time(t[name]):
                            step(dve.tensor_scalar(dst, rows[r, cols], bias[r], None, ALU.add))
                    step.wait()
                    dve.sem_inc(f_ready, 1)
                    step(dve.tensor_scalar(t["jump"][:], t["log_f"][:], 0.0, None, ALU.min))
                    step.wait()
                    dve.wait_ge(log_done, 1)
                    step(dve.tensor_tensor(t["log_f"][:], t["jump"][:], t["tmp"][:], ALU.subtract))
                    step.wait()
                    dve.wait_ge(loaded, 32)
                    step(dve.tensor_tensor_scan(t["b"][:], t["keep"][:], t["log_f"][:], 0.0, ALU.mult, ALU.add))
                    step(dve.memset(t["jump"][:], 0.0))
                    step.wait()
                    last_b = chunks(t["b"][:])[:, :, CHUNK - 1]
                    step(dve.tensor_copy(chunks(t["jump"][:])[:, 1:, 0], last_b[:, 0:ALLCH - 1]))
                    step(dve.tensor_tensor(t["g"][:], t["log_i"][:], t["b"][:], ALU.subtract))
                    step.wait()
                    step(dve.tensor_tensor_scan(t["run_max"][:], t["jump"][:], t["g"][:], 0.0, ALU.add, ALU.max))
                    step(dve.memset(start_m[:], 0.0))
                    step.wait()
                    last_max = chunks(t["run_max"][:])[:, :, CHUNK - 1]
                    step(dve.tensor_tensor(start_m[:, 1:], last_b[:, 0:ALLCH - 1], last_max[:, 0:ALLCH - 1], ALU.add))
                    for dst, r, cols in by_time(neg_m[:]):
                        step(dve.tensor_scalar(dst, t["run_max"][r, cols], -1.0, None, ALU.mult))
                    step.wait()
                    dve.sem_inc(neg_m_done, 1)
                    wide = [GATE_ROWS, ALLCH, CHUNK]
                    step(dve.tensor_tensor(step_decay[:], start_m[:], last_max, ALU.subtract))
                    step(dve.tensor_tensor(chunks(t["pre_ws"][:]), chunks(t["g"][:]), last_max.unsqueeze(2).to_broadcast(wide), ALU.subtract))
                    step(dve.tensor_tensor(chunks(t["pre_decay"][:]), start_m[:].unsqueeze(2).to_broadcast(wide), chunks(t["run_max"][:]), ALU.subtract))
                    step(dve.tensor_tensor(t["pre_floor"][:], t["b"][:], t["run_max"][:], ALU.add))
                    step.wait()
                    dve.sem_inc(pre_done, 1)
                    for dst, r, cols in by_time(t["time_gate"][:, GG, :]):
                        step(dve.tensor_copy(dst, t["g"][r, cols]))
                    step.wait()
                    dve.sem_inc(g_done, 1)
                    dve.wait_ge(turned, 6)
                    step(dve.tensor_copy(carry[:], cps[:, 0:8 * ALLCH].rearrange("p (r c) -> p r c", c=ALLCH)))
                    dve.wait_ge(copied, 5)
                    step(dve.tensor_scalar(tok_gate[:, DECAY], tok_gate[:, DECAY], M_DIM ** -0.5, None, ALU.mult))
                    modulation.dve_add(dve, mod_columns, 0, modulation.count)

                @block.scalar
                def _(act):
                    step = Steps(act, act_step)
                    act.wait_ge(f_ready, 1)
                    step(act.activation(t["tmp"][:], t["log_f"][:], ACT.Abs))
                    step.wait()
                    step(act.activation(t["tmp"][:], t["tmp"][:], ACT.Exp, scale=-1.0))
                    step.wait()
                    act.activation(t["tmp"][:], t["tmp"][:], ACT.Ln, bias=1.0).then_inc(log_done, 1)
                    for j in range(EARLY):
                        modulation.act(act, j, mod_rows)
                    act.wait_ge(turned, 1)
                    act.copy(tok_gate[:, NEG_MAX], by_chunk(FLOOR)).then_inc(copied, 1)
                    act.wait_ge(pre_done, 1)
                    act.activation(step_decay[:], step_decay[:], ACT.Exp).then_inc(exp_done, 1)
                    for q, name, sign in ((WS, "pre_ws", 1.0), (DECAY, "pre_decay", 1.0), (FLOOR, "pre_floor", -1.0)):
                        for dst, r, cols in by_time(t["time_gate"][:, q, :]):
                            act.activation(dst, t[name][r, cols], ACT.Exp, scale=sign).then_inc(exp_done, 1)
                    for i, q in enumerate((GG, WS, DECAY, FLOOR)):
                        act.wait_ge(turned, i + 3)
                        act.copy(tok_gate[:, q], by_chunk(q)).then_inc(copied, 1)
                    for j in range(EARLY, modulation.count):
                        modulation.act(act, j, mod_rows)

                @block.tensor
                def _(pe):
                    for j in range(EARLY):
                        modulation.pe(pe, j, mod_rows, mod_columns)

                    def turn_rows(bank, rows):
                        for c in range(ALLCH):
                            ins = pe.transpose(turn[:, bank, c * GATE_ROWS:(c + 1) * GATE_ROWS], rows[:, c * CHUNK:(c + 1) * CHUNK],
                                               ident[0:GATE_ROWS, 0:GATE_ROWS])
                        ins.then_inc(turned, 1)

                    pe.wait_ge(neg_m_done, 1)
                    turn_rows(FLOOR, neg_m)
                    pe.wait_ge(loaded, 32)
                    pe.wait_ge(exp_done, 1)
                    for r in range(8):
                        ins = pe.matmul(cps[:, r * ALLCH:(r + 1) * ALLCH], pick[:, r, :], step_decay[:], start=True, stop=True)
                    ins.then_inc(turned, 1)
                    for i, q in enumerate((GG, WS, DECAY, FLOOR)):
                        if q == GG:
                            pe.wait_ge(g_done, 1)
                        else:
                            pe.wait_ge(exp_done, 1 + 3 * i)
                        if q == FLOOR:
                            pe.wait_ge(copied, 1)
                        turn_rows(q, t["time_gate"][:, q, :])
                    for j in range(EARLY, modulation.count):
                        modulation.pe(pe, j, mod_rows, mod_columns)

        r_mem = Arena(nc, s_mem.at)
        h_sum = r_mem("h_sum", [P, XCH, M_HEADS, M_DIM])

        def phase_mlstm():
            phases.start()
            mem = Arena(nc, r_mem.at)
            E1 = M_DIM + 1
            state = mem("state", [P, 8, E1])
            k_now = mem("k_now", [P, 2, 2, M_HEADS, CHUNK])
            q_now = mem("mq_now", [P, 2, 2, M_HEADS, CHUNK])
            g_now = mem("g_now", [P, 2, 2, 5, M_HEADS])
            masked = mem("m_masked", [P, 2, 2, M_HEADS, CHUNK])
            a_now = mem("a_now", [P, 2, 8])
            weight = mem("m_weight", [P, 2, CHUNK])
            w_qk = mem("m_w_qk", [P, 2, CHUNK])
            k_w = mem("m_k_w", [P, 2, M_DIM])
            inter = mem("m_inter", [P, 2, E1])
            total = mem("m_total", [P, 2, M_HEADS, E1])
            size = mem("m_size", [P, 2, M_HEADS, 1])
            fetched = sem("mlc_fetched")
            first_done = sem("mlc_first_done")
            second_done = sem("mlc_second_done")
            weight_done = sem("mlc_weight_done")
            k_w_done = sem("mlc_k_w_done")
            w_qk_done = sem("mlc_w_qk_done")
            inter_done = sem("mlc_inter_done")
            state_done = sem("mlc_state_done")
            total_done = sem("mlc_total_done")
            group_done = sem("mlc_group_done")
            dve_step = sem("mlc_dve_step")
            cleared = sem("mlc_cleared")
            U = 16
            with nc.psum_tensor("mlc_wk", [P, 2, HALF], F32) as p_wk, nc.psum_tensor("mlc_qk", [P, 2, HALF], F32) as p_qk, \
                    nc.psum_tensor("mlc_num", [P, 2, HALF], F32) as p_num, nc.psum_tensor("mlc_inter", [P, 2, HALF], F32) as p_int, nc.Block() as block:

                def unit(u):
                    return u // 8, u % 8, (u % 8) // M_HEADS, u % M_HEADS, u % 2

                C_FETCH, X_FETCH = 5, 9

                @block.gpsimd
                def _(pool):
                    pool.wait_ge(cleared, 1)

                    def fetch(par, chunk, s, with_q, done=None):
                        for d in range(2):
                            for now, all_, off in ((k_now, mk_cm, 0),) + (((q_now, mq_cm, CTX),) if with_q else ()):
                                at = chunk[d] * CHUNK - off
                                pool.tensor_tensor(now[:, par, d], all_[:, :, bass.ds(at, CHUNK)], zero_col[:, 0:1].unsqueeze(2).to_broadcast([P, M_HEADS, CHUNK]),
                                                   ALU.add).then_inc(fetched, 1)
                            pool.tensor_copy(g_now[:, par, d].rearrange("p q (c h) -> p q c h", c=1),
                                             tok_gate[:, :, bass.ds(chunk[d], 1), 32 * d:32 * d + M_HEADS]).then_inc(fetched, 1)
                            if with_q:
                                wide = [P, M_HEADS, CHUNK]
                                pool.wait_ge(fetched, done + 4 * d + 3)
                                pool.tensor_tensor(masked[:, par, d], cst("chunk_mask")[:, (1 - d) * P:(2 - d) * P].unsqueeze(1).to_broadcast(wide),
                                                   g_now[:, par, d, NEG_MAX, :].unsqueeze(2).to_broadcast(wide), ALU.add).then_inc(fetched, 1)
                        pool.tensor_copy(a_now[:, par, :].rearrange("p (r c) -> p r c", c=1), carry[:, :, bass.ds(s, 1)]).then_inc(fetched, 1)

                    for s in range(CCH):
                        fetch(s % 2, (s, CCH - 1 - s), s, False)
                    with pool.Fori(0, XCH // 2) as i:
                        for par in range(2):
                            pool.wait_ge(state_done, i * U + 8 * (par + 1) + 2)
                            pool.wait_ge(group_done, 4 * i + 2 * (par + 1))
                            pass_waits(pool)
                            fetch(par, (2 * i + par + CCH, ALLCH - 1 - par - 2 * i), 2 * i + par + CCH, True,
                                  2 * C_FETCH + X_FETCH * (2 * i + par))

                @block.tensor
                def _(pe):
                    def first(u, base, x):
                        par, r, d, h, b = unit(u)
                        pe.wait_ge(k_w_done, base + u + 1)
                        if x is not None:
                            pe.wait_ge(weight_done, x * U + u + 1)
                            pe.wait_ge(w_qk_done, x * U + u + 1)
                            pe.transpose(p_wk[:, b, 0:CHUNK], masked[:, par, d, h, :], ident)
                            pe.matmul(p_qk[:, b, 0:CHUNK], k_now[:, par, d, h, :], q_now[:, par, d, h, :], start=True, stop=True)
                        pe.transpose(p_wk[:, b, CHUNK:2 * CHUNK], k_now[:, par, d, h, :], ident).then_inc(first_done, 1)

                    def second(u, base, x):
                        par, r, d, h, b = unit(u)
                        pe.wait_ge(state_done, base + u + 1)
                        if x is not None:
                            pe.wait_ge(total_done, x * U + u + 1)
                            c = 2 * x + par + CCH if d == 0 else ALLCH - 1 - par - 2 * x
                            values = v_ext[:, bass.ds(c, 1), h, :].rearrange("p o n -> p (o n)")
                            pe.wait_ge(inter_done, x * U + u + 1)
                            pe.wait_ge(w_qk_done, x * U + u + 3)
                            pass_waits(pe)
                            pe.matmul(p_num[:, b, 0:E1], w_qk[:, b, :], values, start=True, stop=True)
                            pe.matmul(p_int[:, b, 0:E1], q_now[:, par, d, h, :], state[:, r, :], start=True, stop=True)
                        else:
                            c = par if d == 0 else CCH - 1 - par
                            values = v_ext[:, c, h, :]
                        pe.wait_ge(k_w_done, base + u + 3)
                        if x is not None:
                            pass_waits(pe)
                        pe.matmul(p_num[:, b, 256:256 + E1], k_w[:, b, :], values, start=True, stop=True).then_inc(second_done, 1)

                    def units(base, x, fetches):
                        pe.wait_ge(fetched, fetches[0])
                        first(0, base, x)
                        first(1, base, x)
                        for u in range(U):
                            second(u, base, x)
                            if u + 2 < U:
                                if u + 2 == U // 2:
                                    pe.wait_ge(fetched, fetches[1])
                                first(u + 2, base, x)

                    units(0, None, (C_FETCH, 2 * C_FETCH))
                    with pe.Fori(0, XCH // 2) as i:
                        done = 2 * C_FETCH + 2 * X_FETCH * i
                        units((i + 1) * U, i, (done + X_FETCH, done + 2 * X_FETCH))

                @block.scalar
                def _(act):
                    act.sem_inc(k_w_done, 2)
                    act.sem_inc(weight_done, 2)
                    act.sem_inc(inter_done, 2)

                    def first(u, base, x):
                        par, r, d, h, b = unit(u)
                        act.wait_ge(first_done, base + u + 1)
                        if x is not None:
                            act.wait_ge(w_qk_done, x * U + u + 1)
                            act.activation(weight[:, b, :], p_wk[:, b, 0:CHUNK], ACT.Exp, bias=g_now[:, par, d, GG, h:h + 1]).then_inc(weight_done, 1)
                        act.wait_ge(state_done, base + u + 1)
                        act.activation(k_w[:, b, :], p_wk[:, b, CHUNK:2 * CHUNK], ACT.Copy, scale=g_now[:, par, d, WS, h:h + 1]).then_inc(k_w_done, 1)

                    def second(u, base, x):
                        par, r, d, h, b = unit(u)
                        if x is not None:
                            act.wait_ge(second_done, base + u + 1)
                            act.activation(inter[:, b, :], p_int[:, b, 0:E1], ACT.Copy, scale=g_now[:, par, d, DECAY, h:h + 1]).then_inc(inter_done, 1)

                    def units(base, x):
                        first(0, base, x)
                        first(1, base, x)
                        for u in range(U):
                            second(u, base, x)
                            if u + 2 < U:
                                first(u + 2, base, x)

                    units(0, None)
                    with act.Fori(0, XCH // 2) as i:
                        units((i + 1) * U, i)

                @block.vector
                def _(dve):
                    dve.memset(state[:], 0.0).then_inc(dve_step, 1)
                    dve.wait_ge(dve_step, 1)
                    dve.sem_inc(w_qk_done, 2)
                    dve.sem_inc(total_done, 2)
                    dve.sem_inc(group_done, 4)
                    dve.sem_inc(state_done, 2)
                    dve.sem_inc(cleared, 1)
                    dve.memset(h_sum[:], 0.0).then_inc(dve_step, 1)
                    dve.wait_ge(dve_step, 2)

                    def first(u, base, x):
                        par, r, d, h, b = unit(u)
                        if x is not None:
                            dve.wait_ge(weight_done, x * U + u + 3)
                            dve.wait_ge(second_done, base + u - 1)
                            dve.scalar_tensor_tensor(out=w_qk[:, b, :], in0=p_qk[:, b, 0:CHUNK], scalar=M_DIM ** -0.5, in1=weight[:, b, :],
                                                     op0=ALU.mult, op1=ALU.mult).then_inc(w_qk_done, 1)

                    def second(u, base, x, steps):
                        par, r, d, h, b = unit(u)
                        dve.wait_ge(second_done, base + u + 1)
                        dve.scalar_tensor_tensor(out=state[:, r, :], in0=state[:, r, :], scalar=a_now[:, par, r:r + 1], in1=p_num[:, b, 256:256 + E1],
                                                 op0=ALU.mult, op1=ALU.add).then_inc(state_done, 1)
                        if x is not None:
                            dve.wait_ge(inter_done, x * U + u + 3)
                            dve.tensor_tensor(total[:, (u // M_HEADS) % 2, h, :], p_num[:, b, 0:E1], inter[:, b, :], ALU.add).then_inc(total_done, 1)
                            if h == M_HEADS - 1:
                                for op in left:
                                    op()
                                left[:] = finish(u // M_HEADS, par, d, x, steps)
                            elif left:
                                left.pop(0)()

                    left = []

                    def finish(q, par, d, x, steps):
                        sums, den, by = total[:, q % 2, :, 0:M_DIM], total[:, q % 2, :, M_DIM:E1], size[:, q % 2]

                        def size_of():
                            dve.wait_ge(total_done, x * U + (q + 1) * M_HEADS + 2)
                            steps(dve.scalar_tensor_tensor(out=by, in0=den, scalar=-1.0, in1=den, op0=ALU.mult, op1=ALU.max))

                        def at_least():
                            steps.wait()
                            steps(dve.tensor_tensor(by, by, g_now[:, par, d, FLOOR, :].unsqueeze(2), ALU.max))

                        def invert():
                            steps.wait()
                            steps(dve.reciprocal(by, by))

                        def divide_and_add():
                            steps.wait()
                            steps(dve.tensor_tensor(sums, sums, by.to_broadcast([P, M_HEADS, M_DIM]), ALU.mult))
                            steps.wait()
                            pass_waits(dve)
                            c = 2 * x + par if d == 0 else XCH - 1 - par - 2 * x
                            to = h_sum[:, bass.ds(c, 1), :, :].rearrange("p o h n -> p (o h) n")
                            steps(dve.tensor_tensor(to, to, sums, ALU.add))
                            steps.wait()
                            dve.sem_inc(group_done, 1)

                        return [size_of, at_least, invert, divide_and_add]

                    def units(base, x):
                        steps = Steps(dve, dve_step, 2 + (0 if x is None else x * (5 * U // M_HEADS)))
                        first(0, base, x)
                        for u in range(U):
                            if u + 1 < U:
                                first(u + 1, base, x)
                            second(u, base, x, steps)
                        for op in left:
                            op()
                        left.clear()

                    units(0, None)
                    with dve.Fori(0, XCH // 2) as i:
                        units((i + 1) * U, i)

        mix_at = nc.sbuf_usable_end // 32 * 32 - 2 * KT * SEQ * 4
        mix_mem = Arena(nc, mix_at)
        mix_hi = mix_mem("mix_hi", [P, KT, SEQ], F32R)
        mix_lo = mix_mem("mix_lo", [P, KT, SEQ], F32R)

        def mix_weights(n):
            src = A["w_out"].rearrange("o k n -> (o k) n")
            cols = slice(n * P, (n + 1) * P)
            half = N_HEADS // 2 * HEAD_DIM
            parts = [(w_raw[HEAD_DIM * a:HEAD_DIM * (a + 1), n % 2, 0:4, :],
                      src[half * a:half * (a + 1), cols].rearrange("(k p) n -> p k n", p=HEAD_DIM)) for a in range(2)]
            return parts + [(w_raw[:, n % 2, 4:, :], src[2 * half:, cols].rearrange("(k p) n -> p k n", p=P))]

        def phase_mix():
            phases.start()
            mem = Arena(nc, free_at)
            att = mem("mix_att", [P, M_HEADS, SEQ])
            normed = mem("mix_normed", [P, XCH * M_HEADS, M_DIM])
            mixed = mem("mix_mixed", [P, 2, HALF])
            sums = mem("mix_sums", [P, XCH * M_HEADS])
            mod_mem = Arena(nc, out_gate_end)
            modulation = Modulation("mix", mod_mem, [a(f"mix_w_mod{u}", [P, KT, Modulation.WIDTH]) for u, a in enumerate((mem, mem, mod_mem, mod_mem))],
                                    MIX_MOD, END_MOD - MIX_MOD)
            assert mem.at <= out_gate_at and mod_mem.at <= s_mem.at
            loaded = sem("mix_loaded")
            squared = sem("mix_squared")
            mean_done = sem("mix_mean_done")
            root_done = sem("mix_root_done")
            normed_done = sem("mix_normed_done")
            turned = sem("mix_turned")
            mixed_done = sem("mix_mixed_done")
            hi_done = sem("mix_hi_done")
            lo_done = sem("mix_lo_done")
            att_hi = sem("mix_att_hi")
            dve_step = sem("mix_dve_step")
            EARLY = 1
            LATE = {2 * (j - EARLY) + 1: j for j in range(EARLY, modulation.count)}
            pre = Prefetch("mix", [mix_weights(0), mix_weights(1)])
            rows = h_sum[:].rearrange("p c h n -> p (c h) n")
            halves = [slice(i * XCH * M_HEADS // 2, (i + 1) * XCH * M_HEADS // 2) for i in range(2)]
            with nc.psum_tensor("mix_turn", [P, 2, HALF], F32) as turn, \
                    nc.psum_tensor("mix_mod_rows", [2, 2, HALF], F32) as mod_rows, nc.psum_tensor("mix_mod_columns", [P, HALF], F32) as mod_columns, \
                    nc.Block() as block:
                @block.sync
                def _(sp):
                    modulation.sp(sp, 0)
                    sp.dma_start(att[:], att_cm.rearrange("(j p) t -> p j t", p=P)).then_inc(loaded, 16)
                    for j in range(1, modulation.count):
                        modulation.sp(sp, j)
                    pre.load(sp)

                @block.gpsimd
                def _(pool):
                    for j in range(M_HEADS):
                        pool.wait_ge(att_hi, j + 1)
                        pool.tensor_tensor(mix_lo[:, j, :], att[:, j, :], mix_hi[:, j, :].bitcast(F32), ALU.subtract)
                    pre.split(pool)

                @block.vector
                def _(dve):
                    step = Steps(dve, dve_step)
                    for half in range(2):
                        dve.wait_ge(squared, half + 1)
                        step(dve.tensor_reduce(sums[:, halves[half]], normed[:, halves[half]], AX_X, ALU.add))
                    step.wait()
                    dve.tensor_scalar(sums[:], sums[:], 1.0 / M_DIM, EPS, ALU.mult, ALU.add).then_inc(mean_done, 1)
                    dve.wait_ge(root_done, 1)
                    step(dve.reciprocal(sums[:], sums[:]))
                    step.wait()
                    for half in halves:
                        dve.tensor_tensor(normed[:, half], rows[:, half], sums[:, half].unsqueeze(2).to_broadcast([P, XCH * M_HEADS // 2, M_DIM]),
                                          ALU.mult).then_inc(normed_done, 1)
                    dve.sem_inc(mixed_done, 2)
                    for n in range(2 * M_HEADS):
                        half, h = n // M_HEADS, n % M_HEADS
                        cols = slice(half * HALF, (half + 1) * HALF)
                        dve.wait_ge(turned, n + 1)
                        if n >= 2:
                            dve.wait_ge(lo_done, n - 1)
                        dve.scalar_tensor_tensor(out=mixed[:, n % 2, :], in0=turn[:, n % 2, :], scalar=pb("mlstm_norm_w")[:, h:h + 1],
                                                 in1=out_gate[:, h, cols], op0=ALU.mult, op1=ALU.mult).then_inc(mixed_done, 1)
                        dve.wait_ge(hi_done, n + 1)
                        dve.tensor_tensor(mix_lo[:, M_HEADS + h, cols], mixed[:, n % 2, :], mix_hi[:, M_HEADS + h, cols].bitcast(F32),
                                          ALU.subtract).then_inc(lo_done, 1)
                    modulation.dve_add(dve, mod_columns, 0, modulation.count)
                    dve.wait_ge(modulation.bias_added, 1)
                    dve.scalar_tensor_tensor(out=gain2[:], in0=mod[:, SC2:SC2 + KT, 0], scalar=1.0, in1=pa("norm2_w"), op0=ALU.add, op1=ALU.mult)

                @block.scalar
                def _(act):
                    for half in halves:
                        act.activation(normed[:, half], rows[:, half], ACT.Square).then_inc(squared, 1)
                    act.wait_ge(mean_done, 1)
                    act.activation(sums[:], sums[:], ACT.Sqrt).then_inc(root_done, 1)
                    for j in range(M_HEADS):
                        if j < EARLY:
                            modulation.act(act, j, mod_rows)
                        act.wait_ge(loaded, 16)
                        act.copy(mix_hi[:, j, :], att[:, j, :]).then_inc(att_hi, 1)
                    for n in range(2 * M_HEADS):
                        half, h = n // M_HEADS, n % M_HEADS
                        act.wait_ge(mixed_done, n + 3)
                        act.copy(mix_hi[:, M_HEADS + h, half * HALF:(half + 1) * HALF], mixed[:, n % 2, :]).then_inc(hi_done, 1)
                        if n in LATE:
                            modulation.act(act, LATE[n], mod_rows)

                @block.tensor
                def _(pe):
                    for j in range(EARLY):
                        modulation.pe(pe, j, mod_rows, mod_columns)
                    for n in range(2 * M_HEADS):
                        half, h = n // M_HEADS, n % M_HEADS
                        pe.wait_ge(normed_done, half + 1)
                        pe.wait_ge(mixed_done, n + 1)
                        for c in range(4):
                            ins = pe.transpose(turn[:, n % 2, c * P:(c + 1) * P], normed[:, (4 * half + c) * M_HEADS + h, :], ident)
                        ins.then_inc(turned, 1)
                        if n in LATE:
                            modulation.pe(pe, LATE[n], mod_rows, mod_columns)

        def phase_out(tag, y_hi, y_lo, weights, pieces, gain, next_parts=None, norm=None, split_from=None, result=None):
            phases.start()
            mem = Arena(nc, free_at)
            x = mem(f"{tag}_x", [P, KT, SEQ])
            squares = norm is not None or result is not None
            sq = mem(f"{tag}_sq", [P, 2, SEQ]) if squares else None
            sq_sum = mem(f"{tag}_sq_sum", [P, SEQ]) if squares else None
            SETS = 3
            rows = mem(f"{tag}_rows", [P, SETS, D]) if result else None
            rstd = mem(f"{tag}_rows_rstd", [P, BLOCKS]) if result else None
            ring = Ring(tag, pieces)
            pre = Prefetch(tag, next_parts, ring, KT) if next_parts else None
            tail = NormTail(tag, mem, x, SEQ, norm["affines"], norm.get("h_hi"), norm.get("h_lo"), norm.get("h_plain")) if norm else None
            z_free = sem(f"{tag}_z_free")
            x_loaded = [sem(f"{tag}_x_loaded{n}") for n in range(KT)]
            x_done = sem(f"{tag}_x_done")
            stored = [sem(f"{tag}_stored{u}") for u in range(2)]
            y_hi_done = sem(f"{tag}_y_hi_done")
            y_ready = sem(f"{tag}_y_ready")
            sq_done = sem(f"{tag}_sq_done")
            sum_done = sem(f"{tag}_sum_done")
            summed = tail.summed if norm else sem(f"{tag}_summed")
            gained = sem(f"{tag}_gained")
            mean_done = sem(f"{tag}_mean_done")
            root_done = sem(f"{tag}_root_done")
            inverse_done = sem(f"{tag}_inverse_done")
            rows_turned = sem(f"{tag}_rows_turned")
            rows_out = [sem(f"{tag}_rows_out{half}") for half in range(2)]
            rows_stored = [sem(f"{tag}_rows_stored{r}") for r in range(SETS)]
            with nc.psum_tensor(f"{tag}_z", [P, 2, 2, HALF], F32) as z, nc.psum_tensor(f"{tag}_sums", [P, HALF], F32) as sums, \
                    nc.psum_tensor(f"{tag}_spread", [P, 2, HALF], F32) as spread, nc.Block() as block:
                row_banks = [spread, z[:, 0], z[:, 1]]

                @block.sync
                def _(sp):
                    for n in range(KT):
                        sp.dma_start(x[:, n, :], x_cm_k[:, n, :]).then_inc(x_loaded[n], 16)
                        if n >= 2:
                            ring.load(sp, n, n % 2, weights(n))
                    if pre:
                        pre.load(sp)
                    if result:
                        for j in range(BLOCKS):
                            for half in range(2):
                                sp.wait_ge(rows_out[half], j + 1)
                            sp.dma_start(result[0][j * P:(j + 1) * P, :], rows[:, j % SETS, :]).then_inc(rows_stored[j % SETS], 16)
                        for u in range(SETS):
                            sp.wait_ge(rows_stored[u], 16 * len(range(u, BLOCKS, SETS)))

                @block.gpsimd
                def _(pool):
                    ring.credits(pool, None)
                    for n in range(2, KT):
                        ring.do_split(pool, n, n % 2, n // 2)
                    if pre:
                        pre.split(pool)
                    if norm:
                        tail.pool(pool)

                @block.tensor
                def _(pe):
                    ring.credits(None, pe)

                    def proj(n, u, between=None):
                        ring.project(pe, n, u, z_free, [(z[:, u, b, :], b * HALF, HALF) for b in range(2)], y_hi, y_lo, between)

                    if split_from is not None:
                        pe.wait_ge(y_ready, 1)
                        proj(0, 0, {kt: (lambda kt=kt: pe.wait_ge(y_ready, kt + 2)) for kt in range(KT - 1)})
                        proj(1, 1)
                    with pe.Fori(0 if split_from is None else 1, KT // 2) as i:
                        for u in range(2):
                            proj(2 * i + u, u)
                    if squares:
                        pe.wait_ge(sum_done, KT)
                        for j in range(BLOCKS):
                            ins = pe.matmul(sums[:, j:j + 1], sq_sum[:, j * P:(j + 1) * P], ones[:, 0:1], start=True, stop=True)
                        ins.then_inc(summed, 1)
                    if norm:
                        tail.pe(pe, spread)
                    if result:
                        pe.wait_ge(gained, KT)
                        for j in range(BLOCKS):
                            if j >= SETS:
                                for half in range(2):
                                    pe.wait_ge(rows_out[half], j - SETS + 1)
                            for kt in range(KT):
                                ins = pe.transpose(row_banks[j % SETS][:, kt // 4, kt % 4 * P:(kt % 4 + 1) * P], x[:, kt, j * P:(j + 1) * P], ident)
                            ins.then_inc(rows_turned, 1)

                @block.vector
                def _(dve):
                    dve.sem_inc(z_free, 2)

                    def add_up(n):
                        dve.wait_ge(sq_done, n + 1)
                        if n:
                            dve.wait_ge(sum_done, n)
                            dve.tensor_tensor(sq_sum[:], sq_sum[:], sq[:, n % 2, :], ALU.add).then_inc(sum_done, 1)
                        else:
                            dve.tensor_copy(sq_sum[:], sq[:, 0, :]).then_inc(sum_done, 1)

                    if split_from is not None:
                        for kt in range(KT):
                            dve.wait_ge(y_hi_done, kt + 1)
                            dve.tensor_tensor(y_lo[:, kt, :], split_from[:, kt, :], y_hi[:, kt, :].bitcast(F32), ALU.subtract).then_inc(y_ready, 1)
                    for n in range(KT):
                        u = n % 2
                        dve.wait_ge(ring.projected, n + 3)
                        dve.wait_ge(x_loaded[n], 16)
                        for b in range(2):
                            cols = slice(b * HALF, (b + 1) * HALF)
                            dve.scalar_tensor_tensor(out=x[:, n, cols], in0=z[:, u, b, :], scalar=1.0 if gain is None else gain(n),
                                                     in1=x[:, n, cols], op0=ALU.mult, op1=ALU.add).then_inc(x_done, 1)
                        dve.wait_ge(x_done, 2 * n + 2)
                        dve.sem_inc(z_free, 1)
                        if squares and n:
                            add_up(n - 1)
                    if squares:
                        add_up(KT - 1)
                    if result:
                        dve.wait_ge(summed, 1)
                        dve.tensor_scalar(rstd[:], sums[:, 0:BLOCKS], 1.0 / D, EPS, ALU.mult, ALU.add).then_inc(mean_done, 1)
                        dve.wait_ge(root_done, 1)
                        dve.reciprocal(rstd[:], rstd[:]).then_inc(inverse_done, 1)
                        dve.wait_ge(inverse_done, 1)
                        for j in range(BLOCKS):
                            dve.wait_ge(rows_turned, j + 1)
                            if j >= SETS:
                                dve.wait_ge(rows_stored[j % SETS], 16 * (j // SETS))
                            dve.tensor_scalar(rows[:, j % SETS, 0:HALF], row_banks[j % SETS][:, 0, :], rstd[:, j:j + 1], None, ALU.mult).then_inc(rows_out[0], 1)
                    if norm:
                        tail.dve(dve, sums[:, 0:BLOCKS], spread, lambda kt: dve.wait_ge(stored[kt % 2], 16 * (kt // 2 + 1)))

                @block.scalar
                def _(act):
                    if split_from is not None:
                        for kt in range(KT):
                            act.copy(y_hi[:, kt, :], split_from[:, kt, :]).then_inc(y_hi_done, 1)
                    for n in range(KT):
                        act.wait_ge(x_done, 2 * n + 2)
                        if not result:
                            act.dma_start(x_cm_k[:, n, :], x[:, n, :]).then_inc(stored[n % 2], 16)
                        if squares:
                            if n >= 2:
                                act.wait_ge(sum_done, n - 1)
                            act.activation(sq[:, n % 2, :], x[:, n, :], ACT.Square).then_inc(sq_done, 1)
                        if result:
                            act.wait_ge(sq_done, n + 1)
                            act.activation(x[:, n, :], x[:, n, :], ACT.Copy, scale=result[1](n)).then_inc(gained, 1)
                    if result:
                        act.wait_ge(mean_done, 1)
                        act.activation(rstd[:], rstd[:], ACT.Sqrt).then_inc(root_done, 1)
                        act.wait_ge(inverse_done, 1)
                        for j in range(BLOCKS):
                            act.wait_ge(rows_turned, j + 1)
                            if j >= SETS:
                                act.wait_ge(rows_stored[j % SETS], 16 * (j // SETS))
                            act.activation(rows[:, j % SETS, HALF:], row_banks[j % SETS][:, 1, :], ACT.Copy, scale=rstd[:, j:j + 1]).then_inc(rows_out[1], 1)
                    else:
                        for u in range(2):
                            act.wait_ge(stored[u], 16 * (KT // 2))
                    if norm:
                        tail.act(act)

        phase_mlstm_inputs()
        phase_gate_scans()
        phase_mlstm()
        phase_mix()
        h2_at = nc.sbuf_usable_end // 32 * 32 - KT * SEQ * 4
        h2_cm = Arena(nc, h2_at)("h2_cm", [P, KT, SEQ])
        phase_out("out1", mix_hi, mix_lo, mix_weights, 3, lambda n: mod[:, G1 + n, 0:1],
                  norm=dict(affines=[(0, SEQ, lambda kt: gain2[:, kt:kt + 1], lambda kt: mod[:, SH2 + kt, 0:1])], h_plain=h2_cm))

        route_mem = Arena(nc, free_at)
        slot_gate = route_mem("slot_gate", [P, N_EXPERTS])
        slot_token = route_mem("slot_token", [P, N_EXPERTS], U32)
        FFK = EXPERT_FF // P
        EXP_SHAPES = {"gate": [P, KT, EXPERT_FF], "up": [P, KT, EXPERT_FF], "down": [P, FFK, D]}
        exp_mem = Arena(nc, route_mem.at)
        exp_hi = {w: exp_mem(f"hi_{w}", s, F32R) for w, s in EXP_SHAPES.items()}
        exp_raw, exp_lo = {}, {}
        for w, s in EXP_SHAPES.items():
            for u in range(2):
                at = Arena(nc, ring_at) if (w, u) == ("down", 0) else exp_mem
                again = Arena(nc, at.at)
                exp_raw[w, u] = at(f"raw_{w}{u}", s)
                exp_lo[w, u] = again(f"lo_{w}{u}", s, F32R)
        exp_src = {w: A[f"w_{w}"].rearrange("o e (k p) n -> p (o e) k n", p=P) for w in EXP_SHAPES}

        def phase_router():
            phases.start()
            mem = Arena(nc, exp_mem.at)
            ROWS = 32 + N_EXPERTS
            w_router = mem("w_router", [P, KT, N_EXPERTS])
            rows = mem("h2_rows_sb", [P, 2, HALF])
            aff = mem("aff", [P, BLOCKS, N_EXPERTS])
            peak = mem("aff_peak", [P, BLOCKS])
            total = mem("aff_total", [P, BLOCKS])
            by_half = mem("aff_by_half", [P, BLOCKS // 2, ROWS])
            left = [mem(f"aff_left{u}", [ROWS, HALF]) for u in range(2)]
            top = mem("aff_top", [ROWS, SLOTS])
            top_at = mem("aff_top_at", [ROWS, SLOTS], U32)
            top_at_f = mem("aff_top_at_f", [ROWS, SLOTS])
            top_back, top_at_back = mem("aff_top_back", [ROWS, SLOTS]), mem("aff_top_at_back", [ROWS, SLOTS])
            second = mem("aff_second", [P, 2, N_EXPERTS])
            of_first = mem("aff_of_first", [P, N_EXPERTS])
            apart = mem("aff_apart", [P, N_EXPERTS])
            w_loaded = sem("route_w_loaded")
            products_done = sem("route_products_done")
            products_out = sem("route_products_out")
            logits_done = sem("route_logits_done")
            shifted = sem("route_shifted")
            exp_done = sem("route_exp_done")
            aff_done = sem("route_aff_done")
            aff_turned = sem("route_aff_turned")
            rows_turned = sem("route_rows_turned")
            rows_out = sem("route_rows_out")
            stored = [sem(f"route_stored{u}") for u in range(2)]
            top_done = sem("route_top_done")
            top_turned = sem("route_top_turned")
            raw_loaded = [sem(f"route_{w}_loaded") for w in EXP_SHAPES]
            next_loaded = sem("route_next_loaded")
            hi_done = sem("route_hi_done")
            assert mem.at <= h2_at, (mem.at, h2_at, free_at)
            dve_step = sem("route_dve_step")
            wide = [P, BLOCKS, N_EXPERTS]
            after = {2 * n + 1: w for n, w in enumerate(EXP_SHAPES)}
            with nc.psum_tensor("route_logits", [P, HALF], F32) as logits, nc.psum_tensor("route_aff_t", [ROWS, HALF], F32) as aff_t, \
                    nc.psum_tensor("route_turn", [P, 2, 2, HALF], F32) as turn, nc.psum_tensor("route_top_t", [P, 4, N_EXPERTS], F32) as top_t, \
                    nc.Block() as block:
                @block.sync
                def _(sp):
                    sp.dma_start(w_router[:], A["w_router"].rearrange("o (k p) n -> p (o k) n", p=P)).then_inc(w_loaded, 16)
                    for n, w in enumerate(EXP_SHAPES):
                        sp.dma_start(exp_raw[w, 0][:], exp_src[w][:, 0]).then_inc(raw_loaded[n], 16)
                    for j in range(BLOCKS):
                        for half in range(2):
                            sp.wait_ge(rows_out, 2 * j + half + 1)
                            sp.dma_start(h2_rows[j * P:(j + 1) * P, half * HALF:(half + 1) * HALF], rows[:, half, :]).then_inc(stored[half], 16)
                        if j in after:
                            w = after[j]
                            sp.dma_start(exp_raw[w, 1][:], exp_src[w][:, 1]).then_inc(next_loaded, 16)
                    for half in range(2):
                        sp.wait_ge(stored[half], 16 * BLOCKS)
                    sp.wait_ge(next_loaded, 16 * len(EXP_SHAPES))

                @block.gpsimd
                def _(pool):
                    for n, w in enumerate(EXP_SHAPES):
                        pool.wait_ge(hi_done, n + 1)
                        pool.tensor_tensor(exp_lo[w, 0][:], exp_raw[w, 0][:], exp_hi[w][:].bitcast(F32), ALU.subtract)

                @block.tensor
                def _(pe):
                    pe.wait_ge(w_loaded, 16)
                    for kt in range(KT):
                        for half in range(2):
                            ins = pe.matmul(turn[0:N_EXPERTS, 1, half, :], w_router[:, kt, :], h2_cm[:, kt, half * HALF:(half + 1) * HALF],
                                            start=(kt == 0), stop=(kt == KT - 1))
                    ins.then_inc(products_done, 1)
                    pe.wait_ge(products_out, 2)
                    for j in range(BLOCKS):
                        ins = pe.transpose(logits[:, j * N_EXPERTS:(j + 1) * N_EXPERTS], left[j // 4][0:N_EXPERTS, j % 4 * P:(j % 4 + 1) * P],
                                           ident[0:N_EXPERTS, 0:N_EXPERTS])
                    ins.then_inc(logits_done, 1)
                    for j in range(BLOCKS):
                        if j >= 2:
                            pe.wait_ge(rows_out, 2 * (j - 1))
                        for kt in range(KT):
                            ins = pe.transpose(turn[:, j % 2, kt // 4, (kt % 4) * P:(kt % 4 + 1) * P], h2_cm[:, kt, j * P:(j + 1) * P], ident)
                            if kt % 4 == 3:
                                ins.then_inc(rows_turned, 1)
                        if j == 2:
                            pe.wait_ge(aff_done, 1)
                            for b in range(BLOCKS // 2):
                                ins = pe.transpose(aff_t[:, b * P:(b + 1) * P], by_half[:, b, :], ident)
                            ins.then_inc(aff_turned, 1)
                    pe.wait_ge(top_done, 1)
                    for n, (x, back) in enumerate(((top, top_back), (top_at_f, top_at_back))):
                        pe.matmul(top_t[:, 2 * n, :], x[:], ident[0:ROWS, 0:N_EXPERTS], start=True, stop=True)
                        ins = pe.matmul(top_t[:, 2 * n + 1, :], back[:], ident[0:ROWS, 32:ROWS], start=True, stop=True)
                    ins.then_inc(top_turned, 1)

                @block.scalar
                def _(act):
                    act.wait_ge(products_done, 1)
                    act.copy(left[0][0:N_EXPERTS, :], turn[0:N_EXPERTS, 1, 0, :]).then_inc(products_out, 1)
                    act.wait_ge(shifted, 1)
                    act.activation(aff[:], aff[:], ACT.Exp).then_inc(exp_done, 1)
                    for j in range(BLOCKS):
                        for half in range(2):
                            act.wait_ge(rows_turned, 2 * j + half + 1)
                            if j:
                                act.wait_ge(stored[half], 16 * j)
                            act.copy(rows[:, half, :], turn[:, j % 2, half, :]).then_inc(rows_out, 1)
                        if j in after:
                            w = after[j]
                            act.wait_ge(raw_loaded[list(EXP_SHAPES).index(w)], 16)
                            act.copy(exp_hi[w][:], exp_raw[w, 0][:]).then_inc(hi_done, 1)

                @block.vector
                def _(dve):
                    step = Steps(dve, dve_step)
                    step(dve.memset(by_half[:], 0.0))
                    dve.wait_ge(products_done, 1)
                    dve.tensor_copy(left[1][0:N_EXPERTS, :], turn[0:N_EXPERTS, 1, 1, :]).then_inc(products_out, 1)
                    dve.wait_ge(logits_done, 1)
                    lg = logits[:, 0:BLOCKS * N_EXPERTS].rearrange("p (j n) -> p j n", n=N_EXPERTS)
                    step(dve.tensor_reduce(peak[:], lg, AX_X, ALU.max))
                    step.wait()
                    dve.tensor_tensor(aff[:], lg, peak[:].unsqueeze(2).to_broadcast(wide), ALU.subtract).then_inc(shifted, 1)
                    dve.wait_ge(exp_done, 1)
                    step(dve.tensor_reduce(total[:], aff[:], AX_X, ALU.add))
                    step.wait()
                    step(dve.reciprocal(total[:], total[:]))
                    step.wait()
                    for half in range(2):
                        blocks = slice(half * (BLOCKS // 2), (half + 1) * (BLOCKS // 2))
                        step(dve.tensor_tensor(by_half[:, :, 32 * half:32 * half + N_EXPERTS], aff[:, blocks, :],
                                               total[:, blocks].unsqueeze(2).to_broadcast([P, BLOCKS // 2, N_EXPERTS]), ALU.mult))
                    step.wait()
                    dve.sem_inc(aff_done, 1)
                    dve.wait_ge(aff_turned, 1)
                    step(dve.tensor_copy(left[0][:], aff_t[:]))
                    step.wait()
                    for r in range(SLOTS // 8):
                        now, nxt = left[r % 2], left[(r + 1) % 2]
                        eight = slice(8 * r, 8 * (r + 1))
                        step(dve.max(top[:, eight], now[:]))
                        step.wait()
                        step(dve.max_index(top_at[:, eight], top[:, eight], now[:]))
                        if r + 1 < SLOTS // 8:
                            step(dve.match_replace(nxt[:], top[:, eight], now[:], -1.0))
                        step.wait()
                    step(dve.tensor_copy(top_at_f[:], top_at[:]))
                    step(dve.tensor_copy(top_back[:], top[:, ::-1]))
                    step(dve.tensor_copy(top_at_back[:], top_at[:, ::-1]))
                    step.wait()
                    dve.sem_inc(top_done, 1)
                    dve.wait_ge(top_turned, 1)
                    step(dve.tensor_copy(second[:, 0, :], top_t[:, 1, :]))
                    step(dve.tensor_scalar(second[:, 1, :], top_t[:, 3, :], float(HALF), None, ALU.add))
                    step.wait()
                    step(dve.tensor_tensor(of_first[:], top_t[:, 0, :], second[:, 0, :], ALU.is_ge))
                    step(dve.tensor_tensor(slot_gate[:], top_t[:, 0, :], second[:, 0, :], ALU.max))
                    step(dve.tensor_tensor(apart[:], top_t[:, 2, :], second[:, 1, :], ALU.subtract))
                    step.wait()
                    step(dve.tensor_tensor(apart[:], apart[:], of_first[:], ALU.mult))
                    step.wait()
                    step(dve.tensor_tensor(slot_token[:], apart[:], second[:, 1, :], ALU.add))

        def phase_experts():
            phases.start()
            mem = Arena(nc, exp_mem.at)
            FK, shapes, raw, w_hi_, w_lo_ = FFK, EXP_SHAPES, exp_raw, exp_hi, exp_lo
            xg = mem("x_gathered", [P, 2, D])
            x_hi = mem("x_hi", [P, 2, KT, P], F32R)
            x_lo = mem("x_lo", [P, 2, KT, P], F32R)
            silu = mem("silu_gate", [P, EXPERT_FF])
            prod = mem("gate_up", [P, EXPERT_FF])
            f_hi = mem("f_hi", [P, FK, P], F32R)
            f_lo = mem("f_lo", [P, FK, P], F32R)
            y = mem("expert_y", [P, 2, D])
            token_in = mem("token_in", [P, 2], U32)
            token_out = mem("token_out", [P, 2], U32)
            gate_now = mem("gate_now", [P, 2])
            loaded = {(w, u): sem(f"exp_{w}_loaded{u}") for w in shapes for u in range(2)}
            hi_done = {w: sem(f"exp_{w}_hi_done") for w in shapes}
            split = {w: sem(f"exp_{w}_split") for w in shapes}
            used = {w: sem(f"exp_{w}_used") for w in shapes}
            token_in_copied = sem("exp_token_in_copied")
            token_out_copied = sem("exp_token_out_copied")
            gathered = [phases.keep(f"exp_gathered{u}") for u in range(2)]
            turned = sem("exp_turned")
            x_hi_done = sem("exp_x_hi_done")
            x_lo_done = sem("exp_x_lo_done")
            silu_done = sem("exp_silu_done")
            prod_done = sem("exp_prod_done")
            f_turned = sem("exp_f_turned")
            f_hi_done = sem("exp_f_hi_done")
            f_lo_done = sem("exp_f_lo_done")
            gate_copied = sem("exp_gate_copied")
            y_out = sem("exp_y_out")
            y_free = sem("exp_y_free")
            scattered = phases.keep("exp_scattered")
            PAIRS = N_EXPERTS // 2
            parts_of = {"gate": 2, "up": 1, "down": 1}
            gate_half = [slice(0, KT // 2), slice(KT // 2, KT)]
            with nc.psum_tensor("exp_turn", [P, 2, HALF], F32) as p_x, nc.psum_tensor("exp_gate", [P, 2, HALF], F32) as p_gu, \
                    nc.psum_tensor("exp_f", [P, FK, P], F32) as p_f, nc.psum_tensor("exp_y", [P, 2, HALF], F32) as p_y, nc.Block() as block:

                def pairs(eng, run):
                    with eng.Fori(0, PAIRS - 1) as i:
                        for u in range(2):
                            run(2 * i + u, u, i, False)
                    for u in range(2):
                        run(2 * (PAIRS - 1) + u, u, PAIRS - 1, u == 1)

                @block.sync
                def _(sp):
                    for place in loaded.values():
                        sp.sem_inc(place, 16)
                    with sp.Fori(1, PAIRS) as i:
                        for u in range(2):
                            for w in shapes:
                                sp.wait_ge(used[w], 2 * i + u)
                                pass_waits(sp)
                                sp.dma_start(raw[w, u][:].rearrange("p (o k) n -> p o k n", o=1), exp_src[w][:, bass.ds(2 * i + u, 1)]).then_inc(loaded[w, u], 16)

                @block.gpsimd
                def _(pool):
                    pool.sem_inc(split["down"], 2)

                    def gather(e, slot, round_):
                        pool.wait_ge(turned, e + 1)
                        pass_waits(pool)
                        pool.tensor_copy(token_in[:, slot:slot + 1], slot_token[:, bass.ds(e, 1)]).then_inc(token_in_copied, 1)
                        pool.wait_ge(token_in_copied, e + 1)
                        pass_waits(pool)
                        pool.indirect_dma_start(xg[:, slot, :], None, h2_rows, bass.IndirectOffsetOnAxis(ap=token_in[:, slot:slot + 1], axis=0),
                                                bounds_check=SEQ - 1).then_inc(gathered[slot], 16)

                    def lo_down(e, slot):
                        pool.wait_ge(hi_done["down"], e + 1)
                        pool.tensor_tensor(w_lo_["down", slot][:], raw["down", slot][:], w_hi_["down"][:].bitcast(F32), ALU.subtract).then_inc(split["down"], 1)

                    def scatter(e, slot):
                        pass_waits(pool)
                        pool.tensor_copy(token_out[:, slot:slot + 1], slot_token[:, bass.ds(e, 1)]).then_inc(token_out_copied, 1)
                        pool.wait_ge(token_out_copied, e + 1)
                        pool.wait_ge(y_out, e + 2)
                        if not (isinstance(e, int) and e == 0):
                            pool.wait_ge(scattered, 16 * e)
                        pool.sem_inc(y_free, 1)
                        pass_waits(pool)
                        pool.indirect_dma_start(ffn_rows, bass.IndirectOffsetOnAxis(ap=token_out[:, slot:slot + 1], axis=0), y[:, slot, :], None,
                                                bounds_check=SEQ - 1, compute_op=ALU.add).then_inc(scattered, 16)

                    pool.sem_inc(turned, 2)
                    pool.sem_inc(y_free, 1)
                    gather(0, 0, 0)
                    gather(1, 1, 0)
                    gather(2, 0, 1)
                    lo_down(1, 1)
                    scatter(0, 0)
                    with pool.Fori(1, PAIRS - 1) as i:
                        for u in range(2):
                            gather(2 * i + u + 1, (u + 1) % 2, i + u)
                            lo_down(2 * i + u, u)
                            scatter(2 * i + u - 1, (u + 1) % 2)
                    for e in (N_EXPERTS - 2, N_EXPERTS - 1):
                        if e + 1 < N_EXPERTS:
                            gather(e + 1, (e + 1) % 2, (e + 1) // 2)
                        lo_down(e, e % 2)
                        scatter(e - 1, (e - 1) % 2)
                    scatter(N_EXPERTS - 1, 1)
                    pool.wait_ge(scattered, 16 * N_EXPERTS)

                @block.tensor
                def _(pe):
                    for w in shapes:
                        pe.sem_inc(used[w], 1)

                    def turn(e, slot, round_):
                        pe.wait_ge(gathered[slot], 16 * (round_ + 1))
                        pe.wait_ge(x_lo_done, e + 1)
                        for kt in range(KT):
                            ins = pe.transpose(p_x[:, kt // 4, (kt % 4) * P:(kt % 4 + 1) * P], xg[:, slot, kt * P:(kt + 1) * P], ident)
                        ins.then_inc(turned, 1)

                    def product(to, w, slot, x_hi, x_lo, kts, cols, lo_ready=None):
                        for kt in range(kts):
                            pe.matmul(to, x_hi[:, kt, :], w_hi_[w][:, kt, cols], start=(kt == 0), stop=False)
                            pe.matmul(to, x_hi[:, kt, :], w_lo_[w, slot][:, kt, cols], start=False, stop=False)
                        if lo_ready:
                            lo_ready()
                        for kt in range(kts):
                            ins = pe.matmul(to, x_lo[:, kt, :], w_hi_[w][:, kt, cols], start=False, stop=(kt == kts - 1))
                        return ins

                    def run(e, slot, round_, last):
                        pe.wait_ge(x_lo_done, e + 2)
                        pe.wait_ge(prod_done, e + 1)
                        for b, w in enumerate(("gate", "up")):
                            pe.wait_ge(split[w], parts_of[w] * (e + 2))
                            product(p_gu[:, b, :], w, slot, x_hi[:, slot], x_lo[:, slot], KT, slice(None)).then_inc(used[w], 1)
                        if not last:
                            turn(e + 1, 1 - slot, round_ + slot)
                        pe.wait_ge(prod_done, e + 2)
                        pe.wait_ge(f_lo_done, e + 1)
                        for kt in range(FK):
                            ins = pe.transpose(p_f[:, kt, :], prod[:, kt * P:(kt + 1) * P], ident)
                        ins.then_inc(f_turned, 1)
                        pe.wait_ge(f_hi_done, e + 1)
                        pe.wait_ge(split["down"], e + 2)
                        pe.wait_ge(y_out, e + 1)
                        for half in range(2):
                            ins = product(p_y[:, half, :], "down", slot, f_hi, f_lo, FK, slice(half * HALF, (half + 1) * HALF),
                                          lambda: pe.wait_ge(f_lo_done, e + 2))
                        ins.then_inc(used["down"], 1)

                    turn(0, 0, 0)
                    pairs(pe, run)

                @block.scalar
                def _(act):
                    def hi(w, e, slot, round_):
                        act.wait_ge(loaded[w, slot], 16 * (round_ + 1))
                        act.wait_ge(used[w], e + 1)
                        for kts in gate_half if w == "gate" else [slice(None)]:
                            act.copy(w_hi_[w][:, kts], raw[w, slot][:, kts]).then_inc(hi_done[w], 1)

                    def hi_x(e, slot):
                        act.wait_ge(turned, e + 3)
                        act.copy(x_hi[:, slot].rearrange("p (a k) n -> p a (k n)", a=2), p_x[:]).then_inc(x_hi_done, 1)

                    def run(e, slot, round_, last):
                        act.wait_ge(used["gate"], e + 2)
                        act.wait_ge(prod_done, e + 1)
                        act.activation(silu[:], p_gu[:, 0, :], ACT.Silu).then_inc(silu_done, 1)
                        if not last:
                            hi("gate", e + 1, 1 - slot, round_ + slot)
                        act.wait_ge(f_turned, e + 1)
                        act.copy(f_hi[:], p_f[:]).then_inc(f_hi_done, 1)
                        if not last:
                            hi_x(e + 1, 1 - slot)
                            hi("up", e + 1, 1 - slot, round_ + slot)
                            hi("down", e + 1, 1 - slot, round_ + slot)

                    for w in shapes:
                        act.sem_inc(hi_done[w], parts_of[w])
                    hi_x(0, 0)
                    pairs(act, run)

                @block.vector
                def _(dve):
                    dve.sem_inc(split["gate"], 4)
                    dve.sem_inc(split["up"], 2)
                    dve.sem_inc(x_lo_done, 1)
                    dve.sem_inc(prod_done, 1)
                    dve.sem_inc(f_lo_done, 1)
                    dve.sem_inc(y_out, 1)
                    dve.sem_inc(gate_copied, 1)

                    def lo_up(e, slot):
                        dve.wait_ge(hi_done["up"], e + 1)
                        dve.tensor_tensor(w_lo_["up", slot][:], raw["up", slot][:], w_hi_["up"][:].bitcast(F32), ALU.subtract).then_inc(split["up"], 1)

                    def lo_gate(e, slot, half):
                        kts = gate_half[half]
                        dve.wait_ge(hi_done["gate"], 2 * e + half + 1)
                        dve.tensor_tensor(w_lo_["gate", slot][:, kts], raw["gate", slot][:, kts], w_hi_["gate"][:, kts].bitcast(F32), ALU.subtract).then_inc(split["gate"], 1)

                    def lo_x(e, slot):
                        dve.wait_ge(x_hi_done, e + 1)
                        dve.tensor_tensor(x_lo[:, slot].rearrange("p (a k) n -> p a (k n)", a=2), p_x[:],
                                          x_hi[:, slot].rearrange("p (a k) n -> p a (k n)", a=2).bitcast(F32), ALU.subtract).then_inc(x_lo_done, 1)

                    def run(e, slot, round_, last):
                        if not last:
                            lo_gate(e + 1, 1 - slot, 0)
                        dve.wait_ge(silu_done, e + 1)
                        dve.wait_ge(used["up"], e + 2)
                        dve.tensor_tensor(prod[:], silu[:], p_gu[:, 1, :], ALU.mult).then_inc(prod_done, 1)
                        dve.wait_ge(f_hi_done, e + 1)
                        dve.tensor_tensor(f_lo[:], p_f[:], f_hi[:].bitcast(F32), ALU.subtract).then_inc(f_lo_done, 1)
                        if not last:
                            lo_x(e + 1, 1 - slot)
                            lo_gate(e + 1, 1 - slot, 1)
                            lo_up(e + 1, 1 - slot)
                        pass_waits(dve)
                        dve.tensor_scalar(gate_now[:, slot:slot + 1], slot_gate[:, bass.ds(e, 1)], 0.0, None, ALU.add).then_inc(gate_copied, 1)
                        dve.wait_ge(gate_copied, e + 2)
                        dve.wait_ge(used["down"], e + 2)
                        dve.wait_ge(y_free, e + 1)
                        dve.tensor_scalar(y[:, slot, :], p_y[:].rearrange("p a b -> p (a b)"), gate_now[:, slot:slot + 1], None,
                                          ALU.mult).then_inc(y_out, 1)

                    lo_x(0, 0)
                    pairs(dve, run)

        phase_router()
        phase_experts()

        top = nc.sbuf_usable_end // 32 * 32
        h_split = Arena(nc, top - 2 * KT * SEQ * 4)
        h_hi = h_split("h_hi", [P, KT, SEQ], F32R)
        h_lo = h_split("h_lo", [P, KT, SEQ], F32R)
        y_split = Arena(nc, top - 4 * KT * SEQ * 4)
        y_hi = y_split("y_hi", [P, KT, SEQ], F32R)
        y_lo = y_split("y_lo", [P, KT, SEQ], F32R)
        work_end = top - 4 * KT * SEQ * 4
        BOTH = [(0, 0, HALF), (1, HALF, HALF)]

        def weight_cols(w, first_row=0):
            src = w.rearrange("o (k p) n -> p (o k) n", p=P)
            return lambda u, cols: [(w_raw[:, u], src[:, first_row // P:first_row // P + KT, cols])]

        def out_weights(w, first_row):
            part = weight_cols(w, first_row)
            return lambda n: part(n % 2, slice(n * P, (n + 1) * P))

        even_cols = weight_cols(A["even_w_in_2"])

        def pool_col(t):
            return t // 4 * 2 * P + (t % 4) // 2 * D + t % 2 * P

        SPATIAL_COLS = (3 * D, 4 * D, 2 * D)

        def phase_pool(next_parts):
            phases.start()
            mem = Arena(nc, free_at)
            PAD, G = max(POOL_SIZES), len(POOL_SIZES)
            a_pad = mem("pool_a", [P, 2, PAD + SEQ])
            sums = mem("pool_sums", [P, 2, PAD + SEQ])
            pooled = mem("pool_pooled", [P, 2, SEQ])
            silu = mem("pool_silu", [P, 2, SEQ])
            y = mem("pool_y", [P, 2, SEQ])
            w_pool = mem("pool_w", [P, 2, 2, 2 * P])
            assert mem.at <= work_end
            ring = Ring("pool")
            pre = Prefetch("pool", next_parts, ring, 4 * G)
            z_out = sem("pool_z_out")
            w_loaded = [sem(f"pool_matrix_loaded{u}") for u in range(2)]
            pooled_done = sem("pool_pooled_done")
            mixed_done = sem("pool_mixed_done")
            y_done = sem("pool_y_done")
            hi_done = sem("pool_hi_done")
            lo_done = sem("pool_lo_done")
            cleared = sem("pool_cleared")
            dve_step = sem("pool_dve_step")
            w_cols = even_cols
            src_pool = A["even_pool_w_2"].rearrange("o g (k p) n -> p (o g) k n", p=P)
            with nc.psum_tensor("pool_z", [P, 2, 2, HALF], F32) as z, nc.psum_tensor("pool_mixed", [P, 2, 2, HALF], F32) as mixed, nc.Block() as block:
                @block.sync
                def _(sp):
                    def matrices(i):
                        for s in range(2):
                            sp.wait_ge(mixed_done, 2 * i + s + 1)
                            if not isinstance(i, int):
                                pass_waits(sp)
                            sp.dma_start(w_pool[:, s].rearrange("p (o k) n -> p o k n", o=1), src_pool[:, bass.ds(2 * i + s, 1)]).then_inc(w_loaded[s], 16)

                    ring.load_all(sp, G // 2, 8, lambda i, t: w_cols(t % 2, bass.ds(i * 4 * P + pool_col(t), P)), matrices)
                    pre.load(sp)

                @block.gpsimd
                def _(pool):
                    ring.credits(pool, None)
                    ring.split_all(pool, G // 2, 8)
                    pre.split(pool)

                @block.tensor
                def _(pe):
                    ring.credits(None, pe)
                    pe.sem_inc(mixed_done, 2)
                    with pe.Fori(0, G // 2) as i:
                        for s in range(2):
                            g = 2 * i + s
                            for t in range(4):
                                ring.project(pe, 4 * g + t, t % 2, z_out, [(z[:, t % 2, b, :], c0, w) for b, c0, w in BOTH], h_hi, h_lo)
                            pe.wait_ge(w_loaded[s], 16 * (i + 1))
                            pe.wait_ge(pooled_done, 2 * g + 2)
                            pe.wait_ge(y_done, 2 * g + 2)
                            for d in range(2):
                                for b, c0, w in BOTH:
                                    for k in range(2):
                                        ins = pe.matmul(mixed[:, d, b, :], w_pool[:, s, k, d * P:(d + 1) * P], pooled[:, k, c0:c0 + w],
                                                        start=(k == 0), stop=(k == 1))
                            ins.then_inc(mixed_done, 1)

                @block.scalar
                def _(act):
                    act.sem_inc(z_out, 2)
                    act.wait_ge(cleared, 1)
                    for g in range(G):
                        for t in range(4):
                            act.wait_ge(ring.projected, 4 * g + t + 3)
                            tile = z[:, t % 2].rearrange("p b n -> p (b n)")
                            if t < 2:
                                if g:
                                    act.wait_ge(pooled_done, 2 * (g - 1) + t + 1)
                                act.copy(a_pad[:, t, PAD:], tile).then_inc(z_out, 1)
                            else:
                                act.wait_ge(y_done, 2 * g + t - 2 + 1)
                                act.activation(silu[:, t - 2, :], tile, ACT.Silu).then_inc(z_out, 1)
                        for d in range(2):
                            act.wait_ge(y_done, 2 * g + d + 3)
                            act.copy(y_hi[:, 2 * g + d, :], y[:, d, :]).then_inc(hi_done, 1)

                @block.vector
                def _(dve):
                    step = Steps(dve, dve_step)
                    dve.sem_inc(y_done, 2)
                    step(dve.memset(a_pad[:], 0.0))
                    step(dve.memset(sums[:], 0.0))
                    step.wait()
                    dve.sem_inc(cleared, 1)
                    for g, w in enumerate(POOL_SIZES):
                        for t in range(2):
                            dve.wait_ge(z_out, 4 * g + t + 3)
                            now = a_pad[:, t]
                            for k in range(g + 1):
                                nxt = sums[:, k % 2]
                                step(dve.tensor_tensor(nxt[:, PAD:], now[:, PAD:], now[:, PAD - (1 << k):PAD + SEQ - (1 << k)], ALU.add))
                                step.wait()
                                now = nxt
                            dve.wait_ge(mixed_done, g + 2)
                            head = pooled[:, t, 0:PAD]
                            step(dve.tensor_tensor(head, now[:, PAD:2 * PAD], cst("pool_inv")[:, g * PAD:(g + 1) * PAD], ALU.mult))
                            step.wait()
                            step(dve.tensor_tensor(head, head, a_pad[:, t, PAD:2 * PAD], ALU.subtract))
                            step.wait()
                            dve.scalar_tensor_tensor(out=pooled[:, t, PAD:], in0=now[:, 2 * PAD:], scalar=1.0 / w, in1=a_pad[:, t, 2 * PAD:],
                                                     op0=ALU.mult, op1=ALU.subtract).then_inc(pooled_done, 1)
                            dve.wait_ge(pooled_done, 2 * g + t + 1)
                        dve.wait_ge(mixed_done, g + 3)
                        for d in range(2):
                            dve.wait_ge(z_out, 4 * g + 2 + d + 3)
                            if g:
                                dve.wait_ge(lo_done, 2 * (g - 1) + d + 1)
                            dve.scalar_tensor_tensor(out=y[:, d, :], in0=mixed[:, d].rearrange("p b n -> p (b n)"),
                                                     scalar=pa("even_pool_scale_2")[:, 2 * g + d:2 * g + d + 1], in1=silu[:, d, :],
                                                     op0=ALU.mult, op1=ALU.mult).then_inc(y_done, 1)
                        for d in range(2):
                            dve.wait_ge(hi_done, 2 * g + d + 1)
                            dve.tensor_tensor(y_lo[:, 2 * g + d, :], y[:, d, :], y_hi[:, 2 * g + d, :].bitcast(F32), ALU.subtract).then_inc(lo_done, 1)

        def phase_spatial(next_parts):
            phases.start()
            mem = Arena(nc, free_at)
            G = 4
            ws = mem("spat_ws", [P, G, CHUNK])
            ws_low = mem("spat_ws_low", [P, G, CHUNK])
            ws_t = mem("spat_ws_t", [P, G, CHUNK])
            bias = mem("spat_bias", [1, G, 4, CHUNK])
            v_cm = mem("spat_v_cm", [P, SEQ])
            v_rows_ = mem("spat_v_rows", [P, XCH, P])
            u_cm = mem("spat_u_cm", [P, SEQ])
            silu = mem("spat_silu", [P, SEQ])
            gated = mem("spat_gated", [P, SEQ])
            y = mem("spat_y", [P, SEQ])
            assert mem.at <= work_end
            ring = Ring("spat")
            pre = Prefetch("spat", next_parts, ring, 6 * G)
            z_out = sem("spat_z_out")
            loaded = sem("spat_loaded")
            masked = sem("spat_masked")
            ws_turned = sem("spat_ws_turned")
            ws_ready = sem("spat_ws_ready")
            v_turned = sem("spat_v_turned")
            rows_out = sem("spat_rows_out")
            gated_done = sem("spat_gated_done")
            mixed_done = sem("spat_mixed_done")
            y_done = sem("spat_y_done")
            hi_done = sem("spat_hi_done")
            lo_done = sem("spat_lo_done")
            w_cols = even_cols
            with nc.psum_tensor("spat_z", [P, 2, 2, HALF], F32) as z, nc.psum_tensor("spat_turn", [P, 2, HALF], F32) as turn, \
                    nc.psum_tensor("spat_mixed", [P, 2, HALF], F32) as mixed, nc.Block() as block:
                @block.sync
                def _(sp):
                    sp.dma_start(ws[:], A["even_ws_2"].rearrange("o g t s -> t (o g) s")).then_inc(loaded, 16)
                    for r in range(4):
                        sp.dma_start(bias[:, :, r, :], A["even_bs_2"]).then_inc(loaded, 16)
                    ring.load_all(sp, G, 6, lambda i, m: w_cols(m % 2, bass.ds(i * 2 * P + m // 3 * P + SPATIAL_COLS[m % 3], P)))
                    pre.load(sp)

                @block.gpsimd
                def _(pool):
                    ring.credits(pool, None)
                    pool.wait_ge(loaded, 16 * 5)
                    pool.affine_select(ws_low[:], ws[:], [[0, G], [-1, CHUNK]], ALU.is_ge, 0.0, base=0, channel_multiplier=1).then_inc(masked, 1)
                    ring.split_all(pool, G, 6)
                    pre.split(pool)

                @block.tensor
                def _(pe):
                    ring.credits(None, pe)
                    pe.wait_ge(masked, 1)
                    for g in range(G):
                        ins = pe.transpose(turn[:, 0, g * CHUNK:(g + 1) * CHUNK], ws_low[:, g, :], ident)
                    ins.then_inc(ws_turned, 1)

                    def proj(n, m):
                        ring.project(pe, n, m % 2, z_out, [(z[:, m % 2, b, :], c0, w) for b, c0, w in BOTH], h_hi, h_lo)

                    with pe.Fori(0, G) as i:
                        for s in range(2):
                            c = 2 * i + s
                            proj(6 * i + 3 * s, 3 * s)
                            proj(6 * i + 3 * s + 1, 3 * s + 1)
                            pe.wait_ge(z_out, 6 * i + 3 * s + 3)
                            pe.wait_ge(rows_out, c + 1)
                            for j in range(XCH):
                                ins = pe.transpose(turn[:, j // 4, (j % 4) * P:(j % 4 + 1) * P], v_cm[:, j * P:(j + 1) * P], ident)
                            ins.then_inc(v_turned, 1)
                            proj(6 * i + 3 * s + 2, 3 * s + 2)
                            pe.wait_ge(rows_out, c + 2)
                            pe.wait_ge(y_done, c + 1)
                            pass_waits(pe)
                            for b in range(2):
                                pe.matmul(mixed[:, b, :], ones[0:1, :], bias[:, bass.ds(i, 1), :, :].rearrange("p o r t -> p (o r t)"), start=True, stop=False)
                                for j in range(4):
                                    ins = pe.matmul(mixed[:, b, j * CHUNK:(j + 1) * CHUNK], v_rows_[:, 4 * b + j, :],
                                                    ws_t[:, bass.ds(i, 1), :].rearrange("p o t -> p (o t)"), start=False, stop=(j == 3))
                            ins.then_inc(mixed_done, 1)

                @block.scalar
                def _(act):
                    act.sem_inc(z_out, 2)
                    with act.Fori(0, G) as i:
                        for s in range(2):
                            c = 2 * i + s
                            for t, to in enumerate((v_cm, silu, u_cm)):
                                m = 3 * s + t
                                act.wait_ge(ring.projected, 6 * i + m + 3)
                                if t == 0:
                                    act.wait_ge(v_turned, c + 1)
                                else:
                                    act.wait_ge(gated_done, c + 1)
                                act.activation(to[:], z[:, m % 2].rearrange("p b n -> p (b n)"), ACT.Silu if t == 1 else ACT.Copy).then_inc(z_out, 1)
                            act.wait_ge(y_done, c + 2)
                            pass_waits(act)
                            act.copy(y_hi[:, bass.ds(c, 1), :].rearrange("p o t -> p (o t)"), y[:]).then_inc(hi_done, 1)

                @block.vector
                def _(dve):
                    dve.sem_inc(v_turned, 1)
                    dve.sem_inc(gated_done, 1)
                    dve.sem_inc(y_done, 1)
                    dve.sem_inc(lo_done, 1)
                    dve.wait_ge(ws_turned, 1)
                    dve.tensor_copy(ws_t[:], turn[:, 0, :].rearrange("p (g t) -> p g t", g=G)).then_inc(rows_out, 1)
                    with dve.Fori(0, G) as i:
                        for s in range(2):
                            c = 2 * i + s
                            dve.wait_ge(v_turned, c + 2)
                            dve.tensor_copy(v_rows_[:].rearrange("p (a j) n -> p a (j n)", a=2), turn[:]).then_inc(rows_out, 1)
                            dve.wait_ge(z_out, 6 * i + 3 * s + 2 + 3)
                            dve.wait_ge(y_done, c + 1)
                            dve.tensor_tensor(gated[:], u_cm[:], silu[:], ALU.mult).then_inc(gated_done, 1)
                            dve.wait_ge(mixed_done, c + 1)
                            dve.wait_ge(gated_done, c + 2)
                            dve.wait_ge(lo_done, c + 1)
                            dve.tensor_tensor(y[:], mixed[:].rearrange("p b n -> p (b n)"), gated[:], ALU.mult).then_inc(y_done, 1)
                            dve.wait_ge(hi_done, c + 1)
                            at = bass.ds(c, 1)
                            dve.tensor_tensor(y_lo[:, at, :].rearrange("p o t -> p (o t)"), y[:], y_hi[:, at, :].rearrange("p o t -> p (o t)").bitcast(F32),
                                              ALU.subtract).then_inc(lo_done, 1)

        even_a_out, even_b_out = (out_weights(A["even_w_out_2"], row) for row in (0, D))
        odd_a_out, odd_b_out = (out_weights(A["odd_w_out_2"], row) for row in (0, D))
        phases.start()
        phase_rows_norm("even", Arena(nc, free_at), SEQ, [(0, SEQ, plain_gain("even_norm_2"), None)], h_hi, h_lo,
                        [even_cols(u, slice(pool_col(u), pool_col(u) + P)) for u in range(2)])
        phase_pool([even_a_out(u) for u in range(2)])
        phase_out("even_a_out", y_hi, y_lo, even_a_out, 1, None, [even_cols(u, slice(SPATIAL_COLS[u], SPATIAL_COLS[u] + P)) for u in range(2)])
        phase_spatial([even_b_out(u) for u in range(2)])
        odd_cols = weight_cols(A["odd_w_in_2"])
        GC_COL = 3 * N_DIL * C_SLOTS * P
        DB_COL, DC_COL, DX_COL, GD_COL = (GC_COL + (1 + k) * D for k in range(4))
        CONV_COLS = (DC_COL, DX_COL, GD_COL, DB_COL)
        phase_out("even_b_out", y_hi, y_lo, even_b_out, 1, None, [odd_cols(u, slice(CONV_COLS[u], CONV_COLS[u] + P)) for u in range(2)],
                  norm=dict(affines=[(0, SEQ, plain_gain("odd_norm_2"), None)], h_hi=h_hi, h_lo=h_lo))

        def phase_conv(next_parts):
            phases.start()
            mem = Arena(nc, free_at)
            PAD, TAPS = 2, 3
            taken = [mem(f"conv_{name}", [P, SEQ]) for name in ("c", "x", "silu", "b")]
            c_cm, x_cm_, silu, b_cm = taken
            prod = mem("conv_prod", [P, PAD + SEQ])
            acc = mem("conv_acc", [P, SEQ])
            gated = mem("conv_gated", [P, SEQ])
            y = mem("conv_y", [P, SEQ])
            taps = mem("gated_conv_taps", [P, TAPS, 1])
            assert mem.at <= work_end
            ring = Ring("conv")
            pre = Prefetch("conv", next_parts, ring, 4 * KT)
            z_out = sem("conv_z_out")
            taken_used = sem("conv_taken_used")
            y_done = sem("conv_y_done")
            hi_done = sem("conv_hi_done")
            lo_done = sem("conv_lo_done")
            dve_step = sem("conv_dve_step")
            with nc.psum_tensor("conv_z", [P, 2, 2, HALF], F32) as z, nc.Block() as block:
                @block.sync
                def _(sp):
                    ring.load_all(sp, KT, 4, lambda c, t: odd_cols(t % 2, bass.ds(c * P + CONV_COLS[t], P)))
                    pre.load(sp)

                @block.gpsimd
                def _(pool):
                    ring.credits(pool, None)
                    ring.split_all(pool, KT, 4)
                    pre.split(pool)

                @block.tensor
                def _(pe):
                    ring.credits(None, pe)
                    with pe.Fori(0, KT) as c:
                        for t in range(4):
                            ring.project(pe, 4 * c + t, t % 2, z_out, [(z[:, t % 2, b, :], c0, w) for b, c0, w in BOTH], h_hi, h_lo)

                @block.scalar
                def _(act):
                    act.sem_inc(z_out, 2)
                    with act.Fori(0, KT) as c:
                        for t, to in enumerate(taken):
                            act.wait_ge(ring.projected, 4 * c + t + 3)
                            act.wait_ge(taken_used, c + 1)
                            act.activation(to[:], z[:, t % 2].rearrange("p b n -> p (b n)"), ACT.Silu if to is silu else ACT.Copy).then_inc(z_out, 1)
                        act.wait_ge(y_done, c + 1)
                        pass_waits(act)
                        act.copy(y_hi[:, bass.ds(c, 1), :].rearrange("p o t -> p (o t)"), y[:]).then_inc(hi_done, 1)

                @block.vector
                def _(dve):
                    dve.memset(prod[:], 0.0).then_inc(dve_step, 1)
                    dve.wait_ge(dve_step, 1)
                    dve.sem_inc(taken_used, 1)
                    N_STEP = TAPS + 3
                    with dve.Fori(0, KT) as c:
                        step = Steps(dve, dve_step, N_STEP * c + 1)
                        step.wait()
                        pass_waits(dve)
                        step(dve.tensor_copy(taps[:], pb("odd_conv_w_2").rearrange("p (j c) -> p j c", j=TAPS)[:, :, bass.ds(c, 1)]))
                        dve.wait_ge(z_out, 4 * c + 1 + 3)
                        step(dve.tensor_tensor(prod[:, PAD:], c_cm[:], x_cm_[:], ALU.mult))
                        step.wait()
                        step(dve.tensor_scalar(acc[:], prod[:, 0:SEQ], taps[:, 0, :], None, ALU.mult))
                        step.wait()
                        for j in range(1, TAPS):
                            step(dve.scalar_tensor_tensor(out=acc[:], in0=prod[:, j:j + SEQ], scalar=taps[:, j, :], in1=acc[:], op0=ALU.mult, op1=ALU.add))
                            step.wait()
                        dve.wait_ge(z_out, 4 * c + 3 + 3)
                        step(dve.tensor_tensor(gated[:], b_cm[:], silu[:], ALU.mult))
                        step.wait()
                        dve.sem_inc(taken_used, 1)
                        assert step.done == N_STEP
                        dve.tensor_tensor(y[:], acc[:], gated[:], ALU.mult).then_inc(y_done, 1)
                        dve.wait_ge(hi_done, c + 1)
                        at = bass.ds(c, 1)
                        dve.tensor_tensor(y_lo[:, at, :].rearrange("p o t -> p (o t)"), y[:], y_hi[:, at, :].rearrange("p o t -> p (o t)").bitcast(F32),
                                          ALU.subtract).then_inc(lo_done, 1)
                        dve.wait_ge(lo_done, c + 1)

        y_plain = Arena(nc, top - 3 * KT * SEQ * 4)("y_plain", [P, KT, SEQ])

        DIL_COLS = [first + g * D for g in range(N_DIL) for first in (N_DIL * D, 0)]
        DIL_COLS += [2 * N_DIL * D + g * D for g in range(N_DIL)] + [GC_COL]

        def phase_dilated(next_parts):
            phases.start()
            mem = Arena(nc, free_at)
            q_cm_ = mem("dil_q", [P, N_DIL, SEQ])
            k_cm_ = mem("dil_k", [P, N_DIL, SEQ])
            v_cm = mem("dil_v", [P, SEQ])
            v_rows_ = mem("dil_v_rows", [P, N_DIL, BLOCKS, P])
            silu = mem("dil_silu", [P, SEQ])
            biased = mem("dil_biased", [P, 2, 2 * P])
            p_t = mem("dil_p_t", [P, 2, 2 * P])
            NU = N_DIL * BLOCKS
            neg_max = mem("dil_neg_max", [P, NU])
            den = mem("dil_den", [P, NU])
            log_den = mem("dil_log_den", [P, NU])
            lse = mem("dil_lse", [P, NU])
            slope_now = mem("dil_slope_now", [P, N_DIL, 1])
            joint = mem("dil_joint", [P, N_DIL, 8])
            joint_max = mem("dil_joint_max", [P, 8])
            joint_sum = mem("dil_joint_sum", [P, 8])
            share = mem("dil_share", [P, NU])

            units = []
            for g in range(N_DIL):
                for b in range(BLOCKS):
                    has_prev = (b > 0, b % 2 == 1, False)[g]
                    units.append((g, b, b - 1 if has_prev else b, 2 if has_prev else 1))
            probs = [mem(f"dil_p{u}", [P, n * P]) for u, (_, _, _, n) in enumerate(units)]
            assert mem.at <= top - 3 * KT * SEQ * 4
            ring = Ring("dil")
            pre = Prefetch("dil", next_parts, ring, C_SLOTS * len(DIL_COLS))
            z_out = sem("dil_z_out")
            scores = sem("dil_scores")
            bias_done = sem("dil_bias_done")
            max_done = sem("dil_max_done")
            exp_done = sem("dil_exp_done")
            aux_free = [sem(f"dil_aux_free{b}") for b in range(2)]
            log_done = sem("dil_log_done")
            lse_done = sem("dil_lse_done")
            lse_stored = sem("dil_lse_stored")
            joint_loaded = sem("dil_joint_loaded")
            joint_shifted = sem("dil_joint_shifted")
            joint_exp = sem("dil_joint_exp")
            share_done = sem("dil_share_done")
            share_stored = sem("dil_share_stored")
            share_loaded = sem("dil_share_loaded")
            factor_done = sem("dil_factor_done")
            scaled = sem("dil_scaled")
            v_turned = sem("dil_v_turned")
            rows_out = sem("dil_rows_out")
            p_turned = sem("dil_p_turned")
            p_t_out = sem("dil_p_t_out")
            summed = sem("dil_summed")
            y_done = sem("dil_y_done")
            dve_step = sem("dil_dve_step")
            NT = len(DIL_COLS)
            VT, GT = 2 * N_DIL, 3 * N_DIL
            AUX = NU + 2 * N_DIL + NU

            def reordered(x, g):
                r = DILATION[g]
                return x.rearrange("p (r b m) -> p b m r", r=r, b=2) if g else x.rearrange("p (b m) -> p b m", b=2)

            def in_banks(x, g):
                return x.rearrange("p b (m r) -> p b m r", r=DILATION[g]) if g else x

            def token_order(row, tile, g):
                if g == 0:
                    return [(row.rearrange("(b p) -> p b", p=P), tile)]
                if g == 1:
                    return [(row.rearrange("(m p r) -> p r m", p=P, r=4)[:, r, :], tile[:, 2 * r:2 * r + 2]) for r in range(4)]
                by_half = row.rearrange("(i b a) -> a i b", b=8, a=2)
                return [(by_half[a], tile[a * 64:(a + 1) * 64, :]) for a in range(2)]

            moves = sum(len(token_order(stat_dram[0, g], share[:, 0:8], g)) for g in range(N_DIL))

            with nc.psum_tensor("dil_z", [P, 2, 2, HALF], F32) as z, nc.psum_tensor("dil_aux", [P, 2, HALF], F32) as aux, \
                    nc.psum_tensor("dil_acc", [P, 2, HALF], F32) as acc, nc.Block() as block:
                @block.sync
                def _(sp):
                    ring.load_all(sp, C_SLOTS, NT, lambda h, t: odd_cols(t % 2, bass.ds(h * P + DIL_COLS[t], P)))
                    pre.load(sp)

                @block.gpsimd
                def _(pool):
                    ring.credits(pool, None)
                    ring.split_all(pool, C_SLOTS, NT)
                    pre.split(pool)

                @block.tensor
                def _(pe):
                    ring.credits(None, pe)
                    class Aux:

                        def __init__(self, h, used=0):
                            self.h, self.used = h, used

                        def take(self):
                            a = self.used
                            pe.wait_ge(aux_free[a % 2], AUX // 2 * self.h + a // 2 + 1)
                            self.used += 1
                            return aux[:, a % 2, :]

                    def proj(h, t, between=None):
                        ring.project(pe, NT * h + t, t % 2, z_out, [(z[:, t % 2, b, :], c0, w) for b, c0, w in BOTH], h_hi, h_lo, between)

                    def score(h, banks, u):
                        g, b, k0, n = units[u]
                        to = banks.take()
                        pe.wait_ge(z_out, NT * h + 2 * g + 2 + 2)
                        pe.matmul(to[:, 0:n * P], q_cm_[:, g, b * P:(b + 1) * P], k_cm_[:, g, k0 * P:(k0 + n) * P], start=True, stop=True).then_inc(scores, 1)

                    def turn_v(h, banks, g):
                        pe.wait_ge(z_out, NT * h + VT + g + 3)
                        for half in range(2):
                            to = banks.take()
                            for j in range(4):
                                at = (4 * half + j) * P
                                ins = pe.transpose(to[:, j * P:(j + 1) * P], v_cm[:, at:at + P], ident)
                            ins.then_inc(v_turned, 1)

                    def turn_p(h, banks, u):
                        to = banks.take()
                        pe.wait_ge(scaled, NU * h + u + 1)
                        for j in range(units[u][3]):
                            ins = pe.transpose(to[:, j * P:(j + 1) * P], probs[u][:, j * P:(j + 1) * P], ident)
                        ins.then_inc(p_turned, 1)

                    def weigh_v(h, u):
                        g, b, k0, n = units[u]
                        pe.wait_ge(p_t_out, NU * h + u + 1)
                        for j in range(n):
                            pt = p_t[:, u % 2, j * P:(j + 1) * P]
                            v = v_rows_[:, g, k0 + j, :]
                            if g == 0:
                                ins = pe.matmul(acc[:, b // 4, (b % 4) * P:(b % 4 + 1) * P], v, pt, start=False, stop=False)
                            elif g == 1:
                                ins = pe.matmul(acc[:, b % 2, :].rearrange("p (m r) -> p r m", r=4)[:, b // 2, :], v, pt, start=False, stop=False)
                            else:
                                for bank in range(2):
                                    to = acc[:, bank, :].rearrange("p (i c a) -> p c a i", c=8, a=2)[:, b]
                                    ins = pe.matmul(to, v, pt.rearrange("p (a s i) -> p s a i", a=2, s=2)[:, bank], start=False, stop=(b == BLOCKS - 1))
                        ins.then_inc(summed, 1)

                    def scores_and_values(h):
                        banks = Aux(h)
                        for t in range(6):
                            proj(h, 2 + t, {2 * k + 1: (lambda u=4 * t + k: score(h, banks, u)) for k in range(4)})
                        turn_v(h, banks, 0)
                        proj(h, VT + 2)
                        turn_v(h, banks, 1)
                        proj(h, GT)
                        turn_v(h, banks, 2)
                        return banks

                    def begin_sums(h, banks):
                        pe.wait_ge(y_done, h + 1)
                        for bank in range(2):
                            pe.matmul(acc[:, bank, :], ones[0:1, :], zero_col[0:1, :].to_broadcast([1, HALF]), start=True, stop=False)
                        turn_p(h, banks, 0)
                        turn_p(h, banks, 1)
                        pe.wait_ge(rows_out, 6 * h + 6)

                    def sum_pair(h, banks, u):
                        weigh_v(h, u)
                        weigh_v(h, u + 1)
                        if u + 2 < NU:
                            turn_p(h, banks, u + 2)
                            turn_p(h, banks, u + 3)
                        else:
                            assert banks.used == AUX

                    for t in range(2):
                        proj(0, t)
                    with pe.Fori(0, C_SLOTS - 1) as h:
                        banks = scores_and_values(h)
                        steps = [lambda: begin_sums(h, banks)] + [lambda u=u: sum_pair(h, banks, u) for u in range(0, NU, 2)]
                        for t in range(2):
                            proj(h + 1, t, {kt: steps[KT * t + kt - 1] for kt in range(KT) if 0 <= KT * t + kt - 1 < len(steps)})
                    banks = scores_and_values(C_SLOTS - 1)
                    begin_sums(C_SLOTS - 1, banks)
                    for u in range(0, NU, 2):
                        sum_pair(C_SLOTS - 1, banks, u)

                @block.scalar
                def _(act):
                    act.sem_inc(z_out, 2)
                    with act.Fori(0, C_SLOTS) as h:
                        def take(t, to):
                            act.wait_ge(ring.projected, NT * h + t + 3)
                            act.activation(to, in_banks(z[:, t % 2], t // 2) if t < VT else in_banks(z[:, t % 2], t - VT), ACT.Copy,
                                           scale=P ** -0.5 if t < VT and t % 2 else 1.0).then_inc(z_out, 1)

                        def exps(u0):
                            for u in range(u0, u0 + 4):
                                w = units[u][3] * P
                                act.wait_ge(max_done, NU * h + u + 1)
                                act.activation(probs[u][:], biased[:, u % 2, 0:w], ACT.Exp, bias=neg_max[:, u:u + 1],
                                               accum_out=den[:, u:u + 1]).then_inc(exp_done, 1)

                        for t in range(2 * N_DIL):
                            if t >= 2:
                                exps(4 * (t - 2))
                            take(t, reordered((q_cm_ if t % 2 else k_cm_)[:, t // 2, :], t // 2))
                        for g in range(N_DIL):
                            if g < 2:
                                exps(16 + 4 * g)
                            if g == 2:
                                act.wait_ge(exp_done, NU * h + NU + 2)
                                act.activation(log_den[:], den[:], ACT.Ln).then_inc(log_done, 1)
                                act.wait_ge(lse_done, h + 1)
                                for q in range(N_DIL):
                                    for row, tile in token_order(stat_dram[0, q], lse[:, 8 * q:8 * q + 8], q):
                                        act.dma_start(row, tile, allow_slow_non_contiguous=True).then_inc(lse_stored, 16)
                                act.wait_ge(lse_stored, 16 * moves * (h + 1))
                                act.dma_start(joint[:], stat_dram[0].rearrange("q (p j) -> p q j", j=8)).then_inc(joint_loaded, 16)
                                act.wait_ge(joint_shifted, h + 1)
                                act.activation(joint[:], joint[:], ACT.Exp).then_inc(joint_exp, 1)
                                act.wait_ge(share_done, h + 1)
                                act.dma_start(factor_dram.rearrange("q (p j) -> p q j", j=8), joint[:]).then_inc(share_stored, 16)
                                act.wait_ge(share_stored, 16 * (h + 1))
                                for q in range(N_DIL):
                                    for row, tile in token_order(factor_dram[q], share[:, 8 * q:8 * q + 8], q):
                                        act.dma_start(tile, row, allow_slow_non_contiguous=True).then_inc(share_loaded, 16)
                            act.wait_ge(v_turned, 6 * h + 2 * g)
                            take(VT + g, reordered(v_cm[:], g))
                        act.wait_ge(ring.projected, NT * h + GT + 3)
                        act.wait_ge(y_done, h + 1)
                        act.activation(silu[:], z[:, GT % 2].rearrange("p b n -> p (b n)"), ACT.Silu).then_inc(z_out, 1)
                        act.wait_ge(factor_done, h + 1)
                        for u in range(NU):
                            act.activation(probs[u][:], probs[u][:], ACT.Copy, scale=share[:, u:u + 1]).then_inc(scaled, 1)

                @block.vector
                def _(dve):
                    for b in range(2):
                        dve.sem_inc(aux_free[b], 1)
                    dve.sem_inc(exp_done, 2)
                    dve.sem_inc(y_done, 1)
                    dve.sem_inc(dve_step, 1)
                    N_STEP = 10
                    with dve.Fori(0, C_SLOTS) as h:
                        step = Steps(dve, dve_step, N_STEP * h + 1)
                        uses = 0
                        step.wait()
                        pass_waits(dve)
                        step(dve.tensor_copy(slope_now[:], cst("slopes").rearrange("p (g s) -> p g s", g=N_DIL)[:, :, bass.ds(h, 1)]))
                        step.wait()
                        for u, (g, b, k0, n) in enumerate(units):
                            w = n * P
                            dist = cst("dist16") if g == 2 else cst("dist")[:, (2 - n) * P:]
                            dve.wait_ge(scores, NU * h + u + 1)
                            dve.wait_ge(exp_done, NU * h + u + 1)
                            dve.scalar_tensor_tensor(out=biased[:, u % 2, 0:w], in0=dist, scalar=slope_now[:, g, :], in1=aux[:, uses % 2, 0:w],
                                                     op0=ALU.mult, op1=ALU.add).then_inc(aux_free[uses % 2], 1)
                            uses += 1
                            dve.wait_ge(aux_free[u % 2], AUX // 2 * h + u // 2 + 2)
                            dve.tensor_reduce(neg_max[:, u:u + 1], biased[:, u % 2, 0:w], AX_X, ALU.max, negate=True).then_inc(max_done, 1)

                        def rows(g):
                            nonlocal uses
                            for half in range(2):
                                dve.wait_ge(v_turned, 6 * h + 2 * g + half + 1)
                                dve.tensor_copy(v_rows_[:, g, 4 * half:4 * half + 4, :].rearrange("p j n -> p (j n)"), aux[:, uses % 2, :]).then_inc(aux_free[uses % 2], 1)
                                uses += 1
                                dve.wait_ge(aux_free[(uses - 1) % 2], AUX // 2 * h + (uses - 1) // 2 + 2)
                                dve.sem_inc(rows_out, 1)

                        dve.wait_ge(log_done, h + 1)
                        dve.wait_ge(max_done, NU * h + NU)
                        dve.tensor_tensor(lse[:], log_den[:], neg_max[:], ALU.subtract).then_inc(lse_done, 1)
                        step(dve.reciprocal(den[:], den[:]))
                        rows(0)
                        dve.wait_ge(joint_loaded, 16 * (h + 1))
                        step(dve.tensor_tensor(joint_max[:], joint[:, 0], joint[:, 1], ALU.max))
                        step.wait()
                        step(dve.tensor_tensor(joint_max[:], joint_max[:], joint[:, 2], ALU.max))
                        step.wait()
                        dve.tensor_tensor(joint[:], joint[:], joint_max[:].unsqueeze(1).to_broadcast([P, N_DIL, 8]), ALU.subtract).then_inc(joint_shifted, 1)
                        dve.wait_ge(joint_exp, h + 1)
                        step(dve.tensor_tensor(joint_sum[:], joint[:, 0], joint[:, 1], ALU.add))
                        step.wait()
                        step(dve.tensor_tensor(joint_sum[:], joint_sum[:], joint[:, 2], ALU.add))
                        step.wait()
                        step(dve.reciprocal(joint_sum[:], joint_sum[:]))
                        step.wait()
                        dve.tensor_tensor(joint[:], joint[:], joint_sum[:].unsqueeze(1).to_broadcast([P, N_DIL, 8]), ALU.mult).then_inc(share_done, 1)
                        rows(1)
                        rows(2)
                        dve.wait_ge(share_loaded, 16 * moves * (h + 1))
                        dve.tensor_tensor(share[:], share[:], den[:], ALU.mult).then_inc(factor_done, 1)
                        for u in range(NU):
                            w = units[u][3] * P
                            dve.wait_ge(p_turned, NU * h + u + 1)
                            if u >= 2:
                                dve.wait_ge(summed, NU * h + u - 1)
                            dve.tensor_copy(p_t[:, u % 2, 0:w], aux[:, uses % 2, 0:w]).then_inc(aux_free[uses % 2], 1)
                            uses += 1
                            dve.wait_ge(aux_free[(uses - 1) % 2], AUX // 2 * h + (uses - 1) // 2 + 2)
                            dve.sem_inc(p_t_out, 1)
                        dve.wait_ge(summed, NU * h + NU)
                        dve.wait_ge(z_out, NT * h + NT + 2)
                        dve.tensor_tensor(y_plain[:, bass.ds(h, 1), :].rearrange("p o t -> p (o t)"), acc[:].rearrange("p b n -> p (b n)"), silu[:],
                                          ALU.mult).then_inc(y_done, 1)
                        dve.wait_ge(y_done, h + 2)
                        dve.sem_inc(dve_step, N_STEP - step.done)

        phase_conv([odd_b_out(u) for u in range(2)])
        phase_out("odd_b_out", y_hi, y_lo, odd_b_out, 1, None, [odd_cols(u, slice(DIL_COLS[u], DIL_COLS[u] + P)) for u in range(2)])
        phase_dilated([odd_a_out(u) for u in range(2)])
        phase_out("odd_a_out", h_hi, h_lo, odd_a_out, 1, None, split_from=y_plain, result=(out[0], plain_gain("final_norm_2")))


_USED = ["x", "c", "ctx", "c_ctx", "w_mod", "b_mod", "norm1_w", "norm2_w", "w_in", "b_gates", "conv_qk", "q_norm_w", "k_norm_w",
         "sink", "mlstm_norm_w", "w_out", "w_router", "w_gate", "w_up", "w_down", "even_norm_2", "even_w_in_2", "even_pool_w_2",
         "even_pool_scale_2", "even_ws_2", "even_bs_2", "even_w_out_2", "odd_norm_2", "odd_w_in_2", "odd_conv_w_2", "odd_w_out_2",
         "final_norm_2"]


def declare(nc, inputs):
    arrays, args = {}, {}
    for name, a in {**{n: inputs[n] for n in _USED}, **constant_tables()}.items():
        a = np.ascontiguousarray(a)
        arrays[f"in_{name}"] = a
        args[name] = nc.dram_tensor(f"in_{name}", a.shape, F32, kind="ExternalInput").ap()
    out = nc.dram_tensor("out", (1, SEQ, D), F32, kind="ExternalOutput").ap()
    return arrays, args, out


def kernel(**inputs):
    import concourse.bacc as bacc
    from concourse.bass_utils import run_bass_kernel_spmd

    nc = bacc.Bacc("TRN2", target_bir_lowering=False, num_devices=1)
    arrays, args, out = declare(nc, inputs)
    build_program(nc, args, out)
    result = run_bass_kernel_spmd(nc, [arrays], core_ids=[0])
    return result.results[0]["out"]
```
